# Optimizing a Trainium2 kernel written in Bass

```python
import jax
import jax.numpy as jnp
from jax import lax
import numpy as np
import math
import jax, jax.numpy as jnp

D_MODEL = 1024
BATCH = 1
SEQ = 256
DEPTH = 2

N_GROUPS = 4
GROUP_WIDTH = D_MODEL // N_GROUPS
D_MIX = N_GROUPS * GROUP_WIDTH
HEAD_DIM = 64
CHUNK = 64
EPS = 1e-6
MASK_VALUE = -1e30
MIN_POS = 1e-30

HA = GROUP_WIDTH // HEAD_DIM
DK_A = HEAD_DIM
DV_A = HEAD_DIM
HB = GROUP_WIDTH // HEAD_DIM
DK_B = HEAD_DIM // 2
DV_B = HEAD_DIM
GLA_GATE_RANK = 16
GLA_GATE_NORMALIZER = 16.0
HC = GROUP_WIDTH // HEAD_DIM
MLA_Q_RANK = 256
MLA_KV_RANK = 128
MLA_NOPE = 64
MLA_ROPE = 32
MLA_V = HEAD_DIM
ROPE_THETA = 10000.0
Q_BLOCK = 128
HD = GROUP_WIDTH // HEAD_DIM
DK_D = HEAD_DIM
DV_D = HEAD_DIM
GDN_CONV = 4
D_FF = 2816
FFN_CONV = 3

IN_SPLITS = (
    HA * DK_A, HA * DK_A, HA * DV_A, HA * DV_A,
    HB * DK_B, HB * DK_B, HB * DV_B, GLA_GATE_RANK, HB * DV_B,
    MLA_Q_RANK, MLA_KV_RANK, MLA_ROPE,
    HD * DK_D, HD * DK_D, HD * DV_D, HD, HD, HD * DV_D,
)
D_IN = sum(IN_SPLITS)


def rms_norm(x, g):
    xf = x.astype(jnp.float32)
    y = xf * lax.rsqrt(jnp.mean(xf * xf, axis=-1, keepdims=True) + EPS)
    return (y * g).astype(x.dtype)

def l2_norm(x):
    xf = x.astype(jnp.float32)
    return xf * lax.rsqrt(jnp.sum(xf * xf, axis=-1, keepdims=True) + EPS)

def heads(t, h, d):
    return t.reshape(t.shape[:-1] + (h, d))

def split_columns(z):
    out = []
    start = 0
    for w in IN_SPLITS:
        out.append(z[..., start:start + w])
        start += w
    return out

def causal_dwconv(x, w):
    k, c = w.shape
    return lax.conv_general_dilated(
        x, w[:, None, :].astype(x.dtype), window_strides=(1,), padding=[(k - 1, 0)],
        dimension_numbers=('NWC', 'WIO', 'NWC'), feature_group_count=c)

def rope_tables(s):
    inv = ROPE_THETA ** (-jnp.arange(0, MLA_ROPE, 2, dtype=jnp.float32) / MLA_ROPE)
    ang = jnp.arange(s, dtype=jnp.float32)[:, None] * inv[None, :]
    return jnp.cos(ang), jnp.sin(ang)

def apply_rope(x, cos, sin):
    xf = x.astype(jnp.float32)
    x1, x2 = xf[..., :MLA_ROPE // 2], xf[..., MLA_ROPE // 2:]
    return jnp.concatenate([x1 * cos - x2 * sin, x2 * cos + x1 * sin], axis=-1).astype(x.dtype)

def chunk_gla(q, k, v, log_f):
    bsz, s, h, dk = q.shape
    dv = v.shape[-1]
    n = s // CHUNK

    def to_chunks(t):
        return t.astype(jnp.float32).reshape(bsz, n, CHUNK, h, t.shape[-1]).transpose(1, 0, 3, 2, 4)

    qc, kc, vc, gc = to_chunks(q), to_chunks(k), to_chunks(v), to_chunks(log_f)
    bc = jnp.cumsum(gc, axis=3)
    causal = jnp.tril(jnp.ones((CHUNK, CHUNK), bool))[:, :, None]

    def step(state, inp):
        q_, k_, v_, b_ = inp
        diff = b_[:, :, :, None, :] - b_[:, :, None, :, :]
        decay = jnp.where(causal, jnp.exp(jnp.where(causal, diff, 0.0)), 0.0)
        attn = jnp.einsum('bhid,bhjd,bhijd->bhij', q_, k_, decay)
        b_last = b_[:, :, -1, :]
        o = (jnp.einsum('bhij,bhjv->bhiv', attn, v_)
             + jnp.einsum('bhid,bhdv->bhiv', q_ * jnp.exp(b_), state))
        state = (jnp.exp(b_last)[..., None] * state
                 + jnp.einsum('bhjd,bhjv->bhdv', k_ * jnp.exp(b_last[:, :, None, :] - b_), v_))
        return state, o

    s0 = jnp.zeros((bsz, h, dk, dv), jnp.float32)
    _, o = lax.scan(step, s0, (qc, kc, vc, bc))
    return o.transpose(1, 0, 3, 2, 4).reshape(bsz, s, h, dv)

def chunk_gated_delta(q, k, v, beta, log_g):
    bsz, s, h, dk = q.shape
    dv = v.shape[-1]
    n = s // CHUNK

    def to_chunks(t):
        t = t.astype(jnp.float32).reshape((bsz, n, CHUNK, h) + t.shape[3:])
        return jnp.moveaxis(t, (1, 3), (0, 2))

    qc, kc, vc = to_chunks(q), to_chunks(k), to_chunks(v)
    bt, gc = to_chunks(beta), to_chunks(log_g)
    b = jnp.cumsum(gc, axis=-1)
    incl = jnp.tril(jnp.ones((CHUNK, CHUNK), bool))
    strict = jnp.tril(jnp.ones((CHUNK, CHUNK), bool), -1)
    diff = b[..., :, None] - b[..., None, :]
    lmask = jnp.where(incl, jnp.exp(jnp.where(incl, diff, 0.0)), 0.0)
    kb = kc * bt[..., None]
    m = jnp.where(strict, jnp.einsum('nbhid,nbhjd->nbhij', kb, kc) * lmask, 0.0)
    eye = jnp.eye(CHUNK, dtype=jnp.float32)
    rhs = jnp.concatenate([vc * bt[..., None], kb * jnp.exp(b)[..., None]], axis=-1)
    sol = lax.linalg.triangular_solve(m + eye, rhs, left_side=True, lower=True, unit_diagonal=True)
    u, w = sol[..., :dv], sol[..., dv:]
    a_qk = jnp.einsum('nbhid,nbhjd->nbhij', qc, kc) * lmask

    def step(state, inp):
        q_, k_, u_, w_, a_, b_ = inp
        v_new = u_ - jnp.einsum('bhcd,bhdv->bhcv', w_, state)
        o = (jnp.einsum('bhcd,bhdv->bhcv', q_ * jnp.exp(b_)[..., None], state)
             + jnp.einsum('bhij,bhjv->bhiv', a_, v_new))
        b_last = b_[..., -1:]
        state = (jnp.exp(b_last)[..., None] * state
                 + jnp.einsum('bhcd,bhcv->bhdv', k_ * jnp.exp(b_last - b_)[..., None], v_new))
        return state, o

    s0 = jnp.zeros((bsz, h, dk, dv), jnp.float32)
    _, o = lax.scan(step, s0, (qc, kc, u, w, a_qk, b))
    return jnp.moveaxis(o, (0, 2), (1, 3)).reshape(bsz, s, h, dv)

def mla_attention(q_nope, q_rope, k_nope, k_rope, v):
    bsz, s, h, _ = q_nope.shape
    nb = s // Q_BLOCK
    scale = (MLA_NOPE + MLA_ROPE) ** -0.5
    key_pos = jnp.arange(s)

    def blocks(t):
        return jnp.moveaxis(t.reshape((bsz, nb, Q_BLOCK) + t.shape[2:]), 1, 0)

    def attend(args):
        qn, qr, blk = args
        sc = (jnp.einsum('bqhd,bkhd->bhqk', qn, k_nope)
              + jnp.einsum('bqhd,bkd->bhqk', qr, k_rope)).astype(jnp.float32) * scale
        q_pos = blk * Q_BLOCK + jnp.arange(Q_BLOCK)
        mask = key_pos[None, :] <= q_pos[:, None]
        p = jax.nn.softmax(jnp.where(mask, sc, MASK_VALUE), axis=-1)
        return jnp.einsum('bhqk,bkhv->bqhv', p.astype(v.dtype), v)

    o = lax.map(attend, (blocks(q_nope), blocks(q_rope), jnp.arange(nb)))
    return jnp.moveaxis(o, 0, 1).reshape(bsz, s, h, v.shape[-1])

def hgrn_lower_bounds(lb_logits):
    p = jax.nn.softmax(lb_logits.astype(jnp.float32), axis=0)
    return jnp.cumsum(p, axis=0) - p[0]

def hgrn2_mixer(q, f_logit, i, g, lb, norm_g):
    dtype = q.dtype
    zf = f_logit.astype(jnp.float32)
    f = lb + (1.0 - lb) * jax.nn.sigmoid(zf)
    log_f = jnp.log(jnp.maximum(f, MIN_POS))
    k = (1.0 - lb) * jax.nn.sigmoid(-zf)
    qh = heads(jax.nn.silu(q), HA, DK_A) * DK_A ** -0.5
    o = chunk_gla(qh, heads(k, HA, DK_A), heads(i, HA, DV_A), heads(log_f, HA, DK_A))
    o = rms_norm(o, norm_g) * jax.nn.sigmoid(heads(g, HA, DV_A).astype(jnp.float32))
    return o.reshape(o.shape[:2] + (HA * DV_A,)).astype(dtype)

def gla_mixer(q, k, v, gate_code, g, w_gk2, b_gk, norm_g):
    dtype = q.dtype
    log_gk = jax.nn.log_sigmoid((gate_code @ w_gk2 + b_gk).astype(jnp.float32)) / GLA_GATE_NORMALIZER
    o = chunk_gla(heads(q, HB, DK_B) * DK_B ** -0.5, heads(k, HB, DK_B), heads(v, HB, DV_B),
                  heads(log_gk, HB, DK_B))
    o = rms_norm(o, norm_g) * jax.nn.silu(heads(g, HB, DV_B).astype(jnp.float32))
    return o.reshape(o.shape[:2] + (HB * DV_B,)).astype(dtype)

def mla_mixer(c_q, c_kv, k_rope, q_norm_g, w_uq, kv_norm_g, w_ukv, cos, sin):
    dtype = c_q.dtype
    q = heads(rms_norm(c_q, q_norm_g) @ w_uq, HC, MLA_NOPE + MLA_ROPE)
    kv = heads(rms_norm(c_kv, kv_norm_g) @ w_ukv, HC, MLA_NOPE + MLA_V)
    q_nope = q[..., :MLA_NOPE]
    q_rope = apply_rope(q[..., MLA_NOPE:], cos[:, None, :], sin[:, None, :])
    k_nope, v = kv[..., :MLA_NOPE], kv[..., MLA_NOPE:]
    k_rope = apply_rope(k_rope, cos, sin)
    o = mla_attention(q_nope, q_rope, k_nope, k_rope, v)
    return o.reshape(o.shape[:2] + (HC * MLA_V,)).astype(dtype)

def gdn_mixer(q, k, v, beta_logit, a, z, conv_w, a_log, dt_bias, norm_g):
    dtype = q.dtype
    qkv = jax.nn.silu(causal_dwconv(jnp.concatenate([q, k, v], axis=-1), conv_w))
    qd = l2_norm(heads(qkv[..., :HD * DK_D], HD, DK_D)) * DK_D ** -0.5
    kd = l2_norm(heads(qkv[..., HD * DK_D:2 * HD * DK_D], HD, DK_D))
    vd = heads(qkv[..., 2 * HD * DK_D:], HD, DV_D)
    beta = jax.nn.sigmoid(beta_logit.astype(jnp.float32))
    log_g = -jnp.exp(a_log.astype(jnp.float32)) * jax.nn.softplus(a.astype(jnp.float32) + dt_bias)
    o = chunk_gated_delta(qd, kd, vd, beta, log_g)
    o = rms_norm(o, norm_g) * jax.nn.silu(heads(z, HD, DV_D).astype(jnp.float32))
    return o.reshape(o.shape[:2] + (HD * DV_D,)).astype(dtype)

def conv_glu_ffn(h, w_gate, w_up, conv_w, w_down):
    gate = causal_dwconv(h @ w_gate, conv_w)
    return (jax.nn.gelu(gate, approximate=True) * (h @ w_up)) @ w_down

def first_inputs(seed: int = 0) -> dict:
    key = jax.random.key(seed)
    ks = jax.random.split(key, 26)

    def nrm(k, shape, scale):
        return jax.random.normal(k, shape, jnp.float32) * scale

    def gain(k, shape):
        return 1.0 + 0.1 * jax.random.normal(k, shape, jnp.float32)

    dt = jnp.exp(jax.random.uniform(ks[19], (DEPTH, HD), jnp.float32,
                                    jnp.log(1e-3), jnp.log(1e-1)))
    return {
        'x': jax.random.normal(ks[0], (BATCH, SEQ, D_MODEL), jnp.float32),
        'w_in': nrm(ks[1], (DEPTH, D_MODEL, D_IN), D_MODEL ** -0.5),
        'w_out': nrm(ks[2], (DEPTH, D_MIX, D_MODEL), D_MIX ** -0.5),
        'pre_mix_g': gain(ks[3], (DEPTH, D_MODEL)),
        'post_mix_g': gain(ks[4], (DEPTH, D_MODEL)),
        'pre_ffn_g': gain(ks[5], (DEPTH, D_MODEL)),
        'post_ffn_g': gain(ks[6], (DEPTH, D_MODEL)),
        'hgrn_lb_logits': nrm(ks[7], (DEPTH, HA * DK_A), 1.0),
        'hgrn_norm_g': gain(ks[8], (DEPTH, DV_A)),
        'gla_w_gk2': nrm(ks[9], (DEPTH, GLA_GATE_RANK, HB * DK_B), GLA_GATE_RANK ** -0.5),
        'gla_b_gk': nrm(ks[10], (DEPTH, HB * DK_B), 0.1),
        'gla_norm_g': gain(ks[11], (DEPTH, DV_B)),
        'mla_q_norm_g': gain(ks[12], (DEPTH, MLA_Q_RANK)),
        'mla_w_uq': nrm(ks[13], (DEPTH, MLA_Q_RANK, HC * (MLA_NOPE + MLA_ROPE)), MLA_Q_RANK ** -0.5),
        'mla_kv_norm_g': gain(ks[14], (DEPTH, MLA_KV_RANK)),
        'mla_w_ukv': nrm(ks[15], (DEPTH, MLA_KV_RANK, HC * (MLA_NOPE + MLA_V)), MLA_KV_RANK ** -0.5),
        'gdn_conv_w': nrm(ks[16], (DEPTH, GDN_CONV, HD * (2 * DK_D + DV_D)), GDN_CONV ** -0.5),
        'gdn_a_log': jnp.log(jax.random.uniform(ks[17], (DEPTH, HD), jnp.float32, 1.0, 16.0)),
        'gdn_dt_bias': dt + jnp.log(-jnp.expm1(-dt)),
        'gdn_norm_g': gain(ks[18], (DEPTH, DV_D)),
        'ffn_w_gate': nrm(ks[20], (DEPTH, D_MODEL, D_FF), D_MODEL ** -0.5),
        'ffn_w_up': nrm(ks[21], (DEPTH, D_MODEL, D_FF), D_MODEL ** -0.5),
        'ffn_conv_w': nrm(ks[22], (DEPTH, FFN_CONV, D_FF), FFN_CONV ** -0.5),
        'ffn_w_down': nrm(ks[23], (DEPTH, D_FF, D_MODEL), D_FF ** -0.5),
    }

def first_block(x, w_in, w_out, pre_mix_g, post_mix_g, pre_ffn_g, post_ffn_g,
              hgrn_lb_logits, hgrn_norm_g, gla_w_gk2, gla_b_gk, gla_norm_g,
              mla_q_norm_g, mla_w_uq, mla_kv_norm_g, mla_w_ukv,
              gdn_conv_w, gdn_a_log, gdn_dt_bias, gdn_norm_g,
              ffn_w_gate, ffn_w_up, ffn_conv_w, ffn_w_down):
    s = x.shape[1]
    cos, sin = rope_tables(s)
    lower_bounds = hgrn_lower_bounds(hgrn_lb_logits)
    for l in range(DEPTH):
        h = rms_norm(x, pre_mix_g[l])
        z = h @ w_in[l]
        (a_q, a_f, a_i, a_g,
         b_q, b_k, b_v, b_code, b_g,
         c_q, c_kv, c_kr,
         d_q, d_k, d_v, d_beta, d_a, d_z) = split_columns(z)
        o_a = hgrn2_mixer(a_q, a_f, a_i, a_g, lower_bounds[l], hgrn_norm_g[l])
        o_b = gla_mixer(b_q, b_k, b_v, b_code, b_g, gla_w_gk2[l], gla_b_gk[l], gla_norm_g[l])
        o_c = mla_mixer(c_q, c_kv, c_kr, mla_q_norm_g[l], mla_w_uq[l], mla_kv_norm_g[l], mla_w_ukv[l], cos, sin)
        o_d = gdn_mixer(d_q, d_k, d_v, d_beta, d_a, d_z, gdn_conv_w[l], gdn_a_log[l], gdn_dt_bias[l], gdn_norm_g[l])
        mix = jnp.concatenate([o_a, o_b, o_c, o_d], axis=-1).astype(h.dtype) @ w_out[l]
        x = x + rms_norm(mix, post_mix_g[l])
        h = rms_norm(x, pre_ffn_g[l])
        y = conv_glu_ffn(h, ffn_w_gate[l], ffn_w_up[l], ffn_conv_w[l], ffn_w_down[l])
        x = x + rms_norm(y, post_ffn_g[l])
    return x


N_HEADS_A = 4
N_HEADS_B = 4
N_HEADS_C = 4
N_HEADS_D = 4
N_KV_D = 2
DIFF_DIM = HEAD_DIM // 2
IDX_HEADS = 8
IDX_DIM = 64
TOPK_MAX = 256
WINDOW = 128
BLOCK = 128
D_FF_2 = 4 * D_MODEL
D_PLE = 256
NEG_INF = -1e30
MIX_WIDTH = (N_HEADS_A + N_HEADS_B + N_HEADS_C + N_HEADS_D) * HEAD_DIM
SPLIT_WIDTHS = (
    N_HEADS_A * HEAD_DIM, N_HEADS_A * HEAD_DIM, N_HEADS_A * HEAD_DIM,
    IDX_HEADS * IDX_DIM, IDX_DIM, IDX_HEADS,
    N_HEADS_B * HEAD_DIM, N_HEADS_B * HEAD_DIM, N_HEADS_B * HEAD_DIM,
    N_HEADS_B,
    N_HEADS_C * HEAD_DIM, N_HEADS_C * HEAD_DIM, N_HEADS_C * HEAD_DIM,
    N_HEADS_D * HEAD_DIM, N_KV_D * HEAD_DIM, N_KV_D * HEAD_DIM,
)
D_IN_2 = sum(SPLIT_WIDTHS)


def rmsnorm(x, g):
    xf = x.astype(jnp.float32)
    y = xf * lax.rsqrt(jnp.mean(xf * xf, axis=-1, keepdims=True) + EPS)
    return (y * g.astype(jnp.float32)).astype(x.dtype)

def rope_tables_2(positions, dim):
    half = dim // 2
    inv_freq = ROPE_THETA ** (-jnp.arange(half, dtype=jnp.float32) / half)
    ang = positions.astype(jnp.float32)[..., None] * inv_freq
    return jnp.cos(ang)[:, :, None, :], jnp.sin(ang)[:, :, None, :]

def apply_rope_2(x, tables):
    cos, sin = tables
    half = x.shape[-1] // 2
    xf = x.astype(jnp.float32)
    x1, x2 = xf[..., :half], xf[..., half:]
    return jnp.concatenate([x1 * cos - x2 * sin, x2 * cos + x1 * sin], axis=-1).astype(x.dtype)

def to_blocks(a):
    b, s = a.shape[:2]
    return jnp.moveaxis(a.reshape(b, s // BLOCK, BLOCK, *a.shape[2:]), 1, 0)

def from_blocks(o):
    nb, b = o.shape[:2]
    return jnp.moveaxis(o, 0, 1).reshape(b, nb * BLOCK, *o.shape[3:])

def dsa_attention(q, k, v, iq, ik, iw):
    s_len = k.shape[1]
    topk = min(TOPK_MAX, s_len // 4)
    key_pos = jnp.arange(s_len)
    scale = HEAD_DIM ** -0.5

    def one_block(args):
        qb, iqb, iwb, n = args
        t = n * BLOCK + jnp.arange(BLOCK)
        causal = key_pos[None, :] <= t[:, None]
        dots = jnp.einsum('bthd,bsd->bths', iqb, ik)
        score = jnp.einsum('bth,bths->bts', iwb, jax.nn.relu(dots)).astype(jnp.float32)
        score = jnp.where(causal[None], score, NEG_INF)
        _, idx = lax.top_k(score, topk)
        valid = idx <= t[None, :, None]
        k_sel = jax.vmap(lambda kk, ii: kk[ii])(k, idx)
        v_sel = jax.vmap(lambda vv, ii: vv[ii])(v, idx)
        logits = jnp.einsum('bthd,btjhd->bhtj', qb, k_sel).astype(jnp.float32) * scale
        logits = jnp.where(valid[:, None], logits, NEG_INF)
        probs = jax.nn.softmax(logits, axis=-1).astype(v.dtype)
        return jnp.einsum('bhtj,btjhd->bthd', probs, v_sel)

    nb = s_len // BLOCK
    out = lax.map(one_block, (to_blocks(q), to_blocks(iq), to_blocks(iw), jnp.arange(nb)))
    return from_blocks(out)

def forgetting_attention(q, k, v, log_f):
    s_len = k.shape[1]
    cum_bsh = jnp.cumsum(log_f, axis=1)
    cum = jnp.moveaxis(cum_bsh, 2, 1)
    key_pos = jnp.arange(s_len)
    scale = HEAD_DIM ** -0.5

    def one_block(args):
        qb, cb, n = args
        t = n * BLOCK + jnp.arange(BLOCK)
        causal = key_pos[None, :] <= t[:, None]
        logits = jnp.einsum('bthd,bshd->bhts', qb, k).astype(jnp.float32) * scale
        decay = jnp.moveaxis(cb, 2, 1)[..., :, None] - cum[:, :, None, :]
        logits = jnp.where(causal[None, None], logits + decay, NEG_INF)
        probs = jax.nn.softmax(logits, axis=-1).astype(v.dtype)
        return jnp.einsum('bhts,bshd->bthd', probs, v)

    nb = s_len // BLOCK
    out = lax.map(one_block, (to_blocks(q), to_blocks(cum_bsh), jnp.arange(nb)))
    return from_blocks(out)

def differential_attention(q, k, v, lam, lam_init, subln_g):
    s_len = k.shape[1]
    key_pos = jnp.arange(s_len)
    scale = DIFF_DIM ** -0.5

    def one_block(args):
        qb, n = args
        t = n * BLOCK + jnp.arange(BLOCK)
        causal = key_pos[None, :] <= t[:, None]
        logits = jnp.einsum('bthmd,bshmd->bmhts', qb, k).astype(jnp.float32) * scale
        logits = jnp.where(causal[None, None, None], logits, NEG_INF)
        probs = jax.nn.softmax(logits, axis=-1)
        diff = probs[:, 0] - lam * probs[:, 1]
        return jnp.einsum('bhts,bshd->bthd', diff.astype(v.dtype), v)

    nb = s_len // BLOCK
    out = from_blocks(lax.map(one_block, (to_blocks(q), jnp.arange(nb))))
    return rmsnorm(out, subln_g) * (1.0 - lam_init)

def sliding_window_sink_attention(q, k, v, sinks):
    b, s_len, n_h, dh = q.shape
    n_kv = k.shape[2]
    grp = n_h // n_kv
    nb = s_len // BLOCK
    qb = q.reshape(b, nb, BLOCK, n_kv, grp, dh)
    kb = k.reshape(b, nb, BLOCK, n_kv, dh)
    vb = v.reshape(b, nb, BLOCK, n_kv, dh)
    pad = ((0, 0), (1, 0), (0, 0), (0, 0), (0, 0))
    k_win = jnp.concatenate([jnp.pad(kb, pad)[:, :-1], kb], axis=2)
    v_win = jnp.concatenate([jnp.pad(vb, pad)[:, :-1], vb], axis=2)
    logits = jnp.einsum('bnikgd,bnjkd->bnkgij', qb, k_win).astype(jnp.float32) * (dh ** -0.5)
    i = jnp.arange(BLOCK)[:, None]
    j = jnp.arange(2 * BLOCK)[None, :]
    rel = i + BLOCK - j
    band = (rel >= 0) & (rel < WINDOW)
    in_range = (jnp.arange(nb)[:, None, None] > 0) | (j[None] >= BLOCK)
    mask = band[None] & in_range
    logits = jnp.where(mask[None, :, None, None], logits, NEG_INF)
    sink = jnp.broadcast_to(sinks.astype(jnp.float32).reshape(n_kv, grp)[None, None, :, :, None, None],
                            logits.shape[:-1] + (1,))
    probs = jax.nn.softmax(jnp.concatenate([logits, sink], axis=-1), axis=-1)[..., :-1]
    out = jnp.einsum('bnkgij,bnjkd->bnikgd', probs.astype(v.dtype), v_win)
    return out.reshape(b, s_len, n_h, dh)

def hybrid_layer(x, p_i, rope64, rope32, lam_init, w_in, b_forget, lq1, lk1, lq2, lk2,
                 diff_subln, sinks, w_out, g_pre_mix, g_post_mix, g_pre_mlp, g_post_mlp,
                 w_up, w_down, w_ple_proj, w_ple_gate):
    b, s_len, _ = x.shape
    h = rmsnorm(x, g_pre_mix)
    proj = h @ w_in
    points = np.cumsum(SPLIT_WIDTHS)[:-1].tolist()
    (a_q, a_k, a_v, a_iq, a_ik, a_iw, b_q, b_k, b_v, b_f,
     c_q, c_k, c_v, d_q, d_k, d_v) = jnp.split(proj, points, axis=-1)

    def heads(t, n, d):
        return t.reshape(b, s_len, n, d)

    iw = a_iw * (IDX_HEADS ** -0.5 * IDX_DIM ** -0.5)
    o_a = dsa_attention(apply_rope_2(heads(a_q, N_HEADS_A, HEAD_DIM), rope64),
                        apply_rope_2(heads(a_k, N_HEADS_A, HEAD_DIM), rope64),
                        heads(a_v, N_HEADS_A, HEAD_DIM),
                        apply_rope_2(heads(a_iq, IDX_HEADS, IDX_DIM), rope64),
                        apply_rope_2(a_ik[:, :, None, :], rope64)[:, :, 0],
                        iw)
    log_f = jax.nn.log_sigmoid((b_f + b_forget).astype(jnp.float32))
    o_b = forgetting_attention(heads(b_q, N_HEADS_B, HEAD_DIM), heads(b_k, N_HEADS_B, HEAD_DIM),
                               heads(b_v, N_HEADS_B, HEAD_DIM), log_f)
    cq = apply_rope_2(heads(c_q, 2 * N_HEADS_C, DIFF_DIM), rope32).reshape(b, s_len, N_HEADS_C, 2, DIFF_DIM)
    ck = apply_rope_2(heads(c_k, 2 * N_HEADS_C, DIFF_DIM), rope32).reshape(b, s_len, N_HEADS_C, 2, DIFF_DIM)
    f32 = jnp.float32
    lam = (jnp.exp(jnp.sum(lq1.astype(f32) * lk1.astype(f32)))
           - jnp.exp(jnp.sum(lq2.astype(f32) * lk2.astype(f32))) + lam_init)
    o_c = differential_attention(cq, ck, heads(c_v, N_HEADS_C, HEAD_DIM), lam, lam_init, diff_subln)
    o_d = sliding_window_sink_attention(apply_rope_2(heads(d_q, N_HEADS_D, HEAD_DIM), rope64),
                                        apply_rope_2(heads(d_k, N_KV_D, HEAD_DIM), rope64),
                                        heads(d_v, N_KV_D, HEAD_DIM), sinks)

    mix = jnp.concatenate([o_a.reshape(b, s_len, -1), o_b.reshape(b, s_len, -1),
                           o_c.reshape(b, s_len, -1), o_d.reshape(b, s_len, -1)], axis=-1)
    x = x + rmsnorm(mix @ w_out, g_post_mix)

    h = rmsnorm(x, g_pre_mlp)
    m = jnp.square(jax.nn.relu(h @ w_up)) @ w_down
    x = x + rmsnorm(m, g_post_mlp)

    x = x + jax.nn.sigmoid(x @ w_ple_gate) * (p_i @ w_ple_proj)
    return x

def second_inputs(seed: int = 0) -> dict:
    key = jax.random.key(seed)
    ks = jax.random.split(key, 22)

    def normal(k, shape, scale):
        return jax.random.normal(k, shape, jnp.float32) * scale

    def gain(k, shape):
        return 1.0 + 0.02 * jax.random.normal(k, shape, jnp.float32)

    return {
        'x': normal(ks[0], (BATCH, SEQ, D_MODEL), 1.0),
        'p': normal(ks[1], (DEPTH, BATCH, SEQ, D_PLE), 1.0),
        'positions': jnp.broadcast_to(jnp.arange(SEQ, dtype=jnp.int32), (BATCH, SEQ)),
        'w_in': normal(ks[2], (DEPTH, D_MODEL, D_IN_2), D_MODEL ** -0.5),
        'b_forget': 2.0 + normal(ks[3], (DEPTH, N_HEADS_B), 0.5),
        'lambda_q1': normal(ks[4], (DEPTH, DIFF_DIM), 0.1),
        'lambda_k1': normal(ks[5], (DEPTH, DIFF_DIM), 0.1),
        'lambda_q2': normal(ks[6], (DEPTH, DIFF_DIM), 0.1),
        'lambda_k2': normal(ks[7], (DEPTH, DIFF_DIM), 0.1),
        'diff_subln': gain(ks[8], (DEPTH, HEAD_DIM)),
        'sinks': normal(ks[9], (DEPTH, N_HEADS_D), 1.0),
        'w_out': normal(ks[10], (DEPTH, MIX_WIDTH, D_MODEL), MIX_WIDTH ** -0.5),
        'norm_pre_mix': gain(ks[11], (DEPTH, D_MODEL)),
        'norm_post_mix': gain(ks[12], (DEPTH, D_MODEL)),
        'norm_pre_mlp': gain(ks[13], (DEPTH, D_MODEL)),
        'norm_post_mlp': gain(ks[14], (DEPTH, D_MODEL)),
        'w_mlp_up': normal(ks[15], (DEPTH, D_MODEL, D_FF_2), D_MODEL ** -0.5),
        'w_mlp_down': normal(ks[16], (DEPTH, D_FF_2, D_MODEL), D_FF_2 ** -0.5),
        'w_ple_proj': normal(ks[17], (DEPTH, D_PLE, D_MODEL), D_PLE ** -0.5),
        'w_ple_gate': normal(ks[18], (DEPTH, D_MODEL, D_MODEL), D_MODEL ** -0.5),
    }

def second_block(x, p, positions, w_in, b_forget, lambda_q1, lambda_k1, lambda_q2, lambda_k2,
              diff_subln, sinks, w_out, norm_pre_mix, norm_post_mix, norm_pre_mlp, norm_post_mlp,
              w_mlp_up, w_mlp_down, w_ple_proj, w_ple_gate):
    rope64 = rope_tables_2(positions, HEAD_DIM)
    rope32 = rope_tables_2(positions, DIFF_DIM)
    for i in range(DEPTH):
        lam_init = 0.8 - 0.6 * math.exp(-0.3 * i)
        x = hybrid_layer(x, p[i], rope64, rope32, lam_init, w_in[i], b_forget[i],
                         lambda_q1[i], lambda_k1[i], lambda_q2[i], lambda_k2[i],
                         diff_subln[i], sinks[i], w_out[i], norm_pre_mix[i], norm_post_mix[i],
                         norm_pre_mlp[i], norm_post_mlp[i], w_mlp_up[i], w_mlp_down[i],
                         w_ple_proj[i], w_ple_gate[i])
    return x


def setup_inputs(seed=0):
    out = dict(first_inputs(seed))
    for name, value in second_inputs(seed + 1).items():
        if name != "x":
            out[name + "_2"] = value
    return out


def reference(
    x, w_in, w_out, pre_mix_g, post_mix_g, pre_ffn_g, post_ffn_g, hgrn_lb_logits, hgrn_norm_g,
    gla_w_gk2, gla_b_gk, gla_norm_g, mla_q_norm_g, mla_w_uq, mla_kv_norm_g, mla_w_ukv,
    gdn_conv_w, gdn_a_log, gdn_dt_bias, gdn_norm_g, ffn_w_gate, ffn_w_up, ffn_conv_w,
    ffn_w_down, p_2, positions_2, w_in_2, b_forget_2, lambda_q1_2, lambda_k1_2, lambda_q2_2,
    lambda_k2_2, diff_subln_2, sinks_2, w_out_2, norm_pre_mix_2, norm_post_mix_2,
    norm_pre_mlp_2, norm_post_mlp_2, w_mlp_up_2, w_mlp_down_2, w_ple_proj_2, w_ple_gate_2,
):
    x = first_block(
        x, w_in, w_out, pre_mix_g, post_mix_g, pre_ffn_g, post_ffn_g, hgrn_lb_logits,
        hgrn_norm_g, gla_w_gk2, gla_b_gk, gla_norm_g, mla_q_norm_g, mla_w_uq, mla_kv_norm_g,
        mla_w_ukv, gdn_conv_w, gdn_a_log, gdn_dt_bias, gdn_norm_g, ffn_w_gate, ffn_w_up,
        ffn_conv_w, ffn_w_down,
    )
    return second_block(
        x, p_2, positions_2, w_in_2, b_forget_2, lambda_q1_2, lambda_k1_2, lambda_q2_2,
        lambda_k2_2, diff_subln_2, sinks_2, w_out_2, norm_pre_mix_2, norm_post_mix_2,
        norm_pre_mlp_2, norm_post_mlp_2, w_mlp_up_2, w_mlp_down_2, w_ple_proj_2, w_ple_gate_2,
    )


_drawn_inputs = setup_inputs


def setup_inputs(seed=0):
    import zlib

    import numpy as np

    out = dict(_drawn_inputs(seed))
    spreads = {}
    factors = {'lambda_k1_2': 4.733,
     'lambda_q2_2': 3.273,
     'lambda_k2_2': 3.541,
     'diff_subln_2': 46.564,
     'sinks_2': 32.013,
     'norm_post_mix_2': 4.28,
     'norm_pre_mlp_2': 4.3,
     'norm_post_mlp_2': 14.652,
     'b_forget_2': 26.36}
    for name, (base, spread) in spreads.items():
        noise = np.random.default_rng([zlib.crc32(name.encode()), seed]).standard_normal(out[name].shape)
        drawn = base * np.exp(spread * noise) if base else spread * noise
        out[name] = jnp.asarray(drawn.astype(out[name].dtype))
    for name, factor in factors.items():
        out[name] = (out[name] * factor).astype(out[name].dtype)
    return out
```

```python
from contextlib import ExitStack

import numpy as np

import concourse.bass as bass
from concourse import mybir

F32 = mybir.dt.float32
ALU = mybir.AluOpType
ACT = mybir.ActivationFunctionType
AX = mybir.AxisListType

P = 128
T = 256
NT = T // P
DM = 1024
KT = DM // P
DEPTH = 2
GW = 256
HD = 64
EPS = 1e-6
NEG = -1e30
SUB = 16
NSUB = T // SUB
SUBP = P // SUB
CHUNK = 64
D_FF = 2816
FT = D_FF // P
MEMORY = 51160
PANEL = 528
SLOTS = 4


class Psum:

    def __init__(self, nc, ctx, tag, banks):
        self.t = banks
        self.full = [ctx.enter_context(nc.semaphore(f"{tag}_bank{b}_filled")) for b in range(8)]
        self.free = [ctx.enter_context(nc.semaphore(f"{tag}_bank{b}_freed")) for b in range(8)]
        self.at, self.given_back = {}, set()

    def claim(self, pe, name):
        assert name not in self.at, name
        n = len(self.at)
        self.at[name] = (n % 8, n // 8 + 1)
        if n >= 8:
            pe.wait_ge(self.free[n % 8], n // 8)
        return self.t[:, n % 8, :]

    def check(self):
        assert set(self.at) == self.given_back, set(self.at) ^ self.given_back

    def known(self, name):
        return name in self.at

    def bank(self, name):
        return self.t[:, self.at[name][0], :]

    def full_of(self, name):
        return self.full[self.at[name][0]]

    def filled(self, name):
        b, n = self.at[name]
        return self.full[b], n

    def freed(self, name):
        assert name not in self.given_back, name
        self.given_back.add(name)
        return self.free[self.at[name][0]], 1


class Chain:

    def __init__(self, eng, sem):
        self.eng, self.sem, self.n = eng, sem, 0

    def __call__(self, ins):
        self.n += 1
        ins.then_inc(self.sem, 1)
        self.eng.wait_ge(self.sem, self.n)


class Ring:

    def __init__(self, nc, ctx, tag, panels, slots):
        self.t = slots
        self.full = [ctx.enter_context(nc.semaphore(f"{tag}_slot{s}_filled")) for s in range(SLOTS)]
        self.free = [ctx.enter_context(nc.semaphore(f"{tag}_slot{s}_freed")) for s in range(SLOTS)]
        self.panels, self.names = panels, [p[0] for p in panels]
        self.per_layer = [len(range(s, len(panels), SLOTS)) for s in range(SLOTS)]

    def view(self, name):
        n = self.names.index(name)
        _, _, k, c0, c1 = self.panels[n]
        return self.t[:, n % SLOTS, 0:k * (c1 - c0)].rearrange("p (k n) -> p k n", k=k)

    def load_all(self, sp, layer):
        for n, (name, source, k, c0, c1) in enumerate(self.panels):
            s = n % SLOTS
            sp.wait_ge(self.free[s], layer * self.per_layer[s] + (n // SLOTS + 1))
            sp.dma_start(self.view(name), source(layer)).then_inc(self.full[s], 16)

    def wait(self, eng, layer, name):
        n = self.names.index(name)
        s = n % SLOTS
        eng.wait_ge(self.full[s], layer * (16 * self.per_layer[s]) + 16 * (n // SLOTS + 1))
        return self.view(name)

    def freed(self, name):
        return self.free[self.names.index(name) % SLOTS], 1


def table(columns):
    out, at = {}, 0
    for name, width in columns:
        out[name] = (at, at + width)
        at += width
    return out, at


def bands(a, d):
    return a.rearrange("p r (s c) -> p (r s) c", c=SUB)[:, :, d:SUB]


def shifted(a, d):
    return a.rearrange("p r (s c) -> p (r s) c", c=SUB)[:, :, 0:SUB - d]


def shaped(ap, *shape):
    if len(shape) == 1:
        return ap
    names = "abcd"[:len(shape)]
    sizes = {n: s for n, s in zip(names[1:], shape[1:])}
    return ap.rearrange(f"p ({' '.join(names)}) -> p {' '.join(names)}", **sizes)


class Area:

    def __init__(self, tensor, width, at=0):
        self.tensor, self.width, self.at = tensor, width, at

    def __call__(self, *shape):
        n = int(np.prod(shape))
        lo, self.at = self.at, self.at + n
        assert self.at <= self.width, (self.at, self.width)
        return shaped(self.tensor[:, lo:lo + n], *shape)


class Group:
    pass


def sem_ranges(numbers):
    out = []
    for n in sorted(numbers):
        if out and out[-1].stop == n:
            out[-1] = range(out[-1].start, n + 1)
        else:
            out.append(range(n, n + 1))
    return out


CONST1, N_CONST1 = table([
    ("ident", P), ("cum", P), ("ones", P), ("heads64", P), ("to_pair", 2 * P),
    ("rot96", 96), ("cos96", T), ("sin96", T), ("causal", NT * T), ("hide_strict", P),
    ("hide_incl", P), ("level", 7 * P), ("restart", T), ("sub", SUBP), ("eps", 1),
])
PAR1, N_PAR1 = table([
    ("pre_mix", KT), ("pre_ffn", KT), ("lb_logits", 2 * DEPTH), ("lb_of", 2 * DEPTH), ("hgrn_norm", 1),
    ("b_gk", 1), ("gla_norm", 1), ("q_norm", 2), ("kv_norm", 1), ("conv", 4 * 6), ("gdn_norm", 1),
    ("ffn_conv", 3 * FT), ("a_log", 4), ("dt_bias", 4), ("post_mix", DM), ("post_ffn", DM),
])
IN1 = [(0, 512), (512, 1024), (1024, 1536), (1536, 2064), (2064, 2480), (2480, 2992), (2992, 3256)]


def shape_constants1():
    c = np.zeros((P, N_CONST1), np.float32)

    def put(name, a):
        lo, hi = CONST1[name]
        c[:a.shape[0], lo:hi] = a.reshape(a.shape[0], -1)

    i = np.arange(P)
    same = (i[:, None] // CHUNK) == (i[None, :] // CHUNK)
    put("ident", np.eye(P, dtype=np.float32))
    put("cum", (same & (i[:, None] <= i[None, :])).astype(np.float32))
    put("ones", np.ones((P, P), np.float32))
    put("heads64", same.astype(np.float32))
    pair = np.zeros((P, 2, P), np.float32)
    for p in range(2):
        pair[:, p] = (i[:, None] // 32) == (2 * p + i[None, :] // 64)
    put("to_pair", pair)
    rot = np.zeros((96, 96), np.float32)
    for m in range(16):
        rot[64 + 16 + m, 64 + m] = -1.0
        rot[64 + m, 64 + 16 + m] = 1.0
    put("rot96", rot)
    inv = (np.float32(10000.0) ** (-np.arange(0, 32, 2, dtype=np.float32) / np.float32(32))).astype(np.float32)
    ang = (np.arange(T, dtype=np.float32)[None, :] * inv[:, None]).astype(np.float32)
    cos, sin = np.ones((96, T), np.float32), np.zeros((96, T), np.float32)
    cos[64:80] = cos[80:96] = np.cos(ang)
    sin[64:80] = sin[80:96] = np.sin(ang)
    put("cos96", cos)
    put("sin96", sin)
    key = np.arange(T)
    put("causal", np.stack([np.where(key[None, :] <= (i[:, None] + P * t), 0.0, NEG) for t in range(NT)], 1).astype(np.float32))
    put("hide_strict", np.where(same & (i[None, :] < i[:, None]), 0.0, -NEG).astype(np.float32))
    put("hide_incl", np.where(same & (i[None, :] >= i[:, None]), 0.0, NEG).astype(np.float32))
    level = np.zeros((P, 7, P), np.float32)
    for n in range(6):
        c_ = 1 << n
        row, col = i[:, None], i[None, :]
        m = (row // (2 * c_) == col // (2 * c_)) & (row % (2 * c_) >= c_) & (col % (2 * c_) < c_)
        level[:, n] = m.T
        if n == 0:
            level[:, 6] = m
    put("level", level)
    put("restart", np.broadcast_to((np.arange(T) % SUB != 0).astype(np.float32), (P, T)))
    put("sub", (i[:, None] // SUB == np.arange(SUBP)[None, :]).astype(np.float32))
    put("eps", np.full((P, 1), EPS, np.float32))
    return c


def params1(a):
    out = np.zeros((DEPTH, P, N_PAR1), np.float32)

    def put(name, layer, v):
        lo, hi = PAR1[name]
        out[layer, :, lo:hi] = v

    def cols(v):
        return np.asarray(v).reshape(-1, P).T

    def rows(v):
        v = np.asarray(v)
        return np.broadcast_to(v, (P,) + v.shape)

    for l in range(DEPTH):
        put("pre_mix", l, cols(a["pre_mix_g"][l]))
        put("pre_ffn", l, cols(a["pre_ffn_g"][l]))
        lb = np.stack([cols(a["hgrn_lb_logits"][j]) for j in range(DEPTH)], 2)
        put("lb_logits", l, lb.reshape(P, -1))
        of = np.zeros((P, 2, DEPTH), np.float32)
        of[:, :, 1:l + 1] = 1.0
        put("lb_of", l, of.reshape(P, -1))
        put("hgrn_norm", l, np.concatenate([a["hgrn_norm_g"][l]] * 2)[:, None])
        put("b_gk", l, cols(a["gla_b_gk"][l]))
        put("gla_norm", l, np.concatenate([a["gla_norm_g"][l]] * 2)[:, None])
        put("q_norm", l, cols(a["mla_q_norm_g"][l]))
        put("kv_norm", l, cols(a["mla_kv_norm_g"][l]))
        put("conv", l, np.asarray(a["gdn_conv_w"][l]).reshape(4, 6, P).transpose(2, 1, 0).reshape(P, -1))
        put("gdn_norm", l, np.concatenate([a["gdn_norm_g"][l]] * 2)[:, None])
        put("ffn_conv", l, np.asarray(a["ffn_conv_w"][l]).reshape(3, FT, P).transpose(2, 1, 0).reshape(P, -1))
        put("a_log", l, rows(a["gdn_a_log"][l]))
        put("dt_bias", l, rows(a["gdn_dt_bias"][l]))
        put("post_mix", l, rows(a["post_mix_g"][l]))
        put("post_ffn", l, rows(a["post_ffn_g"][l]))
    return out



SIGNALS1 = """normed hT v_T kdT kd_tok vexp state q_decayed weighted o_sq mla_sq mla_c mla_cn rot_in qT kT probs
PT mla_v l2_sq g_ready qk_norm lmat level_T level_X tok_D uw qe state_D v_new params code mixT gT
rstd oT_ready o_rstd scan exp_b scan_end kd_exp vtok diff decay act lb_max lb_exp aq_tanh af_sig
gate_th bg_th dz_th af_f af_ln gk_abs gk_ln gla_done mla_rstd scores_max exps conv conv_th conv_silu
l2_rstd ba_in ba_exp b_small b_exp erow hid decays nt y_ss y_sum y_rstd x_new ff_conv ff_gate
ff_gelu qk dve kr_done gpad_zero""".split()


def block1(nc, kept, memory, banks, x, x_in, A):
    with ExitStack() as ctx:
        buf = Area(memory, MEMORY)

        S = {n: ctx.enter_context(nc.semaphore("b1_" + n)) for n in SIGNALS1}
        psum = Psum(nc, ctx, "b1", banks)
        layer_done = kept.enter_context(nc.semaphore("b1_layer_done"))
        layer_open = kept.enter_context(nc.semaphore("b1_layer_open"))
        barrier_taken = kept.enter_context(nc.semaphore("b1_barrier_taken"))
        once = kept.enter_context(nc.semaphore("b1_constants_in"))

        def cols(src, k):
            return lambda l, c0, c1, k0=0: src.rearrange("l (k p) n -> l p k n", p=P)[l, :, k0:k0 + k, c0:c1]

        win, wout = cols(A["w_in"], KT), cols(A["w_out"], KT)
        wg, wu = cols(A["ffn_w_gate"], KT), cols(A["ffn_w_up"], KT)
        wd = A["ffn_w_down"].rearrange("l (k p) n -> l p k n", p=P)
        panels = [(f"in{i}", lambda l, c0=c0, c1=c1: win(l, c0, c1), KT, c0, c1) for i, (c0, c1) in enumerate(IN1)]
        panels += [(f"out{i}", lambda l, i=i: wout(l, 512 * i, 512 * i + 512), KT, 0, 512) for i in range(2)]
        for i in range(6):
            c0, c1 = 512 * i, min(512 * i + 512, D_FF)
            panels.append((f"gate{i}", lambda l, c0=c0, c1=c1: wg(l, c0, c1), KT, c0, c1))
            panels.append((f"up{i}", lambda l, c0=c0, c1=c1: wu(l, c0, c1), KT, c0, c1))
        for i in range(6):
            k = min(4, FT - 4 * i)
            panels.append((f"down{i}", lambda l, i=i, k=k: wd[l, :, 4 * i:4 * i + k, :], k, 0, DM))
        ring = Ring(nc, kept, "b1", panels, buf(SLOTS, KT * PANEL))

        const = buf(N_CONST1)
        par = buf(N_PAR1)

        def C(name, rows=P):
            lo, hi = CONST1[name]
            return const[0:rows, lo:hi]

        def PAR(name, i=None, n=1):
            lo, hi = PAR1[name]
            return par[:, lo:hi] if i is None else par[:, lo + i:lo + i + n]

        w_uq = buf(2, 384)
        w_ukv = buf(512)
        w_gk2 = buf(P)
        hT = buf(KT, T)
        mixT = buf(KT, T)
        stat = buf(64)

        G = {}
        for m, R in (("A", 2), ("B", 1)):
            g = G[m] = Group()
            g.name, g.R = m, R
            g.q, g.k, g.lf = (buf(R, T) for n in ("q", "k", "lf"))
            g.vT, g.gate = (buf(2, T) for n in ("vT", "gate"))
        cT = buf(3, T)
        kr = buf(T)
        cin = buf(6, 3 + T)
        oD = Group()
        oD.gate = buf(2, T)
        code = buf(T)
        lb = buf(32)
        zb = buf(NT, 8)
        sm = {n: buf(NT, 4) for n in ("beta", "x", "e", "l", "g", "b", "nb", "eb", "be", "fd", "bl")}
        ea = buf(4)
        SD = buf(4, 2, HD)

        WORK = 13440
        work = buf(WORK)
        area = Area(work, WORK)
        for g in G.values():
            area.at = 0
            g.b, g.eb, g.qe, g.kd, g.e2 = (area(g.R, T) for _ in range(5))
            area.at = 10 * T
            g.vtok, g.oT, g.sq, g.rs = (area(2, T) for _ in range(4))
            g.kdtok = area(NT, g.R * P)
            area.at = 20 * T
            g.S = area(g.R, NSUB, HD)
            area.at = 28 * T
            vexp = area(NT, SUBP, GW)
            area.at = 28 * T
            band = {n: area(2, 2 * T) for n in ("diff", "exp", "qk", "w", "o")}
        area.at = 0
        cn, crs = area(3, T), area(2, T)
        qT, kT, rtmp = (area(4, T) for _ in range(3))
        vtokC = area(NT, GW)
        L, Pr, PT = area(4, T), area(4, T), area(NT, 4, T)
        area.at = 0
        cv = area(6, T)
        ktok, vtokD, kbe, vb, kdec = (area(NT, GW) for _ in range(5))
        row, lstr, lincT, erow, Tm, Um, NTm = (area(8, P) for _ in range(7))
        Xm = row
        pm = lstr
        cth = shaped(work[:, area.at - 6 * T:area.at], 6, T)
        lrs = erow.rearrange("p a b -> p (a b)").rearrange("p (a b) -> p a b", a=4)
        qeD, wT = area(2, T), area(2, T)
        uD, vnew = area(NT, GW), area(NT, GW)
        area.at = 0
        oD.oT, oD.sq, oD.rs = (area(2, T) for _ in range(3))
        area.at = 0
        gT = area(FT, T)
        gpad = area(2, 2 + T)
        gcv = area(2, 3, T)
        ysq, yn = area(512), area(4, 512)
        xn = shaped(work[:, WORK - NT * DM:WORK], NT, DM)

        IN_USES = [
            ("a_q", "in0", [(0, P, 0, 0), (0, P, 1, 128)]), ("a_f", "in0", [(0, P, 0, 256), (0, P, 1, 384)]),
            ("a_i", "in1", [(0, P, 0, 512), (0, P, 1, 640)]), ("a_g", "in1", [(0, P, 0, 768), (0, P, 1, 896)]),
            ("b_qk", "in2", [(0, P, 0, 1024), (0, P, 1, 1152)]), ("b_v", "in2", [(0, P, 0, 1280), (0, P, 1, 1408)]),
            ("code", "in3", [(0, 16, 0, 1536)]), ("b_g", "in3", [(0, P, 0, 1552), (0, P, 1, 1680)]),
            ("c_q", "in3", [(0, P, 0, 1808), (0, P, 1, 1936)]),
            ("c_kvr", "in4", [(0, P, 0, 2064), (64, 32, 1, 2192)]),
            ("d_q", "in4", [(0, P, 0, 2224), (0, P, 1, 2352)]),
            ("d_k", "in5", [(0, P, 0, 2480), (0, P, 1, 2608)]), ("d_v", "in5", [(0, P, 0, 2736), (0, P, 1, 2864)]),
            ("d_z", "in6", [(0, P, 0, 3000), (0, P, 1, 3128)]),
        ]
        block = ctx.enter_context(nc.Block())

        @block.sync
        def _(sp):
            for s in range(SLOTS):
                sp.sem_inc(ring.free[s], 1)
            sp.dma_start(const[:, :], A["const1"]).then_inc(once, 16)
            with sp.Fori(0, DEPTH) as layer:
                ring.load_all(sp, layer)

        @block.tensor
        def _(pe):
            used = [None]

            def mm(out, lhsT, rhs, start=True, stop=True):
                ins = nc.tensor.matmul(out, lhsT, rhs, start=start, stop=stop)
                if used[0]:
                    ins.then_inc(*ring.freed(used[0]))
                    used[0] = None
                return ins

            def transpose(out, a):
                return nc.tensor.transpose(out, a, C("ident"))

            def norm_transposes(k):
                pe.wait_ge(S["normed"], k + 1)
                for j in range(4):
                    b = psum.claim(pe, f"hT{k}_{j}")
                    for i in range(4):
                        last = transpose(b[:, i * P:(i + 1) * P], xn[:, i % 2, (2 * j + i // 2) * P:(2 * j + i // 2 + 1) * P])
                    last.then_inc(psum.full_of(f"hT{k}_{j}"), 1)

            def project(layer):
                pe.wait_ge(S["hT"], 4)
                held = None
                for name, panel, parts in IN_USES:
                    if panel != held:
                        used[0], held = held, panel
                        w = ring.wait(pe, layer, panel)
                        base = IN1[int(panel[2:])][0]
                    if panel == "in6" and name == "d_z":
                        b = psum.claim(pe, "d_ba")
                        for t in range(NT):
                            for k in range(KT):
                                last = mm(b[:, 8 * t:8 * t + 8], hT[:, k, t * P:(t + 1) * P], w[:, k, 0:8], k == 0, k == KT - 1)
                        last.then_inc(psum.full_of("d_ba"), 1)
                    b = psum.claim(pe, name)
                    for row0, m, half, c0 in parts:
                        for k in range(KT):
                            last = mm(b[row0:row0 + m, half * T:(half + 1) * T], w[:, k, c0 - base:c0 - base + m],
                                      hT[:, k, :], k == 0, k == KT - 1)
                    last.then_inc(psum.full_of(name), 1)
                pe.drain().then_inc(*ring.freed(held))

            def gla(g, m):
                pe.wait_ge(S["v_T"], m + 1)
                b = psum.claim(pe, g.name + "_vt")
                for t in range(NT):
                    for p in range(2):
                        last = transpose(b[:, t * T + p * P:t * T + (p + 1) * P], g.vT[:, p, t * P:(t + 1) * P])
                last.then_inc(psum.full_of(g.name + "_vt"), 1)
                pe.wait_ge(S["kdT"], m + 1)
                b = psum.claim(pe, g.name + "_kdt")
                for t in range(NT):
                    for r in range(g.R):
                        at = (t * g.R + r) * P
                        last = transpose(b[:, at:at + P], g.kd[:, r, t * P:(t + 1) * P])
                last.then_inc(psum.full_of(g.name + "_kdt"), 1)
                pe.wait_ge(S["kd_tok"], m + 1)
                pe.wait_ge(S["vexp"], m + 1)
                d = g.R * P // 4
                for t in range(NT):
                    for r in range(g.R):
                        name = f"{g.name}_G{r}{t}"
                        b = psum.claim(pe, name)
                        for h in range(4 // g.R * r, 4 // g.R * (r + 1)):
                            row0 = d * h - P * r
                            last = mm(shaped(b, SUBP, HD)[row0:row0 + d, :, :], g.kdtok[:, t, d * h:d * h + d],
                                      vexp[:, t, :, HD * h:HD * h + HD])
                        last.then_inc(psum.full_of(name), 1)
                pe.wait_ge(S["state"], m + 1)
                pe.wait_ge(S["q_decayed"], m + 1)
                for p in range(2):
                    name = f"{g.name}_o{p}"
                    b = psum.claim(pe, name)
                    for s in range(NSUB):
                        for h in (2 * p, 2 * p + 1):
                            r, row0 = (d * h) // P, (d * h) % P
                            last = mm(b[HD * (h % 2):HD * (h % 2) + HD, SUB * s:SUB * s + SUB], g.S[row0:row0 + d, r, s, :],
                                      g.qe[row0:row0 + d, r, SUB * s:SUB * s + SUB])
                    last.then_inc(psum.full_of(name), 1)
                for i in range(SUB):
                    pe.wait_ge(S["weighted"], SUB * m + i + 1)
                    name, n = f"{g.name}_band{i}", NSUB * (SUB - i)
                    b = psum.claim(pe, name)
                    w = band["w"][:, i % 2, :]
                    if g.R == 2:
                        last = mm(b[:, 0:2 * n], C("heads64"), w[:, 0:2 * n])
                    else:
                        for p in range(2):
                            last = mm(b[:, p * n:(p + 1) * n], C("to_pair")[:, p * P:(p + 1) * P], w[:, 0:n])
                    last.then_inc(psum.full_of(name), 1)

            def head_norm(g, n, name):
                pe.wait_ge(S["o_sq"], n + 1)
                b = psum.claim(pe, name)
                mm(b[:, :], C("heads64"), g.sq[:, :, :]).then_inc(psum.full_of(name), 1)

            def mla():
                pe.wait_ge(S["mla_sq"], 1)
                b = psum.claim(pe, "c_ss")
                mm(b[:, 0:T], C("ones"), crs[:, 0, :], True, False)
                mm(b[:, 0:T], C("ones"), crs[:, 1, :], False, True)
                mm(b[:, T:2 * T], C("ones"), rtmp[:, 0, :]).then_inc(psum.full_of("c_ss"), 1)
                pe.wait_ge(S["mla_c"], 2)
                b = psum.claim(pe, "kr_rot")
                mm(b[64:96, 0:T], C("rot96")[64:96, 64:96], kr[64:96, :]).then_inc(psum.full_of("kr_rot"), 1)
                pe.wait_ge(S["mla_cn"], 1)
                for j in range(2):
                    b = psum.claim(pe, f"qT{j}")
                    for i in range(2):
                        h = 2 * j + i
                        for k in range(2):
                            last = mm(b[0:96, i * T:(i + 1) * T], w_uq[:, k, 96 * h:96 * h + 96], cn[:, k, :], k == 0, k == 1)
                    last.then_inc(psum.full_of(f"qT{j}"), 1)
                for j in range(2):
                    b = psum.claim(pe, f"kT{j}")
                    for i in range(2):
                        h = 2 * j + i
                        last = mm(b[0:64, i * T:(i + 1) * T], w_ukv[:, P * h:P * h + 64], cn[:, 2, :])
                    last.then_inc(psum.full_of(f"kT{j}"), 1)
                b = psum.claim(pe, "c_v")
                for t in range(NT):
                    last = mm(shaped(b[:, t * T:(t + 1) * T], 4, HD), cn[:, 2, t * P:(t + 1) * P],
                              shaped(w_ukv, 4, P)[:, :, 64:P])
                last.then_inc(psum.full_of("c_v"), 1)
                pe.wait_ge(S["rot_in"], 2)
                for j in range(2):
                    b = psum.claim(pe, f"rot{j}")
                    mm(b[0:96, :], C("rot96", 96), qT[0:96, 2 * j:2 * j + 2, :]).then_inc(psum.full_of(f"rot{j}"), 1)
                pe.wait_ge(S["qT"], 1)
                pe.wait_ge(S["kT"], 2)
                for t in range(NT):
                    n = P * (t + 1)
                    for j in range(2):
                        b = psum.claim(pe, f"c_sc{t}{j}")
                        for i in range(2):
                            h = 2 * j + i
                            last = mm(b[:, i * n:(i + 1) * n], qT[0:96, h, t * P:(t + 1) * P], kT[0:96, h, 0:n])
                        last.then_inc(psum.full_of(f"c_sc{t}{j}"), 1)
                for t in range(NT):
                    pe.wait_ge(S["probs"], t + 1)
                    for kt in range(t + 1):
                        b = psum.claim(pe, f"c_pt{t}{kt}")
                        for h in range(4):
                            last = transpose(b[:, h * P:(h + 1) * P], Pr[:, h, kt * P:(kt + 1) * P])
                        last.then_inc(psum.full_of(f"c_pt{t}{kt}"), 1)
                pe.wait_ge(S["PT"], 3)
                pe.wait_ge(S["mla_v"], 1)
                b = psum.claim(pe, "c_o")
                for h in range(4):
                    o = b[HD * (h % 2):HD * (h % 2) + HD, T * (h // 2):T * (h // 2) + T]
                    mm(o, vtokC[:, 0, HD * h:HD * h + HD], PT[:, 0, h, :], True, False)
                    last = mm(o[:, P:T], vtokC[:, 1, HD * h:HD * h + HD], PT[:, 1, h, P:T], False, True)
                last.then_inc(psum.full_of("c_o"), 1)

            def gdn():
                pe.wait_ge(S["l2_sq"], 1)
                for j in range(2):
                    b = psum.claim(pe, f"l2_{j}")
                    mm(b[:, :], C("heads64"), cth[:, 2 * j:2 * j + 2, :]).then_inc(psum.full_of(f"l2_{j}"), 1)
                pe.wait_ge(S["g_ready"], 1)
                b = psum.claim(pe, "bsum")
                mm(b[:, 0:8], C("cum"), sm["g"][:, :, :])
                mm(b[:, 8:16], C("heads64"), sm["g"][:, :, :]).then_inc(psum.full_of("bsum"), 1)
                for par_ in range(2):
                    name = f"brow{par_}"
                    b = psum.claim(pe, name)
                    for t in range(NT):
                        for hp in range(2):
                            at = (2 * t + hp) * P
                            h = 2 * hp + par_
                            last = mm(b[:, at:at + P], sm["g"][:, t, h:h + 1].broadcast_to([P, P]), C("cum"))
                    last.then_inc(psum.full_of(name), 1)
                pe.wait_ge(S["qk_norm"], 1)
                for what, base in (("k_tok", 2), ("v_tok", 4)):
                    b = psum.claim(pe, what)
                    for t in range(NT):
                        for p in range(2):
                            last = transpose(b[:, t * T + p * P:t * T + (p + 1) * P], cv[:, base + p, t * P:(t + 1) * P])
                    last.then_inc(psum.full_of(what), 1)
                for what, base in (("kk", 2), ("kq", 0)):
                    for par_ in range(2):
                        name = f"{what}{par_}"
                        b = psum.claim(pe, name)
                        for t in range(NT):
                            for hp in range(2):
                                at, row0 = (2 * t + hp) * P, HD * par_
                                last = mm(b[:, at:at + P], cv[row0:row0 + HD, 2 + hp, t * P:(t + 1) * P],
                                          cv[row0:row0 + HD, base + hp, t * P:(t + 1) * P])
                        last.then_inc(psum.full_of(name), 1)

                def eight(what, f):
                    for j in range(2):
                        b = psum.claim(pe, f"{what}{j}")
                        for i in range(4):
                            last = f(b[:, i * P:(i + 1) * P], 4 * j + i)
                        last.then_inc(psum.full_of(f"{what}{j}"), 1)

                pe.wait_ge(S["lmat"], 1)
                eight("nt", lambda o, e: transpose(o, lstr[:, e, :]))
                for n in range(1, 6):
                    pe.wait_ge(S["level_T"], n)
                    eight(f"X{n}_", lambda o, e: mm(o, pm[:, e, :], Tm[:, e, :]))
                    pe.wait_ge(S["level_X"], 2 * n)
                    if n < 5:
                        eight(f"TX{n}_", lambda o, e: mm(o, Um[:, e, :], Xm[:, e, :]))
                    eight(f"UX{n}_", lambda o, e: mm(o, Xm[:, e, :], Um[:, e, :]))
                pe.wait_ge(S["level_T"], 6)
                pe.wait_ge(S["tok_D"], 1)
                b = psum.claim(pe, "u")
                for par_ in range(2):
                    for t in range(NT):
                        for hp in range(2):
                            h, e = 2 * hp + par_, 4 * par_ + 2 * t + hp
                            last = mm(b[:, t * T + HD * h:t * T + HD * h + HD], Um[:, e, :], vb[:, t, HD * h:HD * h + HD])
                last.then_inc(psum.full_of("u"), 1)
                b = psum.claim(pe, "wT")
                for par_ in range(2):
                    for t in range(NT):
                        for hp in range(2):
                            h, e = 2 * hp + par_, 4 * par_ + 2 * t + hp
                            last = mm(b[HD * par_:HD * par_ + HD, hp * T + t * P:hp * T + (t + 1) * P],
                                      kbe[:, t, HD * h:HD * h + HD], Um[:, e, :])
                last.then_inc(psum.full_of("wT"), 1)
                pe.wait_ge(S["uw"], 2)
                pe.wait_ge(S["qe"], 1)
                for c in range(4):
                    t, tok0, chunk = c // 2, CHUNK * (c % 2), slice(CHUNK * c, CHUNK * (c + 1))
                    pe.wait_ge(S["state_D"], c + 1)
                    for par_ in range(2):
                        rows = slice(HD * par_, HD * par_ + HD)
                        b = psum.claim(pe, f"ws{c}{par_}")
                        for hp in range(2):
                            last = mm(b[tok0:tok0 + CHUNK, hp * HD:(hp + 1) * HD], wT[rows, hp, chunk], SD[rows, c, hp, :])
                        last.then_inc(psum.full_of(f"ws{c}{par_}"), 1)
                    if c < 3:
                        pe.wait_ge(S["v_new"], c + 1)
                        b = psum.claim(pe, f"su{c}")
                        for par_ in range(2):
                            for hp in range(2):
                                h = 2 * hp + par_
                                last = mm(b[HD * par_:HD * par_ + HD, hp * HD:(hp + 1) * HD],
                                          kdec[tok0:tok0 + CHUNK, t, HD * h:HD * h + HD],
                                          vnew[tok0:tok0 + CHUNK, t, HD * h:HD * h + HD])
                        last.then_inc(psum.full_of(f"su{c}"), 1)
                o = psum.claim(pe, "D_o")
                for par_ in range(2):
                    rows = slice(HD * par_, HD * par_ + HD)
                    for c in range(4):
                        chunk = slice(CHUNK * c, CHUNK * (c + 1))
                        for hp in range(2):
                            last = mm(shaped(o, 2, T)[rows, hp, chunk], SD[rows, c, hp, :], qeD[rows, hp, chunk])
                last.then_inc(psum.full_of("D_o"), 1)
                pe.wait_ge(S["v_new"], 4)
                b = psum.claim(pe, "D_o2")
                for par_ in range(2):
                    for t in range(NT):
                        for hp in range(2):
                            h, e = 2 * hp + par_, 4 * par_ + 2 * t + hp
                            last = mm(b[HD * par_:HD * par_ + HD, hp * T + t * P:hp * T + (t + 1) * P],
                                      vnew[:, t, HD * h:HD * h + HD], lincT[:, e, :])
                last.then_inc(psum.full_of("D_o2"), 1)

            def wide(layer, what, lhs, tiles):
                banks = [psum.claim(pe, f"{what}{i}") for i in range(4)]
                held = None
                for k, (panel, cut) in enumerate(tiles):
                    if panel != held:
                        used[0], held = held or used[0], panel
                        w = ring.wait(pe, layer, panel)
                    for t in range(NT):
                        for half in range(2):
                            last = mm(banks[2 * t + half], lhs[:, k, t * P:(t + 1) * P], w[:, cut, half * 512:half * 512 + 512],
                                      k == 0, k == len(tiles) - 1)
                            if k == len(tiles) - 1:
                                last.then_inc(psum.full_of(f"{what}{2 * t + half}"), 1)
                return held

            with pe.Fori(0, DEPTH) as layer:
                pe.wait_ge(once, 16)
                pe.wait_ge(S["params"], 64)
                norm_transposes(0)
                project(layer)
                pe.wait_ge(S["code"], 1)
                b = psum.claim(pe, "gk")
                mm(b[:, 0:T], w_gk2[0:16, :], code[0:16, :]).then_inc(psum.full_of("gk"), 1)
                gla(G["A"], 0)
                head_norm(G["A"], 0, "A_ss")
                gla(G["B"], 1)
                head_norm(G["B"], 1, "B_ss")
                mla()
                gdn()
                head_norm(oD, 2, "D_ss")
                pe.wait_ge(S["mixT"], 4)
                banks = {}
                for half in range(2):
                    w = ring.wait(pe, layer, f"out{half}")
                    for t in range(NT):
                        b = psum.claim(pe, f"mix{half}{t}")
                        for k in range(KT):
                            last = mm(b[:, :], mixT[:, k, t * P:(t + 1) * P], w[:, k, :], k == 0, k == KT - 1)
                        last.then_inc(psum.full_of(f"mix{half}{t}"), 1)
                    used[0] = f"out{half}"
                norm_transposes(1)
                pe.wait_ge(S["hT"], 8)
                for c in range(6):
                    w1 = ring.wait(pe, layer, f"gate{c}")
                    w2 = ring.wait(pe, layer, f"up{c}")
                    last_tile = min(4 * c + 4, FT) - 1
                    for j in range(4 * c, last_tile + 1):
                        b = psum.claim(pe, f"ff{j}")
                        for half, w in ((0, w1), (1, w2)):
                            for k in range(KT):
                                last = mm(b[:, half * T:(half + 1) * T], w[:, k, (j % 4) * P:(j % 4 + 1) * P], hT[:, k, :],
                                          k == 0, k == KT - 1)
                            if half == 0 and j == last_tile:
                                used[0] = f"gate{c}"
                        last.then_inc(psum.full_of(f"ff{j}"), 1)
                    used[0] = f"up{c}"
                pe.wait_ge(S["gT"], FT)
                held = wide(layer, "y", gT, [(f"down{k // 4}", k % 4) for k in range(FT)])
                pe.drain().then_inc(ring.free[ring.names.index(held) % SLOTS], 1)
                pe.drain().then_inc(layer_done, 1)
                pe.wait_ge(layer_open, layer + 1)

        @block.scalar
        def _(act):
            A_ = nc.scalar.activation

            def norm_stats(k, step):
                for t in range(NT):
                    A_(xn[:, t, :], x[:, t, :], ACT.Square, accum_out=stat[:, t:t + 1])
                act.drain()
                step(A_(stat[:, 2:4], stat[:, 0:2], ACT.Ln, bias=C("eps"), scale=1.0 / DM))
                A_(stat[:, 4:6], stat[:, 2:4], ACT.Exp, scale=-0.5).then_inc(S["rstd"], 1)

            def norm_gain(k, gain):
                for j in (1, 3):
                    name = f"hT{k}_{j}"
                    act.wait_ge(*psum.filled(name))
                    for i in range(2):
                        last = A_(hT[:, 2 * j + i, :], psum.bank(name)[:, i * T:(i + 1) * T], ACT.Copy,
                                  scale=PAR(gain, 2 * j + i))
                    last.then_inc(*psum.freed(name))
                    act.drain().then_inc(S["hT"], 1)

            def drain_bank(name, out, signal, rows=slice(0, P), part=slice(0, 512), func=ACT.Copy, scale=1.0):
                act.wait_ge(*psum.filled(name))
                A_(out, psum.bank(name)[rows, part], func, scale=scale).then_inc(*psum.freed(name))
                if signal:
                    act.drain().then_inc(S[signal], 1)

            def post_norm(g, n, name, step):
                act.wait_ge(S["oT_ready"], n + 1)
                A_(g.sq[:, :, :], g.oT[:, :, :], ACT.Square).then_inc(S["o_sq"], 1)
                act.wait_ge(*psum.filled(name))
                ins = A_(g.rs[:, :, :], shaped(psum.bank(name), 2, T), ACT.Ln, bias=C("eps"), scale=1.0 / HD)
                ins.then_inc(*psum.freed(name))
                act.drain()
                A_(g.rs[:, :, :], g.rs[:, :, :], ACT.Exp, scale=-0.5).then_inc(S["o_rstd"], 1)

            def gla(g, m):
                act.wait_ge(S["scan"], m + 1)
                A_(g.eb[:, :, :], g.b[:, :, :], ACT.Exp).then_inc(S["exp_b"], 1)
                act.wait_ge(S["scan_end"], m + 1)
                A_(g.e2[:, :, :], g.e2[:, :, :], ACT.Exp, scale=-1.0).then_inc(S["kd_exp"], 1)
                drain_bank(g.name + "_vt", g.vtok[:, :, :], "vtok")
                for i in range(SUB):
                    n = SUB * m + i
                    act.wait_ge(S["diff"], n + 1)
                    if n >= 2:
                        act.wait_ge(S["weighted"], n - 1)
                    w = g.R * NSUB * (SUB - i)
                    A_(band["exp"][:, i % 2, 0:w], band["diff"][:, i % 2, 0:w], ACT.Exp).then_inc(S["decay"], 1)

            with act.Fori(0, DEPTH) as layer:
                step = Chain(act, S["act"])
                act.dma_start(par[:, :], A["par1"][layer, :, :]).then_inc(S["params"], 16)
                act.dma_start(w_uq, A["mla_w_uq"].rearrange("l (k p) n -> l p k n", p=P)[layer, :, :, :]).then_inc(S["params"], 16)
                act.dma_start(w_ukv, A["mla_w_ukv"][layer, :, :]).then_inc(S["params"], 16)
                act.dma_start(w_gk2[0:16, :], A["gla_w_gk2"][layer, :, :]).then_inc(S["params"], 16)
                act.wait_ge(once, 16)
                act.wait_ge(x_in, 32)
                norm_stats(0, step)
                act.wait_ge(S["params"], 64)
                A_(ea, PAR("a_log"), ACT.Exp)
                act.wait_ge(S["lb_max"], 1)
                A_(lb[:, 0:2 * DEPTH], lb[:, 0:2 * DEPTH], ACT.Exp).then_inc(S["lb_exp"], 1)
                norm_gain(0, "pre_mix")
                a, bb = G["A"], G["B"]
                act.wait_ge(*psum.filled("a_q"))
                A_(a.q[:, :, :], shaped(psum.bank("a_q"), 2, T), ACT.Tanh, scale=0.5).then_inc(S["aq_tanh"], 1)
                act.wait_ge(*psum.filled("a_f"))
                A_(a.lf[:, :, :], shaped(psum.bank("a_f"), 2, T), ACT.Sigmoid)
                A_(a.k[:, :, :], shaped(psum.bank("a_f"), 2, T), ACT.Sigmoid, scale=-1.0).then_inc(*psum.freed("a_f"))
                act.drain().then_inc(S["af_sig"], 1)
                drain_bank("a_i", a.vT[:, :, :], "v_T")
                drain_bank("a_g", a.gate[:, :, :], "gate_th", func=ACT.Tanh, scale=0.5)
                drain_bank("b_v", bb.vT[:, :, :], "v_T")
                drain_bank("code", code[0:16, :], "code", slice(0, 16), slice(0, T))
                act.wait_ge(*psum.filled("b_g"))
                A_(bb.gate[:, :, :], shaped(psum.bank("b_g"), 2, T), ACT.Tanh, scale=0.5).then_inc(S["bg_th"], 1)
                drain_bank("c_q", cT[:, 0:2, :], "mla_c")
                act.wait_ge(*psum.filled("c_kvr"))
                A_(cT[:, 2, :], psum.bank("c_kvr")[:, 0:T], ACT.Copy)
                A_(kr[64:96, :], psum.bank("c_kvr")[64:96, T:2 * T], ACT.Copy).then_inc(*psum.freed("c_kvr"))
                act.drain().then_inc(S["mla_c"], 1)
                act.wait_ge(*psum.filled("d_z"))
                A_(oD.gate[:, :, :], shaped(psum.bank("d_z"), 2, T), ACT.Tanh, scale=0.5).then_inc(S["dz_th"], 1)

                act.wait_ge(S["af_f"], 1)
                A_(a.lf[:, :, :], a.lf[:, :, :], ACT.Ln)
                A_(a.b[:, :, :], a.b[:, :, :], ACT.Ln, scale=2.0 ** 40).then_inc(S["af_ln"], 1)
                act.wait_ge(S["gk_abs"], 1)
                step(A_(bb.e2[:, :, :], bb.e2[:, :, :], ACT.Exp, scale=-1.0))
                A_(bb.e2[:, :, :], bb.e2[:, :, :], ACT.Ln, bias=C("ones")[:, 0:1]).then_inc(S["gk_ln"], 1)
                for m, g in enumerate((a, bb)):
                    gla(g, m)
                    post_norm(g, m, g.name + "_ss", step)

                act.wait_ge(S["gla_done"], 1)
                A_(crs[:, :, :], cT[:, 0:2, :], ACT.Square)
                A_(rtmp[:, 0, :], cT[:, 2, :], ACT.Square).then_inc(S["mla_sq"], 1)
                act.wait_ge(*psum.filled("c_ss"))
                A_(crs[:, 0, :], psum.bank("c_ss")[:, 0:T], ACT.Ln, bias=C("eps"), scale=1.0 / 256)
                A_(crs[:, 1, :], psum.bank("c_ss")[:, T:2 * T], ACT.Ln, bias=C("eps"), scale=1.0 / 128).then_inc(*psum.freed("c_ss"))
                act.drain()
                A_(crs[:, :, :], crs[:, :, :], ACT.Exp, scale=-0.5).then_inc(S["mla_rstd"], 1)
                for j in range(2):
                    act.wait_ge(*psum.filled(f"qT{j}"))
                    A_(qT[0:96, 2 * j:2 * j + 2, :], shaped(psum.bank(f"qT{j}"), 2, T)[0:96], ACT.Copy).then_inc(*psum.freed(f"qT{j}"))
                    act.drain().then_inc(S["rot_in"], 1)
                drain_bank("c_v", vtokC[:, :, :], "mla_v")
                for t in range(NT):
                    n = P * (t + 1)
                    act.wait_ge(S["scores_max"], t + 1)
                    for h in range(4):
                        last = A_(Pr[:, h, 0:n], L[:, h, 0:n], ACT.Exp, bias=stat[:, 16 + 4 * t + h:17 + 4 * t + h],
                                  accum_out=stat[:, 24 + 4 * t + h:25 + 4 * t + h])
                    act.drain().then_inc(S["exps"], 1)
                for t, kt in ((0, 0), (1, 0), (1, 1)):
                    name = f"c_pt{t}{kt}"
                    drain_bank(name, PT[:, kt, :, t * P:(t + 1) * P], "PT")
                drain_bank("c_o", mixT[:, 4:6, :], "mixT")

                act.wait_ge(S["conv"], 1)
                A_(cth[:, :, :], cv[:, :, :], ACT.Tanh, scale=0.5).then_inc(S["conv_th"], 1)
                act.wait_ge(S["conv_silu"], 1)
                A_(cth[:, 0:4, :], cv[:, 0:4, :], ACT.Square).then_inc(S["l2_sq"], 1)
                for j in range(2):
                    act.wait_ge(*psum.filled(f"l2_{j}"))
                    A_(lrs[:, 2 * j:2 * j + 2, :], shaped(psum.bank(f"l2_{j}"), 2, T), ACT.Ln, bias=C("eps")).then_inc(*psum.freed(f"l2_{j}"))
                act.drain()
                A_(lrs[:, :, :], lrs[:, :, :], ACT.Exp, scale=-0.5).then_inc(S["l2_rstd"], 1)
                act.wait_ge(S["ba_in"], 1)
                A_(sm["beta"][:, :, :], zb[:, :, 0:4], ACT.Tanh, scale=0.5)
                step(A_(sm["l"][:, :, :], sm["e"][:, :, :], ACT.Exp, scale=-1.0))
                A_(sm["l"][:, :, :], sm["l"][:, :, :], ACT.Ln, bias=C("ones")[:, 0:1]).then_inc(S["ba_exp"], 1)
                act.wait_ge(S["b_small"], 1)
                A_(sm["eb"][:, :, :], sm["b"][:, :, :], ACT.Exp)
                A_(sm["fd"][:, :, :], sm["bl"][:, :, :], ACT.Exp).then_inc(S["b_exp"], 1)
                act.wait_ge(S["qk_norm"], 1)
                for j in range(2):
                    name = f"brow{j}"
                    act.wait_ge(*psum.filled(name))
                    A_(erow[:, 4 * j:4 * j + 4, :], shaped(psum.bank(name), 4, P), ACT.Exp)
                act.drain().then_inc(S["erow"], 1)
                act.wait_ge(S["hid"], 1)
                for par_ in range(2):
                    for t in range(NT):
                        for hp in range(2):
                            h, e = 2 * hp + par_, 4 * par_ + 2 * t + hp
                            A_(lstr[:, e, :], lstr[:, e, :], ACT.Exp, scale=-1.0, bias=sm["b"][:, t, h:h + 1])
                            last = A_(lincT[:, e, :], lincT[:, e, :], ACT.Exp, bias=sm["nb"][:, t, h:h + 1])
                last.then_inc(S["decays"], 1)
                for j in range(2):
                    drain_bank(f"nt{j}", NTm[:, 4 * j:4 * j + 4, :], "nt")
                for n in range(1, 6):
                    for j in range(2):
                        drain_bank(f"X{n}_{j}", Xm[:, 4 * j:4 * j + 4, :], "level_X")
                drain_bank("u", uD[:, :, :], "uw")
                drain_bank("wT", wT[:, :, :], "uw")
                post_norm(oD, 2, "D_ss", step)

                def y_stats(k, names):
                    for i, name in enumerate(names):
                        act.wait_ge(*psum.filled(name))
                        A_(ysq[:, 0:512], psum.bank(name), ACT.Square, accum_out=stat[:, 40 + i:41 + i])
                        act.drain()
                    act.drain().then_inc(S["y_ss"], 1)
                    act.wait_ge(S["y_sum"], k + 1)
                    step(A_(stat[:, 46:48], stat[:, 44:46], ACT.Ln, bias=C("eps"), scale=1.0 / DM))
                    A_(stat[:, 48:50], stat[:, 46:48], ACT.Exp, scale=-0.5).then_inc(S["y_rstd"], 1)

                y_stats(0, [f"mix{half}{t}" for half in range(2) for t in range(NT)])
                act.wait_ge(S["x_new"], 1)
                norm_stats(1, step)
                norm_gain(1, "pre_ffn")
                for j in range(FT):
                    act.wait_ge(*psum.filled(f"ff{j}"))
                    if j >= 2:
                        act.wait_ge(S["ff_conv"], j - 1)
                    A_(gpad[:, j % 2, 2:2 + T], psum.bank(f"ff{j}")[:, 0:T], ACT.Copy).then_inc(S["ff_gate"], 1)
                    act.wait_ge(S["ff_conv"], j + 1)
                    A_(gcv[:, j % 2, 2, :], gcv[:, j % 2, 1, :], ACT.Gelu_apprx_tanh).then_inc(S["ff_gelu"], 1)
                y_stats(1, [f"y{i}" for i in (0, 2, 1, 3)])
                act.drain().then_inc(layer_done, 1)
                act.wait_ge(layer_open, layer + 1)

        @block.vector
        def _(dve):
            V = nc.vector

            def wide_of(col, n):
                return col.broadcast_to([P, n])

            def norm(k, gain, step):
                dve.wait_ge(S["rstd"], k + 1)
                for t in range(NT):
                    last = V.tensor_scalar(xn[:, t, :], x[:, t, :], stat[:, 4 + t:5 + t], None, ALU.mult)
                last.then_inc(S["normed"], 1)
                for j in (0, 2):
                    name = f"hT{k}_{j}"
                    dve.wait_ge(*psum.filled(name))
                    for i in range(2):
                        last = V.tensor_scalar(hT[:, 2 * j + i, :], psum.bank(name)[:, i * T:(i + 1) * T],
                                               PAR(gain, 2 * j + i), None, ALU.mult)
                    last.then_inc(*psum.freed(name))
                    dve.drain().then_inc(S["hT"], 1)

            def silu_gate(g, name, signal, step):
                dve.wait_ge(S[signal], 1)
                ins = V.scalar_tensor_tensor(g.gate[:, :, :], g.gate[:, :, :], 1.0, shaped(psum.bank(name), 2, T), ALU.add, ALU.mult)
                ins.then_inc(*psum.freed(name))
                dve.drain()
                step(V.tensor_scalar(g.gate[:, :, :], g.gate[:, :, :], 0.5, None, ALU.mult))

            def gla(g, m, step):
                R = g.R
                flat = "p r (s c) -> p (r s) c"
                for r in range(R):
                    last = V.tensor_tensor_scan(g.b[:, r, :], C("restart"), g.lf[:, r, :], 0.0, ALU.mult, ALU.add)
                last.then_inc(S["scan"], 1)
                dve.wait_ge(S["scan"], m + 1)
                b4 = g.b.rearrange(flat, c=SUB)
                V.tensor_tensor(g.e2.rearrange(flat, c=SUB), b4,
                                b4[:, :, SUB - 1:SUB].broadcast_to([P, R * NSUB, SUB]), ALU.subtract).then_inc(S["scan_end"], 1)
                dve.wait_ge(S["exp_b"], m + 1)
                V.tensor_tensor(g.qe, g.q, g.eb, ALU.mult).then_inc(S["q_decayed"], 1)
                dve.wait_ge(S["kd_exp"], m + 1)
                V.tensor_tensor(g.kd, g.k, g.e2, ALU.mult).then_inc(S["kdT"], 1)
                name = g.name + "_kdt"
                dve.wait_ge(*psum.filled(name))
                V.tensor_copy(g.kdtok, shaped(psum.bank(name)[:, 0:NT * R * P], NT, R * P)).then_inc(*psum.freed(name))
                dve.drain().then_inc(S["kd_tok"], 1)
                dve.wait_ge(S["vtok"], m + 1)
                for t in range(NT):
                    last = V.tensor_tensor(vexp[:, t, :, :], g.vtok[:, t:t + 1, :].broadcast_to([P, SUBP, GW]),
                                           C("sub").unsqueeze(2).broadcast_to([P, SUBP, GW]), ALU.mult)
                last.then_inc(S["vexp"], 1)
                V.memset(g.S[:, :, 0, :], 0.0)
                dve.drain()
                for s in range(NSUB - 1):
                    t = s // SUBP
                    for r in range(R):
                        name = f"{g.name}_G{r}{t}"
                        if s % SUBP == 0:
                            dve.wait_ge(*psum.filled(name))
                        ins = V.scalar_tensor_tensor(g.S[:, r, s + 1, :], g.S[:, r, s, :], g.eb[:, r, SUB * s + SUB - 1:SUB * s + SUB],
                                                     shaped(psum.bank(name), SUBP, HD)[:, s % SUBP, :], ALU.mult, ALU.add)
                        if s % SUBP == SUBP - 1 or s == NSUB - 2:
                            ins.then_inc(*psum.freed(name))
                            dve.drain()
                        elif r == R - 1:
                            step(ins)
                dve.drain().then_inc(S["state"], 1)
                for p in range(2):
                    name = f"{g.name}_o{p}"
                    dve.wait_ge(*psum.filled(name))
                    V.tensor_copy(g.oT[:, p, :], psum.bank(name)[:, 0:T]).then_inc(*psum.freed(name))

                def view(kind, i, n):
                    return band[kind][:, i % 2, 0:n * NSUB * (SUB - i)].rearrange("p (a c) -> p a c", c=SUB - i)

                def apply(i):
                    name, n = f"{g.name}_band{i}", 2 * NSUB * (SUB - i)
                    dve.wait_ge(*psum.filled(name))
                    V.tensor_tensor(view("o", i, 2), psum.bank(name)[:, 0:n].rearrange("p (a c) -> p a c", c=SUB - i),
                                    shifted(g.vT, i), ALU.mult).then_inc(*psum.freed(name))
                    dve.drain()
                    V.tensor_tensor(bands(g.oT, i), bands(g.oT, i), view("o", i, 2), ALU.add)

                for i in range(SUB + 1):
                    n = SUB * m + i
                    if i < SUB:
                        V.tensor_tensor(view("diff", i, R), bands(g.b, i), shifted(g.b, i), ALU.subtract).then_inc(S["diff"], 1)
                    if i > 0:
                        dve.wait_ge(S["decay"], n)
                        dve.wait_ge(S["qk"], n)
                        V.tensor_tensor(view("w", i - 1, R), view("qk", i - 1, R), view("exp", i - 1, R), ALU.mult).then_inc(S["weighted"], 1)
                    if i > 1:
                        apply(i - 2)
                apply(SUB - 1)
                dve.drain().then_inc(S["oT_ready"], 1)

            def head_out(g, n, gain, tile):
                dve.wait_ge(S["o_rstd"], n + 1)
                V.tensor_tensor(g.oT, g.oT, g.rs, ALU.mult)
                dve.drain()
                V.scalar_tensor_tensor(mixT[:, tile:tile + 2, :], g.oT, PAR(gain), g.gate, ALU.mult, ALU.mult)
                dve.drain().then_inc(S["mixT"], 1)

            def residual(k, names, gain, step):
                dve.wait_ge(S["y_ss"], k + 1)
                V.tensor_tensor(stat[:, 44:46], stat[:, 40:42], stat[:, 42:44], ALU.add).then_inc(S["y_sum"], 1)
                dve.wait_ge(S["y_rstd"], k + 1)
                lo = PAR1[gain][0]
                for i, name in enumerate(names):
                    half, t = i // 2, i % 2
                    V.scalar_tensor_tensor(yn[:, i, :], psum.bank(name), stat[:, 48 + t:49 + t],
                                           par[:, lo + 512 * half:lo + 512 * half + 512], ALU.mult, ALU.mult).then_inc(*psum.freed(name))
                dve.drain()
                for i in range(4):
                    half, t = i // 2, i % 2
                    xs = x[:, t, 512 * half:512 * half + 512]
                    V.tensor_tensor(xs, xs, yn[:, i, :], ALU.add)
                dve.drain().then_inc(S["x_new"], 1)

            V.memset(cin[:, :, 0:3], 0.0)
            V.memset(gpad[:, :, 0:2], 0.0)
            with dve.Fori(0, DEPTH) as layer:
                step = Chain(dve, S["dve"])
                dve.wait_ge(once, 16)
                dve.wait_ge(S["params"], 64)
                a, bb = G["A"], G["B"]
                lg = shaped(PAR("lb_logits"), 2, DEPTH)
                step(V.tensor_reduce(lb[:, 8:10], lg, AX.X, ALU.max))
                V.tensor_tensor(shaped(lb[:, 0:4], 2, DEPTH), lg, lb[:, 8:10].unsqueeze(2).broadcast_to([P, 2, DEPTH]),
                                ALU.subtract).then_inc(S["lb_max"], 1)
                norm(0, "pre_mix", step)
                dve.wait_ge(S["lb_exp"], 1)
                step(V.tensor_reduce(lb[:, 8:10], shaped(lb[:, 0:4], 2, DEPTH), AX.X, ALU.add))
                step(V.tensor_tensor(lb[:, 0:4], lb[:, 0:4], PAR("lb_of"), ALU.mult))
                V.tensor_reduce(lb[:, 10:12], shaped(lb[:, 0:4], 2, DEPTH), AX.X, ALU.add)
                step(V.reciprocal(lb[:, 12:14], lb[:, 8:10]))
                step(V.tensor_tensor(lb[:, 14:16], lb[:, 10:12], lb[:, 12:14], ALU.mult))
                step(V.tensor_scalar(lb[:, 16:18], lb[:, 14:16], -1.0, 1.0, ALU.mult, ALU.add))
                lower, rest = lb[:, 14:16], lb[:, 16:18]

                dve.wait_ge(S["aq_tanh"], 1)
                ins = V.scalar_tensor_tensor(a.q, a.q, 1.0, shaped(psum.bank("a_q"), 2, T), ALU.add, ALU.mult)
                ins.then_inc(*psum.freed("a_q"))
                dve.drain()
                V.tensor_scalar(a.q, a.q, 0.5 * HD ** -0.5, None, ALU.mult)
                dve.wait_ge(S["af_sig"], 1)
                for r in range(2):
                    V.tensor_scalar(a.k[:, r, :], a.k[:, r, :], rest[:, r:r + 1], None, ALU.mult)
                    last = V.tensor_scalar(a.lf[:, r, :], a.lf[:, r, :], rest[:, r:r + 1], lower[:, r:r + 1], ALU.mult, ALU.add)
                step(last)
                step(V.tensor_scalar(a.b, a.lf, 1e-30, 2.0 ** -40, ALU.max, ALU.min))
                V.tensor_scalar(a.lf, a.lf, 2.0 ** -40, None, ALU.max).then_inc(S["af_f"], 1)
                dve.wait_ge(S["gate_th"], 1)
                V.tensor_scalar(a.gate, a.gate, 0.5, 0.5, ALU.mult, ALU.add)
                dve.wait_ge(*psum.filled("b_qk"))
                V.tensor_scalar(bb.q[:, 0, :], psum.bank("b_qk")[:, 0:T], 32 ** -0.5, None, ALU.mult)
                V.tensor_copy(bb.k[:, 0, :], psum.bank("b_qk")[:, T:2 * T]).then_inc(*psum.freed("b_qk"))
                silu_gate(bb, "b_g", "bg_th", step)
                for i, name in enumerate(("d_q", "d_k")):
                    dve.wait_ge(*psum.filled(name))
                    V.tensor_copy(cin[:, 2 * i:2 * i + 2, 3:3 + T], shaped(psum.bank(name), 2, T)).then_inc(*psum.freed(name))
                dve.wait_ge(*psum.filled("d_v"))
                V.tensor_copy(cin[:, 4:6, 3:3 + T], shaped(psum.bank("d_v"), 2, T)).then_inc(*psum.freed("d_v"))
                dve.wait_ge(*psum.filled("d_ba"))
                V.tensor_copy(zb, shaped(psum.bank("d_ba")[:, 0:16], NT, 8)).then_inc(*psum.freed("d_ba"))
                silu_gate(oD, "d_z", "dz_th", step)

                dve.wait_ge(S["af_ln"], 1)
                step(V.tensor_tensor(a.lf, a.b, a.lf, ALU.add))
                dve.wait_ge(*psum.filled("gk"))
                V.tensor_scalar(bb.lf[:, 0, :], psum.bank("gk")[:, 0:T], PAR("b_gk"), None, ALU.add).then_inc(*psum.freed("gk"))
                dve.drain()
                V.scalar_tensor_tensor(bb.e2, bb.lf, -1.0, bb.lf, ALU.mult, ALU.max).then_inc(S["gk_abs"], 1)
                step(V.tensor_scalar(bb.lf, bb.lf, 0.0, None, ALU.min))
                dve.wait_ge(S["gk_ln"], 1)
                step(V.tensor_tensor(bb.lf, bb.lf, bb.e2, ALU.subtract))
                step(V.tensor_scalar(bb.lf, bb.lf, 1.0 / 16.0, None, ALU.mult))

                for m, g in enumerate((a, bb)):
                    gla(g, m, step)
                    head_out(g, m, ("hgrn_norm", "gla_norm")[m], 2 * m)
                dve.drain().then_inc(S["gla_done"], 1)

                dve.wait_ge(S["mla_rstd"], 1)
                for i in range(3):
                    gain = PAR("q_norm", i) if i < 2 else PAR("kv_norm")
                    last = V.scalar_tensor_tensor(cn[:, i, :], cT[:, i, :], gain, crs[:, i // 2, :], ALU.mult, ALU.mult)
                last.then_inc(S["mla_cn"], 1)
                cos, sin = C("cos96"), C("sin96")
                dve.wait_ge(*psum.filled("kr_rot"))
                V.tensor_tensor(rtmp[64:96, 1, :], psum.bank("kr_rot")[64:96, 0:T], sin[64:96, :], ALU.mult).then_inc(*psum.freed("kr_rot"))
                step(V.tensor_tensor(rtmp[64:96, 2, :], kr[64:96, :], cos[64:96, :], ALU.mult))
                V.tensor_tensor(kT[64:96, :, :], rtmp[64:96, 1:2, :].broadcast_to([32, 4, T]),
                                rtmp[64:96, 2:3, :].broadcast_to([32, 4, T]), ALU.add).then_inc(S["kr_done"], 1)
                for j in range(2):
                    name = f"kT{j}"
                    dve.wait_ge(*psum.filled(name))
                    V.tensor_copy(kT[0:64, 2 * j:2 * j + 2, :], shaped(psum.bank(name), 2, T)[0:64]).then_inc(*psum.freed(name))
                    dve.drain().then_inc(S["kT"], 1)
                for j in range(2):
                    name = f"rot{j}"
                    dve.wait_ge(*psum.filled(name))
                    V.tensor_tensor(rtmp[0:96, 2 * j:2 * j + 2, :], shaped(psum.bank(name), 2, T)[0:96],
                                    sin[0:96, :].unsqueeze(1).broadcast_to([96, 2, T]), ALU.mult).then_inc(*psum.freed(name))
                step(V.tensor_tensor(qT[0:96], qT[0:96], cos[0:96, :].unsqueeze(1).broadcast_to([96, 4, T]), ALU.mult))
                V.tensor_tensor(qT[0:96], qT[0:96], rtmp[0:96], ALU.add).then_inc(S["qT"], 1)
                mask = shaped(C("causal"), NT, T)
                for t in range(NT):
                    n = P * (t + 1)
                    if t:
                        dve.wait_ge(S["exps"], t)
                    for j in range(2):
                        name = f"c_sc{t}{j}"
                        dve.wait_ge(*psum.filled(name))
                        V.scalar_tensor_tensor(L[:, 2 * j:2 * j + 2, 0:n], shaped(psum.bank(name)[:, 0:2 * n], 2, n), 96 ** -0.5,
                                               mask[:, t:t + 1, 0:n].broadcast_to([P, 2, n]), ALU.mult, ALU.add).then_inc(*psum.freed(name))
                    dve.drain()
                    step(V.tensor_reduce(stat[:, 32:36], L[:, :, 0:n], AX.X, ALU.max))
                    V.tensor_scalar(stat[:, 16 + 4 * t:20 + 4 * t], stat[:, 32:36], -1.0, None, ALU.mult).then_inc(S["scores_max"], 1)
                    dve.wait_ge(S["exps"], t + 1)
                    step(V.reciprocal(stat[:, 36:40], stat[:, 24 + 4 * t:28 + 4 * t]))
                    V.tensor_tensor(Pr[:, :, 0:n], Pr[:, :, 0:n], stat[:, 36:40].unsqueeze(2).broadcast_to([P, 4, n]), ALU.mult)
                    dve.drain().then_inc(S["probs"], 1)
                    dve.wait_ge(*psum.filled(f"c_pt{t}{t}"))
                dve.wait_ge(S["mixT"], 3)

                w = shaped(PAR("conv"), 6, 4)
                for r in range(6):
                    V.tensor_scalar(cv[:, r, :], cin[:, r, 3:3 + T], w[:, r, 3:4], None, ALU.mult)
                for i in range(3):
                    dve.drain()
                    for r in range(6):
                        V.scalar_tensor_tensor(cv[:, r, :], cin[:, r, i:i + T], w[:, r, i:i + 1], cv[:, r, :], ALU.mult, ALU.add)
                dve.drain().then_inc(S["conv"], 1)
                V.tensor_tensor(sm["x"], zb[:, :, 4:8], PAR("dt_bias").unsqueeze(1).broadcast_to([P, NT, 4]), ALU.add)
                dve.drain()
                V.scalar_tensor_tensor(sm["e"], sm["x"], -1.0, sm["x"], ALU.mult, ALU.max)
                dve.drain().then_inc(S["ba_in"], 1)
                dve.wait_ge(S["conv_th"], 1)
                step(V.tensor_scalar(cth, cth, 0.5, 0.5, ALU.mult, ALU.add))
                V.tensor_tensor(cv, cv, cth, ALU.mult).then_inc(S["conv_silu"], 1)
                dve.wait_ge(S["ba_exp"], 1)
                V.tensor_scalar(sm["beta"], sm["beta"], 0.5, 0.5, ALU.mult, ALU.add)
                step(V.scalar_tensor_tensor(sm["g"], sm["x"], 0.0, sm["l"], ALU.max, ALU.add))
                V.scalar_tensor_tensor(sm["g"], sm["g"], -1.0, ea.unsqueeze(1).broadcast_to([P, NT, 4]), ALU.mult, ALU.mult).then_inc(S["g_ready"], 1)
                dve.wait_ge(S["l2_rstd"], 1)
                V.scalar_tensor_tensor(cv[:, 0:2, :], cv[:, 0:2, :], HD ** -0.5, lrs[:, 0:2, :], ALU.mult, ALU.mult)
                V.tensor_tensor(cv[:, 2:4, :], cv[:, 2:4, :], lrs[:, 2:4, :], ALU.mult)
                dve.drain().then_inc(S["qk_norm"], 1)
                dve.wait_ge(*psum.filled("bsum"))
                bs = psum.bank("bsum")
                V.tensor_copy(sm["b"], shaped(bs[:, 0:8], NT, 4))
                V.tensor_copy(sm["x"], shaped(bs[:, 8:16], NT, 4)).then_inc(*psum.freed("bsum"))
                dve.drain()
                V.tensor_scalar(sm["nb"], sm["b"], -1.0, None, ALU.mult)
                V.tensor_tensor(sm["bl"], sm["x"], sm["b"], ALU.subtract)
                dve.drain().then_inc(S["b_small"], 1)
                dve.wait_ge(S["b_exp"], 1)
                step(V.tensor_tensor(sm["be"], sm["beta"], sm["eb"], ALU.mult))
                dve.wait_ge(S["erow"], 1)
                for j in range(2):
                    name = f"brow{j}"
                    brow = shaped(psum.bank(name), 4, P)
                    V.tensor_tensor(lstr[:, 4 * j:4 * j + 4, :], brow, C("hide_strict").unsqueeze(1).broadcast_to([P, 4, P]), ALU.add)
                    V.tensor_tensor(lincT[:, 4 * j:4 * j + 4, :], brow, C("hide_incl").unsqueeze(1).broadcast_to([P, 4, P]), ALU.add).then_inc(*psum.freed(name))
                dve.drain().then_inc(S["hid"], 1)
                V.memset(SD[:, 0], 0.0)
                dve.drain().then_inc(S["state_D"], 1)

                def per_head(sc):
                    return sc.rearrange("p t h -> p (t h)").unsqueeze(2).broadcast_to([P, 8, HD])

                def by_head(tok):
                    return tok.rearrange("p t (h d) -> p (t h) d", d=HD)

                dve.wait_ge(*psum.filled("k_tok"))
                V.tensor_copy(ktok, shaped(psum.bank("k_tok"), NT, GW)).then_inc(*psum.freed("k_tok"))
                dve.wait_ge(*psum.filled("v_tok"))
                V.tensor_copy(vtokD, shaped(psum.bank("v_tok"), NT, GW)).then_inc(*psum.freed("v_tok"))
                dve.drain()
                V.tensor_tensor(by_head(kbe), by_head(ktok), per_head(sm["be"]), ALU.mult)
                V.tensor_tensor(by_head(kdec), by_head(ktok), per_head(sm["fd"]), ALU.mult)
                V.tensor_tensor(by_head(vb), by_head(vtokD), per_head(sm["beta"]), ALU.mult)
                dve.drain().then_inc(S["tok_D"], 1)
                for par_ in range(2):
                    rows = slice(HD * par_, HD * par_ + HD)
                    ev = erow[:, :, :].rearrange("p (q t h) c -> p q h t c", q=2, t=NT)
                    for hp in range(2):
                        V.tensor_tensor(qeD[rows, hp, :].rearrange("p (t c) -> p t c", t=NT), cv[rows, hp, :].rearrange("p (t c) -> p t c", t=NT),
                                        ev[rows, par_, hp, :, :], ALU.mult)
                dve.drain().then_inc(S["qe"], 1)
                dve.wait_ge(S["decays"], 1)
                for par_ in range(2):
                    name = f"kk{par_}"
                    dve.wait_ge(*psum.filled(name))
                    for t in range(NT):
                        for hp in range(2):
                            h, i = 2 * hp + par_, 2 * t + hp
                            e = 4 * par_ + i
                            last = V.scalar_tensor_tensor(lstr[:, e, :], psum.bank(name)[:, i * P:(i + 1) * P], sm["beta"][:, t, h:h + 1],
                                                          lstr[:, e, :], ALU.mult, ALU.mult)
                    last.then_inc(*psum.freed(name))
                dve.drain().then_inc(S["lmat"], 1)
                for par_ in range(2):
                    name = f"kq{par_}"
                    dve.wait_ge(*psum.filled(name))
                    V.tensor_tensor(lincT[:, 4 * par_:4 * par_ + 4, :], shaped(psum.bank(name), 4, P),
                                    lincT[:, 4 * par_:4 * par_ + 4, :], ALU.mult).then_inc(*psum.freed(name))

                lvl = shaped(C("level"), 7, P)

                def eight_of(m):
                    return m.unsqueeze(1).broadcast_to([P, 8, P])

                V.tensor_tensor(Tm, lstr, eight_of(lvl[:, 6, :]), ALU.mult)
                dve.wait_ge(S["nt"], 2)
                V.tensor_tensor(Um, NTm, eight_of(lvl[:, 0, :]), ALU.mult)
                dve.drain()
                V.tensor_tensor(Tm, eight_of(C("ident")), Tm, ALU.subtract)
                V.tensor_tensor(Um, eight_of(C("ident")), Um, ALU.subtract)
                V.tensor_tensor(pm, NTm, eight_of(lvl[:, 1, :]), ALU.mult)
                dve.drain().then_inc(S["level_T"], 1)
                for n in range(1, 6):
                    for what, m in (("TX", Tm), ("UX", Um)):
                        if what == "TX" and n == 5:
                            continue
                        for j in range(2):
                            name = f"{what}{n}_{j}"
                            dve.wait_ge(*psum.filled(name))
                            if what == "TX" and j == 0:
                                dve.wait_ge(*psum.filled(f"UX{n}_1"))
                            if n == 5 and j == 0:
                                dve.wait_ge(*psum.filled(f"UX{n}_1"))
                            mj = m[:, 4 * j:4 * j + 4, :]
                            V.tensor_tensor(mj, mj, shaped(psum.bank(name), 4, P), ALU.subtract).then_inc(*psum.freed(name))
                    if n < 5:
                        V.tensor_tensor(pm, NTm, eight_of(lvl[:, n + 1, :]), ALU.mult)
                    dve.drain().then_inc(S["level_T"], 1)

                dve.wait_ge(S["uw"], 2)
                for c in range(4):
                    t, tok0 = c // 2, CHUNK * (c % 2)
                    toks = slice(tok0, tok0 + CHUNK)
                    for par_ in range(2):
                        name = f"ws{c}{par_}"
                        dve.wait_ge(*psum.filled(name))
                        hv = "p (h q d) -> p q h d"
                        un, vn = (z[toks, t, :].rearrange(hv, q=2, d=HD)[:, par_] for z in (uD, vnew))
                        V.tensor_tensor(vn, un, shaped(psum.bank(name)[:, 0:P], 2, HD)[toks], ALU.subtract).then_inc(*psum.freed(name))
                    dve.drain().then_inc(S["v_new"], 1)
                    if c < 3:
                        name = f"su{c}"
                        dve.wait_ge(*psum.filled(name))
                        for par_ in range(2):
                            rows = slice(HD * par_, HD * par_ + HD)
                            for hp in range(2):
                                e = 4 * par_ + 2 * t + hp
                                last = V.scalar_tensor_tensor(SD[rows, c + 1, hp, :], SD[rows, c, hp, :], erow[rows, e, tok0 + CHUNK - 1:tok0 + CHUNK],
                                                              psum.bank(name)[rows, hp * HD:(hp + 1) * HD], ALU.mult, ALU.add)
                        last.then_inc(*psum.freed(name))
                        dve.drain().then_inc(S["state_D"], 1)
                dve.wait_ge(*psum.filled("D_o"))
                V.tensor_copy(oD.oT, shaped(psum.bank("D_o"), 2, T)).then_inc(*psum.freed("D_o"))
                dve.wait_ge(*psum.filled("D_o2"))
                dve.drain()
                V.tensor_tensor(oD.oT, oD.oT, shaped(psum.bank("D_o2"), 2, T), ALU.add).then_inc(*psum.freed("D_o2"))
                dve.drain().then_inc(S["oT_ready"], 1)
                head_out(oD, 2, "gdn_norm", 6)

                residual(0, [f"mix{half}{t}" for half in range(2) for t in range(NT)], "post_mix", step)
                norm(1, "pre_ffn", step)

                fw = shaped(PAR("ffn_conv"), FT, 3)

                def finish(j):
                    dve.wait_ge(S["ff_gelu"], j + 1)
                    V.tensor_tensor(gT[:, j, :], gcv[:, j % 2, 2, :], psum.bank(f"ff{j}")[:, T:2 * T], ALU.mult).then_inc(*psum.freed(f"ff{j}"))
                    dve.drain().then_inc(S["gT"], 1)

                V.memset(gpad[:, :, 0:2], 0.0)
                dve.drain().then_inc(S["gpad_zero"], 1)
                for j in range(FT):
                    dve.wait_ge(S["ff_gate"], j + 1)
                    step(V.tensor_scalar(gcv[:, j % 2, 0, :], gpad[:, j % 2, 2:2 + T], fw[:, j, 2:3], None, ALU.mult))
                    step(V.scalar_tensor_tensor(gcv[:, j % 2, 1, :], gpad[:, j % 2, 1:1 + T], fw[:, j, 1:2], gcv[:, j % 2, 0, :], ALU.mult, ALU.add))
                    V.scalar_tensor_tensor(gcv[:, j % 2, 1, :], gpad[:, j % 2, 0:T], fw[:, j, 0:1], gcv[:, j % 2, 1, :], ALU.mult, ALU.add).then_inc(S["ff_conv"], 1)
                    if j:
                        finish(j - 1)
                finish(FT - 1)
                residual(1, [f"y{i}" for i in (0, 2, 1, 3)], "post_ffn", step)
                dve.drain().then_inc(layer_done, 1)
                dve.wait_ge(layer_open, layer + 1)

        @block.gpsimd
        def _(pool):
            with pool.Fori(0, DEPTH) as layer:
                for m, g in enumerate((G["A"], G["B"])):
                    pool.wait_ge(S["state"], m + 1)
                    for i in range(SUB):
                        n = SUB * m + i
                        if n >= 2:
                            pool.wait_ge(S["weighted"], n - 1)
                        out = band["qk"][:, i % 2, 0:g.R * NSUB * (SUB - i)].rearrange("p (a c) -> p a c", c=SUB - i)
                        nc.gpsimd.tensor_tensor(out, bands(g.q, i), shifted(g.k, i), ALU.mult).then_inc(S["qk"], 1)
                pool.wait_ge(layer_done, 3 * layer + 3)
                pool.sem_inc(barrier_taken, 1)
                for r in sem_ranges([s.num for s in S.values()] + [s.num for s in psum.full + psum.free]):
                    pool.sem_clear(r)
                pool.sem_inc(layer_open, 1)

        psum.check()


D_FF2 = 4096
UT = D_FF2 // P
IDX_HEADS = 8
TOPK = 64
TAKEN = -3e38
TWO_PI = (6.28125, 0.0019350051879882812, 3.0199159819e-07)
BY_PARITY = (0, 2, 1, 3)
CONST2, N_CONST2 = table([
    ("ident", P), ("cum", P), ("ones", P), ("heads64", P), ("rot64", P), ("rot32", P),
    ("causal", NT * T), ("window", NT * T), ("inv_freq", 2), ("eps", 1),
])
PAR2, N_PAR2 = table([
    ("pre_mix", KT), ("pre_mlp", KT), ("subln", 1), ("lam_q", 64), ("lam_k", 64), ("b_forget", 4),
    ("sinks", 4), ("lam_init", 1), ("lam_rest", 1), ("post_mix", DM), ("post_mlp", DM),
])
IN2 = [(0, 512), (512, 1024), (1024, 1352), (1352, 1864), (1864, 2380), (2380, 2892), (2892, 3404)]


def shape_constants2():
    c = np.zeros((P, N_CONST2), np.float32)

    def put(name, a):
        lo, hi = CONST2[name]
        c[:a.shape[0], lo:hi] = a.reshape(a.shape[0], -1)

    i = np.arange(P)
    put("ident", np.eye(P, dtype=np.float32))
    put("cum", (i[:, None] <= i[None, :]).astype(np.float32))
    put("ones", np.ones((P, P), np.float32))
    put("heads64", ((i[:, None] // 64) == (i[None, :] // 64)).astype(np.float32))
    inv = np.zeros((P, 2), np.float32)
    for n, (name, half) in enumerate((("rot64", 32), ("rot32", 16))):
        rot = np.zeros((P, P), np.float32)
        for m in range(P):
            if m % (2 * half) < half:
                rot[m + half, m] = -1.0
            else:
                rot[m - half, m] = 1.0
        put(name, rot)
        f = (np.float32(10000.0) ** (-np.arange(half, dtype=np.float32) / np.float32(half))).astype(np.float32)
        inv[:, n] = f[i % half]
    put("inv_freq", inv)
    key, q = np.arange(T)[None, :], i[:, None]
    put("causal", np.stack([np.where(key <= q + P * t, 0.0, NEG) for t in range(NT)], 1).astype(np.float32))
    put("window", np.stack([np.where((key <= q + P * t) & (q + P * t - key < P), 0.0, NEG) for t in range(NT)], 1).astype(np.float32))
    put("eps", np.full((P, 1), EPS, np.float32))
    return c


def params2(a):
    out = np.zeros((DEPTH, P, N_PAR2), np.float32)

    def put(name, layer, v):
        lo, hi = PAR2[name]
        out[layer, :, lo:hi] = v

    def cols(v):
        return np.asarray(v).reshape(-1, P).T

    def rows(v):
        v = np.asarray(v)
        return np.broadcast_to(v, (P,) + v.shape)

    for l in range(DEPTH):
        lam_init = 0.8 - 0.6 * float(np.exp(-0.3 * l))
        put("pre_mix", l, cols(a["norm_pre_mix_2"][l]))
        put("pre_mlp", l, cols(a["norm_pre_mlp_2"][l]))
        put("subln", l, np.concatenate([a["diff_subln_2"][l]] * 2)[:, None])
        put("lam_q", l, rows(np.concatenate([a["lambda_q1_2"][l], a["lambda_q2_2"][l]])))
        put("lam_k", l, rows(np.concatenate([a["lambda_k1_2"][l], a["lambda_k2_2"][l]])))
        put("b_forget", l, rows(a["b_forget_2"][l]))
        put("sinks", l, rows(np.asarray(a["sinks_2"][l])[list(BY_PARITY)]))
        put("lam_init", l, np.float32(lam_init))
        put("lam_rest", l, np.float32(1.0 - lam_init))
        put("post_mix", l, rows(a["norm_post_mix_2"][l]))
        put("post_mlp", l, rows(a["norm_post_mlp_2"][l]))
    return out

SIGNALS2 = """raw hT probs PT nlf normed roped copied o_sq mixT params gT pT_in proj x_new rstd score_max exps
c_oT o_rstd y_ss y_sum y_rstd act lam_sum lam_exp gate_abs gate_ln relu_used relu gates cosined""".split()


def block2(nc, kept, memory, banks, x, A):
    with ExitStack() as ctx:
        buf = Area(memory, MEMORY)

        S = {n: ctx.enter_context(nc.semaphore("b2_" + n)) for n in SIGNALS2}
        psum = Psum(nc, ctx, "b2", banks)
        layer_done = kept.enter_context(nc.semaphore("b2_layer_done"))
        layer_open = kept.enter_context(nc.semaphore("b2_layer_open"))
        barrier_taken = kept.enter_context(nc.semaphore("b2_barrier_taken"))
        once = kept.enter_context(nc.semaphore("b2_constants_in"))
        tables_made = kept.enter_context(nc.semaphore("b2_tables_made"))
        angles = kept.enter_context(nc.semaphore("b2_angles"))

        def cols(src):
            return src.rearrange("l (k p) n -> l p k n", p=P)

        win, wout, wup, wgate = cols(A["w_in_2"]), cols(A["w_out_2"]), cols(A["w_mlp_up_2"]), cols(A["w_ple_gate_2"])
        wdown, wproj = cols(A["w_mlp_down_2"]), cols(A["w_ple_proj_2"])
        panels = [(f"in{i}", lambda l, c0=c0, c1=c1: win[l, :, :, c0:c1], KT, c0, c1) for i, (c0, c1) in enumerate(IN2)]
        panels += [(f"out{i}", lambda l, i=i: wout[l, :, :, 512 * i:512 * i + 512], KT, 0, 512) for i in range(2)]
        panels += [(f"up{i}", lambda l, i=i: wup[l, :, :, 512 * i:512 * i + 512], KT, 0, 512) for i in range(8)]
        panels += [(f"down{i}", lambda l, i=i: wdown[l, :, 4 * i:4 * i + 4, :], 4, 0, DM) for i in range(8)]
        panels += [("proj", lambda l: wproj[l, :, :, :], 2, 0, DM)]
        panels += [(f"ple{i}", lambda l, i=i: wgate[l, :, :, 512 * i:512 * i + 512], KT, 0, 512) for i in range(2)]
        ring = Ring(nc, kept, "b2", panels, buf(SLOTS, KT * PANEL))

        const = buf(N_CONST2)
        par = buf(N_PAR2)

        def C(name, rows=P):
            lo, hi = CONST2[name]
            return const[0:rows, lo:hi]

        def PAR(name, i=None, n=1):
            lo, hi = PAR2[name]
            return par[:, lo:hi] if i is None else par[:, lo + i:lo + i + n]

        hT = buf(KT, T)
        mixT = buf(KT, T)
        stat = buf(128)
        ptok = buf(NT, T)
        pT = buf(2, T)
        positions = buf(T).bitcast(mybir.dt.int32)
        rope = buf(2, 2, T)
        qk = {n: buf(w, T) for n, w in (("a_q", 2), ("a_k", 2), ("a_iq", 4), ("a_ik", 1), ("b_q", 2), ("b_k", 2),
                                           ("c_q", 2), ("c_k", 2), ("d_q", 2), ("d_k", 2))}
        vtok = {n: buf(NT, w) for n, w in (("a_v", GW), ("b_v", GW), ("c_v", GW), ("d_v", P))}
        iw = buf(NT, IDX_HEADS)
        fl = {n: buf(NT, 4) for n in ("x", "e", "n", "cum")}
        lam = buf(80)

        WORK = 16128
        work = buf(WORK)
        area = Area(work, WORK)
        raw, turned = area(2, 2, T), area(2, 2, T)
        LN = 8 * P * 3
        Ls = [area(LN), area(LN)]
        PTs = [area(NT, 4, T), area(NT, 4, T)]
        Dm = area(4 * P * 3)
        sel, acc = [area(P), area(T)], [area(P), area(T)]
        dots = area(2, 512)
        ysq = area(512)
        area.at -= 512 + 1024 + 2 * 3 * P + 4 * P * 3
        oT, osq, ors = area(2, T), area(2, T), area(2, T)
        area.at = 0
        xn = area(NT, DM)
        area.at = 0
        gT = area(UT, T)
        gates, proj = area(4, 512), area(4, 512)
        area.at = NT * DM
        yn = area(4, 512)

        def scores_of(buffer, t, maps):
            n = P * (t + 1)
            lo = maps * P * t
            return buffer[:, lo:lo + maps * n].rearrange("p (e n) -> p e n", n=n)

        IN_USES = [
            ("a_q", "in0", "T", [(0, P, 0, 0), (0, P, 1, 128)]), ("a_k", "in0", "T", [(0, P, 0, 256), (0, P, 1, 384)]),
            ("a_v", "in1", "tok", (512, GW)), ("a_iq0", "in1", "T", [(0, P, 0, 768), (0, P, 1, 896)]),
            ("a_iq1", "in2", "T", [(0, P, 0, 1024), (0, P, 1, 1152)]), ("a_ik", "in2", "T", [(0, 64, 0, 1280), (64, 64, 0, 1280)]),
            ("a_iw", "in2", "tok", (1344, 8)),
            ("b_q", "in3", "T", [(0, P, 0, 1352), (0, P, 1, 1480)]), ("b_k", "in3", "T", [(0, P, 0, 1608), (0, P, 1, 1736)]),
            ("b_v", "in4", "tok", (1864, GW)), ("b_f", "in4", "tok", (2120, 4)),
            ("c_q", "in4", "T", [(0, P, 0, 2124), (0, P, 1, 2252)]),
            ("c_k", "in5", "T", [(0, P, 0, 2380), (0, P, 1, 2508)]), ("c_v", "in5", "tok", (2636, GW)),
            ("d_q", "in6", "T", [(0, P, 0, 2892), (0, P, 1, 3020)]),
            ("d_k", "in6", "T", [(0, 64, 0, 3148), (64, 64, 0, 3148), (0, 64, 1, 3212), (64, 64, 1, 3212)]),
            ("d_v", "in6", "tok", (3276, P)),
        ]
        ROPED = [("a_q", qk["a_q"], 0, 2), ("a_k", qk["a_k"], 0, 2), ("a_iq0", qk["a_iq"][:, 0:2, :], 0, 2),
                 ("a_iq1", qk["a_iq"][:, 2:4, :], 0, 2), ("a_ik", qk["a_ik"], 0, 1), ("c_q", qk["c_q"], 1, 2),
                 ("c_k", qk["c_k"], 1, 2), ("d_q", qk["d_q"], 0, 2), ("d_k", qk["d_k"], 0, 2)]
        ROPED_AT = {r[0]: i for i, r in enumerate(ROPED)}
        ATTENDED = [("b", 4, HD ** -0.5, 2), ("c", 8, 32 ** -0.5, 4), ("d", 4, HD ** -0.5, 6), ("a", 4, HD ** -0.5, 0)]
        block = ctx.enter_context(nc.Block())

        @block.sync
        def _(sp):
            for s in range(SLOTS):
                sp.sem_inc(ring.free[s], 1)
            sp.dma_start(const[:, :], A["const2"]).then_inc(once, 16)
            sp.dma_start(positions[:, :], A["positions_2"][0, :].partition_broadcast(P)).then_inc(once, 16)
            with sp.Fori(0, DEPTH) as layer:
                ring.load_all(sp, layer)

        @block.tensor
        def _(pe):
            used = [None]

            def mm(out, lhsT, rhs, start=True, stop=True):
                ins = nc.tensor.matmul(out, lhsT, rhs, start=start, stop=stop)
                if used[0]:
                    ins.then_inc(*ring.freed(used[0]))
                    used[0] = None
                return ins

            def transpose(out, a):
                return nc.tensor.transpose(out, a, C("ident"))

            def transposes(name, source):
                for j in range(4):
                    b = psum.claim(pe, f"{name}_{j}")
                    for i in range(4):
                        last = transpose(b[:, i * P:(i + 1) * P], source[:, i % 2, (2 * j + i // 2) * P:(2 * j + i // 2 + 1) * P])
                    last.then_inc(psum.full_of(f"{name}_{j}"), 1)

            def turn(i):
                name, _, width, tiles = ROPED[i]
                pe.wait_ge(S["raw"], i + 1)
                b = psum.claim(pe, name + "_rot")
                mm(b[:, 0:tiles * T], C(("rot64", "rot32")[width]), raw[:, i % 2, 0:tiles, :]).then_inc(psum.full_of(name + "_rot"), 1)

            def project(layer):
                pe.wait_ge(S["hT"], 4)
                held, turned_n = None, 0
                for name, panel, kind, parts in IN_USES:
                    if panel != held:
                        used[0], held = held, panel
                        w = ring.wait(pe, layer, panel)
                        base = IN2[int(panel[2:])][0]
                    b = psum.claim(pe, name)
                    if kind == "T":
                        for row0, m, half, c0 in parts:
                            for k in range(KT):
                                last = mm(b[row0:row0 + m, half * T:(half + 1) * T], w[:, k, c0 - base:c0 - base + m],
                                          hT[:, k, :], k == 0, k == KT - 1)
                    else:
                        c0, n = parts
                        for t in range(NT):
                            for k in range(KT):
                                last = mm(b[:, t * n:(t + 1) * n], hT[:, k, t * P:(t + 1) * P], w[:, k, c0 - base:c0 - base + n],
                                          k == 0, k == KT - 1)
                    last.then_inc(psum.full_of(name), 1)
                    while turned_n < len(ROPED) and psum.known(ROPED[turned_n][0]) and ROPED[turned_n][0] != name:
                        turn(turned_n)
                        turned_n += 1
                pe.drain().then_inc(*ring.freed(held))
                for i in range(turned_n, len(ROPED)):
                    turn(i)

            def scores(name):
                size = 32 if name == "c" else HD
                q, k = qk[name + "_q"], qk[name + "_k"]
                for t in range(NT):
                    n = P * (t + 1)
                    for g in range(P // size):
                        b = psum.claim(pe, f"{name}_sc{t}{g}")
                        rows = slice(size * g, size * (g + 1))
                        for hp in range(2):
                            last = mm(b[:, hp * n:(hp + 1) * n], q[rows, hp, t * P:(t + 1) * P], k[rows, hp, 0:n])
                        last.then_inc(psum.full_of(f"{name}_sc{t}{g}"), 1)

            def values(i):
                name, maps, _, _ = ATTENDED[i]
                L, PT = Ls[i % 2], PTs[i % 2]
                for t in range(NT):
                    pe.wait_ge(S["probs"], 2 * i + t + 1)
                    for kt in range(t + 1):
                        b = psum.claim(pe, f"{name}_pt{t}{kt}")
                        for e in range(4):
                            m = e if maps == 4 else 4 * (e // 2) + e % 2
                            last = transpose(b[:, e * P:(e + 1) * P], scores_of(L, t, maps)[:, m, kt * P:(kt + 1) * P])
                        last.then_inc(psum.full_of(f"{name}_pt{t}{kt}"), 1)
                pe.wait_ge(S["PT"], 3 * i + 3)
                b = psum.claim(pe, name + "_o")
                v = vtok[name + "_v"]
                for e, h in enumerate(BY_PARITY):
                    c = HD * (h // 2) if name == "d" else HD * h
                    o = b[HD * (h % 2):HD * (h % 2) + HD, T * (h // 2):T * (h // 2) + T]
                    mm(o, v[:, 0, c:c + HD], PT[:, 0, e, :], True, False)
                    last = mm(o[:, P:T], v[:, 1, c:c + HD], PT[:, 1, e, P:T], False, True)
                last.then_inc(psum.full_of(name + "_o"), 1)

            def forget_sums():
                pe.wait_ge(S["nlf"], 1)
                b = psum.claim(pe, "f_col")
                mm(b[:, 0:4], C("cum"), fl["n"][:, 0, :])
                mm(b[:, 4:8], C("ones"), fl["n"][:, 0, :], True, False)
                mm(b[:, 4:8], C("cum"), fl["n"][:, 1, :], False, True).then_inc(psum.full_of("f_col"), 1)
                for g in range(2):
                    b = psum.claim(pe, f"f_row{g}")
                    for hp in range(2):
                        h = BY_PARITY[2 * g + hp]
                        first, second = (fl["n"][:, t, h:h + 1].broadcast_to([P, P]) for t in range(NT))
                        mm(b[:, hp * T:hp * T + P], first, C("cum"))
                        mm(b[:, hp * T + P:(hp + 1) * T], first, C("ones"), True, False)
                        last = mm(b[:, hp * T + P:(hp + 1) * T], second, C("cum"), False, True)
                    last.then_inc(psum.full_of(f"f_row{g}"), 1)

            def index_dots():
                for t in range(NT):
                    n = P * (t + 1)
                    each = 512 // n
                    for g in range(2):
                        rows = slice(HD * g, HD * (g + 1))
                        for j in range(4 // each):
                            name = f"dots{t}{g}{j}"
                            b = psum.claim(pe, name)
                            for i in range(each):
                                last = mm(b[:, i * n:(i + 1) * n], qk["a_iq"][rows, each * j + i, t * P:(t + 1) * P],
                                          qk["a_ik"][rows, 0, 0:n])
                            last.then_inc(psum.full_of(name), 1)

            def wide(layer, what, lhs, tiles):
                banks = [psum.claim(pe, f"{what}{i}") for i in range(4)]
                held = None
                for k, (panel, cut) in enumerate(tiles):
                    if panel != held:
                        used[0], held = held or used[0], panel
                        w = ring.wait(pe, layer, panel)
                    for t in range(NT):
                        for half in range(2):
                            last = mm(banks[2 * t + half], lhs[:, k, t * P:(t + 1) * P], w[:, cut, half * 512:half * 512 + 512],
                                      k == 0, k == len(tiles) - 1)
                            if k == len(tiles) - 1:
                                last.then_inc(psum.full_of(f"{what}{2 * t + half}"), 1)
                pe.drain().then_inc(*ring.freed(held))

            with pe.Fori(0, DEPTH) as layer:
                pe.wait_ge(once, 32)
                pe.wait_ge(S["normed"], 1)
                transposes("hT0", xn)
                project(layer)
                pe.wait_ge(S["roped"], len(ROPED))
                forget_sums()
                pe.wait_ge(S["copied"], 6)
                index_dots()
                scores("b")
                scores("c")
                values(0)
                scores("d")
                values(1)
                pe.wait_ge(S["o_sq"], 1)
                b = psum.claim(pe, "c_ss")
                mm(b[:, :], C("heads64"), osq).then_inc(psum.full_of("c_ss"), 1)
                scores("a")
                values(2)
                values(3)
                pe.wait_ge(S["mixT"], 4)
                for half in range(2):
                    w = ring.wait(pe, layer, f"out{half}")
                    for t in range(NT):
                        b = psum.claim(pe, f"mix{half}{t}")
                        for k in range(KT):
                            last = mm(b[:, :], mixT[:, k, t * P:(t + 1) * P], w[:, k, :], k == 0, k == KT - 1)
                        last.then_inc(psum.full_of(f"mix{half}{t}"), 1)
                    used[0] = f"out{half}"
                pe.wait_ge(S["params"], 32)
                b = psum.claim(pe, "pT")
                for i in range(4):
                    last = transpose(b[:, i * P:(i + 1) * P], ptok[:, i % 2, (i // 2) * P:(i // 2 + 1) * P])
                last.then_inc(psum.full_of("pT"), 1)
                pe.wait_ge(S["normed"], 2)
                transposes("hT1", xn)
                pe.wait_ge(S["hT"], 8)
                for c in range(8):
                    w = ring.wait(pe, layer, f"up{c}")
                    for j in range(4 * c, 4 * c + 4):
                        if j % 2 == 0:
                            b = psum.claim(pe, f"ff{j // 2}")
                        for k in range(KT):
                            last = mm(b[:, (j % 2) * T:(j % 2 + 1) * T], w[:, k, (j % 4) * P:(j % 4 + 1) * P], hT[:, k, :],
                                      k == 0, k == KT - 1)
                        if j % 2:
                            last.then_inc(psum.full_of(f"ff{j // 2}"), 1)
                    used[0] = f"up{c}"
                pe.wait_ge(S["gT"], UT // 2)
                wide(layer, "y", gT, [(f"down{k // 4}", k % 4) for k in range(UT)])
                pe.wait_ge(S["pT_in"], 1)
                wide(layer, "proj", pT, [("proj", k) for k in range(2)])
                pe.wait_ge(S["x_new"], 2)
                transposes("xT", x)
                pe.wait_ge(S["hT"], 12)
                for half in range(2):
                    w = ring.wait(pe, layer, f"ple{half}")
                    for t in range(NT):
                        b = psum.claim(pe, f"ple{half}{t}")
                        for k in range(KT):
                            last = mm(b[:, :], hT[:, k, t * P:(t + 1) * P], w[:, k, :], k == 0, k == KT - 1)
                        last.then_inc(psum.full_of(f"ple{half}{t}"), 1)
                    pe.drain().then_inc(*ring.freed(f"ple{half}"))
                pe.drain().then_inc(layer_done, 1)
                pe.wait_ge(layer_open, layer + 1)

        def stat_of(i, t, what, n):
            lo = 16 + 48 * (i % 2) + 8 * t + {"neg": 0, "den": 16, "rec": 32, "sink": 36}[what]
            return stat[:, lo:lo + n]

        @block.scalar
        def _(act):
            A_ = nc.scalar.activation

            def norm_stats(step):
                for t in range(NT):
                    A_(xn[:, t, :], x[:, t, :], ACT.Square, accum_out=stat[:, t:t + 1])
                act.drain()
                step(A_(stat[:, 2:4], stat[:, 0:2], ACT.Ln, bias=C("eps"), scale=1.0 / DM))
                A_(stat[:, 4:6], stat[:, 2:4], ACT.Exp, scale=-0.5).then_inc(S["rstd"], 1)

            def half_of_hT(name, gain):
                for j in (1, 3):
                    act.wait_ge(*psum.filled(f"{name}_{j}"))
                    for i in range(2):
                        last = A_(hT[:, 2 * j + i, :], psum.bank(f"{name}_{j}")[:, i * T:(i + 1) * T], ACT.Copy,
                                  scale=PAR(gain, 2 * j + i) if gain else 1.0)
                    last.then_inc(*psum.freed(f"{name}_{j}"))
                    act.drain().then_inc(S["hT"], 1)

            def drain_bank(name, out, signal, rows=slice(0, P), part=slice(0, 512)):
                act.wait_ge(*psum.filled(name))
                A_(out, psum.bank(name)[rows, part], ACT.Copy).then_inc(*psum.freed(name))
                act.drain().then_inc(S[signal], 1)

            def exps(i):
                name, maps, _, _ = ATTENDED[i]
                for t in range(NT):
                    act.wait_ge(S["score_max"], 2 * i + t + 1)
                    L = scores_of(Ls[i % 2], t, maps)
                    for e in range(maps):
                        A_(L[:, e, :], L[:, e, :], ACT.Exp, bias=stat_of(i, t, "neg", maps)[:, e:e + 1],
                           accum_out=stat_of(i, t, "den", maps)[:, e:e + 1])
                    if name == "d":
                        A_(stat_of(i, t, "sink", 4), stat_of(i, t, "sink", 4), ACT.Exp)
                    act.drain().then_inc(S["exps"], 1)

            def turned_probs(i):
                name, _, _, tile = ATTENDED[i]
                for t, kt in ((0, 0), (1, 0), (1, 1)):
                    drain_bank(f"{name}_pt{t}{kt}", PTs[i % 2][:, kt, :, t * P:(t + 1) * P], "PT")
                if name == "c":
                    drain_bank("c_o", oT, "c_oT")
                    A_(osq, oT, ACT.Square).then_inc(S["o_sq"], 1)
                    act.wait_ge(*psum.filled("c_ss"))
                    A_(ors, shaped(psum.bank("c_ss"), 2, T), ACT.Ln, bias=C("eps"), scale=1.0 / HD).then_inc(*psum.freed("c_ss"))
                    act.drain()
                    A_(ors, ors, ACT.Exp, scale=-0.5).then_inc(S["o_rstd"], 1)
                else:
                    drain_bank(name + "_o", mixT[:, tile:tile + 2, :], "mixT")

            def y_stats(k, names):
                for i, name in enumerate(names):
                    act.wait_ge(*psum.filled(name))
                    A_(ysq, psum.bank(name), ACT.Square, accum_out=stat[:, 112 + i:113 + i])
                    act.drain()
                act.drain().then_inc(S["y_ss"], 1)
                act.wait_ge(S["y_sum"], k + 1)
                A_(stat[:, 118:120], stat[:, 116:118], ACT.Ln, bias=C("eps"), scale=1.0 / DM)
                act.drain()
                A_(stat[:, 120:122], stat[:, 118:120], ACT.Exp, scale=-0.5).then_inc(S["y_rstd"], 1)

            act.wait_ge(angles, 1)
            A_(rope, rope, ACT.Sin).then_inc(tables_made, 1)
            with act.Fori(0, DEPTH) as layer:
                step = Chain(act, S["act"])
                act.dma_start(par[:, :], A["par2"][layer, :, :]).then_inc(S["params"], 16)
                act.dma_start(ptok, A["p_2"][layer, 0, :, :].rearrange("(t q) n -> q t n", q=P)).then_inc(S["params"], 16)
                act.wait_ge(once, 32)
                norm_stats(step)
                act.wait_ge(S["params"], 32)
                act.wait_ge(S["lam_sum"], 1)
                A_(lam[:, 66:68], lam[:, 64:66], ACT.Exp).then_inc(S["lam_exp"], 1)
                half_of_hT("hT0", "pre_mix")
                for name, panel, kind, parts in IN_USES:
                    if name in ROPED_AT:
                        i = ROPED_AT[name]
                        tiles = ROPED[i][3]
                        if i >= 2:
                            act.wait_ge(S["roped"], i - 1)
                        drain_bank(name, raw[:, i % 2, 0:tiles, :], "raw", part=slice(0, tiles * T))
                    elif name in ("b_q", "b_k"):
                        drain_bank(name, qk[name], "copied")
                    elif name in vtok:
                        drain_bank(name, vtok[name], "copied", part=slice(0, NT * parts[1]))
                act.wait_ge(S["gate_abs"], 1)
                A_(fl["e"], fl["e"], ACT.Exp, scale=-1.0)
                act.drain()
                A_(fl["e"], fl["e"], ACT.Ln, bias=C("ones")[:, 0:1]).then_inc(S["gate_ln"], 1)
                at = 0
                for t in range(NT):
                    for g in range(2):
                        for j in range(t + 1):
                            if at >= 2:
                                act.wait_ge(S["relu_used"], at - 1)
                            act.wait_ge(*psum.filled(f"dots{t}{g}{j}"))
                            A_(dots[:, at % 2, :], psum.bank(f"dots{t}{g}{j}"), ACT.Relu).then_inc(*psum.freed(f"dots{t}{g}{j}"))
                            act.drain().then_inc(S["relu"], 1)
                            at += 1
                exps(0)
                exps(1)
                turned_probs(0)
                exps(2)
                turned_probs(1)
                exps(3)
                turned_probs(2)
                turned_probs(3)
                y_stats(0, [f"mix{half}{t}" for half in range(2) for t in range(NT)])
                drain_bank("pT", pT, "pT_in")
                act.wait_ge(S["x_new"], 1)
                norm_stats(step)
                half_of_hT("hT1", "pre_mlp")
                y_stats(1, [f"y{i}" for i in (0, 2, 1, 3)])
                for i in (0, 2, 1, 3):
                    t, half = i // 2, i % 2
                    drain_bank(f"proj{i}", proj[:, 2 * half + t, :], "proj")
                half_of_hT("xT", None)
                for half in range(2):
                    for t in range(NT):
                        name, i = f"ple{half}{t}", 2 * half + t
                        act.wait_ge(*psum.filled(name))
                        A_(gates[:, i, :], psum.bank(name), ACT.Sigmoid).then_inc(*psum.freed(name))
                        act.drain().then_inc(S["gates"], 1)
                act.drain().then_inc(layer_done, 1)
                act.wait_ge(layer_open, layer + 1)

        @block.vector
        def _(dve):
            V = nc.vector

            def norm(k, name, gain):
                dve.wait_ge(S["rstd"], k + 1)
                for t in range(NT):
                    last = V.tensor_scalar(xn[:, t, :], x[:, t, :], stat[:, 4 + t:5 + t], None, ALU.mult)
                last.then_inc(S["normed"], 1)
                half_of_hT(name, gain)

            def half_of_hT(name, gain):
                for j in (0, 2):
                    dve.wait_ge(*psum.filled(f"{name}_{j}"))
                    bank = psum.bank(f"{name}_{j}")
                    for i in range(2):
                        src = bank[:, i * T:(i + 1) * T]
                        if gain:
                            last = V.tensor_scalar(hT[:, 2 * j + i, :], src, PAR(gain, 2 * j + i), None, ALU.mult)
                        else:
                            last = V.tensor_copy(hT[:, 2 * j + i, :], src)
                    last.then_inc(*psum.freed(f"{name}_{j}"))
                    dve.drain().then_inc(S["hT"], 1)

            def turn(i):
                name, out, width, tiles = ROPED[i]
                dve.wait_ge(*psum.filled(name + "_rot"))
                if i >= 2:
                    dve.drain()
                sin = rope[:, width, 1:2, :].broadcast_to([P, tiles, T])
                V.tensor_tensor(turned[:, i % 2, 0:tiles, :], shaped(psum.bank(name + "_rot")[:, 0:tiles * T], tiles, T), sin,
                                ALU.mult).then_inc(*psum.freed(name + "_rot"))
                dve.wait_ge(S["cosined"], i + 1)
                dve.drain()
                V.tensor_tensor(out, out, turned[:, i % 2, 0:tiles, :], ALU.add).then_inc(S["roped"], 1)

            def masked_scores(i):
                name, maps, scale, _ = ATTENDED[i]
                if i >= 2:
                    dve.wait_ge(*psum.filled(ATTENDED[i - 2][0] + "_pt11"))
                for t in range(NT):
                    n = P * (t + 1)
                    L = scores_of(Ls[i % 2], t, maps)
                    for g in range(maps // 2):
                        bank = f"{name}_sc{t}{g}"
                        dve.wait_ge(*psum.filled(bank))
                        if name == "a":
                            mask = sel[t].unsqueeze(1).broadcast_to([P, 2, n])
                        elif name == "b":
                            mask = scores_of(Dm, t, 4)[:, 2 * g:2 * g + 2, :]
                        else:
                            all_ = shaped(C("window" if name == "d" else "causal"), NT, T)
                            mask = all_[:, t:t + 1, 0:n].broadcast_to([P, 2, n])
                        V.scalar_tensor_tensor(L[:, 2 * g:2 * g + 2, :], shaped(psum.bank(bank)[:, 0:2 * n], 2, n), scale, mask,
                                               ALU.mult, ALU.add).then_inc(*psum.freed(bank))
                    dve.drain()
                    neg, rec = stat_of(i, t, "neg", maps), stat_of(i, t, "rec", maps)
                    V.tensor_reduce(rec, L, AX.X, ALU.max)
                    dve.drain()
                    if name == "d":
                        V.tensor_tensor(rec, rec, PAR("sinks"), ALU.max)
                        dve.drain()
                    V.tensor_scalar(neg, rec, -1.0, None, ALU.mult)
                    if name == "d":
                        dve.drain()
                        V.tensor_tensor(stat_of(i, t, "sink", 4), PAR("sinks"), neg, ALU.add)
                    dve.drain().then_inc(S["score_max"], 1)

            def probs(i):
                name, maps, _, _ = ATTENDED[i]
                for t in range(NT):
                    n = P * (t + 1)
                    L = scores_of(Ls[i % 2], t, maps)
                    den, rec = stat_of(i, t, "den", maps), stat_of(i, t, "rec", maps)
                    dve.wait_ge(S["exps"], 2 * i + t + 1)
                    if name == "d":
                        V.tensor_tensor(den, den, stat_of(i, t, "sink", 4), ALU.add)
                        dve.drain()
                    V.reciprocal(rec, den)
                    dve.drain()
                    V.tensor_tensor(L, L, rec.unsqueeze(2).broadcast_to([P, maps, n]), ALU.mult)
                    if name == "c":
                        dve.drain()
                        for g in range(2):
                            V.scalar_tensor_tensor(L[:, 4 * g:4 * g + 2, :], L[:, 4 * g + 2:4 * g + 4, :], lam[:, 68:69],
                                                   L[:, 4 * g:4 * g + 2, :], ALU.mult, ALU.add)
                    dve.drain().then_inc(S["probs"], 1)

            def select(t):
                n = P * (t + 1)
                best = stat[:, 8:16]
                V.tensor_tensor(acc[t], acc[t], shaped(C("causal"), NT, T)[:, t, 0:n], ALU.add)
                for _ in range(TOPK // 8):
                    dve.drain()
                    V.max(best, acc[t])
                    dve.drain()
                    V.match_replace(acc[t], best, acc[t], TAKEN)
                dve.drain()
                V.tensor_scalar(sel[t], acc[t], -1e35, NEG, ALU.is_gt, ALU.mult)
                dve.drain()
                V.tensor_tensor(sel[t], sel[t], shaped(C("causal"), NT, T)[:, t, 0:n], ALU.add)
                dve.drain()

            def residual(k, names, gain):
                dve.wait_ge(S["y_ss"], k + 1)
                V.tensor_tensor(stat[:, 116:118], stat[:, 112:114], stat[:, 114:116], ALU.add).then_inc(S["y_sum"], 1)
                dve.wait_ge(S["y_rstd"], k + 1)
                lo = PAR2[gain][0]
                for i, name in enumerate(names):
                    half, t = i // 2, i % 2
                    V.scalar_tensor_tensor(yn[:, i, :], psum.bank(name), stat[:, 120 + t:121 + t],
                                           par[:, lo + 512 * half:lo + 512 * half + 512], ALU.mult, ALU.mult).then_inc(*psum.freed(name))
                add_to_x()

            def add_to_x():
                dve.drain()
                for i in range(4):
                    half, t = i // 2, i % 2
                    xs = x[:, t, 512 * half:512 * half + 512]
                    V.tensor_tensor(xs, xs, yn[:, i, :], ALU.add)
                dve.drain().then_inc(S["x_new"], 1)

            dve.wait_ge(once, 32)
            pos, turns = acc[1], sel[1]
            V.tensor_copy(pos, positions[:, :])
            for w in range(2):
                ang = rope[:, w, 1, :]
                dve.drain()
                V.tensor_scalar(ang, pos, C("inv_freq")[:, w:w + 1], None, ALU.mult)
                dve.drain()
                V.tensor_scalar(turns, ang, float(1 / (2 * np.pi)), 1.5 * 2.0 ** 23, ALU.mult, ALU.add)
                dve.drain()
                V.tensor_scalar(turns, turns, -1.5 * 2.0 ** 23, None, ALU.add)
                for part in TWO_PI:
                    dve.drain()
                    V.scalar_tensor_tensor(ang, turns, -part, ang, ALU.mult, ALU.add)
                dve.drain()
                V.tensor_scalar(ang, ang, -3.1415925, 3.1415925, ALU.max, ALU.min)
                dve.drain()
                V.scalar_tensor_tensor(rope[:, w, 0, :], ang, -1.0, ang, ALU.mult, ALU.max)
                dve.drain()
                V.tensor_scalar(rope[:, w, 0, :], rope[:, w, 0, :], -1.0, float(np.pi / 2), ALU.mult, ALU.add)
            dve.drain().then_inc(angles, 1)
            with dve.Fori(0, DEPTH) as layer:
                dve.wait_ge(tables_made, 1)
                dve.wait_ge(S["params"], 32)
                V.tensor_tensor(lam[:, 0:64], PAR("lam_q"), PAR("lam_k"), ALU.mult)
                dve.drain()
                V.tensor_reduce(lam[:, 64:66], shaped(lam[:, 0:64], 2, 32), AX.X, ALU.add).then_inc(S["lam_sum"], 1)
                norm(0, "hT0", "pre_mix")
                dve.wait_ge(S["lam_exp"], 1)
                V.tensor_tensor(lam[:, 68:69], lam[:, 67:68], lam[:, 66:67], ALU.subtract)
                dve.drain()
                V.tensor_tensor(lam[:, 68:69], lam[:, 68:69], PAR("lam_init"), ALU.subtract)
                for i in range(4):
                    turn(i)
                dve.wait_ge(*psum.filled("a_iw"))
                V.tensor_scalar(iw, shaped(psum.bank("a_iw")[:, 0:16], NT, 8), IDX_HEADS ** -0.5 * 64 ** -0.5, None,
                                ALU.mult).then_inc(*psum.freed("a_iw"))
                turn(4)
                dve.wait_ge(*psum.filled("b_f"))
                V.tensor_tensor(fl["x"], shaped(psum.bank("b_f")[:, 0:8], NT, 4),
                                PAR("b_forget").unsqueeze(1).broadcast_to([P, NT, 4]), ALU.add).then_inc(*psum.freed("b_f"))
                dve.drain()
                V.scalar_tensor_tensor(fl["e"], fl["x"], -1.0, fl["x"], ALU.mult, ALU.max)
                dve.drain().then_inc(S["gate_abs"], 1)
                for i in range(5, 9):
                    turn(i)
                dve.wait_ge(S["gate_ln"], 1)
                V.tensor_scalar(fl["x"], fl["x"], 0.0, None, ALU.min)
                dve.drain()
                V.tensor_tensor(fl["n"], fl["e"], fl["x"], ALU.subtract).then_inc(S["nlf"], 1)
                dve.wait_ge(*psum.filled("f_col"))
                V.tensor_scalar(fl["cum"], shaped(psum.bank("f_col")[:, 0:8], NT, 4), -1.0, None, ALU.mult).then_inc(*psum.freed("f_col"))
                dve.drain()
                for g in range(2):
                    name = f"f_row{g}"
                    dve.wait_ge(*psum.filled(name))
                    for t in range(NT):
                        n = P * (t + 1)
                        for hp in range(2):
                            h = BY_PARITY[2 * g + hp]
                            last = V.scalar_tensor_tensor(scores_of(Dm, t, 4)[:, 2 * g + hp, :], psum.bank(name)[:, hp * T:hp * T + n],
                                                          fl["cum"][:, t, h:h + 1], shaped(C("causal"), NT, T)[:, t, 0:n], ALU.add, ALU.add)
                    last.then_inc(*psum.freed(name))
                at = 0
                for t in range(NT):
                    n = P * (t + 1)
                    each = 512 // n
                    for g in range(2):
                        for j in range(4 // each):
                            dve.wait_ge(S["relu"], at + 1)
                            for i in range(each):
                                head = 2 * (each * j + i) + g
                                r, weight = dots[:, at % 2, i * n:(i + 1) * n], iw[:, t, head:head + 1]
                                dve.drain()
                                if g == j == i == 0:
                                    last = V.tensor_scalar(acc[t], r, weight, None, ALU.mult)
                                else:
                                    last = V.scalar_tensor_tensor(acc[t], r, weight, acc[t], ALU.mult, ALU.add)
                            last.then_inc(S["relu_used"], 1)
                            at += 1
                dve.drain()
                masked_scores(0)
                masked_scores(1)
                probs(0)
                select(0)
                masked_scores(2)
                probs(1)
                select(1)
                masked_scores(3)
                probs(2)
                probs(3)
                dve.wait_ge(S["o_rstd"], 1)
                V.scalar_tensor_tensor(oT, oT, PAR("subln"), ors, ALU.mult, ALU.mult)
                dve.drain()
                V.tensor_scalar(mixT[:, 4:6, :], oT, PAR("lam_rest"), None, ALU.mult)
                dve.drain().then_inc(S["mixT"], 1)
                residual(0, [f"mix{half}{t}" for half in range(2) for t in range(NT)], "post_mix")
                norm(1, "hT1", "pre_mlp")
                for j in range(UT // 2):
                    name = f"ff{j}"
                    dve.wait_ge(*psum.filled(name))
                    V.tensor_scalar(gT[:, 2 * j:2 * j + 2, :], shaped(psum.bank(name), 2, T), 0.0, None, ALU.max).then_inc(*psum.freed(name))
                    dve.drain()
                    V.tensor_tensor(gT[:, 2 * j:2 * j + 2, :], gT[:, 2 * j:2 * j + 2, :], gT[:, 2 * j:2 * j + 2, :], ALU.mult).then_inc(S["gT"], 1)
                residual(1, [f"y{i}" for i in (0, 2, 1, 3)], "post_mlp")
                half_of_hT("xT", None)
                for i in range(4):
                    dve.wait_ge(S["gates"], i + 1)
                    V.tensor_tensor(yn[:, i, :], gates[:, i, :], proj[:, i, :], ALU.mult)
                add_to_x()
                dve.drain().then_inc(layer_done, 1)
                dve.wait_ge(layer_open, layer + 1)

        @block.gpsimd
        def _(pool):
            pool.wait_ge(tables_made, 1)
            with pool.Fori(0, DEPTH) as layer:
                for i, (name, out, width, tiles) in enumerate(ROPED):
                    pool.wait_ge(S["raw"], i + 1)
                    cos = rope[:, width, 0:1, :].broadcast_to([P, tiles, T])
                    nc.gpsimd.tensor_tensor(out, raw[:, i % 2, 0:tiles, :], cos, ALU.mult).then_inc(S["cosined"], 1)
                pool.wait_ge(layer_done, 3 * layer + 3)
                pool.sem_inc(barrier_taken, 1)
                for r in sem_ranges([s.num for s in S.values()] + [s.num for s in psum.full + psum.free]):
                    pool.sem_clear(r)
                pool.sem_inc(layer_open, 1)

        psum.check()


def two_blocks(nc, A, out):
    with ExitStack() as ctx:
        x = shaped(ctx.enter_context(nc.sbuf_tensor("x_state", [P, NT * DM], F32))[:, :], NT, DM)
        memory = ctx.enter_context(nc.sbuf_tensor("memory", [P, MEMORY], F32))[:, :]
        banks = ctx.enter_context(nc.psum_tensor("banks", [P, 8, 512], F32))
        x_in = ctx.enter_context(nc.semaphore("x_in"))
        x_out = ctx.enter_context(nc.semaphore("x_out"))
        with nc.Block() as block:
            @block.sync
            def _(sp):
                for t in range(NT):
                    sp.dma_start(x[:, t, :], A["x"][0, t * P:(t + 1) * P, :]).then_inc(x_in, 16)
                sp.wait_ge(x_in, 16 * NT)
        block1(nc, ctx, memory, banks, x, x_in, A)
        block2(nc, ctx, memory, banks, x, A)
        with nc.Block() as block:
            @block.sync
            def _(sp):
                for t in range(NT):
                    sp.dma_start(out[0, t * P:(t + 1) * P, :], x[:, t, :]).then_inc(x_out, 16)
                sp.wait_ge(x_out, 16 * NT)


_LARGE = ["x", "w_in", "w_out", "mla_w_uq", "mla_w_ukv", "gla_w_gk2", "ffn_w_gate", "ffn_w_up", "ffn_w_down",
          "p_2", "positions_2", "w_in_2", "w_out_2", "w_mlp_up_2", "w_mlp_down_2", "w_ple_proj_2", "w_ple_gate_2"]


def kernel(**inputs):
    import concourse.bacc as bacc
    from concourse.bass_utils import run_bass_kernel_spmd

    nc = bacc.Bacc("TRN2", target_bir_lowering=False, num_devices=1)
    host = {name: np.ascontiguousarray(inputs[name]) for name in _LARGE}
    host["const1"], host["const2"] = shape_constants1(), shape_constants2()
    host["par1"], host["par2"] = params1(inputs), params2(inputs)
    arrays, A = {}, {}
    for name, a in host.items():
        arrays[f"in_{name}"] = a
        A[name] = nc.dram_tensor(f"in_{name}", a.shape, mybir.dt.from_np(a.dtype), kind="ExternalInput").ap()
    out = nc.dram_tensor("out_x", (1, T, DM), F32, kind="ExternalOutput").ap()
    two_blocks(nc, A, out)
    result = run_bass_kernel_spmd(nc, [arrays], core_ids=[0])
    return result.results[0]["out_x"]
```

```python
from contextlib import ExitStack

import numpy as np

import concourse.bass as bass
from concourse import mybir

F32 = mybir.dt.float32
ALU = mybir.AluOpType
ACT = mybir.ActivationFunctionType
AX = mybir.AxisListType

P = 128
T = 256
NT = T // P
DM = 1024
KT = DM // P
DEPTH = 2
GW = 256
HD = 64
EPS = 1e-6
NEG = -1e30
SUB = 16
NSUB = T // SUB
SUBP = P // SUB
CHUNK = 64
D_FF = 2816
FT = D_FF // P
PANEL = 272
SLOTS = 8


class Psum:

    def __init__(self, nc, ctx, tag, banks):
        self.t = banks
        self.full = [ctx.enter_context(nc.semaphore(f"{tag}_bank{b}_filled")) for b in range(8)]
        self.free = [ctx.enter_context(nc.semaphore(f"{tag}_bank{b}_freed")) for b in range(8)]
        self.at, self.given_back = {}, set()

    def claim(self, pe, name):
        assert name not in self.at, name
        n = len(self.at)
        self.at[name] = (n % 8, n // 8 + 1)
        if n >= 8:
            pe.wait_ge(self.free[n % 8], n // 8)
        return self.t[:, n % 8, :]

    def check(self):
        assert set(self.at) == self.given_back, set(self.at) ^ self.given_back

    def known(self, name):
        return name in self.at

    def bank(self, name):
        return self.t[:, self.at[name][0], :]

    def full_of(self, name):
        return self.full[self.at[name][0]]

    def filled(self, name):
        b, n = self.at[name]
        return self.full[b], n

    def freed(self, name):
        assert name not in self.given_back, name
        self.given_back.add(name)
        return self.free[self.at[name][0]], 1


class Chain:

    def __init__(self, eng, sem):
        self.eng, self.sem, self.n = eng, sem, 0

    def __call__(self, ins):
        self.n += 1
        ins.then_inc(self.sem, 1)
        self.eng.wait_ge(self.sem, self.n)


class Ring:

    def __init__(self, nc, ctx, tag, entries, slots):
        self.t = slots
        self.full = [ctx.enter_context(nc.semaphore(f"{tag}_slot{s}_filled")) for s in range(SLOTS)]
        self.free = [ctx.enter_context(nc.semaphore(f"{tag}_slot{s}_freed")) for s in range(SLOTS)]
        self.entries, self.names = entries, [p[0] for p in entries]
        self.uses = [len(range(s, len(entries), SLOTS)) for s in range(SLOTS)]
        self.loads = [self.loads_to(s, len(entries)) for s in range(SLOTS)]
        self.split = [n[:-3] for n in self.names if n.endswith("_hi")]

    def loads_to(self, s, end):
        return sum(self.entries[n][1] is not None for n in range(s, end, SLOTS))

    def view(self, name):
        n = self.names.index(name)
        _, _, k, c0, c1 = self.entries[n]
        return self.t[:, n % SLOTS, 0:k * (c1 - c0)].rearrange("p (k n) -> p k n", k=k)

    def wait_free(self, eng, layer, name):
        n = self.names.index(name)
        eng.wait_ge(self.free[n % SLOTS], layer * self.uses[n % SLOTS] + (n // SLOTS + 1))

    def load_all(self, sp, layer):
        for n, (name, source, k, c0, c1) in enumerate(self.entries):
            if source is not None:
                self.wait_free(sp, layer, name)
                sp.dma_start(self.view(name), source(layer)).then_inc(self.full[n % SLOTS], 16)

    def wait(self, eng, layer, name):
        n = self.names.index(name)
        s = n % SLOTS
        eng.wait_ge(self.full[s], layer * (16 * self.loads[s]) + 16 * self.loads_to(s, n + 1))
        return self.view(name)

    def freed(self, name):
        return self.free[self.names.index(name) % SLOTS], 1


def with_parts(panels):
    return [e for name, source, k, c0, c1 in panels for e in ((name, source, k, c0, c1), (name + "_hi", None, k, c0, c1))]


class Memory:

    def __init__(self, nc, ctx, tag, parts):
        with ExitStack() as plain:
            self.plain = {n: plain.enter_context(nc.sbuf_tensor(f"{tag}_{n}", [P, w], F32)) for n, w in parts.items()}
        self.other = {f"{tag}_{n}": ctx.enter_context(nc.sbuf_tensor(f"{tag}_{n}_rounded", [P, w], mybir.dt.float32r))
                      for n, w in parts.items()}
        self.parts = parts

    def area(self, name):
        return Area(self.plain[name][:, :], self.parts[name])

    def rounded(self, ap):
        return bass.AP(tensor=self.other[ap.tensor.name], offset=ap.offset, ap=ap.ap)


def as_float32(ap):
    return ap.bitcast(F32)


def table(columns):
    out, at = {}, 0
    for name, width in columns:
        out[name] = (at, at + width)
        at += width
    return out, at


def bands(a, d):
    return a.rearrange("p r (s c) -> p (r s) c", c=SUB)[:, :, d:SUB]


def shifted(a, d):
    return a.rearrange("p r (s c) -> p (r s) c", c=SUB)[:, :, 0:SUB - d]


def shaped(ap, *shape):
    if len(shape) == 1:
        return ap
    names = "abcd"[:len(shape)]
    sizes = {n: s for n, s in zip(names[1:], shape[1:])}
    return ap.rearrange(f"p ({' '.join(names)}) -> p {' '.join(names)}", **sizes)


class Area:

    def __init__(self, tensor, width, at=0):
        self.tensor, self.width, self.at = tensor, width, at

    def __call__(self, *shape):
        n = int(np.prod(shape))
        lo, self.at = self.at, self.at + n
        assert self.at <= self.width, (self.at, self.width)
        return shaped(self.tensor[:, lo:lo + n], *shape)


class Group:
    pass


def interleave(a, b):
    places = [((i + 0.5) / len(a), x) for i, x in enumerate(a)] + [((i + 0.5) / len(b), x) for i, x in enumerate(b)]
    return [x for _, x in sorted(places, key=lambda place: place[0])]


def emit(order, parts):
    for name in order:
        next(parts[name])
    for name, part in parts.items():
        assert next(part, "over") == "over", name


def sem_ranges(numbers):
    out = []
    for n in sorted(numbers):
        if out and out[-1].stop == n:
            out[-1] = range(out[-1].start, n + 1)
        else:
            out.append(range(n, n + 1))
    return out


CONST1, N_CONST1 = table([
    ("ident", P), ("cum", P), ("ones", P), ("heads64", P), ("to_pair", 2 * P),
    ("rot96", 96), ("cos96", T), ("sin96", T), ("causal", NT * T), ("hide_strict", P),
    ("hide_incl", P), ("level", 7 * P), ("restart", T), ("sub", SUBP), ("eps", 1),
])
PAR1, N_PAR1 = table([
    ("pre_mix", KT), ("pre_ffn", KT), ("lb_logits", 2 * DEPTH), ("lb_of", 2 * DEPTH), ("hgrn_norm", 1),
    ("b_gk", 1), ("gla_norm", 1), ("q_norm", 2), ("kv_norm", 1), ("conv", 4 * 6), ("gdn_norm", 1),
    ("ffn_conv", 3 * FT), ("a_log", 4), ("dt_bias", 4), ("post_mix", DM), ("post_ffn", DM),
])
IN1 = [(0, 256), (256, 512), (512, 768), (768, 1024), (1024, 1280), (1280, 1536), (1536, 1808), (1808, 2064),
       (2064, 2224), (2224, 2480), (2480, 2736), (2736, 2992), (2992, 3256)]


def shape_constants1():
    c = np.zeros((P, N_CONST1), np.float32)

    def put(name, a):
        lo, hi = CONST1[name]
        c[:a.shape[0], lo:hi] = a.reshape(a.shape[0], -1)

    i = np.arange(P)
    same = (i[:, None] // CHUNK) == (i[None, :] // CHUNK)
    put("ident", np.eye(P, dtype=np.float32))
    put("cum", (same & (i[:, None] <= i[None, :])).astype(np.float32))
    put("ones", np.ones((P, P), np.float32))
    put("heads64", same.astype(np.float32))
    pair = np.zeros((P, 2, P), np.float32)
    for p in range(2):
        pair[:, p] = (i[:, None] // 32) == (2 * p + i[None, :] // 64)
    put("to_pair", pair)
    rot = np.zeros((96, 96), np.float32)
    for m in range(16):
        rot[64 + 16 + m, 64 + m] = -1.0
        rot[64 + m, 64 + 16 + m] = 1.0
    put("rot96", rot)
    inv = (np.float32(10000.0) ** (-np.arange(0, 32, 2, dtype=np.float32) / np.float32(32))).astype(np.float32)
    ang = (np.arange(T, dtype=np.float32)[None, :] * inv[:, None]).astype(np.float32)
    cos, sin = np.ones((96, T), np.float32), np.zeros((96, T), np.float32)
    cos[64:80] = cos[80:96] = np.cos(ang)
    sin[64:80] = sin[80:96] = np.sin(ang)
    put("cos96", cos)
    put("sin96", sin)
    key = np.arange(T)
    put("causal", np.stack([np.where(key[None, :] <= (i[:, None] + P * t), 0.0, NEG) for t in range(NT)], 1).astype(np.float32))
    put("hide_strict", np.where(same & (i[None, :] < i[:, None]), 0.0, -NEG).astype(np.float32))
    put("hide_incl", np.where(same & (i[None, :] >= i[:, None]), 0.0, NEG).astype(np.float32))
    level = np.zeros((P, 7, P), np.float32)
    for n in range(6):
        c_ = 1 << n
        row, col = i[:, None], i[None, :]
        m = (row // (2 * c_) == col // (2 * c_)) & (row % (2 * c_) >= c_) & (col % (2 * c_) < c_)
        level[:, n] = m.T
        if n == 0:
            level[:, 6] = m
    put("level", level)
    put("restart", np.broadcast_to((np.arange(T) % SUB != 0).astype(np.float32), (P, T)))
    put("sub", (i[:, None] // SUB == np.arange(SUBP)[None, :]).astype(np.float32))
    put("eps", np.full((P, 1), EPS, np.float32))
    return c


def params1(a):
    out = np.zeros((DEPTH, P, N_PAR1), np.float32)

    def put(name, layer, v):
        lo, hi = PAR1[name]
        out[layer, :, lo:hi] = v

    def cols(v):
        return np.asarray(v).reshape(-1, P).T

    def rows(v):
        v = np.asarray(v)
        return np.broadcast_to(v, (P,) + v.shape)

    for l in range(DEPTH):
        put("pre_mix", l, cols(a["pre_mix_g"][l]))
        put("pre_ffn", l, cols(a["pre_ffn_g"][l]))
        lb = np.stack([cols(a["hgrn_lb_logits"][j]) for j in range(DEPTH)], 2)
        put("lb_logits", l, lb.reshape(P, -1))
        of = np.zeros((P, 2, DEPTH), np.float32)
        of[:, :, 1:l + 1] = 1.0
        put("lb_of", l, of.reshape(P, -1))
        put("hgrn_norm", l, np.concatenate([a["hgrn_norm_g"][l]] * 2)[:, None])
        put("b_gk", l, cols(a["gla_b_gk"][l]))
        put("gla_norm", l, np.concatenate([a["gla_norm_g"][l]] * 2)[:, None])
        put("q_norm", l, cols(a["mla_q_norm_g"][l]))
        put("kv_norm", l, cols(a["mla_kv_norm_g"][l]))
        put("conv", l, np.asarray(a["gdn_conv_w"][l]).reshape(4, 6, P).transpose(2, 1, 0).reshape(P, -1))
        put("gdn_norm", l, np.concatenate([a["gdn_norm_g"][l]] * 2)[:, None])
        put("ffn_conv", l, np.asarray(a["ffn_conv_w"][l]).reshape(3, FT, P).transpose(2, 1, 0).reshape(P, -1))
        put("a_log", l, rows(a["gdn_a_log"][l]))
        put("dt_bias", l, rows(a["gdn_dt_bias"][l]))
        put("post_mix", l, rows(a["post_mix_g"][l]))
        put("post_ffn", l, rows(a["post_ffn_g"][l]))
    return out



SIGNALS1 = """w_split normed hT o_sq code v_T kdT kd_tok vexp state q_decayed weighted mla_sq mla_c mla_cn rot_in
qT kT probs PT mla_v l2_sq g_ready qk_norm level_X lmat level_T tok_D uw qe state_D v_new params
mix_split h_split gT w_hi rstd oT_ready o_rstd af_f af_ln gk_abs gk_ln scan exp_b scan_end kd_exp
vtok diff decay aq_tanh af_sig gate_th bg_th dz_th gla_done mla_rstd scores_max exps mixT_C conv
conv_th ba_in ba_exp conv_silu l2_rstd b_small b_exp erow hid decays nt act lb_max lb_exp y_ss y_sum
y_rstd x_new ff_conv ff_gate ff_gelu qk kr_done dve gpad_zero""".split()


def block1(nc, kept, banks, x, x_in, A):
    with ExitStack() as ctx:
        A_LEFT, BETWEEN, D_WORK, LEFT = 10 * T, 14 * T, 42 * T, 5534
        memory = Memory(nc, ctx, "b1", {"ring": SLOTS * KT * PANEL, "front": KT * T + A_LEFT + BETWEEN, "back": D_WORK + LEFT,
                                        "small": N_CONST1 + N_PAR1 + 768 + 512 + P + KT * T + 64})
        rounded, buf = memory.rounded, memory.area("small")

        S = {n: ctx.enter_context(nc.semaphore("b1_" + n)) for n in SIGNALS1}
        psum = Psum(nc, ctx, "b1", banks)
        layer_done = kept.enter_context(nc.semaphore("b1_layer_done"))
        layer_open = kept.enter_context(nc.semaphore("b1_layer_open"))
        barrier_taken = kept.enter_context(nc.semaphore("b1_barrier_taken"))
        once = kept.enter_context(nc.semaphore("b1_constants_in"))

        def cols(src, k):
            return lambda l, c0, c1, k0=0: src.rearrange("l (k p) n -> l p k n", p=P)[l, :, k0:k0 + k, c0:c1]

        win, wout = cols(A["w_in"], KT), cols(A["w_out"], KT)
        wg, wu = cols(A["ffn_w_gate"], KT), cols(A["ffn_w_up"], KT)
        wd = A["ffn_w_down"].rearrange("l (k p) n -> l p k n", p=P)
        panels = [(f"in{i}", lambda l, c0=c0, c1=c1: win(l, c0, c1), KT, c0, c1) for i, (c0, c1) in enumerate(IN1)]
        late = [(f"out{i}", lambda l, i=i: wout(l, 256 * i, 256 * i + 256), KT, 0, 256) for i in range(4)]
        for i in range(FT // 2):
            late.append((f"gate{i}", lambda l, i=i: wg(l, 256 * i, 256 * i + 256), KT, 0, 256))
            late.append((f"up{i}", lambda l, i=i: wu(l, 256 * i, 256 * i + 256), KT, 0, 256))
        late += [(f"down{i}", lambda l, i=i: wd[l, :, 2 * i:2 * i + 2, :], 2, 0, DM) for i in range(FT // 2)]
        panels += with_parts(late)
        ring = Ring(nc, kept, "b1", panels, memory.area("ring")(SLOTS, KT * PANEL))

        const = buf(N_CONST1)
        par = buf(N_PAR1)

        def C(name, rows=P):
            lo, hi = CONST1[name]
            return const[0:rows, lo:hi]

        def PAR(name, i=None, n=1):
            lo, hi = PAR1[name]
            return par[:, lo:hi] if i is None else par[:, lo + i:lo + i + n]

        w_uq = buf(2, 384)
        w_ukv = buf(512)
        w_gk2 = buf(P)
        mixT = buf(KT, T)
        stat = buf(64)

        front, back = memory.area("front"), memory.area("back")
        hT = front(KT, T)
        a_left = Area(front(A_LEFT), A_LEFT)
        between = front(BETWEEN)
        d_work = back(D_WORK)
        area = Area(back(LEFT), LEFT)
        G = {}
        for m, R, left in (("A", 2, a_left), ("B", 1, area)):
            g = G[m] = Group()
            g.name, g.R = m, R
            g.q, g.k, g.lf = (left(R, T) for _ in range(3))
            g.vT, g.gate = left(2, T), left(2, T)
        cT = area(3, T)
        kr = area(T)
        cin = area(6, 3 + T)
        oD = Group()
        oD.gate = area(2, T)
        code = kr
        lb = area(32)
        zb = area(NT, 8)
        sm = {n: area(NT, 4) for n in ("beta", "x", "e", "l", "g", "b", "nb", "eb", "be", "fd", "bl")}
        ea = area(4)
        SD = area(4, 2, HD)

        whole = memory.plain["front"][:, :]
        for g, area, rest in ((G["A"], Area(between, BETWEEN), Area(d_work, D_WORK)),
                              (G["B"], memory.area("front"), None)):
            R = g.R
            g.b, g.eb, g.qe, g.kd, g.e2 = (area(R, T) for _ in range(5))
            g.rs = shaped(area.tensor[:, 3 * R * T:(3 * R + 2) * T], 2, T)
            g.vtok, g.oT = area(2, T), area(2, T)
            area = rest or area
            g.sq = area(2, T)
            g.kdtok = area(NT, R * P)
            g.S = area(R, NSUB, HD)
            at = area.at
            g.vexp = area(NT, SUBP, GW)
            area.at = at
            g.band = {n: area(2, (2 if n == "o" else R) * T) for n in ("diff", "exp", "qk", "w", "o")}
        area = memory.area("front")
        cn = area(3, T)
        qT, kT = area(4, T), area(4, T)
        vtokC = area(NT, GW)
        L, Pr, PT = area(4, T), area(4, T), area(NT, 4, T)
        crs, rtmp = Pr[:, 0:2, :], PT[:, 0]
        area = Area(d_work, D_WORK)
        cv = area(6, T)
        ktok, vtokD, kbe = (area(NT, GW) for _ in range(3))
        kdec, vb = ktok, vtokD
        row, lstr, lincT, erow, Tm, Um, NTm = (area(8, P) for _ in range(7))
        Xm = row
        pm = lstr
        uD = vnew = area(NT, GW)
        cth = shaped(area.tensor[:, area.at - NT * GW - 6 * T:area.at - NT * GW], 6, T)
        lrs = erow.rearrange("p a b -> p (a b)").rearrange("p (a b) -> p a b", a=4)
        area.at = 0
        oD.oT, oD.sq, oD.rs = (area(2, T) for _ in range(3))
        qeD, wT = (shaped(cin.rearrange("p a b -> p (a b)")[:, i * 2 * T:(i + 1) * 2 * T], 2, T) for i in range(2))
        xn = shaped(between[:, 0:NT * DM], NT, DM)
        front, back = Area(whole[:, KT * T:], A_LEFT + BETWEEN), memory.area("back")
        gh, gl = front(FT, T), back(FT, T)
        gpad = back(2, 2 + T)
        gcv = back(2, 3, T)
        ysq, yn = back(512), back(4, 512)

        IN_USES = [
            ("a_q", "in0", [(0, P, 0, 0), (0, P, 1, 128)]), ("a_f", "in1", [(0, P, 0, 256), (0, P, 1, 384)]),
            ("a_i", "in2", [(0, P, 0, 512), (0, P, 1, 640)]), ("a_g", "in3", [(0, P, 0, 768), (0, P, 1, 896)]),
            ("b_qk", "in4", [(0, P, 0, 1024), (0, P, 1, 1152)]), ("b_v", "in5", [(0, P, 0, 1280), (0, P, 1, 1408)]),
            ("code", "in6", [(0, 16, 0, 1536)]), ("b_g", "in6", [(0, P, 0, 1552), (0, P, 1, 1680)]),
            ("c_q", "in7", [(0, P, 0, 1808), (0, P, 1, 1936)]),
            ("c_kvr", "in8", [(0, P, 0, 2064), (64, 32, 1, 2192)]),
            ("d_q", "in9", [(0, P, 0, 2224), (0, P, 1, 2352)]),
            ("d_k", "in10", [(0, P, 0, 2480), (0, P, 1, 2608)]), ("d_v", "in11", [(0, P, 0, 2736), (0, P, 1, 2864)]),
            ("d_z", "in12", [(0, P, 0, 3000), (0, P, 1, 3128)]),
        ]
        LEAD = 7
        IN_STEPS, GLA_STEPS, MLA_STEPS = sum(len(parts) for _, _, parts in IN_USES) + 1, SUB + 10, 12
        GDN_STEPS = 11 + 3 * 5 + 1 + 7 + 2
        ORDER = (["in"] * LEAD + interleave(["A"] * GLA_STEPS, ["in"] * (IN_STEPS - LEAD))
                 + interleave(["D"] * GDN_STEPS, ["B"] * GLA_STEPS + ["C"] * MLA_STEPS + ["out"] * 5))
        block = ctx.enter_context(nc.Block())

        @block.sync
        def _(sp):
            for s in range(SLOTS):
                sp.sem_inc(ring.free[s], 1)
            sp.dma_start(const[:, :], A["const1"]).then_inc(once, 16)
            with sp.Fori(0, DEPTH) as layer:
                ring.load_all(sp, layer)

        @block.tensor
        def _(pe):
            used = []

            def mm(out, lhsT, rhs, start=True, stop=True):
                ins = nc.tensor.matmul(out, lhsT, rhs, start=start, stop=stop)
                if used:
                    ins.then_inc(*ring.freed(used.pop(0)))
                return ins

            def mm3(out, a, b, start, stop):
                mm(out, a[0], b[0], start, False)
                mm(out, a[0], b[1], False, False)
                return mm(out, a[1], b[0], False, stop)

            def split_panel(name):
                pe.wait_ge(S["w_split"], ring.split.index(name) + 1)
                return rounded(ring.view(name + "_hi")), rounded(ring.view(name))

            def give_back():
                for name in used:
                    pe.drain().then_inc(*ring.freed(name))
                used.clear()

            def transpose(out, a):
                return nc.tensor.transpose(out, a, C("ident"))

            def norm_transposes(k):
                pe.wait_ge(S["normed"], k + 1)
                for j in range(4):
                    b = psum.claim(pe, f"hT{k}_{j}")
                    for i in range(4):
                        last = transpose(b[:, i * P:(i + 1) * P], xn[:, i % 2, (2 * j + i // 2) * P:(2 * j + i // 2 + 1) * P])
                    last.then_inc(psum.full_of(f"hT{k}_{j}"), 1)

            def project(layer):
                pe.wait_ge(S["hT"], 4)
                held = None
                for name, panel, parts in IN_USES:
                    if panel != held:
                        if held:
                            used.append(held)
                        held = panel
                        w = ring.wait(pe, layer, panel)
                        base = IN1[int(panel[2:])][0]
                    if name == "d_z":
                        b = psum.claim(pe, "d_ba")
                        for t in range(NT):
                            for k in range(KT):
                                last = mm(b[:, 8 * t:8 * t + 8], hT[:, k, t * P:(t + 1) * P], w[:, k, 0:8], k == 0, k == KT - 1)
                        last.then_inc(psum.full_of("d_ba"), 1)
                    b = psum.claim(pe, name)
                    for row0, m, half, c0 in parts:
                        for k in range(KT):
                            last = mm(b[row0:row0 + m, half * T:(half + 1) * T], w[:, k, c0 - base:c0 - base + m],
                                      hT[:, k, :], k == 0, k == KT - 1)
                        if len(parts) == 2 and not half:
                            yield
                    last.then_inc(psum.full_of(name), 1)
                    yield
                used.append(held)
                give_back()
                yield

            def head_norm(g, n, name):
                pe.wait_ge(S["o_sq"], n + 1)
                b = psum.claim(pe, name)
                mm(b[:, :], C("heads64"), g.sq[:, :, :]).then_inc(psum.full_of(name), 1)

            def gla(g, m):
                if m:
                    pe.wait_ge(S["code"], 1)
                    b = psum.claim(pe, "gk")
                    mm(b[:, 0:T], w_gk2[0:16, :], code[0:16, :]).then_inc(psum.full_of("gk"), 1)
                yield
                pe.wait_ge(S["v_T"], m + 1)
                b = psum.claim(pe, g.name + "_vt")
                for t in range(NT):
                    for p in range(2):
                        last = transpose(b[:, t * T + p * P:t * T + (p + 1) * P], g.vT[:, p, t * P:(t + 1) * P])
                last.then_inc(psum.full_of(g.name + "_vt"), 1)
                yield
                yield
                pe.wait_ge(S["kdT"], m + 1)
                b = psum.claim(pe, g.name + "_kdt")
                for t in range(NT):
                    for r in range(g.R):
                        at = (t * g.R + r) * P
                        last = transpose(b[:, at:at + P], g.kd[:, r, t * P:(t + 1) * P])
                last.then_inc(psum.full_of(g.name + "_kdt"), 1)
                yield
                pe.wait_ge(S["kd_tok"], m + 1)
                pe.wait_ge(S["vexp"], m + 1)
                d = g.R * P // 4
                for t in range(NT):
                    for r in range(g.R):
                        name = f"{g.name}_G{r}{t}"
                        b = psum.claim(pe, name)
                        for h in range(4 // g.R * r, 4 // g.R * (r + 1)):
                            row0 = d * h - P * r
                            last = mm(shaped(b, SUBP, HD)[row0:row0 + d, :, :], g.kdtok[:, t, d * h:d * h + d],
                                      g.vexp[:, t, :, HD * h:HD * h + HD])
                        last.then_inc(psum.full_of(name), 1)
                    yield
                pe.wait_ge(S["state"], m + 1)
                pe.wait_ge(S["q_decayed"], m + 1)
                for p in range(2):
                    name = f"{g.name}_o{p}"
                    b = psum.claim(pe, name)
                    for s in range(NSUB):
                        for h in (2 * p, 2 * p + 1):
                            r, row0 = (d * h) // P, (d * h) % P
                            last = mm(b[HD * (h % 2):HD * (h % 2) + HD, SUB * s:SUB * s + SUB], g.S[row0:row0 + d, r, s, :],
                                      g.qe[row0:row0 + d, r, SUB * s:SUB * s + SUB])
                    last.then_inc(psum.full_of(name), 1)
                yield
                yield
                for i in range(SUB):
                    pe.wait_ge(S["weighted"], SUB * m + i + 1)
                    name, n = f"{g.name}_band{i}", NSUB * (SUB - i)
                    b = psum.claim(pe, name)
                    w = g.band["w"][:, i % 2, :]
                    if g.R == 2:
                        last = mm(b[:, 0:2 * n], C("heads64"), w[:, 0:2 * n])
                    else:
                        for p in range(2):
                            last = mm(b[:, p * n:(p + 1) * n], C("to_pair")[:, p * P:(p + 1) * P], w[:, 0:n])
                    last.then_inc(psum.full_of(name), 1)
                    yield
                yield
                head_norm(g, m, g.name + "_ss")
                yield

            def mla():
                yield
                pe.wait_ge(S["mla_sq"], 1)
                b = psum.claim(pe, "c_ss")
                mm(b[:, 0:T], C("ones"), crs[:, 0, :], True, False)
                mm(b[:, 0:T], C("ones"), crs[:, 1, :], False, True)
                mm(b[:, T:2 * T], C("ones"), rtmp[:, 0, :]).then_inc(psum.full_of("c_ss"), 1)
                pe.wait_ge(S["mla_c"], 2)
                b = psum.claim(pe, "kr_rot")
                mm(b[64:96, 0:T], C("rot96")[64:96, 64:96], kr[64:96, :]).then_inc(psum.full_of("kr_rot"), 1)
                yield
                yield
                pe.wait_ge(S["mla_cn"], 1)
                for j in range(2):
                    b = psum.claim(pe, f"qT{j}")
                    for i in range(2):
                        h = 2 * j + i
                        for k in range(2):
                            last = mm(b[0:96, i * T:(i + 1) * T], w_uq[:, k, 96 * h:96 * h + 96], cn[:, k, :], k == 0, k == 1)
                    last.then_inc(psum.full_of(f"qT{j}"), 1)
                for j in range(2):
                    b = psum.claim(pe, f"kT{j}")
                    for i in range(2):
                        h = 2 * j + i
                        last = mm(b[0:64, i * T:(i + 1) * T], w_ukv[:, P * h:P * h + 64], cn[:, 2, :])
                    last.then_inc(psum.full_of(f"kT{j}"), 1)
                b = psum.claim(pe, "c_v")
                for t in range(NT):
                    last = mm(shaped(b[:, t * T:(t + 1) * T], 4, HD), cn[:, 2, t * P:(t + 1) * P],
                              shaped(w_ukv, 4, P)[:, :, 64:P])
                last.then_inc(psum.full_of("c_v"), 1)
                yield
                pe.wait_ge(S["rot_in"], 2)
                for j in range(2):
                    b = psum.claim(pe, f"rot{j}")
                    mm(b[0:96, :], C("rot96", 96), qT[0:96, 2 * j:2 * j + 2, :]).then_inc(psum.full_of(f"rot{j}"), 1)
                yield
                pe.wait_ge(S["qT"], 1)
                pe.wait_ge(S["kT"], 2)
                for t in range(NT):
                    n = P * (t + 1)
                    for j in range(2):
                        b = psum.claim(pe, f"c_sc{t}{j}")
                        for i in range(2):
                            h = 2 * j + i
                            last = mm(b[:, i * n:(i + 1) * n], qT[0:96, h, t * P:(t + 1) * P], kT[0:96, h, 0:n])
                        last.then_inc(psum.full_of(f"c_sc{t}{j}"), 1)
                    yield
                    yield
                    pe.wait_ge(S["probs"], t + 1)
                    for kt in range(t + 1):
                        b = psum.claim(pe, f"c_pt{t}{kt}")
                        for h in range(4):
                            last = transpose(b[:, h * P:(h + 1) * P], Pr[:, h, kt * P:(kt + 1) * P])
                        last.then_inc(psum.full_of(f"c_pt{t}{kt}"), 1)
                    yield
                pe.wait_ge(S["PT"], 3)
                pe.wait_ge(S["mla_v"], 1)
                b = psum.claim(pe, "c_o")
                for h in range(4):
                    o = b[HD * (h % 2):HD * (h % 2) + HD, T * (h // 2):T * (h // 2) + T]
                    mm(o, vtokC[:, 0, HD * h:HD * h + HD], PT[:, 0, h, :], True, False)
                    last = mm(o[:, P:T], vtokC[:, 1, HD * h:HD * h + HD], PT[:, 1, h, P:T], False, True)
                last.then_inc(psum.full_of("c_o"), 1)
                yield

            def gdn():
                yield
                yield
                yield
                pe.wait_ge(S["l2_sq"], 1)
                for j in range(2):
                    b = psum.claim(pe, f"l2_{j}")
                    mm(b[:, :], C("heads64"), cth[:, 2 * j:2 * j + 2, :]).then_inc(psum.full_of(f"l2_{j}"), 1)
                yield
                pe.wait_ge(S["g_ready"], 1)
                b = psum.claim(pe, "bsum")
                mm(b[:, 0:8], C("cum"), sm["g"][:, :, :])
                mm(b[:, 8:16], C("heads64"), sm["g"][:, :, :]).then_inc(psum.full_of("bsum"), 1)
                for par_ in range(2):
                    name = f"brow{par_}"
                    b = psum.claim(pe, name)
                    for t in range(NT):
                        for hp in range(2):
                            at = (2 * t + hp) * P
                            h = 2 * hp + par_
                            last = mm(b[:, at:at + P], sm["g"][:, t, h:h + 1].broadcast_to([P, P]), C("cum"))
                    last.then_inc(psum.full_of(name), 1)
                yield
                yield
                pe.wait_ge(S["qk_norm"], 1)
                for what, base in (("k_tok", 2), ("v_tok", 4)):
                    b = psum.claim(pe, what)
                    for t in range(NT):
                        for p in range(2):
                            last = transpose(b[:, t * T + p * P:t * T + (p + 1) * P], cv[:, base + p, t * P:(t + 1) * P])
                    last.then_inc(psum.full_of(what), 1)
                yield
                for what, base in (("kk", 2), ("kq", 0)):
                    for par_ in range(2):
                        name = f"{what}{par_}"
                        b = psum.claim(pe, name)
                        for t in range(NT):
                            for hp in range(2):
                                at, row0 = (2 * t + hp) * P, HD * par_
                                last = mm(b[:, at:at + P], cv[row0:row0 + HD, 2 + hp, t * P:(t + 1) * P],
                                          cv[row0:row0 + HD, base + hp, t * P:(t + 1) * P])
                        last.then_inc(psum.full_of(name), 1)

                def eight(what, f, copied=None):
                    for j in range(2):
                        if copied:
                            pe.wait_ge(S["level_X"], copied + j)
                        b = psum.claim(pe, f"{what}{j}")
                        for i in range(4):
                            last = f(b[:, i * P:(i + 1) * P], 4 * j + i)
                        last.then_inc(psum.full_of(f"{what}{j}"), 1)

                yield
                yield
                pe.wait_ge(S["lmat"], 1)
                eight("nt", lambda o, e: transpose(o, lstr[:, e, :]))
                yield
                yield
                for n in range(1, 6):
                    pe.wait_ge(S["level_T"], n)
                    eight(f"X{n}_", lambda o, e: mm(o, pm[:, e, :], Tm[:, e, :]))
                    yield
                    if n < 5:
                        eight(f"TX{n}_", lambda o, e: mm(o, Um[:, e, :], Xm[:, e, :]), 2 * n - 1)
                    eight(f"UX{n}_", lambda o, e: mm(o, Xm[:, e, :], Um[:, e, :]), 2 * n - 1)
                    yield
                    yield
                pe.wait_ge(S["level_T"], 6)
                pe.wait_ge(S["tok_D"], 1)
                b = psum.claim(pe, "u")
                for par_ in range(2):
                    for t in range(NT):
                        for hp in range(2):
                            h, e = 2 * hp + par_, 4 * par_ + 2 * t + hp
                            last = mm(b[:, t * T + HD * h:t * T + HD * h + HD], Um[:, e, :], vb[:, t, HD * h:HD * h + HD])
                last.then_inc(psum.full_of("u"), 1)
                b = psum.claim(pe, "wT")
                for par_ in range(2):
                    for t in range(NT):
                        for hp in range(2):
                            h, e = 2 * hp + par_, 4 * par_ + 2 * t + hp
                            last = mm(b[HD * par_:HD * par_ + HD, hp * T + t * P:hp * T + (t + 1) * P],
                                      kbe[:, t, HD * h:HD * h + HD], Um[:, e, :])
                last.then_inc(psum.full_of("wT"), 1)
                yield
                pe.wait_ge(S["uw"], 2)
                pe.wait_ge(S["qe"], 1)
                for c in range(4):
                    t, tok0, chunk = c // 2, CHUNK * (c % 2), slice(CHUNK * c, CHUNK * (c + 1))
                    pe.wait_ge(S["state_D"], c + 1)
                    for par_ in range(2):
                        rows = slice(HD * par_, HD * par_ + HD)
                        b = psum.claim(pe, f"ws{c}{par_}")
                        for hp in range(2):
                            last = mm(b[tok0:tok0 + CHUNK, hp * HD:(hp + 1) * HD], wT[rows, hp, chunk], SD[rows, c, hp, :])
                        last.then_inc(psum.full_of(f"ws{c}{par_}"), 1)
                    yield
                    if c < 3:
                        pe.wait_ge(S["v_new"], c + 1)
                        b = psum.claim(pe, f"su{c}")
                        for par_ in range(2):
                            for hp in range(2):
                                h = 2 * hp + par_
                                last = mm(b[HD * par_:HD * par_ + HD, hp * HD:(hp + 1) * HD],
                                          kdec[tok0:tok0 + CHUNK, t, HD * h:HD * h + HD],
                                          vnew[tok0:tok0 + CHUNK, t, HD * h:HD * h + HD])
                        last.then_inc(psum.full_of(f"su{c}"), 1)
                        yield
                o = psum.claim(pe, "D_o")
                for par_ in range(2):
                    rows = slice(HD * par_, HD * par_ + HD)
                    for c in range(4):
                        chunk = slice(CHUNK * c, CHUNK * (c + 1))
                        for hp in range(2):
                            last = mm(shaped(o, 2, T)[rows, hp, chunk], SD[rows, c, hp, :], qeD[rows, hp, chunk])
                last.then_inc(psum.full_of("D_o"), 1)
                pe.wait_ge(S["v_new"], 4)
                b = psum.claim(pe, "D_o2")
                for par_ in range(2):
                    for t in range(NT):
                        for hp in range(2):
                            h, e = 2 * hp + par_, 4 * par_ + 2 * t + hp
                            last = mm(b[HD * par_:HD * par_ + HD, hp * T + t * P:hp * T + (t + 1) * P],
                                      vnew[:, t, HD * h:HD * h + HD], lincT[:, e, :])
                last.then_inc(psum.full_of("D_o2"), 1)
                yield
                head_norm(oD, 2, "D_ss")
                yield

            def wide(what, lhs, tiles):
                banks = [psum.claim(pe, f"{what}{i}") for i in range(4)]
                held = None
                for k, (panel, cut) in enumerate(tiles):
                    if panel != held:
                        if held:
                            used.extend((held, held + "_hi"))
                        held = panel
                        w = split_panel(panel)
                    for t in range(NT):
                        for half in range(2):
                            last = mm3(banks[2 * t + half], [a[:, k, t * P:(t + 1) * P] for a in lhs],
                                       [a[:, cut, half * 512:half * 512 + 512] for a in w], k == 0, k == len(tiles) - 1)
                            if k == len(tiles) - 1:
                                last.then_inc(psum.full_of(f"{what}{2 * t + half}"), 1)
                used.extend((held, held + "_hi"))
                give_back()

            def rows_by(what, lhs, panel):
                for half in range(2):
                    banks = [psum.claim(pe, f"{what}{half}{t}") for t in range(NT)]
                    for quarter in range(2):
                        name = f"{panel}{2 * half + quarter}"
                        w = split_panel(name)
                        for t in range(NT):
                            for k in range(KT):
                                last = mm3(banks[t][:, quarter * 256:quarter * 256 + 256], [a[:, k, t * P:(t + 1) * P] for a in lhs],
                                           [a[:, k, :] for a in w], k == 0, k == KT - 1)
                            if quarter:
                                last.then_inc(psum.full_of(f"{what}{half}{t}"), 1)
                        used.extend((name, name + "_hi"))

            with pe.Fori(0, DEPTH) as layer:
                pe.wait_ge(once, 16)
                pe.wait_ge(S["params"], 64)
                norm_transposes(0)
                emit(ORDER, {"in": project(layer), "A": gla(G["A"], 0), "B": gla(G["B"], 1), "C": mla(), "D": gdn(), "out": iter(range(5))})
                pe.wait_ge(S["mix_split"], 1)
                rows_by("mix", (rounded(hT), rounded(mixT)), "out")
                norm_transposes(1)
                pe.wait_ge(S["h_split"], 1)
                h = (rounded(mixT), rounded(hT))
                for j in range(FT):
                    b = psum.claim(pe, f"ff{j}")
                    for half, what in enumerate(("gate", "up")):
                        name = f"{what}{j // 2}"
                        w = split_panel(name)
                        c = (j % 2) * P
                        for k in range(KT):
                            last = mm3(b[:, half * T:(half + 1) * T], [a[:, k, c:c + P] for a in w], [a[:, k, :] for a in h],
                                       k == 0, k == KT - 1)
                        if j % 2 and not half:
                            used.extend((name, name + "_hi"))
                    last.then_inc(psum.full_of(f"ff{j}"), 1)
                    if j % 2:
                        used.extend((name, name + "_hi"))
                pe.wait_ge(S["gT"], FT)
                wide("y", (rounded(gh), rounded(gl)), [(f"down{k // 2}", k % 2) for k in range(FT)])
                pe.drain().then_inc(layer_done, 1)
                pe.wait_ge(layer_open, layer + 1)

        @block.scalar
        def _(act):
            A_ = nc.scalar.activation

            def round_weights(layer, *names):
                for name in names:
                    raw = ring.wait(act, layer, name)
                    ring.wait_free(act, layer, name + "_hi")
                    A_(rounded(ring.view(name + "_hi")), raw, ACT.Copy).then_inc(S["w_hi"], 1)

            def norm_stats(k, step):
                for t in range(NT):
                    A_(xn[:, t, :], x[:, t, :], ACT.Square, accum_out=stat[:, t:t + 1])
                act.drain()
                step(A_(stat[:, 2:4], stat[:, 0:2], ACT.Ln, bias=C("eps"), scale=1.0 / DM))
                A_(stat[:, 4:6], stat[:, 2:4], ACT.Exp, scale=-0.5).then_inc(S["rstd"], 1)

            def norm_gain(k, gain):
                for j in (1, 3):
                    name = f"hT{k}_{j}"
                    act.wait_ge(*psum.filled(name))
                    for i in range(2):
                        last = A_(hT[:, 2 * j + i, :], psum.bank(name)[:, i * T:(i + 1) * T], ACT.Copy,
                                  scale=PAR(gain, 2 * j + i))
                    last.then_inc(*psum.freed(name))
                    act.drain().then_inc(S["hT"], 1)

            def drain_bank(name, out, signal, rows=slice(0, P), part=slice(0, 512), func=ACT.Copy, scale=1.0):
                act.wait_ge(*psum.filled(name))
                A_(out, psum.bank(name)[rows, part], func, scale=scale).then_inc(*psum.freed(name))
                if signal:
                    act.drain().then_inc(S[signal], 1)

            def post_norm(g, n, name, step):
                act.wait_ge(S["oT_ready"], n + 1)
                A_(g.sq[:, :, :], g.oT[:, :, :], ACT.Square).then_inc(S["o_sq"], 1)
                act.wait_ge(*psum.filled(name))
                ins = A_(g.rs[:, :, :], shaped(psum.bank(name), 2, T), ACT.Ln, bias=C("eps"), scale=1.0 / HD)
                ins.then_inc(*psum.freed(name))
                act.drain()
                A_(g.rs[:, :, :], g.rs[:, :, :], ACT.Exp, scale=-0.5).then_inc(S["o_rstd"], 1)

            def gla(g, m, step):
                if m == 0:
                    act.wait_ge(S["af_f"], 1)
                    A_(g.lf[:, :, :], g.lf[:, :, :], ACT.Ln)
                    A_(g.b[:, :, :], g.b[:, :, :], ACT.Ln, scale=2.0 ** 40).then_inc(S["af_ln"], 1)
                else:
                    act.wait_ge(S["gk_abs"], 1)
                    step(A_(g.e2[:, :, :], g.e2[:, :, :], ACT.Exp, scale=-1.0))
                    A_(g.e2[:, :, :], g.e2[:, :, :], ACT.Ln, bias=C("ones")[:, 0:1]).then_inc(S["gk_ln"], 1)
                yield
                act.wait_ge(S["scan"], m + 1)
                A_(g.eb[:, :, :], g.b[:, :, :], ACT.Exp).then_inc(S["exp_b"], 1)
                act.wait_ge(S["scan_end"], m + 1)
                A_(g.e2[:, :, :], g.e2[:, :, :], ACT.Exp, scale=-1.0).then_inc(S["kd_exp"], 1)
                yield
                drain_bank(g.name + "_vt", g.vtok[:, :, :], "vtok")
                yield
                yield
                yield
                yield
                yield
                for i in range(SUB):
                    n = SUB * m + i
                    act.wait_ge(S["diff"], n + 1)
                    if n >= 2:
                        act.wait_ge(S["weighted"], n - 1)
                    w = g.R * NSUB * (SUB - i)
                    A_(g.band["exp"][:, i % 2, 0:w], g.band["diff"][:, i % 2, 0:w], ACT.Exp).then_inc(S["decay"], 1)
                    yield
                yield
                yield
                post_norm(g, m, g.name + "_ss", step)
                yield

            def project():
                a, bb = G["A"], G["B"]
                yield
                yield
                act.wait_ge(*psum.filled("a_q"))
                A_(a.q[:, :, :], shaped(psum.bank("a_q"), 2, T), ACT.Tanh, scale=0.5).then_inc(S["aq_tanh"], 1)
                yield
                yield
                act.wait_ge(*psum.filled("a_f"))
                A_(a.lf[:, :, :], shaped(psum.bank("a_f"), 2, T), ACT.Sigmoid)
                A_(a.k[:, :, :], shaped(psum.bank("a_f"), 2, T), ACT.Sigmoid, scale=-1.0).then_inc(*psum.freed("a_f"))
                act.drain().then_inc(S["af_sig"], 1)
                yield
                yield
                drain_bank("a_i", a.vT[:, :, :], "v_T")
                yield
                yield
                drain_bank("a_g", a.gate[:, :, :], "gate_th", func=ACT.Tanh, scale=0.5)
                yield
                yield
                yield
                yield
                drain_bank("b_v", bb.vT[:, :, :], "v_T")
                yield
                drain_bank("code", code[0:16, :], "code", slice(0, 16), slice(0, T))
                yield
                yield
                act.wait_ge(*psum.filled("b_g"))
                A_(bb.gate[:, :, :], shaped(psum.bank("b_g"), 2, T), ACT.Tanh, scale=0.5).then_inc(S["bg_th"], 1)
                yield
                yield
                drain_bank("c_q", cT[:, 0:2, :], "mla_c")
                yield
                yield
                act.wait_ge(*psum.filled("c_kvr"))
                A_(cT[:, 2, :], psum.bank("c_kvr")[:, 0:T], ACT.Copy)
                A_(kr[64:96, :], psum.bank("c_kvr")[64:96, T:2 * T], ACT.Copy).then_inc(*psum.freed("c_kvr"))
                act.drain().then_inc(S["mla_c"], 1)
                for _ in range(6):
                    yield
                yield
                yield
                act.wait_ge(*psum.filled("d_z"))
                A_(oD.gate[:, :, :], shaped(psum.bank("d_z"), 2, T), ACT.Tanh, scale=0.5).then_inc(S["dz_th"], 1)
                yield

            def mla():
                act.wait_ge(S["gla_done"], 1)
                A_(crs[:, :, :], cT[:, 0:2, :], ACT.Square)
                A_(rtmp[:, 0, :], cT[:, 2, :], ACT.Square).then_inc(S["mla_sq"], 1)
                yield
                act.wait_ge(*psum.filled("c_ss"))
                A_(crs[:, 0, :], psum.bank("c_ss")[:, 0:T], ACT.Ln, bias=C("eps"), scale=1.0 / 256)
                A_(crs[:, 1, :], psum.bank("c_ss")[:, T:2 * T], ACT.Ln, bias=C("eps"), scale=1.0 / 128).then_inc(*psum.freed("c_ss"))
                act.drain()
                A_(crs[:, :, :], crs[:, :, :], ACT.Exp, scale=-0.5).then_inc(S["mla_rstd"], 1)
                yield
                yield
                for j in range(2):
                    act.wait_ge(*psum.filled(f"qT{j}"))
                    A_(qT[0:96, 2 * j:2 * j + 2, :], shaped(psum.bank(f"qT{j}"), 2, T)[0:96], ACT.Copy).then_inc(*psum.freed(f"qT{j}"))
                    act.drain().then_inc(S["rot_in"], 1)
                drain_bank("c_v", vtokC[:, :, :], "mla_v")
                yield
                yield
                for t in range(NT):
                    n = P * (t + 1)
                    yield
                    act.wait_ge(S["scores_max"], t + 1)
                    for h in range(4):
                        last = A_(Pr[:, h, 0:n], L[:, h, 0:n], ACT.Exp, bias=stat[:, 16 + 4 * t + h:17 + 4 * t + h],
                                  accum_out=stat[:, 24 + 4 * t + h:25 + 4 * t + h])
                    act.drain().then_inc(S["exps"], 1)
                    yield
                    for kt in range(t + 1):
                        drain_bank(f"c_pt{t}{kt}", PT[:, kt, :, t * P:(t + 1) * P], "PT")
                    yield
                drain_bank("c_o", mixT[:, 4:6, :], "mixT_C")
                yield

            def gdn(step):
                yield
                act.wait_ge(S["conv"], 1)
                A_(cth[:, :, :], cv[:, :, :], ACT.Tanh, scale=0.5).then_inc(S["conv_th"], 1)
                act.wait_ge(S["ba_in"], 1)
                A_(sm["beta"][:, :, :], zb[:, :, 0:4], ACT.Tanh, scale=0.5)
                yield
                step(A_(sm["l"][:, :, :], sm["e"][:, :, :], ACT.Exp, scale=-1.0))
                A_(sm["l"][:, :, :], sm["l"][:, :, :], ACT.Ln, bias=C("ones")[:, 0:1]).then_inc(S["ba_exp"], 1)
                act.wait_ge(S["conv_silu"], 1)
                A_(cth[:, 0:4, :], cv[:, 0:4, :], ACT.Square).then_inc(S["l2_sq"], 1)
                yield
                yield
                for j in range(2):
                    act.wait_ge(*psum.filled(f"l2_{j}"))
                    A_(lrs[:, 2 * j:2 * j + 2, :], shaped(psum.bank(f"l2_{j}"), 2, T), ACT.Ln, bias=C("eps")).then_inc(*psum.freed(f"l2_{j}"))
                act.drain()
                A_(lrs[:, :, :], lrs[:, :, :], ACT.Exp, scale=-0.5).then_inc(S["l2_rstd"], 1)
                yield
                act.wait_ge(S["b_small"], 1)
                A_(sm["eb"][:, :, :], sm["b"][:, :, :], ACT.Exp)
                A_(sm["fd"][:, :, :], sm["bl"][:, :, :], ACT.Exp).then_inc(S["b_exp"], 1)
                yield
                act.wait_ge(S["qk_norm"], 1)
                for j in range(2):
                    name = f"brow{j}"
                    act.wait_ge(*psum.filled(name))
                    A_(erow[:, 4 * j:4 * j + 4, :], shaped(psum.bank(name), 4, P), ACT.Exp)
                act.drain().then_inc(S["erow"], 1)
                yield
                act.wait_ge(S["hid"], 1)
                for par_ in range(2):
                    for t in range(NT):
                        for hp in range(2):
                            h, e = 2 * hp + par_, 4 * par_ + 2 * t + hp
                            A_(lstr[:, e, :], lstr[:, e, :], ACT.Exp, scale=-1.0, bias=sm["b"][:, t, h:h + 1])
                            last = A_(lincT[:, e, :], lincT[:, e, :], ACT.Exp, bias=sm["nb"][:, t, h:h + 1])
                last.then_inc(S["decays"], 1)
                yield
                yield
                for j in range(2):
                    drain_bank(f"nt{j}", NTm[:, 4 * j:4 * j + 4, :], "nt")
                yield
                yield
                for n in range(1, 6):
                    for j in range(2):
                        drain_bank(f"X{n}_{j}", Xm[:, 4 * j:4 * j + 4, :], "level_X")
                    yield
                    yield
                    yield
                drain_bank("u", uD[:, :, :], "uw")
                drain_bank("wT", wT[:, :, :], "uw")
                yield
                for _ in range(7):
                    yield
                yield
                post_norm(oD, 2, "D_ss", step)
                yield

            def split_out(layer):
                yield
                for i in range(4):
                    round_weights(layer, f"out{i}")
                    yield

            with act.Fori(0, DEPTH) as layer:
                step = Chain(act, S["act"])
                act.dma_start(par[:, :], A["par1"][layer, :, :]).then_inc(S["params"], 16)
                act.dma_start(w_uq, A["mla_w_uq"].rearrange("l (k p) n -> l p k n", p=P)[layer, :, :, :]).then_inc(S["params"], 16)
                act.dma_start(w_ukv, A["mla_w_ukv"][layer, :, :]).then_inc(S["params"], 16)
                act.dma_start(w_gk2[0:16, :], A["gla_w_gk2"][layer, :, :]).then_inc(S["params"], 16)
                act.wait_ge(once, 16)
                act.wait_ge(x_in, 32)
                norm_stats(0, step)
                act.wait_ge(S["params"], 64)
                A_(ea, PAR("a_log"), ACT.Exp)
                act.wait_ge(S["lb_max"], 1)
                A_(lb[:, 0:2 * DEPTH], lb[:, 0:2 * DEPTH], ACT.Exp).then_inc(S["lb_exp"], 1)
                norm_gain(0, "pre_mix")
                emit(ORDER, {"in": project(), "A": gla(G["A"], 0, step), "B": gla(G["B"], 1, step), "C": mla(), "D": gdn(step),
                             "out": split_out(layer)})
                def y_stats(k, names):
                    for i, name in enumerate(names):
                        act.wait_ge(*psum.filled(name))
                        A_(ysq[:, 0:512], psum.bank(name), ACT.Square, accum_out=stat[:, 40 + i:41 + i])
                        act.drain()
                    act.drain().then_inc(S["y_ss"], 1)
                    act.wait_ge(S["y_sum"], k + 1)
                    step(A_(stat[:, 46:48], stat[:, 44:46], ACT.Ln, bias=C("eps"), scale=1.0 / DM))
                    A_(stat[:, 48:50], stat[:, 46:48], ACT.Exp, scale=-0.5).then_inc(S["y_rstd"], 1)

                y_stats(0, [f"mix{half}{t}" for half in range(2) for t in range(NT)])
                act.wait_ge(S["x_new"], 1)
                norm_stats(1, step)
                norm_gain(1, "pre_ffn")
                round_weights(layer, "gate0", "up0")
                for j in range(FT):
                    q = j // 2 + 1
                    name = f"{('gate', 'up')[j % 2]}{q}" if q < FT // 2 else f"down{j - FT + 2}"
                    round_weights(layer, name)
                    act.wait_ge(*psum.filled(f"ff{j}"))
                    if j >= 2:
                        act.wait_ge(S["ff_conv"], j - 1)
                    A_(gpad[:, j % 2, 2:2 + T], psum.bank(f"ff{j}")[:, 0:T], ACT.Copy).then_inc(S["ff_gate"], 1)
                    act.wait_ge(S["ff_conv"], j + 1)
                    A_(gcv[:, j % 2, 2, :], gcv[:, j % 2, 1, :], ACT.Gelu_apprx_tanh).then_inc(S["ff_gelu"], 1)
                round_weights(layer, *[f"down{i}" for i in range(2, FT // 2)])
                y_stats(1, [f"y{i}" for i in (0, 2, 1, 3)])
                act.drain().then_inc(layer_done, 1)
                act.wait_ge(layer_open, layer + 1)

        @block.vector
        def _(dve):
            V = nc.vector

            def subtract_rounded(*names):
                for name in names:
                    dve.wait_ge(S["w_hi"], ring.split.index(name) + 1)
                    V.tensor_tensor(rounded(ring.view(name)), ring.view(name), as_float32(rounded(ring.view(name + "_hi"))), ALU.subtract).then_inc(S["w_split"], 1)

            def split(hi, lo, a):
                dve.drain()
                V.tensor_copy(rounded(hi), a)
                dve.drain()
                V.tensor_tensor(rounded(lo), a, as_float32(rounded(hi)), ALU.subtract)

            def wide_of(col, n):
                return col.broadcast_to([P, n])

            def norm(k, gain, step):
                dve.wait_ge(S["rstd"], k + 1)
                for t in range(NT):
                    last = V.tensor_scalar(xn[:, t, :], x[:, t, :], stat[:, 4 + t:5 + t], None, ALU.mult)
                last.then_inc(S["normed"], 1)
                for j in (0, 2):
                    name = f"hT{k}_{j}"
                    dve.wait_ge(*psum.filled(name))
                    for i in range(2):
                        last = V.tensor_scalar(hT[:, 2 * j + i, :], psum.bank(name)[:, i * T:(i + 1) * T],
                                               PAR(gain, 2 * j + i), None, ALU.mult)
                    last.then_inc(*psum.freed(name))
                    dve.drain().then_inc(S["hT"], 1)

            def silu_gate(g, name, signal, step):
                dve.wait_ge(S[signal], 1)
                ins = V.scalar_tensor_tensor(g.gate[:, :, :], g.gate[:, :, :], 1.0, shaped(psum.bank(name), 2, T), ALU.add, ALU.mult)
                ins.then_inc(*psum.freed(name))
                dve.drain()
                step(V.tensor_scalar(g.gate[:, :, :], g.gate[:, :, :], 0.5, None, ALU.mult))

            def head_out(g, n, gain, tile):
                dve.wait_ge(S["o_rstd"], n + 1)
                V.tensor_tensor(g.oT, g.oT, g.rs, ALU.mult)
                dve.drain()
                V.scalar_tensor_tensor(mixT[:, tile:tile + 2, :], g.oT, PAR(gain), g.gate, ALU.mult, ALU.mult)

            def gla(g, m, step):
                R = g.R
                flat = "p r (s c) -> p (r s) c"
                if m:
                    dve.wait_ge(*psum.filled("gk"))
                    V.tensor_scalar(g.lf[:, 0, :], psum.bank("gk")[:, 0:T], PAR("b_gk"), None, ALU.add).then_inc(*psum.freed("gk"))
                    dve.drain()
                    V.scalar_tensor_tensor(g.e2, g.lf, -1.0, g.lf, ALU.mult, ALU.max).then_inc(S["gk_abs"], 1)
                    step(V.tensor_scalar(g.lf, g.lf, 0.0, None, ALU.min))
                    yield
                    dve.wait_ge(S["gk_ln"], 1)
                    step(V.tensor_tensor(g.lf, g.lf, g.e2, ALU.subtract))
                    step(V.tensor_scalar(g.lf, g.lf, 1.0 / 16.0, None, ALU.mult))
                else:
                    yield
                    dve.wait_ge(S["af_ln"], 1)
                    step(V.tensor_tensor(g.lf, g.b, g.lf, ALU.add))
                for r in range(R):
                    last = V.tensor_tensor_scan(g.b[:, r, :], C("restart"), g.lf[:, r, :], 0.0, ALU.mult, ALU.add)
                last.then_inc(S["scan"], 1)
                dve.wait_ge(S["scan"], m + 1)
                b4 = g.b.rearrange(flat, c=SUB)
                V.tensor_tensor(g.e2.rearrange(flat, c=SUB), b4,
                                b4[:, :, SUB - 1:SUB].broadcast_to([P, R * NSUB, SUB]), ALU.subtract).then_inc(S["scan_end"], 1)
                yield
                dve.wait_ge(S["exp_b"], m + 1)
                V.tensor_tensor(g.qe, g.q, g.eb, ALU.mult).then_inc(S["q_decayed"], 1)
                dve.wait_ge(S["kd_exp"], m + 1)
                V.tensor_tensor(g.kd, g.k, g.e2, ALU.mult).then_inc(S["kdT"], 1)
                yield
                name = g.name + "_kdt"
                dve.wait_ge(*psum.filled(name))
                V.tensor_copy(g.kdtok, shaped(psum.bank(name)[:, 0:NT * R * P], NT, R * P)).then_inc(*psum.freed(name))
                dve.drain().then_inc(S["kd_tok"], 1)
                dve.wait_ge(S["vtok"], m + 1)
                for t in range(NT):
                    last = V.tensor_tensor(g.vexp[:, t, :, :], g.vtok[:, t:t + 1, :].broadcast_to([P, SUBP, GW]),
                                           C("sub").unsqueeze(2).broadcast_to([P, SUBP, GW]), ALU.mult)
                last.then_inc(S["vexp"], 1)
                V.memset(g.S[:, :, 0, :], 0.0)
                dve.drain()
                yield
                for s in range(NSUB - 1):
                    t = s // SUBP
                    if s == SUBP:
                        yield
                    for r in range(R):
                        name = f"{g.name}_G{r}{t}"
                        if s % SUBP == 0:
                            dve.wait_ge(*psum.filled(name))
                        ins = V.scalar_tensor_tensor(g.S[:, r, s + 1, :], g.S[:, r, s, :], g.eb[:, r, SUB * s + SUB - 1:SUB * s + SUB],
                                                     shaped(psum.bank(name), SUBP, HD)[:, s % SUBP, :], ALU.mult, ALU.add)
                        if s % SUBP == SUBP - 1 or s == NSUB - 2:
                            ins.then_inc(*psum.freed(name))
                            dve.drain()
                        elif r == R - 1:
                            step(ins)
                dve.drain().then_inc(S["state"], 1)
                yield
                for p in range(2):
                    name = f"{g.name}_o{p}"
                    dve.wait_ge(*psum.filled(name))
                    V.tensor_copy(g.oT[:, p, :], psum.bank(name)[:, 0:T]).then_inc(*psum.freed(name))

                yield

                def view(kind, i, n):
                    return g.band[kind][:, i % 2, 0:n * NSUB * (SUB - i)].rearrange("p (a c) -> p a c", c=SUB - i)

                def apply(i):
                    name, n = f"{g.name}_band{i}", 2 * NSUB * (SUB - i)
                    dve.wait_ge(*psum.filled(name))
                    V.tensor_tensor(view("o", i, 2), psum.bank(name)[:, 0:n].rearrange("p (a c) -> p a c", c=SUB - i),
                                    shifted(g.vT, i), ALU.mult).then_inc(*psum.freed(name))
                    dve.drain()
                    V.tensor_tensor(bands(g.oT, i), bands(g.oT, i), view("o", i, 2), ALU.add)

                for i in range(SUB + 1):
                    n = SUB * m + i
                    if i < SUB:
                        V.tensor_tensor(view("diff", i, R), bands(g.b, i), shifted(g.b, i), ALU.subtract).then_inc(S["diff"], 1)
                    if i > 0:
                        dve.wait_ge(S["decay"], n)
                        dve.wait_ge(S["qk"], n)
                        V.tensor_tensor(view("w", i - 1, R), view("qk", i - 1, R), view("exp", i - 1, R), ALU.mult).then_inc(S["weighted"], 1)
                    if i > 1:
                        apply(i - 2)
                    yield
                apply(SUB - 1)
                dve.drain().then_inc(S["oT_ready"], 1)
                yield
                head_out(g, m, ("hgrn_norm", "gla_norm")[m], 2 * m)
                if m:
                    dve.drain().then_inc(S["gla_done"], 1)
                yield

            def project(a, bb, lower, rest, step):
                yield
                yield
                dve.wait_ge(S["aq_tanh"], 1)
                ins = V.scalar_tensor_tensor(a.q, a.q, 1.0, shaped(psum.bank("a_q"), 2, T), ALU.add, ALU.mult)
                ins.then_inc(*psum.freed("a_q"))
                dve.drain()
                V.tensor_scalar(a.q, a.q, 0.5 * HD ** -0.5, None, ALU.mult)
                yield
                yield
                dve.wait_ge(S["af_sig"], 1)
                for r in range(2):
                    V.tensor_scalar(a.k[:, r, :], a.k[:, r, :], rest[:, r:r + 1], None, ALU.mult)
                    last = V.tensor_scalar(a.lf[:, r, :], a.lf[:, r, :], rest[:, r:r + 1], lower[:, r:r + 1], ALU.mult, ALU.add)
                step(last)
                step(V.tensor_scalar(a.b, a.lf, 1e-30, 2.0 ** -40, ALU.max, ALU.min))
                V.tensor_scalar(a.lf, a.lf, 2.0 ** -40, None, ALU.max).then_inc(S["af_f"], 1)
                for _ in range(4):
                    yield
                dve.wait_ge(S["gate_th"], 1)
                V.tensor_scalar(a.gate, a.gate, 0.5, 0.5, ALU.mult, ALU.add)
                yield
                yield
                dve.wait_ge(*psum.filled("b_qk"))
                V.tensor_scalar(bb.q[:, 0, :], psum.bank("b_qk")[:, 0:T], 32 ** -0.5, None, ALU.mult)
                V.tensor_copy(bb.k[:, 0, :], psum.bank("b_qk")[:, T:2 * T]).then_inc(*psum.freed("b_qk"))
                for _ in range(5):
                    yield
                silu_gate(bb, "b_g", "bg_th", step)
                for _ in range(4):
                    yield
                V.memset(cin[:, :, 0:3], 0.0)
                for i, name in enumerate(("d_q", "d_k", "d_v")):
                    yield
                    yield
                    dve.wait_ge(*psum.filled(name))
                    V.tensor_copy(cin[:, 2 * i:2 * i + 2, 3:3 + T], shaped(psum.bank(name), 2, T)).then_inc(*psum.freed(name))
                yield
                yield
                dve.wait_ge(*psum.filled("d_ba"))
                V.tensor_copy(zb, shaped(psum.bank("d_ba")[:, 0:16], NT, 8)).then_inc(*psum.freed("d_ba"))
                silu_gate(oD, "d_z", "dz_th", step)
                yield

            def mla(step):
                yield
                yield
                dve.wait_ge(S["mla_rstd"], 1)
                for i in range(3):
                    gain = PAR("q_norm", i) if i < 2 else PAR("kv_norm")
                    last = V.scalar_tensor_tensor(cn[:, i, :], cT[:, i, :], gain, crs[:, i // 2, :], ALU.mult, ALU.mult)
                last.then_inc(S["mla_cn"], 1)
                cos, sin = C("cos96"), C("sin96")
                dve.wait_ge(*psum.filled("kr_rot"))
                V.tensor_tensor(rtmp[64:96, 1, :], psum.bank("kr_rot")[64:96, 0:T], sin[64:96, :], ALU.mult).then_inc(*psum.freed("kr_rot"))
                step(V.tensor_tensor(rtmp[64:96, 2, :], kr[64:96, :], cos[64:96, :], ALU.mult))
                V.tensor_tensor(kT[64:96, :, :], rtmp[64:96, 1:2, :].broadcast_to([32, 4, T]),
                                rtmp[64:96, 2:3, :].broadcast_to([32, 4, T]), ALU.add).then_inc(S["kr_done"], 1)
                yield
                for j in range(2):
                    name = f"kT{j}"
                    dve.wait_ge(*psum.filled(name))
                    V.tensor_copy(kT[0:64, 2 * j:2 * j + 2, :], shaped(psum.bank(name), 2, T)[0:64]).then_inc(*psum.freed(name))
                    dve.drain().then_inc(S["kT"], 1)
                yield
                for j in range(2):
                    name = f"rot{j}"
                    dve.wait_ge(*psum.filled(name))
                    V.tensor_tensor(rtmp[0:96, 2 * j:2 * j + 2, :], shaped(psum.bank(name), 2, T)[0:96],
                                    sin[0:96, :].unsqueeze(1).broadcast_to([96, 2, T]), ALU.mult).then_inc(*psum.freed(name))
                step(V.tensor_tensor(qT[0:96], qT[0:96], cos[0:96, :].unsqueeze(1).broadcast_to([96, 4, T]), ALU.mult))
                V.tensor_tensor(qT[0:96], qT[0:96], rtmp[0:96], ALU.add).then_inc(S["qT"], 1)
                mask = shaped(C("causal"), NT, T)
                for t in range(NT):
                    n = P * (t + 1)
                    yield
                    if t:
                        dve.wait_ge(*psum.filled("c_pt00"))
                        dve.wait_ge(S["exps"], t)
                    for j in range(2):
                        name = f"c_sc{t}{j}"
                        dve.wait_ge(*psum.filled(name))
                        V.scalar_tensor_tensor(L[:, 2 * j:2 * j + 2, 0:n], shaped(psum.bank(name)[:, 0:2 * n], 2, n), 96 ** -0.5,
                                               mask[:, t:t + 1, 0:n].broadcast_to([P, 2, n]), ALU.mult, ALU.add).then_inc(*psum.freed(name))
                    dve.drain()
                    step(V.tensor_reduce(stat[:, 32:36], L[:, :, 0:n], AX.X, ALU.max))
                    V.tensor_scalar(stat[:, 16 + 4 * t:20 + 4 * t], stat[:, 32:36], -1.0, None, ALU.mult).then_inc(S["scores_max"], 1)
                    yield
                    dve.wait_ge(S["exps"], t + 1)
                    step(V.reciprocal(stat[:, 36:40], stat[:, 24 + 4 * t:28 + 4 * t]))
                    V.tensor_tensor(Pr[:, :, 0:n], Pr[:, :, 0:n], stat[:, 36:40].unsqueeze(2).broadcast_to([P, 4, n]), ALU.mult)
                    dve.drain().then_inc(S["probs"], 1)
                    yield
                yield
                yield

            def gdn(step):
                w = shaped(PAR("conv"), 6, 4)
                for r in range(6):
                    V.tensor_scalar(cv[:, r, :], cin[:, r, 3:3 + T], w[:, r, 3:4], None, ALU.mult)
                for i in range(3):
                    dve.drain()
                    for r in range(6):
                        V.scalar_tensor_tensor(cv[:, r, :], cin[:, r, i:i + T], w[:, r, i:i + 1], cv[:, r, :], ALU.mult, ALU.add)
                dve.drain().then_inc(S["conv"], 1)
                V.tensor_tensor(sm["x"], zb[:, :, 4:8], PAR("dt_bias").unsqueeze(1).broadcast_to([P, NT, 4]), ALU.add)
                dve.drain()
                V.scalar_tensor_tensor(sm["e"], sm["x"], -1.0, sm["x"], ALU.mult, ALU.max)
                dve.drain().then_inc(S["ba_in"], 1)
                yield
                dve.wait_ge(S["conv_th"], 1)
                step(V.tensor_scalar(cth, cth, 0.5, 0.5, ALU.mult, ALU.add))
                V.tensor_tensor(cv, cv, cth, ALU.mult).then_inc(S["conv_silu"], 1)
                yield
                yield
                dve.wait_ge(S["ba_exp"], 1)
                V.tensor_scalar(sm["beta"], sm["beta"], 0.5, 0.5, ALU.mult, ALU.add)
                step(V.scalar_tensor_tensor(sm["g"], sm["x"], 0.0, sm["l"], ALU.max, ALU.add))
                V.scalar_tensor_tensor(sm["g"], sm["g"], -1.0, ea.unsqueeze(1).broadcast_to([P, NT, 4]), ALU.mult, ALU.mult).then_inc(S["g_ready"], 1)
                yield
                yield
                dve.wait_ge(S["l2_rstd"], 1)
                V.scalar_tensor_tensor(cv[:, 0:2, :], cv[:, 0:2, :], HD ** -0.5, lrs[:, 0:2, :], ALU.mult, ALU.mult)
                V.tensor_tensor(cv[:, 2:4, :], cv[:, 2:4, :], lrs[:, 2:4, :], ALU.mult)
                dve.drain().then_inc(S["qk_norm"], 1)
                dve.wait_ge(*psum.filled("bsum"))
                bs = psum.bank("bsum")
                V.tensor_copy(sm["b"], shaped(bs[:, 0:8], NT, 4))
                V.tensor_copy(sm["x"], shaped(bs[:, 8:16], NT, 4)).then_inc(*psum.freed("bsum"))
                dve.drain()
                V.tensor_scalar(sm["nb"], sm["b"], -1.0, None, ALU.mult)
                V.tensor_tensor(sm["bl"], sm["x"], sm["b"], ALU.subtract)
                dve.drain().then_inc(S["b_small"], 1)
                yield
                dve.wait_ge(S["b_exp"], 1)
                step(V.tensor_tensor(sm["be"], sm["beta"], sm["eb"], ALU.mult))
                dve.wait_ge(S["erow"], 1)
                for j in range(2):
                    name = f"brow{j}"
                    brow = shaped(psum.bank(name), 4, P)
                    V.tensor_tensor(lstr[:, 4 * j:4 * j + 4, :], brow, C("hide_strict").unsqueeze(1).broadcast_to([P, 4, P]), ALU.add)
                    V.tensor_tensor(lincT[:, 4 * j:4 * j + 4, :], brow, C("hide_incl").unsqueeze(1).broadcast_to([P, 4, P]), ALU.add).then_inc(*psum.freed(name))
                dve.drain().then_inc(S["hid"], 1)
                V.memset(SD[:, 0], 0.0)
                dve.drain().then_inc(S["state_D"], 1)

                def per_head(sc):
                    return sc.rearrange("p t h -> p (t h)").unsqueeze(2).broadcast_to([P, 8, HD])

                def by_head(tok):
                    return tok.rearrange("p t (h d) -> p (t h) d", d=HD)

                yield
                dve.wait_ge(*psum.filled("k_tok"))
                V.tensor_copy(ktok, shaped(psum.bank("k_tok"), NT, GW)).then_inc(*psum.freed("k_tok"))
                dve.wait_ge(*psum.filled("v_tok"))
                V.tensor_copy(vtokD, shaped(psum.bank("v_tok"), NT, GW)).then_inc(*psum.freed("v_tok"))
                dve.drain()
                V.tensor_tensor(by_head(kbe), by_head(ktok), per_head(sm["be"]), ALU.mult)
                V.tensor_tensor(by_head(vb), by_head(vtokD), per_head(sm["beta"]), ALU.mult)
                dve.drain()
                V.tensor_tensor(by_head(kdec), by_head(ktok), per_head(sm["fd"]), ALU.mult)
                dve.drain().then_inc(S["tok_D"], 1)
                for par_ in range(2):
                    rows = slice(HD * par_, HD * par_ + HD)
                    ev = erow[:, :, :].rearrange("p (q t h) c -> p q h t c", q=2, t=NT)
                    for hp in range(2):
                        V.tensor_tensor(qeD[rows, hp, :].rearrange("p (t c) -> p t c", t=NT), cv[rows, hp, :].rearrange("p (t c) -> p t c", t=NT),
                                        ev[rows, par_, hp, :, :], ALU.mult)
                dve.drain().then_inc(S["qe"], 1)
                yield
                dve.wait_ge(S["decays"], 1)
                for par_ in range(2):
                    name = f"kk{par_}"
                    dve.wait_ge(*psum.filled(name))
                    for t in range(NT):
                        for hp in range(2):
                            h, i = 2 * hp + par_, 2 * t + hp
                            e = 4 * par_ + i
                            last = V.scalar_tensor_tensor(lstr[:, e, :], psum.bank(name)[:, i * P:(i + 1) * P], sm["beta"][:, t, h:h + 1],
                                                          lstr[:, e, :], ALU.mult, ALU.mult)
                    last.then_inc(*psum.freed(name))
                dve.drain().then_inc(S["lmat"], 1)
                for par_ in range(2):
                    name = f"kq{par_}"
                    dve.wait_ge(*psum.filled(name))
                    V.tensor_tensor(lincT[:, 4 * par_:4 * par_ + 4, :], shaped(psum.bank(name), 4, P),
                                    lincT[:, 4 * par_:4 * par_ + 4, :], ALU.mult).then_inc(*psum.freed(name))

                yield
                yield

                lvl = shaped(C("level"), 7, P)

                def eight_of(m):
                    return m.unsqueeze(1).broadcast_to([P, 8, P])

                V.tensor_tensor(Tm, lstr, eight_of(lvl[:, 6, :]), ALU.mult)
                dve.wait_ge(S["nt"], 2)
                V.tensor_tensor(Um, NTm, eight_of(lvl[:, 0, :]), ALU.mult)
                dve.drain()
                V.tensor_tensor(Tm, eight_of(C("ident")), Tm, ALU.subtract)
                V.tensor_tensor(Um, eight_of(C("ident")), Um, ALU.subtract)
                V.tensor_tensor(pm, NTm, eight_of(lvl[:, 1, :]), ALU.mult)
                dve.drain().then_inc(S["level_T"], 1)
                yield
                for n in range(1, 6):
                    yield
                    if n < 5:
                        dve.wait_ge(*psum.filled(f"X{n}_1"))
                        V.tensor_tensor(pm, NTm, eight_of(lvl[:, n + 1, :]), ALU.mult)
                    yield
                    for what, m in (("TX", Tm), ("UX", Um)):
                        if what == "TX" and n == 5:
                            continue
                        for j in range(2):
                            name = f"{what}{n}_{j}"
                            dve.wait_ge(*psum.filled(name))
                            mj = m[:, 4 * j:4 * j + 4, :]
                            V.tensor_tensor(mj, mj, shaped(psum.bank(name), 4, P), ALU.subtract).then_inc(*psum.freed(name))
                    dve.drain().then_inc(S["level_T"], 1)
                    yield

                yield
                dve.wait_ge(S["uw"], 2)
                for c in range(4):
                    t, tok0 = c // 2, CHUNK * (c % 2)
                    toks = slice(tok0, tok0 + CHUNK)
                    for par_ in range(2):
                        name = f"ws{c}{par_}"
                        dve.wait_ge(*psum.filled(name))
                        hv = "p (h q d) -> p q h d"
                        un, vn = (z[toks, t, :].rearrange(hv, q=2, d=HD)[:, par_] for z in (uD, vnew))
                        V.tensor_tensor(vn, un, shaped(psum.bank(name)[:, 0:P], 2, HD)[toks], ALU.subtract).then_inc(*psum.freed(name))
                    dve.drain().then_inc(S["v_new"], 1)
                    yield
                    if c < 3:
                        name = f"su{c}"
                        dve.wait_ge(*psum.filled(name))
                        for par_ in range(2):
                            rows = slice(HD * par_, HD * par_ + HD)
                            for hp in range(2):
                                e = 4 * par_ + 2 * t + hp
                                last = V.scalar_tensor_tensor(SD[rows, c + 1, hp, :], SD[rows, c, hp, :], erow[rows, e, tok0 + CHUNK - 1:tok0 + CHUNK],
                                                              psum.bank(name)[rows, hp * HD:(hp + 1) * HD], ALU.mult, ALU.add)
                        last.then_inc(*psum.freed(name))
                        dve.drain().then_inc(S["state_D"], 1)
                        yield
                dve.wait_ge(*psum.filled("D_o"))
                V.tensor_copy(oD.oT, shaped(psum.bank("D_o"), 2, T)).then_inc(*psum.freed("D_o"))
                dve.wait_ge(*psum.filled("D_o2"))
                dve.drain()
                V.tensor_tensor(oD.oT, oD.oT, shaped(psum.bank("D_o2"), 2, T), ALU.add).then_inc(*psum.freed("D_o2"))
                dve.drain().then_inc(S["oT_ready"], 1)
                yield
                head_out(oD, 2, "gdn_norm", 6)
                yield

            def split_out():
                dve.wait_ge(S["mixT_C"], 1)
                split(hT[:, 0:6, :], mixT[:, 0:6, :], mixT[:, 0:6, :])
                yield
                for i in range(4):
                    subtract_rounded(f"out{i}")
                    yield

            def residual(k, names, gain, step):
                dve.wait_ge(S["y_ss"], k + 1)
                V.tensor_tensor(stat[:, 44:46], stat[:, 40:42], stat[:, 42:44], ALU.add).then_inc(S["y_sum"], 1)
                dve.wait_ge(S["y_rstd"], k + 1)
                lo = PAR1[gain][0]
                for i, name in enumerate(names):
                    half, t = i // 2, i % 2
                    V.scalar_tensor_tensor(yn[:, i, :], psum.bank(name), stat[:, 48 + t:49 + t],
                                           par[:, lo + 512 * half:lo + 512 * half + 512], ALU.mult, ALU.mult).then_inc(*psum.freed(name))
                dve.drain()
                for i in range(4):
                    half, t = i // 2, i % 2
                    xs = x[:, t, 512 * half:512 * half + 512]
                    V.tensor_tensor(xs, xs, yn[:, i, :], ALU.add)
                dve.drain().then_inc(S["x_new"], 1)

            with dve.Fori(0, DEPTH) as layer:
                step = Chain(dve, S["dve"])
                dve.wait_ge(once, 16)
                dve.wait_ge(S["params"], 64)
                a, bb = G["A"], G["B"]
                lg = shaped(PAR("lb_logits"), 2, DEPTH)
                step(V.tensor_reduce(lb[:, 8:10], lg, AX.X, ALU.max))
                V.tensor_tensor(shaped(lb[:, 0:4], 2, DEPTH), lg, lb[:, 8:10].unsqueeze(2).broadcast_to([P, 2, DEPTH]),
                                ALU.subtract).then_inc(S["lb_max"], 1)
                norm(0, "pre_mix", step)
                dve.wait_ge(S["lb_exp"], 1)
                step(V.tensor_reduce(lb[:, 8:10], shaped(lb[:, 0:4], 2, DEPTH), AX.X, ALU.add))
                step(V.tensor_tensor(lb[:, 0:4], lb[:, 0:4], PAR("lb_of"), ALU.mult))
                V.tensor_reduce(lb[:, 10:12], shaped(lb[:, 0:4], 2, DEPTH), AX.X, ALU.add)
                step(V.reciprocal(lb[:, 12:14], lb[:, 8:10]))
                step(V.tensor_tensor(lb[:, 14:16], lb[:, 10:12], lb[:, 12:14], ALU.mult))
                step(V.tensor_scalar(lb[:, 16:18], lb[:, 14:16], -1.0, 1.0, ALU.mult, ALU.add))
                lower, rest = lb[:, 14:16], lb[:, 16:18]

                emit(ORDER, {"in": project(a, bb, lower, rest, step), "A": gla(a, 0, step), "B": gla(bb, 1, step), "C": mla(step),
                             "D": gdn(step), "out": split_out()})
                split(hT[:, 6:8, :], mixT[:, 6:8, :], mixT[:, 6:8, :])
                dve.drain().then_inc(S["mix_split"], 1)
                residual(0, [f"mix{half}{t}" for half in range(2) for t in range(NT)], "post_mix", step)
                norm(1, "pre_ffn", step)
                dve.wait_ge(S["hT"], 8)
                split(mixT, hT, hT)
                dve.drain().then_inc(S["h_split"], 1)
                subtract_rounded("gate0", "up0")

                fw = shaped(PAR("ffn_conv"), FT, 3)

                def finish(j):
                    dve.wait_ge(S["ff_gelu"], j + 1)
                    V.tensor_tensor(gcv[:, j % 2, 0, :], gcv[:, j % 2, 2, :], psum.bank(f"ff{j}")[:, T:2 * T], ALU.mult).then_inc(*psum.freed(f"ff{j}"))
                    split(gh[:, j, :], gl[:, j, :], gcv[:, j % 2, 0, :])
                    dve.drain().then_inc(S["gT"], 1)

                V.memset(gpad[:, :, 0:2], 0.0)
                dve.drain().then_inc(S["gpad_zero"], 1)
                for j in range(FT):
                    q = j // 2 + 1
                    subtract_rounded(f"{('gate', 'up')[j % 2]}{q}" if q < FT // 2 else f"down{j - FT + 2}")
                    dve.wait_ge(S["ff_gate"], j + 1)
                    step(V.tensor_scalar(gcv[:, j % 2, 0, :], gpad[:, j % 2, 2:2 + T], fw[:, j, 2:3], None, ALU.mult))
                    step(V.scalar_tensor_tensor(gcv[:, j % 2, 1, :], gpad[:, j % 2, 1:1 + T], fw[:, j, 1:2], gcv[:, j % 2, 0, :], ALU.mult, ALU.add))
                    V.scalar_tensor_tensor(gcv[:, j % 2, 1, :], gpad[:, j % 2, 0:T], fw[:, j, 0:1], gcv[:, j % 2, 1, :], ALU.mult, ALU.add).then_inc(S["ff_conv"], 1)
                    if j:
                        finish(j - 1)
                finish(FT - 1)
                subtract_rounded(*[f"down{i}" for i in range(2, FT // 2)])
                residual(1, [f"y{i}" for i in (0, 2, 1, 3)], "post_ffn", step)
                dve.drain().then_inc(layer_done, 1)
                dve.wait_ge(layer_open, layer + 1)

        @block.gpsimd
        def _(pool):
            with pool.Fori(0, DEPTH) as layer:
                for m, g in enumerate((G["A"], G["B"])):
                    pool.wait_ge(S["state"], m + 1)
                    for i in range(SUB):
                        n = SUB * m + i
                        if n >= 2:
                            pool.wait_ge(S["weighted"], n - 1)
                        out = g.band["qk"][:, i % 2, 0:g.R * NSUB * (SUB - i)].rearrange("p (a c) -> p a c", c=SUB - i)
                        nc.gpsimd.tensor_tensor(out, bands(g.q, i), shifted(g.k, i), ALU.mult).then_inc(S["qk"], 1)
                pool.wait_ge(layer_done, 3 * layer + 3)
                pool.sem_inc(barrier_taken, 1)
                for r in sem_ranges([s.num for s in S.values()] + [s.num for s in psum.full + psum.free]):
                    pool.sem_clear(r)
                pool.sem_inc(layer_open, 1)

        psum.check()


D_FF2 = 4096
UT = D_FF2 // P
IDX_HEADS = 8
TOPK = 64
TAKEN = -3e38
TWO_PI = (6.28125, 0.0019350051879882812, 3.0199159819e-07)
BY_PARITY = (0, 2, 1, 3)
CONST2, N_CONST2 = table([
    ("ident", P), ("cum", P), ("ones", P), ("heads64", P), ("rot64", P), ("rot32", P),
    ("causal", NT * T), ("window", NT * T), ("inv_freq", 2), ("eps", 1),
])
PAR2, N_PAR2 = table([
    ("pre_mix", KT), ("pre_mlp", KT), ("subln", 1), ("lam_q", 64), ("lam_k", 64), ("b_forget", 4),
    ("sinks", 4), ("lam_init", 1), ("lam_rest", 1), ("post_mix", DM), ("post_mlp", DM),
])
IN2 = [(0, 256), (256, 512), (512, 768), (768, 1024), (1024, 1280), (1280, 1352), (1352, 1608), (1608, 1864),
       (1864, 2124), (2124, 2380), (2380, 2636), (2636, 2892), (2892, 3148), (3148, 3404)]


def shape_constants2():
    c = np.zeros((P, N_CONST2), np.float32)

    def put(name, a):
        lo, hi = CONST2[name]
        c[:a.shape[0], lo:hi] = a.reshape(a.shape[0], -1)

    i = np.arange(P)
    put("ident", np.eye(P, dtype=np.float32))
    put("cum", (i[:, None] <= i[None, :]).astype(np.float32))
    put("ones", np.ones((P, P), np.float32))
    put("heads64", ((i[:, None] // 64) == (i[None, :] // 64)).astype(np.float32))
    inv = np.zeros((P, 2), np.float32)
    for n, (name, half) in enumerate((("rot64", 32), ("rot32", 16))):
        rot = np.zeros((P, P), np.float32)
        for m in range(P):
            if m % (2 * half) < half:
                rot[m + half, m] = -1.0
            else:
                rot[m - half, m] = 1.0
        put(name, rot)
        f = (np.float32(10000.0) ** (-np.arange(half, dtype=np.float32) / np.float32(half))).astype(np.float32)
        inv[:, n] = f[i % half]
    put("inv_freq", inv)
    key, q = np.arange(T)[None, :], i[:, None]
    put("causal", np.stack([np.where(key <= q + P * t, 0.0, NEG) for t in range(NT)], 1).astype(np.float32))
    put("window", np.stack([np.where((key <= q + P * t) & (q + P * t - key < P), 0.0, NEG) for t in range(NT)], 1).astype(np.float32))
    put("eps", np.full((P, 1), EPS, np.float32))
    return c


def params2(a):
    out = np.zeros((DEPTH, P, N_PAR2), np.float32)

    def put(name, layer, v):
        lo, hi = PAR2[name]
        out[layer, :, lo:hi] = v

    def cols(v):
        return np.asarray(v).reshape(-1, P).T

    def rows(v):
        v = np.asarray(v)
        return np.broadcast_to(v, (P,) + v.shape)

    for l in range(DEPTH):
        lam_init = 0.8 - 0.6 * float(np.exp(-0.3 * l))
        put("pre_mix", l, cols(a["norm_pre_mix_2"][l]))
        put("pre_mlp", l, cols(a["norm_pre_mlp_2"][l]))
        put("subln", l, np.concatenate([a["diff_subln_2"][l]] * 2)[:, None])
        put("lam_q", l, rows(np.concatenate([a["lambda_q1_2"][l], a["lambda_q2_2"][l]])))
        put("lam_k", l, rows(np.concatenate([a["lambda_k1_2"][l], a["lambda_k2_2"][l]])))
        put("b_forget", l, rows(a["b_forget_2"][l]))
        put("sinks", l, rows(np.asarray(a["sinks_2"][l])[list(BY_PARITY)]))
        put("lam_init", l, np.float32(lam_init))
        put("lam_rest", l, np.float32(1.0 - lam_init))
        put("post_mix", l, rows(a["norm_post_mix_2"][l]))
        put("post_mlp", l, rows(a["norm_post_mlp_2"][l]))
    return out

SIGNALS2 = """w_split raw hT probs PT nlf normed roped copied o_sq mix_split params h_split gT p_split x_new w_hi
rstd score_max exps c_oT o_rstd mixT y_ss y_sum y_rstd act lam_sum lam_exp gate_abs gate_ln
relu_used relu pT_in ff_relu ff_squared g_hi proj gates cosined""".split()


def block2(nc, kept, banks, x, A):
    with ExitStack() as ctx:
        QKV, WORK = 28 * T, 16128
        memory = Memory(nc, ctx, "b2", {"ring": SLOTS * KT * PANEL, "zone": QKV + WORK,
                                        "small": N_CONST2 + N_PAR2 + 2 * KT * T + 128 + 4 * T + 4 * T + NT * (8 + 4 * 4) + 80})
        rounded, buf = memory.rounded, memory.area("small")

        S = {n: ctx.enter_context(nc.semaphore("b2_" + n)) for n in SIGNALS2}
        psum = Psum(nc, ctx, "b2", banks)
        layer_done = kept.enter_context(nc.semaphore("b2_layer_done"))
        layer_open = kept.enter_context(nc.semaphore("b2_layer_open"))
        barrier_taken = kept.enter_context(nc.semaphore("b2_barrier_taken"))
        once = kept.enter_context(nc.semaphore("b2_constants_in"))
        tables_made = kept.enter_context(nc.semaphore("b2_tables_made"))
        angles = kept.enter_context(nc.semaphore("b2_angles"))

        def cols(src):
            return src.rearrange("l (k p) n -> l p k n", p=P)

        win, wout, wup, wgate = cols(A["w_in_2"]), cols(A["w_out_2"]), cols(A["w_mlp_up_2"]), cols(A["w_ple_gate_2"])
        wdown, wproj = cols(A["w_mlp_down_2"]), cols(A["w_ple_proj_2"])
        panels = [(f"in{i}", lambda l, c0=c0, c1=c1: win[l, :, :, c0:c1], KT, c0, c1) for i, (c0, c1) in enumerate(IN2)]
        late = [(f"out{i}", lambda l, i=i: wout[l, :, :, 256 * i:256 * i + 256], KT, 0, 256) for i in range(4)]
        late += [(f"up{i}", lambda l, i=i: wup[l, :, :, 256 * i:256 * i + 256], KT, 0, 256) for i in range(UT // 2)]
        late += [(f"down{i}", lambda l, i=i: wdown[l, :, 2 * i:2 * i + 2, :], 2, 0, DM) for i in range(UT // 2)]
        late += [("proj", lambda l: wproj[l, :, :, :], 2, 0, DM)]
        late += [(f"ple{i}", lambda l, i=i: wgate[l, :, :, 256 * i:256 * i + 256], KT, 0, 256) for i in range(4)]
        panels += with_parts(late)
        ring = Ring(nc, kept, "b2", panels, memory.area("ring")(SLOTS, KT * PANEL))

        const = buf(N_CONST2)
        par = buf(N_PAR2)

        def C(name, rows=P):
            lo, hi = CONST2[name]
            return const[0:rows, lo:hi]

        def PAR(name, i=None, n=1):
            lo, hi = PAR2[name]
            return par[:, lo:hi] if i is None else par[:, lo + i:lo + i + n]

        hT = buf(KT, T)
        mixT = buf(KT, T)
        stat = buf(128)
        ptok = buf(NT, T)
        pT = buf(2, T)
        pT_lo = ptok.rearrange("p a b -> p (a b)").rearrange("p (a b) -> p a b", a=2)
        rope = buf(2, 2, T)
        iw = buf(NT, IDX_HEADS)
        fl = {n: buf(NT, 4) for n in ("x", "e", "n", "cum")}
        lam = buf(80)

        zone = memory.plain["zone"][:, :]
        positions = zone[:, 0:T].bitcast(mybir.dt.int32)
        area = Area(zone, QKV)
        qk = {n: area(w, T) for n, w in (("a_q", 2), ("a_k", 2), ("a_iq", 4), ("a_ik", 1), ("b_q", 2), ("b_k", 2),
                                           ("c_q", 2), ("c_k", 2), ("d_q", 2), ("d_k", 2))}
        vtok = {n: area(NT, w) for n, w in (("a_v", GW), ("b_v", GW), ("c_v", GW), ("d_v", P))}
        work = zone[:, QKV:QKV + WORK]
        area = Area(work, WORK)
        raw, turned = area(2, 2, T), area(2, 2, T)
        LN = 8 * P * 3
        Ls = [area(LN), area(LN)]
        PTs = [area(NT, 4, T), area(NT, 4, T)]
        Dm = area(4 * P * 3)
        sel, acc = [area(P), area(T)], [area(P), area(T)]
        dots = area(2, 512)
        area.at -= 1024 + 2 * 3 * P + 4 * P * 3
        oT, osq, ors = area(2, T), area(2, T), area(2, T)
        area.at = 0
        xn = area(NT, DM)
        area = Area(zone, QKV + WORK)
        gh, gl = area(UT, T), area(UT, T)
        gates, proj, yn = area(4, 512), area(4, 512), area(4, 512)
        ysq = area(512)

        def scores_of(buffer, t, maps):
            n = P * (t + 1)
            lo = maps * P * t
            return buffer[:, lo:lo + maps * n].rearrange("p (e n) -> p e n", n=n)

        IN_USES = [
            ("a_q", "in0", "T", [(0, P, 0, 0), (0, P, 1, 128)]), ("a_k", "in1", "T", [(0, P, 0, 256), (0, P, 1, 384)]),
            ("a_v", "in2", "tok", (512, GW)), ("a_iq0", "in3", "T", [(0, P, 0, 768), (0, P, 1, 896)]),
            ("a_iq1", "in4", "T", [(0, P, 0, 1024), (0, P, 1, 1152)]), ("a_ik", "in5", "T", [(0, 64, 0, 1280), (64, 64, 0, 1280)]),
            ("a_iw", "in5", "tok", (1344, 8)),
            ("b_q", "in6", "T", [(0, P, 0, 1352), (0, P, 1, 1480)]), ("b_k", "in7", "T", [(0, P, 0, 1608), (0, P, 1, 1736)]),
            ("b_v", "in8", "tok", (1864, GW)), ("b_f", "in8", "tok", (2120, 4)),
            ("c_q", "in9", "T", [(0, P, 0, 2124), (0, P, 1, 2252)]),
            ("c_k", "in10", "T", [(0, P, 0, 2380), (0, P, 1, 2508)]), ("c_v", "in11", "tok", (2636, GW)),
            ("d_q", "in12", "T", [(0, P, 0, 2892), (0, P, 1, 3020)]),
            ("d_k", "in13", "T", [(0, 64, 0, 3148), (64, 64, 0, 3148), (0, 64, 1, 3212), (64, 64, 1, 3212)]),
            ("d_v", "in13", "tok", (3276, P)),
        ]
        ROPED = [("a_q", qk["a_q"], 0, 2), ("a_k", qk["a_k"], 0, 2), ("a_iq0", qk["a_iq"][:, 0:2, :], 0, 2),
                 ("a_iq1", qk["a_iq"][:, 2:4, :], 0, 2), ("a_ik", qk["a_ik"], 0, 1), ("c_q", qk["c_q"], 1, 2),
                 ("c_k", qk["c_k"], 1, 2), ("d_q", qk["d_q"], 0, 2), ("d_k", qk["d_k"], 0, 2)]
        ROPED_AT = {r[0]: i for i, r in enumerate(ROPED)}
        ATTENDED = [("b", 4, HD ** -0.5, 2), ("c", 8, 32 ** -0.5, 4), ("d", 4, HD ** -0.5, 6), ("a", 4, HD ** -0.5, 0)]
        block = ctx.enter_context(nc.Block())

        @block.sync
        def _(sp):
            for s in range(SLOTS):
                sp.sem_inc(ring.free[s], 1)
            sp.dma_start(const[:, :], A["const2"]).then_inc(once, 16)
            sp.dma_start(positions[:, :], A["positions_2"][0, :].partition_broadcast(P)).then_inc(once, 16)
            with sp.Fori(0, DEPTH) as layer:
                ring.load_all(sp, layer)

        @block.tensor
        def _(pe):
            used = []

            def mm(out, lhsT, rhs, start=True, stop=True):
                ins = nc.tensor.matmul(out, lhsT, rhs, start=start, stop=stop)
                if used:
                    ins.then_inc(*ring.freed(used.pop(0)))
                return ins

            def mm3(out, a, b, start, stop):
                mm(out, a[0], b[0], start, False)
                mm(out, a[0], b[1], False, False)
                return mm(out, a[1], b[0], False, stop)

            def split_panel(name):
                pe.wait_ge(S["w_split"], ring.split.index(name) + 1)
                return rounded(ring.view(name + "_hi")), rounded(ring.view(name))

            def give_back():
                for name in used:
                    pe.drain().then_inc(*ring.freed(name))
                used.clear()

            def transpose(out, a):
                return nc.tensor.transpose(out, a, C("ident"))

            def transposes(name, source):
                for j in range(4):
                    b = psum.claim(pe, f"{name}_{j}")
                    for i in range(4):
                        last = transpose(b[:, i * P:(i + 1) * P], source[:, i % 2, (2 * j + i // 2) * P:(2 * j + i // 2 + 1) * P])
                    last.then_inc(psum.full_of(f"{name}_{j}"), 1)

            def turn(i):
                name, _, width, tiles = ROPED[i]
                pe.wait_ge(S["raw"], i + 1)
                b = psum.claim(pe, name + "_rot")
                mm(b[:, 0:tiles * T], C(("rot64", "rot32")[width]), raw[:, i % 2, 0:tiles, :]).then_inc(psum.full_of(name + "_rot"), 1)

            def project(layer):
                pe.wait_ge(S["hT"], 4)
                held, turned_n = None, 0
                for name, panel, kind, parts in IN_USES:
                    if panel != held:
                        if held:
                            used.append(held)
                        held = panel
                        w = ring.wait(pe, layer, panel)
                        base = IN2[int(panel[2:])][0]
                    b = psum.claim(pe, name)
                    if kind == "T":
                        for row0, m, half, c0 in parts:
                            for k in range(KT):
                                last = mm(b[row0:row0 + m, half * T:(half + 1) * T], w[:, k, c0 - base:c0 - base + m],
                                          hT[:, k, :], k == 0, k == KT - 1)
                    else:
                        c0, n = parts
                        for t in range(NT):
                            for k in range(KT):
                                last = mm(b[:, t * n:(t + 1) * n], hT[:, k, t * P:(t + 1) * P], w[:, k, c0 - base:c0 - base + n],
                                          k == 0, k == KT - 1)
                    last.then_inc(psum.full_of(name), 1)
                    while turned_n < len(ROPED) and psum.known(ROPED[turned_n][0]) and ROPED[turned_n][0] != name:
                        turn(turned_n)
                        turned_n += 1
                used.append(held)
                give_back()
                for i in range(turned_n, len(ROPED)):
                    turn(i)

            def scores(name):
                size = 32 if name == "c" else HD
                q, k = qk[name + "_q"], qk[name + "_k"]
                for t in range(NT):
                    n = P * (t + 1)
                    for g in range(P // size):
                        b = psum.claim(pe, f"{name}_sc{t}{g}")
                        rows = slice(size * g, size * (g + 1))
                        for hp in range(2):
                            last = mm(b[:, hp * n:(hp + 1) * n], q[rows, hp, t * P:(t + 1) * P], k[rows, hp, 0:n])
                        last.then_inc(psum.full_of(f"{name}_sc{t}{g}"), 1)

            def values(i):
                name, maps, _, _ = ATTENDED[i]
                L, PT = Ls[i % 2], PTs[i % 2]
                for t in range(NT):
                    pe.wait_ge(S["probs"], 2 * i + t + 1)
                    for kt in range(t + 1):
                        b = psum.claim(pe, f"{name}_pt{t}{kt}")
                        for e in range(4):
                            m = e if maps == 4 else 4 * (e // 2) + e % 2
                            last = transpose(b[:, e * P:(e + 1) * P], scores_of(L, t, maps)[:, m, kt * P:(kt + 1) * P])
                        last.then_inc(psum.full_of(f"{name}_pt{t}{kt}"), 1)
                pe.wait_ge(S["PT"], 3 * i + 3)
                b = psum.claim(pe, name + "_o")
                v = vtok[name + "_v"]
                for e, h in enumerate(BY_PARITY):
                    c = HD * (h // 2) if name == "d" else HD * h
                    o = b[HD * (h % 2):HD * (h % 2) + HD, T * (h // 2):T * (h // 2) + T]
                    mm(o, v[:, 0, c:c + HD], PT[:, 0, e, :], True, False)
                    last = mm(o[:, P:T], v[:, 1, c:c + HD], PT[:, 1, e, P:T], False, True)
                last.then_inc(psum.full_of(name + "_o"), 1)

            def forget_sums():
                pe.wait_ge(S["nlf"], 1)
                b = psum.claim(pe, "f_col")
                mm(b[:, 0:4], C("cum"), fl["n"][:, 0, :])
                mm(b[:, 4:8], C("ones"), fl["n"][:, 0, :], True, False)
                mm(b[:, 4:8], C("cum"), fl["n"][:, 1, :], False, True).then_inc(psum.full_of("f_col"), 1)
                for g in range(2):
                    b = psum.claim(pe, f"f_row{g}")
                    for hp in range(2):
                        h = BY_PARITY[2 * g + hp]
                        first, second = (fl["n"][:, t, h:h + 1].broadcast_to([P, P]) for t in range(NT))
                        mm(b[:, hp * T:hp * T + P], first, C("cum"))
                        mm(b[:, hp * T + P:(hp + 1) * T], first, C("ones"), True, False)
                        last = mm(b[:, hp * T + P:(hp + 1) * T], second, C("cum"), False, True)
                    last.then_inc(psum.full_of(f"f_row{g}"), 1)

            def index_dots():
                for t in range(NT):
                    n = P * (t + 1)
                    each = 512 // n
                    for g in range(2):
                        rows = slice(HD * g, HD * (g + 1))
                        for j in range(4 // each):
                            name = f"dots{t}{g}{j}"
                            b = psum.claim(pe, name)
                            for i in range(each):
                                last = mm(b[:, i * n:(i + 1) * n], qk["a_iq"][rows, each * j + i, t * P:(t + 1) * P],
                                          qk["a_ik"][rows, 0, 0:n])
                            last.then_inc(psum.full_of(name), 1)

            def wide(what, lhs, tiles):
                banks = [psum.claim(pe, f"{what}{i}") for i in range(4)]
                held = None
                for k, (panel, cut) in enumerate(tiles):
                    if panel != held:
                        if held:
                            used.extend((held, held + "_hi"))
                        held = panel
                        w = split_panel(panel)
                    for t in range(NT):
                        for half in range(2):
                            last = mm3(banks[2 * t + half], [a[:, k, t * P:(t + 1) * P] for a in lhs],
                                       [a[:, cut, half * 512:half * 512 + 512] for a in w], k == 0, k == len(tiles) - 1)
                            if k == len(tiles) - 1:
                                last.then_inc(psum.full_of(f"{what}{2 * t + half}"), 1)
                used.extend((held, held + "_hi"))
                give_back()

            def rows_by(what, lhs, panel):
                for half in range(2):
                    banks = [psum.claim(pe, f"{what}{half}{t}") for t in range(NT)]
                    for quarter in range(2):
                        name = f"{panel}{2 * half + quarter}"
                        w = split_panel(name)
                        for t in range(NT):
                            for k in range(KT):
                                last = mm3(banks[t][:, quarter * 256:quarter * 256 + 256], [a[:, k, t * P:(t + 1) * P] for a in lhs],
                                           [a[:, k, :] for a in w], k == 0, k == KT - 1)
                            if quarter:
                                last.then_inc(psum.full_of(f"{what}{half}{t}"), 1)
                        used.extend((name, name + "_hi"))

            with pe.Fori(0, DEPTH) as layer:
                pe.wait_ge(once, 32)
                pe.wait_ge(S["normed"], 1)
                transposes("hT0", xn)
                project(layer)
                pe.wait_ge(S["roped"], len(ROPED))
                forget_sums()
                pe.wait_ge(S["copied"], 6)
                index_dots()
                scores("b")
                scores("c")
                values(0)
                scores("d")
                values(1)
                pe.wait_ge(S["o_sq"], 1)
                b = psum.claim(pe, "c_ss")
                mm(b[:, :], C("heads64"), osq).then_inc(psum.full_of("c_ss"), 1)
                scores("a")
                values(2)
                values(3)
                pe.wait_ge(S["mix_split"], 1)
                rows_by("mix", (rounded(hT), rounded(mixT)), "out")
                pe.wait_ge(S["params"], 32)
                b = psum.claim(pe, "pT")
                for i in range(4):
                    last = transpose(b[:, i * P:(i + 1) * P], ptok[:, i % 2, (i // 2) * P:(i // 2 + 1) * P])
                last.then_inc(psum.full_of("pT"), 1)
                pe.wait_ge(S["normed"], 2)
                transposes("hT1", xn)
                pe.wait_ge(S["h_split"], 1)
                h = (rounded(mixT), rounded(hT))
                for c in range(UT // 2):
                    w = split_panel(f"up{c}")
                    b = psum.claim(pe, f"ff{c}")
                    for half in range(2):
                        for k in range(KT):
                            last = mm3(b[:, half * T:(half + 1) * T], [a[:, k, half * P:(half + 1) * P] for a in w],
                                       [a[:, k, :] for a in h], k == 0, k == KT - 1)
                    last.then_inc(psum.full_of(f"ff{c}"), 1)
                    used.extend((f"up{c}", f"up{c}_hi"))
                pe.wait_ge(S["gT"], UT // 2)
                wide("y", (rounded(gh), rounded(gl)), [(f"down{k // 2}", k % 2) for k in range(UT)])
                pe.wait_ge(S["p_split"], 1)
                wide("proj", (rounded(pT), rounded(pT_lo)), [("proj", k) for k in range(2)])
                pe.wait_ge(S["x_new"], 2)
                transposes("xT", x)
                pe.wait_ge(S["h_split"], 2)
                rows_by("ple", h, "ple")
                give_back()
                pe.drain().then_inc(layer_done, 1)
                pe.wait_ge(layer_open, layer + 1)

        def stat_of(i, t, what, n):
            lo = 16 + 48 * (i % 2) + 8 * t + {"neg": 0, "den": 16, "rec": 32, "sink": 36}[what]
            return stat[:, lo:lo + n]

        @block.scalar
        def _(act):
            A_ = nc.scalar.activation

            def round_weights(layer, *names):
                for name in names:
                    raw = ring.wait(act, layer, name)
                    ring.wait_free(act, layer, name + "_hi")
                    A_(rounded(ring.view(name + "_hi")), raw, ACT.Copy).then_inc(S["w_hi"], 1)

            def norm_stats(step):
                for t in range(NT):
                    A_(xn[:, t, :], x[:, t, :], ACT.Square, accum_out=stat[:, t:t + 1])
                act.drain()
                step(A_(stat[:, 2:4], stat[:, 0:2], ACT.Ln, bias=C("eps"), scale=1.0 / DM))
                A_(stat[:, 4:6], stat[:, 2:4], ACT.Exp, scale=-0.5).then_inc(S["rstd"], 1)

            def half_of_hT(name, gain):
                for j in (1, 3):
                    act.wait_ge(*psum.filled(f"{name}_{j}"))
                    for i in range(2):
                        last = A_(hT[:, 2 * j + i, :], psum.bank(f"{name}_{j}")[:, i * T:(i + 1) * T], ACT.Copy,
                                  scale=PAR(gain, 2 * j + i) if gain else 1.0)
                    last.then_inc(*psum.freed(f"{name}_{j}"))
                    act.drain().then_inc(S["hT"], 1)

            def drain_bank(name, out, signal, rows=slice(0, P), part=slice(0, 512)):
                act.wait_ge(*psum.filled(name))
                A_(out, psum.bank(name)[rows, part], ACT.Copy).then_inc(*psum.freed(name))
                act.drain().then_inc(S[signal], 1)

            def exps(i):
                name, maps, _, _ = ATTENDED[i]
                for t in range(NT):
                    act.wait_ge(S["score_max"], 2 * i + t + 1)
                    L = scores_of(Ls[i % 2], t, maps)
                    for e in range(maps):
                        A_(L[:, e, :], L[:, e, :], ACT.Exp, bias=stat_of(i, t, "neg", maps)[:, e:e + 1],
                           accum_out=stat_of(i, t, "den", maps)[:, e:e + 1])
                    if name == "d":
                        A_(stat_of(i, t, "sink", 4), stat_of(i, t, "sink", 4), ACT.Exp)
                    act.drain().then_inc(S["exps"], 1)

            def turned_probs(i):
                name, _, _, tile = ATTENDED[i]
                for t, kt in ((0, 0), (1, 0), (1, 1)):
                    drain_bank(f"{name}_pt{t}{kt}", PTs[i % 2][:, kt, :, t * P:(t + 1) * P], "PT")
                if name == "c":
                    drain_bank("c_o", oT, "c_oT")
                    A_(osq, oT, ACT.Square).then_inc(S["o_sq"], 1)
                    act.wait_ge(*psum.filled("c_ss"))
                    A_(ors, shaped(psum.bank("c_ss"), 2, T), ACT.Ln, bias=C("eps"), scale=1.0 / HD).then_inc(*psum.freed("c_ss"))
                    act.drain()
                    A_(ors, ors, ACT.Exp, scale=-0.5).then_inc(S["o_rstd"], 1)
                else:
                    drain_bank(name + "_o", mixT[:, tile:tile + 2, :], "mixT")

            def y_stats(k, names):
                for i, name in enumerate(names):
                    act.wait_ge(*psum.filled(name))
                    A_(ysq, psum.bank(name), ACT.Square, accum_out=stat[:, 112 + i:113 + i])
                    act.drain()
                act.drain().then_inc(S["y_ss"], 1)
                act.wait_ge(S["y_sum"], k + 1)
                A_(stat[:, 118:120], stat[:, 116:118], ACT.Ln, bias=C("eps"), scale=1.0 / DM)
                act.drain()
                A_(stat[:, 120:122], stat[:, 118:120], ACT.Exp, scale=-0.5).then_inc(S["y_rstd"], 1)

            act.wait_ge(angles, 1)
            A_(rope, rope, ACT.Sin).then_inc(tables_made, 1)
            with act.Fori(0, DEPTH) as layer:
                step = Chain(act, S["act"])
                act.dma_start(par[:, :], A["par2"][layer, :, :]).then_inc(S["params"], 16)
                act.dma_start(ptok, A["p_2"][layer, 0, :, :].rearrange("(t q) n -> q t n", q=P)).then_inc(S["params"], 16)
                act.wait_ge(once, 32)
                norm_stats(step)
                act.wait_ge(S["params"], 32)
                act.wait_ge(S["lam_sum"], 1)
                A_(lam[:, 66:68], lam[:, 64:66], ACT.Exp).then_inc(S["lam_exp"], 1)
                half_of_hT("hT0", "pre_mix")
                for name, panel, kind, parts in IN_USES:
                    if name in ROPED_AT:
                        i = ROPED_AT[name]
                        tiles = ROPED[i][3]
                        if i >= 2:
                            act.wait_ge(S["roped"], i - 1)
                        drain_bank(name, raw[:, i % 2, 0:tiles, :], "raw", part=slice(0, tiles * T))
                    elif name in ("b_q", "b_k"):
                        drain_bank(name, qk[name], "copied")
                    elif name in vtok:
                        drain_bank(name, vtok[name], "copied", part=slice(0, NT * parts[1]))
                act.wait_ge(S["gate_abs"], 1)
                A_(fl["e"], fl["e"], ACT.Exp, scale=-1.0)
                act.drain()
                A_(fl["e"], fl["e"], ACT.Ln, bias=C("ones")[:, 0:1]).then_inc(S["gate_ln"], 1)
                at = 0
                for t in range(NT):
                    for g in range(2):
                        for j in range(t + 1):
                            if at >= 2:
                                act.wait_ge(S["relu_used"], at - 1)
                            act.wait_ge(*psum.filled(f"dots{t}{g}{j}"))
                            A_(dots[:, at % 2, :], psum.bank(f"dots{t}{g}{j}"), ACT.Relu).then_inc(*psum.freed(f"dots{t}{g}{j}"))
                            act.drain().then_inc(S["relu"], 1)
                            at += 1
                exps(0)
                exps(1)
                turned_probs(0)
                exps(2)
                turned_probs(1)
                exps(3)
                turned_probs(2)
                round_weights(layer, "out0", "out1", "out2", "out3")
                turned_probs(3)
                y_stats(0, [f"mix{half}{t}" for half in range(2) for t in range(NT)])
                drain_bank("pT", pT_lo, "pT_in")
                act.wait_ge(S["x_new"], 1)
                norm_stats(step)
                half_of_hT("hT1", "pre_mlp")
                round_weights(layer, "up0", "up1")
                for c in range(UT // 2 + 1):
                    if c < UT // 2:
                        round_weights(layer, f"up{c + 2}" if c + 2 < UT // 2 else f"down{c + 2 - UT // 2}")
                        act.wait_ge(*psum.filled(f"ff{c}"))
                        A_(gh[:, 2 * c:2 * c + 2, :], shaped(psum.bank(f"ff{c}"), 2, T), ACT.Relu).then_inc(*psum.freed(f"ff{c}"))
                        act.drain().then_inc(S["ff_relu"], 1)
                    if c:
                        act.wait_ge(S["ff_squared"], c)
                        A_(rounded(gh[:, 2 * c - 2:2 * c, :]), gl[:, 2 * c - 2:2 * c, :], ACT.Copy).then_inc(S["g_hi"], 1)
                round_weights(layer, *[f"down{i}" for i in range(2, UT // 2)])
                round_weights(layer, "proj", "ple0", "ple1")
                y_stats(1, [f"y{i}" for i in (0, 2, 1, 3)])
                for i in (0, 2, 1, 3):
                    t, half = i // 2, i % 2
                    drain_bank(f"proj{i}", proj[:, 2 * half + t, :], "proj")
                half_of_hT("xT", None)
                round_weights(layer, "ple2", "ple3")
                for half in range(2):
                    for t in range(NT):
                        name, i = f"ple{half}{t}", 2 * half + t
                        act.wait_ge(*psum.filled(name))
                        A_(gates[:, i, :], psum.bank(name), ACT.Sigmoid).then_inc(*psum.freed(name))
                        act.drain().then_inc(S["gates"], 1)
                act.drain().then_inc(layer_done, 1)
                act.wait_ge(layer_open, layer + 1)

        @block.vector
        def _(dve):
            V = nc.vector

            def subtract_rounded(*names):
                for name in names:
                    dve.wait_ge(S["w_hi"], ring.split.index(name) + 1)
                    V.tensor_tensor(rounded(ring.view(name)), ring.view(name), as_float32(rounded(ring.view(name + "_hi"))), ALU.subtract).then_inc(S["w_split"], 1)

            def split(hi, lo, a):
                dve.drain()
                V.tensor_copy(rounded(hi), a)
                dve.drain()
                V.tensor_tensor(rounded(lo), a, as_float32(rounded(hi)), ALU.subtract)

            def norm(k, name, gain):
                dve.wait_ge(S["rstd"], k + 1)
                for t in range(NT):
                    last = V.tensor_scalar(xn[:, t, :], x[:, t, :], stat[:, 4 + t:5 + t], None, ALU.mult)
                last.then_inc(S["normed"], 1)
                half_of_hT(name, gain)

            def half_of_hT(name, gain):
                for j in (0, 2):
                    dve.wait_ge(*psum.filled(f"{name}_{j}"))
                    bank = psum.bank(f"{name}_{j}")
                    for i in range(2):
                        src = bank[:, i * T:(i + 1) * T]
                        if gain:
                            last = V.tensor_scalar(hT[:, 2 * j + i, :], src, PAR(gain, 2 * j + i), None, ALU.mult)
                        else:
                            last = V.tensor_copy(hT[:, 2 * j + i, :], src)
                    last.then_inc(*psum.freed(f"{name}_{j}"))
                    dve.drain().then_inc(S["hT"], 1)

            def turn(i):
                name, out, width, tiles = ROPED[i]
                dve.wait_ge(*psum.filled(name + "_rot"))
                if i >= 2:
                    dve.drain()
                sin = rope[:, width, 1:2, :].broadcast_to([P, tiles, T])
                V.tensor_tensor(turned[:, i % 2, 0:tiles, :], shaped(psum.bank(name + "_rot")[:, 0:tiles * T], tiles, T), sin,
                                ALU.mult).then_inc(*psum.freed(name + "_rot"))
                dve.wait_ge(S["cosined"], i + 1)
                dve.drain()
                V.tensor_tensor(out, out, turned[:, i % 2, 0:tiles, :], ALU.add).then_inc(S["roped"], 1)

            def masked_scores(i):
                name, maps, scale, _ = ATTENDED[i]
                if i >= 2:
                    dve.wait_ge(*psum.filled(ATTENDED[i - 2][0] + "_pt11"))
                for t in range(NT):
                    n = P * (t + 1)
                    L = scores_of(Ls[i % 2], t, maps)
                    for g in range(maps // 2):
                        bank = f"{name}_sc{t}{g}"
                        dve.wait_ge(*psum.filled(bank))
                        if name == "a":
                            mask = sel[t].unsqueeze(1).broadcast_to([P, 2, n])
                        elif name == "b":
                            mask = scores_of(Dm, t, 4)[:, 2 * g:2 * g + 2, :]
                        else:
                            all_ = shaped(C("window" if name == "d" else "causal"), NT, T)
                            mask = all_[:, t:t + 1, 0:n].broadcast_to([P, 2, n])
                        V.scalar_tensor_tensor(L[:, 2 * g:2 * g + 2, :], shaped(psum.bank(bank)[:, 0:2 * n], 2, n), scale, mask,
                                               ALU.mult, ALU.add).then_inc(*psum.freed(bank))
                    dve.drain()
                    neg, rec = stat_of(i, t, "neg", maps), stat_of(i, t, "rec", maps)
                    V.tensor_reduce(rec, L, AX.X, ALU.max)
                    dve.drain()
                    if name == "d":
                        V.tensor_tensor(rec, rec, PAR("sinks"), ALU.max)
                        dve.drain()
                    V.tensor_scalar(neg, rec, -1.0, None, ALU.mult)
                    if name == "d":
                        dve.drain()
                        V.tensor_tensor(stat_of(i, t, "sink", 4), PAR("sinks"), neg, ALU.add)
                    dve.drain().then_inc(S["score_max"], 1)

            def probs(i):
                name, maps, _, _ = ATTENDED[i]
                for t in range(NT):
                    n = P * (t + 1)
                    L = scores_of(Ls[i % 2], t, maps)
                    den, rec = stat_of(i, t, "den", maps), stat_of(i, t, "rec", maps)
                    dve.wait_ge(S["exps"], 2 * i + t + 1)
                    if name == "d":
                        V.tensor_tensor(den, den, stat_of(i, t, "sink", 4), ALU.add)
                        dve.drain()
                    V.reciprocal(rec, den)
                    dve.drain()
                    V.tensor_tensor(L, L, rec.unsqueeze(2).broadcast_to([P, maps, n]), ALU.mult)
                    if name == "c":
                        dve.drain()
                        for g in range(2):
                            V.scalar_tensor_tensor(L[:, 4 * g:4 * g + 2, :], L[:, 4 * g + 2:4 * g + 4, :], lam[:, 68:69],
                                                   L[:, 4 * g:4 * g + 2, :], ALU.mult, ALU.add)
                    dve.drain().then_inc(S["probs"], 1)

            def select(t):
                n = P * (t + 1)
                best = stat[:, 8:16]
                V.tensor_tensor(acc[t], acc[t], shaped(C("causal"), NT, T)[:, t, 0:n], ALU.add)
                for _ in range(TOPK // 8):
                    dve.drain()
                    V.max(best, acc[t])
                    dve.drain()
                    V.match_replace(acc[t], best, acc[t], TAKEN)
                dve.drain()
                V.tensor_scalar(sel[t], acc[t], -1e35, NEG, ALU.is_gt, ALU.mult)
                dve.drain()
                V.tensor_tensor(sel[t], sel[t], shaped(C("causal"), NT, T)[:, t, 0:n], ALU.add)
                dve.drain()

            def residual(k, names, gain):
                dve.wait_ge(S["y_ss"], k + 1)
                V.tensor_tensor(stat[:, 116:118], stat[:, 112:114], stat[:, 114:116], ALU.add).then_inc(S["y_sum"], 1)
                dve.wait_ge(S["y_rstd"], k + 1)
                lo = PAR2[gain][0]
                for i, name in enumerate(names):
                    half, t = i // 2, i % 2
                    V.scalar_tensor_tensor(yn[:, i, :], psum.bank(name), stat[:, 120 + t:121 + t],
                                           par[:, lo + 512 * half:lo + 512 * half + 512], ALU.mult, ALU.mult).then_inc(*psum.freed(name))
                add_to_x()

            def add_to_x():
                dve.drain()
                for i in range(4):
                    half, t = i // 2, i % 2
                    xs = x[:, t, 512 * half:512 * half + 512]
                    V.tensor_tensor(xs, xs, yn[:, i, :], ALU.add)
                dve.drain().then_inc(S["x_new"], 1)

            dve.wait_ge(once, 32)
            pos, turns = acc[1], sel[1]
            V.tensor_copy(pos, positions[:, :])
            for w in range(2):
                ang = rope[:, w, 1, :]
                dve.drain()
                V.tensor_scalar(ang, pos, C("inv_freq")[:, w:w + 1], None, ALU.mult)
                dve.drain()
                V.tensor_scalar(turns, ang, float(1 / (2 * np.pi)), 1.5 * 2.0 ** 23, ALU.mult, ALU.add)
                dve.drain()
                V.tensor_scalar(turns, turns, -1.5 * 2.0 ** 23, None, ALU.add)
                for part in TWO_PI:
                    dve.drain()
                    V.scalar_tensor_tensor(ang, turns, -part, ang, ALU.mult, ALU.add)
                dve.drain()
                V.tensor_scalar(ang, ang, -3.1415925, 3.1415925, ALU.max, ALU.min)
                dve.drain()
                V.scalar_tensor_tensor(rope[:, w, 0, :], ang, -1.0, ang, ALU.mult, ALU.max)
                dve.drain()
                V.tensor_scalar(rope[:, w, 0, :], rope[:, w, 0, :], -1.0, float(np.pi / 2), ALU.mult, ALU.add)
            dve.drain().then_inc(angles, 1)
            with dve.Fori(0, DEPTH) as layer:
                dve.wait_ge(tables_made, 1)
                dve.wait_ge(S["params"], 32)
                V.tensor_tensor(lam[:, 0:64], PAR("lam_q"), PAR("lam_k"), ALU.mult)
                dve.drain()
                V.tensor_reduce(lam[:, 64:66], shaped(lam[:, 0:64], 2, 32), AX.X, ALU.add).then_inc(S["lam_sum"], 1)
                norm(0, "hT0", "pre_mix")
                dve.wait_ge(S["lam_exp"], 1)
                V.tensor_tensor(lam[:, 68:69], lam[:, 67:68], lam[:, 66:67], ALU.subtract)
                dve.drain()
                V.tensor_tensor(lam[:, 68:69], lam[:, 68:69], PAR("lam_init"), ALU.subtract)
                for i in range(4):
                    turn(i)
                dve.wait_ge(*psum.filled("a_iw"))
                V.tensor_scalar(iw, shaped(psum.bank("a_iw")[:, 0:16], NT, 8), IDX_HEADS ** -0.5 * 64 ** -0.5, None,
                                ALU.mult).then_inc(*psum.freed("a_iw"))
                turn(4)
                dve.wait_ge(*psum.filled("b_f"))
                V.tensor_tensor(fl["x"], shaped(psum.bank("b_f")[:, 0:8], NT, 4),
                                PAR("b_forget").unsqueeze(1).broadcast_to([P, NT, 4]), ALU.add).then_inc(*psum.freed("b_f"))
                dve.drain()
                V.scalar_tensor_tensor(fl["e"], fl["x"], -1.0, fl["x"], ALU.mult, ALU.max)
                dve.drain().then_inc(S["gate_abs"], 1)
                for i in range(5, 9):
                    turn(i)
                dve.wait_ge(S["gate_ln"], 1)
                V.tensor_scalar(fl["x"], fl["x"], 0.0, None, ALU.min)
                dve.drain()
                V.tensor_tensor(fl["n"], fl["e"], fl["x"], ALU.subtract).then_inc(S["nlf"], 1)
                dve.wait_ge(*psum.filled("f_col"))
                V.tensor_scalar(fl["cum"], shaped(psum.bank("f_col")[:, 0:8], NT, 4), -1.0, None, ALU.mult).then_inc(*psum.freed("f_col"))
                dve.drain()
                for g in range(2):
                    name = f"f_row{g}"
                    dve.wait_ge(*psum.filled(name))
                    for t in range(NT):
                        n = P * (t + 1)
                        for hp in range(2):
                            h = BY_PARITY[2 * g + hp]
                            last = V.scalar_tensor_tensor(scores_of(Dm, t, 4)[:, 2 * g + hp, :], psum.bank(name)[:, hp * T:hp * T + n],
                                                          fl["cum"][:, t, h:h + 1], shaped(C("causal"), NT, T)[:, t, 0:n], ALU.add, ALU.add)
                    last.then_inc(*psum.freed(name))
                at = 0
                for t in range(NT):
                    n = P * (t + 1)
                    each = 512 // n
                    for g in range(2):
                        for j in range(4 // each):
                            dve.wait_ge(S["relu"], at + 1)
                            for i in range(each):
                                head = 2 * (each * j + i) + g
                                r, weight = dots[:, at % 2, i * n:(i + 1) * n], iw[:, t, head:head + 1]
                                dve.drain()
                                if g == j == i == 0:
                                    last = V.tensor_scalar(acc[t], r, weight, None, ALU.mult)
                                else:
                                    last = V.scalar_tensor_tensor(acc[t], r, weight, acc[t], ALU.mult, ALU.add)
                            last.then_inc(S["relu_used"], 1)
                            at += 1
                dve.drain()
                masked_scores(0)
                masked_scores(1)
                probs(0)
                select(0)
                masked_scores(2)
                probs(1)
                select(1)
                masked_scores(3)
                probs(2)
                probs(3)
                dve.wait_ge(S["o_rstd"], 1)
                V.scalar_tensor_tensor(oT, oT, PAR("subln"), ors, ALU.mult, ALU.mult)
                dve.drain()
                V.tensor_scalar(mixT[:, 4:6, :], oT, PAR("lam_rest"), None, ALU.mult)
                subtract_rounded("out0", "out1", "out2", "out3")
                dve.wait_ge(S["mixT"], 3)
                split(hT, mixT, mixT)
                dve.drain().then_inc(S["mix_split"], 1)
                residual(0, [f"mix{half}{t}" for half in range(2) for t in range(NT)], "post_mix")
                norm(1, "hT1", "pre_mlp")
                dve.wait_ge(S["pT_in"], 1)
                split(pT, pT_lo, pT_lo)
                dve.drain().then_inc(S["p_split"], 1)
                dve.wait_ge(S["hT"], 8)
                split(mixT, hT, hT)
                dve.drain().then_inc(S["h_split"], 1)
                subtract_rounded("up0", "up1")
                for c in range(UT // 2 + 1):
                    if c < UT // 2:
                        subtract_rounded(f"up{c + 2}" if c + 2 < UT // 2 else f"down{c + 2 - UT // 2}")
                        dve.wait_ge(S["ff_relu"], c + 1)
                        V.tensor_tensor(gl[:, 2 * c:2 * c + 2, :], gh[:, 2 * c:2 * c + 2, :], gh[:, 2 * c:2 * c + 2, :],
                                        ALU.mult).then_inc(S["ff_squared"], 1)
                    if c:
                        dve.wait_ge(S["g_hi"], c)
                        V.tensor_tensor(rounded(gl[:, 2 * c - 2:2 * c, :]), gl[:, 2 * c - 2:2 * c, :],
                                        as_float32(rounded(gh[:, 2 * c - 2:2 * c, :])), ALU.subtract).then_inc(S["gT"], 1)
                subtract_rounded(*[f"down{i}" for i in range(2, UT // 2)])
                subtract_rounded("proj", "ple0", "ple1")
                residual(1, [f"y{i}" for i in (0, 2, 1, 3)], "post_mlp")
                half_of_hT("xT", None)
                dve.wait_ge(S["hT"], 12)
                split(mixT, hT, hT)
                dve.drain().then_inc(S["h_split"], 1)
                subtract_rounded("ple2", "ple3")
                for i in range(4):
                    dve.wait_ge(S["gates"], i + 1)
                    V.tensor_tensor(yn[:, i, :], gates[:, i, :], proj[:, i, :], ALU.mult)
                add_to_x()
                dve.drain().then_inc(layer_done, 1)
                dve.wait_ge(layer_open, layer + 1)

        @block.gpsimd
        def _(pool):
            pool.wait_ge(tables_made, 1)
            with pool.Fori(0, DEPTH) as layer:
                for i, (name, out, width, tiles) in enumerate(ROPED):
                    pool.wait_ge(S["raw"], i + 1)
                    cos = rope[:, width, 0:1, :].broadcast_to([P, tiles, T])
                    nc.gpsimd.tensor_tensor(out, raw[:, i % 2, 0:tiles, :], cos, ALU.mult).then_inc(S["cosined"], 1)
                pool.wait_ge(layer_done, 3 * layer + 3)
                pool.sem_inc(barrier_taken, 1)
                for r in sem_ranges([s.num for s in S.values()] + [s.num for s in psum.full + psum.free]):
                    pool.sem_clear(r)
                pool.sem_inc(layer_open, 1)

        psum.check()


def two_blocks(nc, A, out):
    with ExitStack() as ctx:
        x = shaped(ctx.enter_context(nc.sbuf_tensor("x_state", [P, NT * DM], F32))[:, :], NT, DM)
        banks = ctx.enter_context(nc.psum_tensor("banks", [P, 8, 512], F32))
        x_in = ctx.enter_context(nc.semaphore("x_in"))
        x_out = ctx.enter_context(nc.semaphore("x_out"))
        with nc.Block() as block:
            @block.sync
            def _(sp):
                for t in range(NT):
                    sp.dma_start(x[:, t, :], A["x"][0, t * P:(t + 1) * P, :]).then_inc(x_in, 16)
                sp.wait_ge(x_in, 16 * NT)
        block1(nc, ctx, banks, x, x_in, A)
        block2(nc, ctx, banks, x, A)
        with nc.Block() as block:
            @block.sync
            def _(sp):
                for t in range(NT):
                    sp.dma_start(out[0, t * P:(t + 1) * P, :], x[:, t, :]).then_inc(x_out, 16)
                sp.wait_ge(x_out, 16 * NT)


_LARGE = ["x", "w_in", "w_out", "mla_w_uq", "mla_w_ukv", "gla_w_gk2", "ffn_w_gate", "ffn_w_up", "ffn_w_down",
          "p_2", "positions_2", "w_in_2", "w_out_2", "w_mlp_up_2", "w_mlp_down_2", "w_ple_proj_2", "w_ple_gate_2"]


def kernel(**inputs):
    import concourse.bacc as bacc
    from concourse.bass_utils import run_bass_kernel_spmd

    nc = bacc.Bacc("TRN2", target_bir_lowering=False, num_devices=1)
    host = {name: np.ascontiguousarray(inputs[name]) for name in _LARGE}
    host["const1"], host["const2"] = shape_constants1(), shape_constants2()
    host["par1"], host["par2"] = params1(inputs), params2(inputs)
    arrays, A = {}, {}
    for name, a in host.items():
        arrays[f"in_{name}"] = a
        A[name] = nc.dram_tensor(f"in_{name}", a.shape, mybir.dt.from_np(a.dtype), kind="ExternalInput").ap()
    out = nc.dram_tensor("out_x", (1, T, DM), F32, kind="ExternalOutput").ap()
    two_blocks(nc, A, out)
    result = run_bass_kernel_spmd(nc, [arrays], core_ids=[0])
    return result.results[0]["out_x"]
```

```python
from contextlib import ExitStack

import numpy as np

import concourse.bass as bass
from concourse import mybir

F32 = mybir.dt.float32
ALU = mybir.AluOpType
ACT = mybir.ActivationFunctionType
AX = mybir.AxisListType

P = 128
T = 256
NT = T // P
DM = 1024
KT = DM // P
DEPTH = 2
GW = 256
HD = 64
EPS = 1e-6
NEG = -1e30
SUB = 16
NSUB = T // SUB
SUBP = P // SUB
CHUNK = 64
D_FF = 2816
FT = D_FF // P
PANEL = 272
SLOTS = 8


class Psum:

    def __init__(self, nc, ctx, tag, banks):
        self.t = banks
        self.full = [ctx.enter_context(nc.semaphore(f"{tag}_bank{b}_filled")) for b in range(8)]
        self.free = [ctx.enter_context(nc.semaphore(f"{tag}_bank{b}_freed")) for b in range(8)]
        self.at, self.given_back = {}, set()

    def claim(self, pe, name):
        assert name not in self.at, name
        n = len(self.at)
        self.at[name] = (n % 8, n // 8 + 1)
        if n >= 8:
            pe.wait_ge(self.free[n % 8], n // 8)
        return self.t[:, n % 8, :]

    def check(self):
        assert set(self.at) == self.given_back, set(self.at) ^ self.given_back

    def known(self, name):
        return name in self.at

    def bank(self, name):
        return self.t[:, self.at[name][0], :]

    def full_of(self, name):
        return self.full[self.at[name][0]]

    def filled(self, name):
        b, n = self.at[name]
        return self.full[b], n

    def freed(self, name):
        assert name not in self.given_back, name
        self.given_back.add(name)
        return self.free[self.at[name][0]], 1


class Chain:

    def __init__(self, eng, sem):
        self.eng, self.sem, self.n = eng, sem, 0

    def __call__(self, ins):
        self.n += 1
        ins.then_inc(self.sem, 1)
        self.eng.wait_ge(self.sem, self.n)


class Ring:

    def __init__(self, nc, ctx, tag, entries, slots):
        self.t = slots
        self.full = [ctx.enter_context(nc.semaphore(f"{tag}_slot{s}_filled")) for s in range(SLOTS)]
        self.free = [ctx.enter_context(nc.semaphore(f"{tag}_slot{s}_freed")) for s in range(SLOTS)]
        self.taken = ctx.enter_context(nc.semaphore(f"{tag}_slots_taken"))
        self.entries, self.names = entries, [p[0] for p in entries]
        self.uses = [len(range(s, len(entries), SLOTS)) for s in range(SLOTS)]
        self.loads = [self.loads_to(s, len(entries)) for s in range(SLOTS)]
        self.split = [n[:-3] for n in self.names if n.endswith("_hi")]

    def loads_to(self, s, end):
        return sum(self.entries[n][1] is not None for n in range(s, end, SLOTS))

    def view(self, name):
        n = self.names.index(name)
        _, _, k, c0, c1 = self.entries[n]
        return self.t[:, n % SLOTS, 0:k * (c1 - c0)].rearrange("p (k n) -> p k n", k=k)

    def wait_free(self, eng, layer, name):
        n = self.names.index(name)
        eng.wait_ge(self.free[n % SLOTS], layer * self.uses[n % SLOTS] + (n // SLOTS + 1))

    def load_all(self, sp, layer):
        for n, (name, source, k, c0, c1) in enumerate(self.entries):
            if source is not None:
                self.wait_free(sp, layer, name)
                sp.sem_inc(self.taken, 1)
                sp.dma_start(self.view(name), source(layer)).then_inc(self.full[n % SLOTS], 16)

    def wait(self, eng, layer, name):
        n = self.names.index(name)
        s = n % SLOTS
        eng.wait_ge(self.full[s], layer * (16 * self.loads[s]) + 16 * self.loads_to(s, n + 1))
        return self.view(name)

    def freed(self, name):
        return self.free[self.names.index(name) % SLOTS], 1


def with_parts(panels):
    return [e for name, source, k, c0, c1 in panels for e in ((name, source, k, c0, c1), (name + "_hi", None, k, c0, c1))]


class Memory:

    def __init__(self, nc, ctx, tag, parts):
        with ExitStack() as plain:
            self.plain = {n: plain.enter_context(nc.sbuf_tensor(f"{tag}_{n}", [P, w], F32)) for n, w in parts.items()}
        self.other = {f"{tag}_{n}": ctx.enter_context(nc.sbuf_tensor(f"{tag}_{n}_rounded", [P, w], mybir.dt.float32r))
                      for n, w in parts.items()}
        self.parts = parts

    def area(self, name):
        return Area(self.plain[name][:, :], self.parts[name])

    def rounded(self, ap):
        return bass.AP(tensor=self.other[ap.tensor.name], offset=ap.offset, ap=ap.ap)


def as_float32(ap):
    return ap.bitcast(F32)


def table(columns):
    out, at = {}, 0
    for name, width in columns:
        out[name] = (at, at + width)
        at += width
    return out, at


def bands(a, d):
    return a.rearrange("p r (s c) -> p (r s) c", c=SUB)[:, :, d:SUB]


def shifted(a, d):
    return a.rearrange("p r (s c) -> p (r s) c", c=SUB)[:, :, 0:SUB - d]


def shaped(ap, *shape):
    if len(shape) == 1:
        return ap
    names = "abcd"[:len(shape)]
    sizes = {n: s for n, s in zip(names[1:], shape[1:])}
    return ap.rearrange(f"p ({' '.join(names)}) -> p {' '.join(names)}", **sizes)


class Area:

    def __init__(self, tensor, width, at=0):
        self.tensor, self.width, self.at = tensor, width, at

    def __call__(self, *shape):
        n = int(np.prod(shape))
        lo, self.at = self.at, self.at + n
        assert self.at <= self.width, (self.at, self.width)
        return shaped(self.tensor[:, lo:lo + n], *shape)


class Group:
    pass


def interleave(a, b, haste=1.0):
    places = [(haste * (i + 0.5) / len(a), x) for i, x in enumerate(a)] + [((i + 0.5) / len(b), x) for i, x in enumerate(b)]
    return [x for _, x in sorted(places, key=lambda place: place[0])]


def emit(order, parts):
    for name in order:
        next(parts[name])
    for name, part in parts.items():
        assert next(part, "over") == "over", name


def sem_ranges(numbers):
    out = []
    for n in sorted(numbers):
        if out and out[-1].stop == n:
            out[-1] = range(out[-1].start, n + 1)
        else:
            out.append(range(n, n + 1))
    return out


CONST1, N_CONST1 = table([
    ("ident", P), ("cum", P), ("ones", P), ("heads64", P), ("to_pair", 2 * P),
    ("rot96", 96), ("cos96", T), ("sin96", T), ("causal", NT * T), ("hide_strict", P),
    ("hide_incl", P), ("level", 7 * P), ("restart", T), ("sub", SUBP), ("eps", 1),
])
PAR1, N_PAR1 = table([
    ("pre_mix", KT), ("pre_ffn", KT), ("lb_logits", 2 * DEPTH), ("lb_of", 2 * DEPTH), ("hgrn_norm", 1),
    ("b_gk", 1), ("gla_norm", 1), ("q_norm", 2), ("kv_norm", 1), ("conv", 4 * 6), ("gdn_norm", 1),
    ("ffn_conv", 3 * FT), ("a_log", 4), ("dt_bias", 4), ("post_mix", DM), ("post_ffn", DM),
])
IN1 = [(0, 256), (256, 512), (512, 768), (768, 1024), (1024, 1280), (1280, 1536), (1536, 1808), (1808, 2064),
       (2064, 2224), (2224, 2480), (2480, 2736), (2736, 2992), (2992, 3256)]


def shape_constants1():
    c = np.zeros((P, N_CONST1), np.float32)

    def put(name, a):
        lo, hi = CONST1[name]
        c[:a.shape[0], lo:hi] = a.reshape(a.shape[0], -1)

    i = np.arange(P)
    same = (i[:, None] // CHUNK) == (i[None, :] // CHUNK)
    put("ident", np.eye(P, dtype=np.float32))
    put("cum", (same & (i[:, None] <= i[None, :])).astype(np.float32))
    put("ones", np.ones((P, P), np.float32))
    put("heads64", same.astype(np.float32))
    pair = np.zeros((P, 2, P), np.float32)
    for p in range(2):
        pair[:, p] = (i[:, None] // 32) == (2 * p + i[None, :] // 64)
    put("to_pair", pair)
    rot = np.zeros((96, 96), np.float32)
    for m in range(16):
        rot[64 + 16 + m, 64 + m] = -1.0
        rot[64 + m, 64 + 16 + m] = 1.0
    put("rot96", rot)
    inv = (np.float32(10000.0) ** (-np.arange(0, 32, 2, dtype=np.float32) / np.float32(32))).astype(np.float32)
    ang = (np.arange(T, dtype=np.float32)[None, :] * inv[:, None]).astype(np.float32)
    cos, sin = np.ones((96, T), np.float32), np.zeros((96, T), np.float32)
    cos[64:80] = cos[80:96] = np.cos(ang)
    sin[64:80] = sin[80:96] = np.sin(ang)
    put("cos96", cos)
    put("sin96", sin)
    key = np.arange(T)
    put("causal", np.stack([np.where(key[None, :] <= (i[:, None] + P * t), 0.0, NEG) for t in range(NT)], 1).astype(np.float32))
    put("hide_strict", np.where(same & (i[None, :] < i[:, None]), 0.0, -NEG).astype(np.float32))
    put("hide_incl", np.where(same & (i[None, :] >= i[:, None]), 0.0, NEG).astype(np.float32))
    level = np.zeros((P, 7, P), np.float32)
    for n in range(6):
        c_ = 1 << n
        row, col = i[:, None], i[None, :]
        m = (row // (2 * c_) == col // (2 * c_)) & (row % (2 * c_) >= c_) & (col % (2 * c_) < c_)
        level[:, n] = m.T
        if n == 0:
            level[:, 6] = m
    put("level", level)
    put("restart", np.broadcast_to((np.arange(T) % SUB != 0).astype(np.float32), (P, T)))
    put("sub", (i[:, None] // SUB == np.arange(SUBP)[None, :]).astype(np.float32))
    put("eps", np.full((P, 1), EPS, np.float32))
    return c


def params1(a):
    out = np.zeros((DEPTH, P, N_PAR1), np.float32)

    def put(name, layer, v):
        lo, hi = PAR1[name]
        out[layer, :, lo:hi] = v

    def cols(v):
        return np.asarray(v).reshape(-1, P).T

    def rows(v):
        v = np.asarray(v)
        return np.broadcast_to(v, (P,) + v.shape)

    for l in range(DEPTH):
        put("pre_mix", l, cols(a["pre_mix_g"][l]))
        put("pre_ffn", l, cols(a["pre_ffn_g"][l]))
        lb = np.stack([cols(a["hgrn_lb_logits"][j]) for j in range(DEPTH)], 2)
        put("lb_logits", l, lb.reshape(P, -1))
        of = np.zeros((P, 2, DEPTH), np.float32)
        of[:, :, 1:l + 1] = 1.0
        put("lb_of", l, of.reshape(P, -1))
        put("hgrn_norm", l, np.concatenate([a["hgrn_norm_g"][l]] * 2)[:, None])
        put("b_gk", l, cols(a["gla_b_gk"][l]))
        put("gla_norm", l, np.concatenate([a["gla_norm_g"][l]] * 2)[:, None])
        put("q_norm", l, cols(a["mla_q_norm_g"][l]))
        put("kv_norm", l, cols(a["mla_kv_norm_g"][l]))
        put("conv", l, np.asarray(a["gdn_conv_w"][l]).reshape(4, 6, P).transpose(2, 1, 0).reshape(P, -1))
        put("gdn_norm", l, np.concatenate([a["gdn_norm_g"][l]] * 2)[:, None])
        put("ffn_conv", l, np.asarray(a["ffn_conv_w"][l]).reshape(3, FT, P).transpose(2, 1, 0).reshape(P, -1))
        put("a_log", l, rows(a["gdn_a_log"][l]))
        put("dt_bias", l, rows(a["gdn_dt_bias"][l]))
        put("post_mix", l, rows(a["post_mix_g"][l]))
        put("post_ffn", l, rows(a["post_ffn_g"][l]))
    return out



SIGNALS1 = """w_split_pool w_split params diagonal hT o_sq code v_T kdT kd_tok vexp state q_decayed weighted
mla_sq mla_c mla_cn rot_in qT kT probs PT mla_v l2_sq g_ready qk_norm level_X lmat level_T tok_D uw
qe state_D v_new mix_split h_split gT w_hi rstd y_ss y_sum y_rstd oT_ready o_rstd af_f af_ln gk_abs
gk_ln scan exp_b scan_end kd_exp vtok diff decay aq_tanh af_sig gate_th bg_th dz_th gla_done
mla_rstd scores_max exps mixT_C conv conv_th ba_in ba_exp conv_silu l2_rstd b_small b_exp erow hid
decays nt act lb_max lb_exp x_new ff_conv ff_gate ff_gelu qk kr_done dve gpad_zero""".split()


def block1(nc, kept, banks, x, x_in, A):
    with ExitStack() as ctx:
        A_LEFT, BETWEEN, D_WORK, LEFT = 10 * T, 14 * T, 42 * T, 5534
        memory = Memory(nc, ctx, "b1", {"ring": SLOTS * KT * PANEL, "front": KT * T + A_LEFT + BETWEEN, "back": D_WORK + LEFT,
                                        "small": N_CONST1 + N_PAR1 + 768 + 512 + P + KT * T + 64})
        rounded, buf = memory.rounded, memory.area("small")

        S = {n: ctx.enter_context(nc.semaphore("b1_" + n)) for n in SIGNALS1}
        psum = Psum(nc, ctx, "b1", banks)
        layer_done = kept.enter_context(nc.semaphore("b1_layer_done"))
        layer_open = kept.enter_context(nc.semaphore("b1_layer_open"))
        barrier_taken = kept.enter_context(nc.semaphore("b1_barrier_taken"))
        once = kept.enter_context(nc.semaphore("b1_constants_in"))

        def cols(src, k):
            return lambda l, c0, c1, k0=0: src.rearrange("l (k p) n -> l p k n", p=P)[l, :, k0:k0 + k, c0:c1]

        win, wout = cols(A["w_in"], KT), cols(A["w_out"], KT)
        wg, wu = cols(A["ffn_w_gate"], KT), cols(A["ffn_w_up"], KT)
        wd = A["ffn_w_down"].rearrange("l (k p) n -> l p k n", p=P)
        panels = [(f"in{i}", lambda l, c0=c0, c1=c1: win(l, c0, c1), KT, c0, c1) for i, (c0, c1) in enumerate(IN1)]
        late = [(f"out{i}", lambda l, i=i: wout(l, 256 * i, 256 * i + 256), KT, 0, 256) for i in range(4)]
        for i in range(FT // 2):
            late.append((f"gate{i}", lambda l, i=i: wg(l, 256 * i, 256 * i + 256), KT, 0, 256))
            late.append((f"up{i}", lambda l, i=i: wu(l, 256 * i, 256 * i + 256), KT, 0, 256))
        late += [(f"down{i}", lambda l, i=i: wd[l, :, 2 * i:2 * i + 2, :], 2, 0, DM) for i in range(FT // 2)]
        panels += with_parts(late)
        ring = Ring(nc, kept, "b1", panels, memory.area("ring")(SLOTS, KT * PANEL))

        const = buf(N_CONST1)
        par = buf(N_PAR1)

        def C(name, rows=P):
            lo, hi = CONST1[name]
            return const[0:rows, lo:hi]

        def PAR(name, i=None, n=1):
            lo, hi = PAR1[name]
            return par[:, lo:hi] if i is None else par[:, lo + i:lo + i + n]

        w_uq = buf(2, 384)
        w_ukv = buf(512)
        w_gk2 = buf(P)
        mixT = buf(KT, T)
        stat = buf(64)

        front, back = memory.area("front"), memory.area("back")
        hT = front(KT, T)
        a_left = Area(front(A_LEFT), A_LEFT)
        between = front(BETWEEN)
        d_work = back(D_WORK)
        area = Area(back(LEFT), LEFT)
        G = {}
        for m, R, left in (("A", 2, a_left), ("B", 1, area)):
            g = G[m] = Group()
            g.name, g.R = m, R
            g.q, g.k, g.lf = (left(R, T) for _ in range(3))
            g.vT, g.gate = left(2, T), left(2, T)
        cT = area(3, T)
        kr = area(T)
        cin = area(6, 3 + T)
        oD = Group()
        oD.gate = area(2, T)
        code = kr
        lb = area(32)
        zb = area(NT, 8)
        sm = {n: area(NT, 4) for n in ("beta", "x", "e", "l", "g", "b", "nb", "eb", "be", "fd", "bl")}
        ea = area(4)
        SD = area(4, 2, HD)

        whole = memory.plain["front"][:, :]
        for g, area, rest in ((G["A"], Area(between, BETWEEN), Area(d_work, D_WORK)),
                              (G["B"], memory.area("front"), None)):
            R = g.R
            g.b, g.eb, g.qe, g.kd, g.e2 = (area(R, T) for _ in range(5))
            g.rs = shaped(area.tensor[:, 3 * R * T:(3 * R + 2) * T], 2, T)
            g.vtok, g.oT = area(2, T), area(2, T)
            area = rest or area
            g.sq = area(2, T)
            g.kdtok = area(NT, R * P)
            g.S = area(R, NSUB, HD)
            at = area.at
            g.vexp = area(NT, SUBP, GW)
            area.at = at
            g.band = {n: area(2, (2 if n == "o" else R) * T) for n in ("diff", "exp", "qk", "w", "o")}
        area = memory.area("front")
        cn = area(3, T)
        qT, kT = area(4, T), area(4, T)
        vtokC = area(NT, GW)
        L, Pr, PT = area(4, T), area(4, T), area(NT, 4, T)
        crs, rtmp = Pr[:, 0:2, :], PT[:, 0]
        area = Area(d_work, D_WORK)
        ktok, vtokD, kbe = (area(NT, GW) for _ in range(3))
        kdec, vb = ktok, vtokD
        row, lstr, lincT, erow, Tm, Um, NTm = (area(8, P) for _ in range(7))
        Xm = row
        pm = lstr
        uD = vnew = area(NT, GW)
        cth = shaped(area.tensor[:, area.at - NT * GW - 6 * T:area.at - NT * GW], 6, T)
        at = area.at
        cv = area(6, T)
        lrs = erow.rearrange("p a b -> p (a b)").rearrange("p (a b) -> p a b", a=4)
        area.at = at
        oD.oT, oD.sq, oD.rs = (area(2, T) for _ in range(3))
        qeD, wT = (shaped(cin.rearrange("p a b -> p (a b)")[:, i * 2 * T:(i + 1) * 2 * T], 2, T) for i in range(2))
        xn = shaped(between[:, 0:NT * DM], NT, DM)
        diagonal = shaped(between[:, NT * DM:NT * DM + NT * P], NT, P)
        front, back = Area(whole[:, KT * T:], A_LEFT + BETWEEN), memory.area("back")
        gh, gl = front(FT, T), back(FT, T)
        gpad = back(2, 2 + T)
        gcv = back(2, 3, T)
        ysq, yn = back(512), back(4, 512)

        IN_USES = [
            ("a_q", "in0", [(0, P, 0, 0), (0, P, 1, 128)]), ("a_f", "in1", [(0, P, 0, 256), (0, P, 1, 384)]),
            ("a_i", "in2", [(0, P, 0, 512), (0, P, 1, 640)]), ("a_g", "in3", [(0, P, 0, 768), (0, P, 1, 896)]),
            ("b_qk", "in4", [(0, P, 0, 1024), (0, P, 1, 1152)]), ("b_v", "in5", [(0, P, 0, 1280), (0, P, 1, 1408)]),
            ("code", "in6", [(0, 16, 0, 1536)]), ("b_g", "in6", [(0, P, 0, 1552), (0, P, 1, 1680)]),
            ("c_q", "in7", [(0, P, 0, 1808), (0, P, 1, 1936)]),
            ("c_kvr", "in8", [(0, P, 0, 2064), (64, 32, 1, 2192)]),
            ("d_q", "in9", [(0, P, 0, 2224), (0, P, 1, 2352)]),
            ("d_k", "in10", [(0, P, 0, 2480), (0, P, 1, 2608)]), ("d_v", "in11", [(0, P, 0, 2736), (0, P, 1, 2864)]),
            ("d_z", "in12", [(0, P, 0, 3000), (0, P, 1, 3128)]),
        ]
        LEAD, TAIL, HASTE = 7, 2, 0.97
        IN_STEPS, GLA_STEPS, MLA_STEPS = sum(len(parts) for _, _, parts in IN_USES) + 1, SUB + 10, 12
        GDN_STEPS = 11 + 3 * 5 + 1 + 7 + 2
        early = interleave(["A"] * (GLA_STEPS - TAIL), ["in"] * (IN_STEPS - LEAD))
        ORDER = (["in"] * LEAD + early + ["A"] * (TAIL - 1) + ["D", "A"]
                 + interleave(["D"] * (GDN_STEPS - 1), ["B"] * (GLA_STEPS - 4) + ["out"] * 4 + ["B"] * 4 + ["C"] * MLA_STEPS + ["mix"], HASTE))
        POOLED = [name for name in ring.split if name.startswith(("out", "gate"))]
        OTHERS = [name for name in ring.split if name not in POOLED]

        def split_done(name):
            if name in POOLED:
                return S["w_split_pool"], POOLED.index(name) + 1
            return S["w_split"], OTHERS.index(name) + 1

        block = ctx.enter_context(nc.Block())

        @block.sync
        def _(sp):
            sp.dma_start(const[:, :], A["const1"]).then_inc(once, 16)
            sp.wait_ge(once, 16)
            sp.wait_ge(S["params"], 64)
            for s in range(SLOTS):
                sp.sem_inc(ring.free[s], 1)
            with sp.Fori(0, DEPTH) as layer:
                ring.load_all(sp, layer)

        @block.tensor
        def _(pe):
            used = []

            def mm(out, lhsT, rhs, start=True, stop=True):
                ins = nc.tensor.matmul(out, lhsT, rhs, start=start, stop=stop)
                if used:
                    ins.then_inc(*ring.freed(used.pop(0)))
                return ins

            def mm3(out, a, b, start, stop):
                mm(out, a[0], b[0], start, False)
                mm(out, a[0], b[1], False, False)
                return mm(out, a[1], b[0], False, stop)

            def split_panel(name):
                pe.wait_ge(*split_done(name))
                return rounded(ring.view(name + "_hi")), rounded(ring.view(name))

            def give_back():
                for name in used:
                    pe.drain().then_inc(*ring.freed(name))
                used.clear()

            def transpose(out, a):
                return nc.tensor.transpose(out, a, C("ident"))

            def normed_transposes(name, k):
                for t in range(NT):
                    pe.wait_ge(S["diagonal"], NT * k + t + 1)
                    for j in range(2):
                        b = psum.claim(pe, f"{name}_{t}{j}")
                        for i in range(4):
                            c = (4 * j + i) * P
                            last = mm(b[:, i * P:(i + 1) * P], x[:, t, c:c + P], diagonal[:, t, :])
                        last.then_inc(psum.full_of(f"{name}_{t}{j}"), 1)

            def project(layer):
                pe.wait_ge(S["hT"], 4)
                held = None
                for name, panel, parts in IN_USES:
                    if panel != held:
                        if held:
                            used.append(held)
                        held = panel
                        w = ring.wait(pe, layer, panel)
                        base = IN1[int(panel[2:])][0]
                    if name == "d_z":
                        b = psum.claim(pe, "d_ba")
                        for t in range(NT):
                            for k in range(KT):
                                last = mm(b[:, 8 * t:8 * t + 8], hT[:, k, t * P:(t + 1) * P], w[:, k, 0:8], k == 0, k == KT - 1)
                        last.then_inc(psum.full_of("d_ba"), 1)
                    b = psum.claim(pe, name)
                    for row0, m, half, c0 in parts:
                        for k in range(KT):
                            last = mm(b[row0:row0 + m, half * T:(half + 1) * T], w[:, k, c0 - base:c0 - base + m],
                                      hT[:, k, :], k == 0, k == KT - 1)
                        if len(parts) == 2 and not half:
                            yield
                    last.then_inc(psum.full_of(name), 1)
                    yield
                used.append(held)
                give_back()
                yield

            def head_norm(g, n, name):
                pe.wait_ge(S["o_sq"], n + 1)
                b = psum.claim(pe, name)
                mm(b[:, :], C("heads64"), g.sq[:, :, :]).then_inc(psum.full_of(name), 1)

            def gla(g, m):
                if m:
                    pe.wait_ge(S["code"], 1)
                    b = psum.claim(pe, "gk")
                    mm(b[:, 0:T], w_gk2[0:16, :], code[0:16, :]).then_inc(psum.full_of("gk"), 1)
                yield
                pe.wait_ge(S["v_T"], m + 1)
                b = psum.claim(pe, g.name + "_vt")
                for t in range(NT):
                    for p in range(2):
                        last = transpose(b[:, t * T + p * P:t * T + (p + 1) * P], g.vT[:, p, t * P:(t + 1) * P])
                last.then_inc(psum.full_of(g.name + "_vt"), 1)
                yield
                yield
                pe.wait_ge(S["kdT"], m + 1)
                b = psum.claim(pe, g.name + "_kdt")
                for t in range(NT):
                    for r in range(g.R):
                        at = (t * g.R + r) * P
                        last = transpose(b[:, at:at + P], g.kd[:, r, t * P:(t + 1) * P])
                last.then_inc(psum.full_of(g.name + "_kdt"), 1)
                yield
                pe.wait_ge(S["kd_tok"], m + 1)
                pe.wait_ge(S["vexp"], m + 1)
                d = g.R * P // 4
                for t in range(NT):
                    for r in range(g.R):
                        name = f"{g.name}_G{r}{t}"
                        b = psum.claim(pe, name)
                        for h in range(4 // g.R * r, 4 // g.R * (r + 1)):
                            row0 = d * h - P * r
                            last = mm(shaped(b, SUBP, HD)[row0:row0 + d, :, :], g.kdtok[:, t, d * h:d * h + d],
                                      g.vexp[:, t, :, HD * h:HD * h + HD])
                        last.then_inc(psum.full_of(name), 1)
                    yield
                pe.wait_ge(S["state"], m + 1)
                pe.wait_ge(S["q_decayed"], m + 1)
                for p in range(2):
                    name = f"{g.name}_o{p}"
                    b = psum.claim(pe, name)
                    for s in range(NSUB):
                        for h in (2 * p, 2 * p + 1):
                            r, row0 = (d * h) // P, (d * h) % P
                            last = mm(b[HD * (h % 2):HD * (h % 2) + HD, SUB * s:SUB * s + SUB], g.S[row0:row0 + d, r, s, :],
                                      g.qe[row0:row0 + d, r, SUB * s:SUB * s + SUB])
                    last.then_inc(psum.full_of(name), 1)
                yield
                yield
                for i in range(SUB):
                    pe.wait_ge(S["weighted"], SUB * m + i + 1)
                    name, n = f"{g.name}_band{i}", NSUB * (SUB - i)
                    b = psum.claim(pe, name)
                    w = g.band["w"][:, i % 2, :]
                    if g.R == 2:
                        last = mm(b[:, 0:2 * n], C("heads64"), w[:, 0:2 * n])
                    else:
                        for p in range(2):
                            last = mm(b[:, p * n:(p + 1) * n], C("to_pair")[:, p * P:(p + 1) * P], w[:, 0:n])
                    last.then_inc(psum.full_of(name), 1)
                    yield
                yield
                head_norm(g, m, g.name + "_ss")
                yield

            def mla():
                yield
                pe.wait_ge(S["mla_sq"], 1)
                b = psum.claim(pe, "c_ss")
                mm(b[:, 0:T], C("ones"), crs[:, 0, :], True, False)
                mm(b[:, 0:T], C("ones"), crs[:, 1, :], False, True)
                mm(b[:, T:2 * T], C("ones"), rtmp[:, 0, :]).then_inc(psum.full_of("c_ss"), 1)
                pe.wait_ge(S["mla_c"], 2)
                b = psum.claim(pe, "kr_rot")
                mm(b[64:96, 0:T], C("rot96")[64:96, 64:96], kr[64:96, :]).then_inc(psum.full_of("kr_rot"), 1)
                yield
                yield
                pe.wait_ge(S["mla_cn"], 1)
                for j in range(2):
                    b = psum.claim(pe, f"qT{j}")
                    for i in range(2):
                        h = 2 * j + i
                        for k in range(2):
                            last = mm(b[0:96, i * T:(i + 1) * T], w_uq[:, k, 96 * h:96 * h + 96], cn[:, k, :], k == 0, k == 1)
                    last.then_inc(psum.full_of(f"qT{j}"), 1)
                for j in range(2):
                    b = psum.claim(pe, f"kT{j}")
                    for i in range(2):
                        h = 2 * j + i
                        last = mm(b[0:64, i * T:(i + 1) * T], w_ukv[:, P * h:P * h + 64], cn[:, 2, :])
                    last.then_inc(psum.full_of(f"kT{j}"), 1)
                b = psum.claim(pe, "c_v")
                for t in range(NT):
                    last = mm(shaped(b[:, t * T:(t + 1) * T], 4, HD), cn[:, 2, t * P:(t + 1) * P],
                              shaped(w_ukv, 4, P)[:, :, 64:P])
                last.then_inc(psum.full_of("c_v"), 1)
                yield
                pe.wait_ge(S["rot_in"], 2)
                for j in range(2):
                    b = psum.claim(pe, f"rot{j}")
                    mm(b[0:96, :], C("rot96", 96), qT[0:96, 2 * j:2 * j + 2, :]).then_inc(psum.full_of(f"rot{j}"), 1)
                yield
                pe.wait_ge(S["qT"], 1)
                pe.wait_ge(S["kT"], 2)
                for t in range(NT):
                    n = P * (t + 1)
                    for j in range(2):
                        b = psum.claim(pe, f"c_sc{t}{j}")
                        for i in range(2):
                            h = 2 * j + i
                            last = mm(b[:, i * n:(i + 1) * n], qT[0:96, h, t * P:(t + 1) * P], kT[0:96, h, 0:n])
                        last.then_inc(psum.full_of(f"c_sc{t}{j}"), 1)
                    yield
                    yield
                    pe.wait_ge(S["probs"], t + 1)
                    for kt in range(t + 1):
                        b = psum.claim(pe, f"c_pt{t}{kt}")
                        for h in range(4):
                            last = transpose(b[:, h * P:(h + 1) * P], Pr[:, h, kt * P:(kt + 1) * P])
                        last.then_inc(psum.full_of(f"c_pt{t}{kt}"), 1)
                    yield
                pe.wait_ge(S["PT"], 3)
                pe.wait_ge(S["mla_v"], 1)
                b = psum.claim(pe, "c_o")
                for h in range(4):
                    o = b[HD * (h % 2):HD * (h % 2) + HD, T * (h // 2):T * (h // 2) + T]
                    mm(o, vtokC[:, 0, HD * h:HD * h + HD], PT[:, 0, h, :], True, False)
                    last = mm(o[:, P:T], vtokC[:, 1, HD * h:HD * h + HD], PT[:, 1, h, P:T], False, True)
                last.then_inc(psum.full_of("c_o"), 1)
                yield

            def gdn():
                yield
                yield
                yield
                pe.wait_ge(S["l2_sq"], 1)
                for j in range(2):
                    b = psum.claim(pe, f"l2_{j}")
                    mm(b[:, :], C("heads64"), cth[:, 2 * j:2 * j + 2, :]).then_inc(psum.full_of(f"l2_{j}"), 1)
                yield
                pe.wait_ge(S["g_ready"], 1)
                b = psum.claim(pe, "bsum")
                mm(b[:, 0:8], C("cum"), sm["g"][:, :, :])
                mm(b[:, 8:16], C("heads64"), sm["g"][:, :, :]).then_inc(psum.full_of("bsum"), 1)
                for par_ in range(2):
                    name = f"brow{par_}"
                    b = psum.claim(pe, name)
                    for t in range(NT):
                        for hp in range(2):
                            at = (2 * t + hp) * P
                            h = 2 * hp + par_
                            last = mm(b[:, at:at + P], sm["g"][:, t, h:h + 1].broadcast_to([P, P]), C("cum"))
                    last.then_inc(psum.full_of(name), 1)
                yield
                yield
                pe.wait_ge(S["qk_norm"], 1)
                for what, base in (("k_tok", 2), ("v_tok", 4)):
                    b = psum.claim(pe, what)
                    for t in range(NT):
                        for p in range(2):
                            last = transpose(b[:, t * T + p * P:t * T + (p + 1) * P], cv[:, base + p, t * P:(t + 1) * P])
                    last.then_inc(psum.full_of(what), 1)
                yield
                for what, base in (("kk", 2), ("kq", 0)):
                    for par_ in range(2):
                        name = f"{what}{par_}"
                        b = psum.claim(pe, name)
                        for t in range(NT):
                            for hp in range(2):
                                at, row0 = (2 * t + hp) * P, HD * par_
                                last = mm(b[:, at:at + P], cv[row0:row0 + HD, 2 + hp, t * P:(t + 1) * P],
                                          cv[row0:row0 + HD, base + hp, t * P:(t + 1) * P])
                        last.then_inc(psum.full_of(name), 1)

                def eight(what, f, copied=None):
                    for j in range(2):
                        if copied:
                            pe.wait_ge(S["level_X"], copied + j)
                        b = psum.claim(pe, f"{what}{j}")
                        for i in range(4):
                            last = f(b[:, i * P:(i + 1) * P], 4 * j + i)
                        last.then_inc(psum.full_of(f"{what}{j}"), 1)

                yield
                yield
                pe.wait_ge(S["lmat"], 1)
                eight("nt", lambda o, e: transpose(o, lstr[:, e, :]))
                yield
                yield
                for n in range(1, 6):
                    pe.wait_ge(S["level_T"], n)
                    eight(f"X{n}_", lambda o, e: mm(o, pm[:, e, :], Tm[:, e, :]))
                    yield
                    if n < 5:
                        eight(f"TX{n}_", lambda o, e: mm(o, Um[:, e, :], Xm[:, e, :]), 2 * n - 1)
                    eight(f"UX{n}_", lambda o, e: mm(o, Xm[:, e, :], Um[:, e, :]), 2 * n - 1)
                    yield
                    yield
                pe.wait_ge(S["level_T"], 6)
                pe.wait_ge(S["tok_D"], 1)
                b = psum.claim(pe, "u")
                for par_ in range(2):
                    for t in range(NT):
                        for hp in range(2):
                            h, e = 2 * hp + par_, 4 * par_ + 2 * t + hp
                            last = mm(b[:, t * T + HD * h:t * T + HD * h + HD], Um[:, e, :], vb[:, t, HD * h:HD * h + HD])
                last.then_inc(psum.full_of("u"), 1)
                b = psum.claim(pe, "wT")
                for par_ in range(2):
                    for t in range(NT):
                        for hp in range(2):
                            h, e = 2 * hp + par_, 4 * par_ + 2 * t + hp
                            last = mm(b[HD * par_:HD * par_ + HD, hp * T + t * P:hp * T + (t + 1) * P],
                                      kbe[:, t, HD * h:HD * h + HD], Um[:, e, :])
                last.then_inc(psum.full_of("wT"), 1)
                yield
                pe.wait_ge(S["uw"], 2)
                pe.wait_ge(S["qe"], 1)
                for c in range(4):
                    t, tok0, chunk = c // 2, CHUNK * (c % 2), slice(CHUNK * c, CHUNK * (c + 1))
                    pe.wait_ge(S["state_D"], c + 1)
                    for par_ in range(2):
                        rows = slice(HD * par_, HD * par_ + HD)
                        b = psum.claim(pe, f"ws{c}{par_}")
                        for hp in range(2):
                            last = mm(b[tok0:tok0 + CHUNK, hp * HD:(hp + 1) * HD], wT[rows, hp, chunk], SD[rows, c, hp, :])
                        last.then_inc(psum.full_of(f"ws{c}{par_}"), 1)
                    yield
                    if c < 3:
                        pe.wait_ge(S["v_new"], c + 1)
                        b = psum.claim(pe, f"su{c}")
                        for par_ in range(2):
                            for hp in range(2):
                                h = 2 * hp + par_
                                last = mm(b[HD * par_:HD * par_ + HD, hp * HD:(hp + 1) * HD],
                                          kdec[tok0:tok0 + CHUNK, t, HD * h:HD * h + HD],
                                          vnew[tok0:tok0 + CHUNK, t, HD * h:HD * h + HD])
                        last.then_inc(psum.full_of(f"su{c}"), 1)
                        yield
                o = psum.claim(pe, "D_o")
                for par_ in range(2):
                    rows = slice(HD * par_, HD * par_ + HD)
                    for c in range(4):
                        chunk = slice(CHUNK * c, CHUNK * (c + 1))
                        for hp in range(2):
                            last = mm(shaped(o, 2, T)[rows, hp, chunk], SD[rows, c, hp, :], qeD[rows, hp, chunk])
                last.then_inc(psum.full_of("D_o"), 1)
                pe.wait_ge(S["v_new"], 4)
                b = psum.claim(pe, "D_o2")
                for par_ in range(2):
                    for t in range(NT):
                        for hp in range(2):
                            h, e = 2 * hp + par_, 4 * par_ + 2 * t + hp
                            last = mm(b[HD * par_:HD * par_ + HD, hp * T + t * P:hp * T + (t + 1) * P],
                                      vnew[:, t, HD * h:HD * h + HD], lincT[:, e, :])
                last.then_inc(psum.full_of("D_o2"), 1)
                yield
                head_norm(oD, 2, "D_ss")
                yield

            def wide(what, lhs, panels):
                banks = [psum.claim(pe, f"{what}{i}") for i in range(4)]
                for n, name in enumerate(panels):
                    w = split_panel(name)
                    end = n == len(panels) - 1
                    for t in range(NT):
                        for cut in range(2):
                            for half in range(2):
                                last = mm3(banks[2 * t + half], [a[:, 2 * n + cut, t * P:(t + 1) * P] for a in lhs],
                                           [a[:, cut, half * 512:half * 512 + 512] for a in w], n == cut == 0, end and cut == 1)
                                if end and cut:
                                    last.then_inc(psum.full_of(f"{what}{2 * t + half}"), 1)
                    used.extend((name, name + "_hi"))
                give_back()

            def rows_by(what, lhs, panel):
                for t in range(NT):
                    banks = [psum.claim(pe, f"{what}{half}{t}") for half in range(2)]
                    for q in range(4):
                        name = f"{panel}{q}"
                        w = split_panel(name)
                        for k in range(KT):
                            last = mm3(banks[q // 2][:, (q % 2) * 256:(q % 2) * 256 + 256], [a[:, k, t * P:(t + 1) * P] for a in lhs],
                                       [a[:, k, :] for a in w], k == 0, k == KT - 1)
                        if q % 2:
                            last.then_inc(psum.full_of(f"{what}{q // 2}{t}"), 1)
                        if t == NT - 1:
                            used.extend((name, name + "_hi"))
                give_back()

            with pe.Fori(0, DEPTH) as layer:
                pe.wait_ge(once, 16)
                pe.wait_ge(S["params"], 64)
                normed_transposes("hT0", 0)
                emit(ORDER, {"in": project(layer), "A": gla(G["A"], 0), "B": gla(G["B"], 1), "C": mla(), "D": gdn(), "out": iter(range(4)), "mix": iter(range(1))})
                pe.wait_ge(S["mix_split"], 1)
                rows_by("mix", (rounded(hT), rounded(mixT)), "out")
                normed_transposes("hT1", 1)
                pe.wait_ge(S["h_split"], 1)
                h = (rounded(mixT), rounded(hT))
                for j in range(FT):
                    b = psum.claim(pe, f"ff{j}")
                    for half, what in enumerate(("gate", "up")):
                        name = f"{what}{j // 2}"
                        w = split_panel(name)
                        c = (j % 2) * P
                        for k in range(KT):
                            last = mm3(b[:, half * T:(half + 1) * T], [a[:, k, c:c + P] for a in w], [a[:, k, :] for a in h],
                                       k == 0, k == KT - 1)
                        if j % 2 and not half:
                            used.extend((name, name + "_hi"))
                    last.then_inc(psum.full_of(f"ff{j}"), 1)
                    if j % 2:
                        used.extend((name, name + "_hi"))
                pe.wait_ge(S["gT"], FT)
                wide("y", (rounded(gh), rounded(gl)), [f"down{i}" for i in range(FT // 2)])
                pe.drain().then_inc(layer_done, 1)
                pe.wait_ge(layer_open, layer + 1)

        @block.scalar
        def _(act):
            A_ = nc.scalar.activation

            def round_weights(layer, *names):
                for name in names:
                    raw = ring.wait(act, layer, name)
                    ring.wait_free(act, layer, name + "_hi")
                    A_(rounded(ring.view(name + "_hi")), raw, ACT.Copy).then_inc(S["w_hi"], 1)

            def norm_stats(k, t):
                A_(xn[:, t, :], x[:, t, :], ACT.Square, accum_out=stat[:, t:t + 1])
                act.drain()
                A_(stat[:, 2 + t:3 + t], stat[:, t:t + 1], ACT.Ln, bias=C("eps"), scale=1.0 / DM)
                act.drain()
                A_(stat[:, 4 + t:5 + t], stat[:, 2 + t:3 + t], ACT.Exp, scale=-0.5).then_inc(S["rstd"], 1)

            def half_of_hT(name, gain):
                for t in range(NT):
                    act.wait_ge(*psum.filled(f"{name}_{t}1"))
                    for i in range(4):
                        last = A_(hT[:, 4 + i, t * P:(t + 1) * P], psum.bank(f"{name}_{t}1")[:, i * P:(i + 1) * P], ACT.Copy,
                                  scale=PAR(gain, 4 + i) if gain else 1.0)
                    last.then_inc(*psum.freed(f"{name}_{t}1"))
                    act.drain().then_inc(S["hT"], 1)

            def y_stats(k, t, names):
                for half, name in enumerate(names):
                    act.wait_ge(*psum.filled(name))
                    A_(ysq[:, 0:512], psum.bank(name), ACT.Square, accum_out=stat[:, 40 + 2 * half + t:41 + 2 * half + t])
                    act.drain()
                act.drain().then_inc(S["y_ss"], 1)
                act.wait_ge(S["y_sum"], NT * k + t + 1)
                A_(stat[:, 46 + t:47 + t], stat[:, 44 + t:45 + t], ACT.Ln, bias=C("eps"), scale=1.0 / DM)
                act.drain()
                A_(stat[:, 48 + t:49 + t], stat[:, 46 + t:47 + t], ACT.Exp, scale=-0.5).then_inc(S["y_rstd"], 1)

            def drain_bank(name, out, signal, rows=slice(0, P), part=slice(0, 512), func=ACT.Copy, scale=1.0):
                act.wait_ge(*psum.filled(name))
                A_(out, psum.bank(name)[rows, part], func, scale=scale).then_inc(*psum.freed(name))
                if signal:
                    act.drain().then_inc(S[signal], 1)

            def post_norm(g, n, name, step):
                act.wait_ge(S["oT_ready"], n + 1)
                A_(g.sq[:, :, :], g.oT[:, :, :], ACT.Square).then_inc(S["o_sq"], 1)
                act.wait_ge(*psum.filled(name))
                ins = A_(g.rs[:, :, :], shaped(psum.bank(name), 2, T), ACT.Ln, bias=C("eps"), scale=1.0 / HD)
                ins.then_inc(*psum.freed(name))
                act.drain()
                A_(g.rs[:, :, :], g.rs[:, :, :], ACT.Exp, scale=-0.5).then_inc(S["o_rstd"], 1)

            def gla(g, m, step):
                if m == 0:
                    act.wait_ge(S["af_f"], 1)
                    A_(g.lf[:, :, :], g.lf[:, :, :], ACT.Ln)
                    A_(g.b[:, :, :], g.b[:, :, :], ACT.Ln, scale=2.0 ** 40).then_inc(S["af_ln"], 1)
                else:
                    act.wait_ge(S["gk_abs"], 1)
                    step(A_(g.e2[:, :, :], g.e2[:, :, :], ACT.Exp, scale=-1.0))
                    A_(g.e2[:, :, :], g.e2[:, :, :], ACT.Ln, bias=C("ones")[:, 0:1]).then_inc(S["gk_ln"], 1)
                yield
                act.wait_ge(S["scan"], m + 1)
                A_(g.eb[:, :, :], g.b[:, :, :], ACT.Exp).then_inc(S["exp_b"], 1)
                act.wait_ge(S["scan_end"], m + 1)
                A_(g.e2[:, :, :], g.e2[:, :, :], ACT.Exp, scale=-1.0).then_inc(S["kd_exp"], 1)
                yield
                drain_bank(g.name + "_vt", g.vtok[:, :, :], "vtok")
                yield
                yield
                yield
                yield
                yield
                for i in range(SUB):
                    n = SUB * m + i
                    act.wait_ge(S["diff"], n + 1)
                    if n >= 2:
                        act.wait_ge(S["weighted"], n - 1)
                    w = g.R * NSUB * (SUB - i)
                    A_(g.band["exp"][:, i % 2, 0:w], g.band["diff"][:, i % 2, 0:w], ACT.Exp).then_inc(S["decay"], 1)
                    yield
                yield
                yield
                post_norm(g, m, g.name + "_ss", step)
                yield

            def project():
                a, bb = G["A"], G["B"]
                yield
                yield
                act.wait_ge(*psum.filled("a_q"))
                A_(a.q[:, :, :], shaped(psum.bank("a_q"), 2, T), ACT.Tanh, scale=0.5).then_inc(S["aq_tanh"], 1)
                yield
                yield
                act.wait_ge(*psum.filled("a_f"))
                A_(a.lf[:, :, :], shaped(psum.bank("a_f"), 2, T), ACT.Sigmoid)
                A_(a.k[:, :, :], shaped(psum.bank("a_f"), 2, T), ACT.Sigmoid, scale=-1.0).then_inc(*psum.freed("a_f"))
                act.drain().then_inc(S["af_sig"], 1)
                yield
                yield
                drain_bank("a_i", a.vT[:, :, :], "v_T")
                yield
                yield
                drain_bank("a_g", a.gate[:, :, :], "gate_th", func=ACT.Tanh, scale=0.5)
                yield
                yield
                yield
                yield
                drain_bank("b_v", bb.vT[:, :, :], "v_T")
                yield
                drain_bank("code", code[0:16, :], "code", slice(0, 16), slice(0, T))
                yield
                yield
                act.wait_ge(*psum.filled("b_g"))
                A_(bb.gate[:, :, :], shaped(psum.bank("b_g"), 2, T), ACT.Tanh, scale=0.5).then_inc(S["bg_th"], 1)
                yield
                yield
                drain_bank("c_q", cT[:, 0:2, :], "mla_c")
                yield
                yield
                act.wait_ge(*psum.filled("c_kvr"))
                A_(cT[:, 2, :], psum.bank("c_kvr")[:, 0:T], ACT.Copy)
                A_(kr[64:96, :], psum.bank("c_kvr")[64:96, T:2 * T], ACT.Copy).then_inc(*psum.freed("c_kvr"))
                act.drain().then_inc(S["mla_c"], 1)
                for _ in range(6):
                    yield
                yield
                yield
                act.wait_ge(*psum.filled("d_z"))
                A_(oD.gate[:, :, :], shaped(psum.bank("d_z"), 2, T), ACT.Tanh, scale=0.5).then_inc(S["dz_th"], 1)
                yield

            def mla():
                act.wait_ge(S["gla_done"], 1)
                A_(crs[:, :, :], cT[:, 0:2, :], ACT.Square)
                A_(rtmp[:, 0, :], cT[:, 2, :], ACT.Square).then_inc(S["mla_sq"], 1)
                yield
                act.wait_ge(*psum.filled("c_ss"))
                A_(crs[:, 0, :], psum.bank("c_ss")[:, 0:T], ACT.Ln, bias=C("eps"), scale=1.0 / 256)
                A_(crs[:, 1, :], psum.bank("c_ss")[:, T:2 * T], ACT.Ln, bias=C("eps"), scale=1.0 / 128).then_inc(*psum.freed("c_ss"))
                act.drain()
                A_(crs[:, :, :], crs[:, :, :], ACT.Exp, scale=-0.5).then_inc(S["mla_rstd"], 1)
                yield
                yield
                for j in range(2):
                    act.wait_ge(*psum.filled(f"qT{j}"))
                    A_(qT[0:96, 2 * j:2 * j + 2, :], shaped(psum.bank(f"qT{j}"), 2, T)[0:96], ACT.Copy).then_inc(*psum.freed(f"qT{j}"))
                    act.drain().then_inc(S["rot_in"], 1)
                drain_bank("c_v", vtokC[:, :, :], "mla_v")
                yield
                yield
                for t in range(NT):
                    n = P * (t + 1)
                    yield
                    act.wait_ge(S["scores_max"], t + 1)
                    for h in range(4):
                        last = A_(Pr[:, h, 0:n], L[:, h, 0:n], ACT.Exp, bias=stat[:, 16 + 4 * t + h:17 + 4 * t + h],
                                  accum_out=stat[:, 24 + 4 * t + h:25 + 4 * t + h])
                    act.drain().then_inc(S["exps"], 1)
                    yield
                    for kt in range(t + 1):
                        drain_bank(f"c_pt{t}{kt}", PT[:, kt, :, t * P:(t + 1) * P], "PT")
                    yield
                drain_bank("c_o", mixT[:, 4:6, :], "mixT_C")
                yield

            def gdn(step):
                yield
                act.wait_ge(S["conv"], 1)
                A_(cth[:, :, :], cv[:, :, :], ACT.Tanh, scale=0.5).then_inc(S["conv_th"], 1)
                act.wait_ge(S["ba_in"], 1)
                A_(sm["beta"][:, :, :], zb[:, :, 0:4], ACT.Tanh, scale=0.5)
                yield
                step(A_(sm["l"][:, :, :], sm["e"][:, :, :], ACT.Exp, scale=-1.0))
                A_(sm["l"][:, :, :], sm["l"][:, :, :], ACT.Ln, bias=C("ones")[:, 0:1]).then_inc(S["ba_exp"], 1)
                act.wait_ge(S["conv_silu"], 1)
                A_(cth[:, 0:4, :], cv[:, 0:4, :], ACT.Square).then_inc(S["l2_sq"], 1)
                yield
                yield
                for j in range(2):
                    act.wait_ge(*psum.filled(f"l2_{j}"))
                    A_(lrs[:, 2 * j:2 * j + 2, :], shaped(psum.bank(f"l2_{j}"), 2, T), ACT.Ln, bias=C("eps")).then_inc(*psum.freed(f"l2_{j}"))
                act.drain()
                A_(lrs[:, :, :], lrs[:, :, :], ACT.Exp, scale=-0.5).then_inc(S["l2_rstd"], 1)
                yield
                act.wait_ge(S["b_small"], 1)
                A_(sm["eb"][:, :, :], sm["b"][:, :, :], ACT.Exp)
                A_(sm["fd"][:, :, :], sm["bl"][:, :, :], ACT.Exp).then_inc(S["b_exp"], 1)
                yield
                act.wait_ge(S["qk_norm"], 1)
                for j in range(2):
                    name = f"brow{j}"
                    act.wait_ge(*psum.filled(name))
                    A_(erow[:, 4 * j:4 * j + 4, :], shaped(psum.bank(name), 4, P), ACT.Exp)
                act.drain().then_inc(S["erow"], 1)
                yield
                act.wait_ge(S["hid"], 1)
                for par_ in range(2):
                    for t in range(NT):
                        for hp in range(2):
                            h, e = 2 * hp + par_, 4 * par_ + 2 * t + hp
                            A_(lstr[:, e, :], lstr[:, e, :], ACT.Exp, scale=-1.0, bias=sm["b"][:, t, h:h + 1])
                            last = A_(lincT[:, e, :], lincT[:, e, :], ACT.Exp, bias=sm["nb"][:, t, h:h + 1])
                last.then_inc(S["decays"], 1)
                yield
                yield
                for j in range(2):
                    drain_bank(f"nt{j}", NTm[:, 4 * j:4 * j + 4, :], "nt")
                yield
                yield
                for n in range(1, 6):
                    for j in range(2):
                        drain_bank(f"X{n}_{j}", Xm[:, 4 * j:4 * j + 4, :], "level_X")
                    yield
                    yield
                    yield
                drain_bank("u", uD[:, :, :], "uw")
                drain_bank("wT", wT[:, :, :], "uw")
                yield
                for _ in range(7):
                    yield
                yield
                post_norm(oD, 2, "D_ss", step)
                yield

            def split_out(layer):
                for i in range(4):
                    round_weights(layer, f"out{i}")
                    yield

            with act.Fori(0, DEPTH) as layer:
                step = Chain(act, S["act"])
                act.dma_start(par[:, :], A["par1"][layer, :, :]).then_inc(S["params"], 16)
                act.dma_start(w_uq, A["mla_w_uq"].rearrange("l (k p) n -> l p k n", p=P)[layer, :, :, :]).then_inc(S["params"], 16)
                act.dma_start(w_ukv, A["mla_w_ukv"][layer, :, :]).then_inc(S["params"], 16)
                act.dma_start(w_gk2[0:16, :], A["gla_w_gk2"][layer, :, :]).then_inc(S["params"], 16)
                act.wait_ge(once, 16)
                act.wait_ge(x_in, 32)
                for t in range(NT):
                    norm_stats(0, t)
                act.wait_ge(S["params"], 64)
                A_(ea, PAR("a_log"), ACT.Exp)
                act.wait_ge(S["lb_max"], 1)
                A_(lb[:, 0:2 * DEPTH], lb[:, 0:2 * DEPTH], ACT.Exp).then_inc(S["lb_exp"], 1)
                half_of_hT("hT0", "pre_mix")
                emit(ORDER, {"in": project(), "A": gla(G["A"], 0, step), "B": gla(G["B"], 1, step), "C": mla(), "D": gdn(step),
                             "out": split_out(layer), "mix": iter(range(1))})
                for t in range(NT):
                    y_stats(0, t, [f"mix{half}{t}" for half in range(2)])
                    act.wait_ge(S["x_new"], t + 1)
                    norm_stats(1, t)
                half_of_hT("hT1", "pre_ffn")
                round_weights(layer, "gate0", "up0")
                for j in range(FT):
                    q = j // 2 + 1
                    name = f"{('gate', 'up')[j % 2]}{q}" if q < FT // 2 else f"down{j - FT + 2}"
                    round_weights(layer, name)
                    act.wait_ge(*psum.filled(f"ff{j}"))
                    if j >= 2:
                        act.wait_ge(S["ff_conv"], j - 1)
                    A_(gpad[:, j % 2, 2:2 + T], psum.bank(f"ff{j}")[:, 0:T], ACT.Copy).then_inc(S["ff_gate"], 1)
                    act.wait_ge(S["ff_conv"], j + 1)
                    A_(gcv[:, j % 2, 2, :], gcv[:, j % 2, 1, :], ACT.Gelu_apprx_tanh).then_inc(S["ff_gelu"], 1)
                round_weights(layer, *[f"down{i}" for i in range(2, FT // 2)])
                for t in range(NT):
                    y_stats(1, t, [f"y{2 * t + half}" for half in range(2)])
                act.drain().then_inc(layer_done, 1)
                act.wait_ge(layer_open, layer + 1)

        @block.vector
        def _(dve):
            V = nc.vector

            def subtract_rounded(*names):
                for name in names:
                    dve.wait_ge(S["w_hi"], ring.split.index(name) + 1)
                    V.tensor_tensor(rounded(ring.view(name)), ring.view(name), as_float32(rounded(ring.view(name + "_hi"))), ALU.subtract).then_inc(S["w_split"], 1)

            def split(hi, lo, a):
                dve.drain()
                V.tensor_copy(rounded(hi), a)
                dve.drain()
                V.tensor_tensor(rounded(lo), a, as_float32(rounded(hi)), ALU.subtract)

            def wide_of(col, n):
                return col.broadcast_to([P, n])

            def scale_rows(k, t):
                dve.wait_ge(S["rstd"], NT * k + t + 1)
                V.tensor_scalar(diagonal[:, t, :], C("ident"), stat[:, 4 + t:5 + t], None, ALU.mult).then_inc(S["diagonal"], 1)

            def half_of_hT(name, gain):
                for t in range(NT):
                    dve.wait_ge(*psum.filled(f"{name}_{t}0"))
                    out, bank = hT[:, 0:4, t * P:(t + 1) * P], shaped(psum.bank(f"{name}_{t}0"), 4, P)
                    if gain:
                        last = V.tensor_tensor(out, bank, PAR(gain)[:, 0:4].unsqueeze(2).broadcast_to([P, 4, P]), ALU.mult)
                    else:
                        last = V.tensor_copy(out, bank)
                    last.then_inc(*psum.freed(f"{name}_{t}0"))
                    dve.drain().then_inc(S["hT"], 1)

            def residual(k, t, names, gain):
                dve.wait_ge(S["y_ss"], NT * k + t + 1)
                V.tensor_tensor(stat[:, 44 + t:45 + t], stat[:, 40 + t:41 + t], stat[:, 42 + t:43 + t],
                                ALU.add).then_inc(S["y_sum"], 1)
                dve.wait_ge(S["y_rstd"], NT * k + t + 1)
                lo = PAR1[gain][0]
                for half, name in enumerate(names):
                    V.scalar_tensor_tensor(yn[:, 2 * t + half, :], psum.bank(name), stat[:, 48 + t:49 + t],
                                           par[:, lo + 512 * half:lo + 512 * half + 512], ALU.mult, ALU.mult).then_inc(*psum.freed(name))
                add_to_x(t)

            def add_to_x(t):
                dve.drain()
                for half in range(2):
                    xs = x[:, t, 512 * half:512 * half + 512]
                    V.tensor_tensor(xs, xs, yn[:, 2 * t + half, :], ALU.add)
                dve.drain().then_inc(S["x_new"], 1)

            def silu_gate(g, name, signal, step):
                dve.wait_ge(S[signal], 1)
                ins = V.scalar_tensor_tensor(g.gate[:, :, :], g.gate[:, :, :], 1.0, shaped(psum.bank(name), 2, T), ALU.add, ALU.mult)
                ins.then_inc(*psum.freed(name))
                dve.drain()
                step(V.tensor_scalar(g.gate[:, :, :], g.gate[:, :, :], 0.5, None, ALU.mult))

            def head_out(g, n, gain, tile):
                dve.wait_ge(S["o_rstd"], n + 1)
                V.tensor_tensor(g.oT, g.oT, g.rs, ALU.mult)
                dve.drain()
                V.scalar_tensor_tensor(mixT[:, tile:tile + 2, :], g.oT, PAR(gain), g.gate, ALU.mult, ALU.mult)

            def gla(g, m, step):
                R = g.R
                flat = "p r (s c) -> p (r s) c"
                if m:
                    dve.wait_ge(*psum.filled("gk"))
                    V.tensor_scalar(g.lf[:, 0, :], psum.bank("gk")[:, 0:T], PAR("b_gk"), None, ALU.add).then_inc(*psum.freed("gk"))
                    dve.drain()
                    V.scalar_tensor_tensor(g.e2, g.lf, -1.0, g.lf, ALU.mult, ALU.max).then_inc(S["gk_abs"], 1)
                    step(V.tensor_scalar(g.lf, g.lf, 0.0, None, ALU.min))
                    yield
                    dve.wait_ge(S["gk_ln"], 1)
                    step(V.tensor_tensor(g.lf, g.lf, g.e2, ALU.subtract))
                    step(V.tensor_scalar(g.lf, g.lf, 1.0 / 16.0, None, ALU.mult))
                else:
                    yield
                    dve.wait_ge(S["af_ln"], 1)
                    step(V.tensor_tensor(g.lf, g.b, g.lf, ALU.add))
                for r in range(R):
                    last = V.tensor_tensor_scan(g.b[:, r, :], C("restart"), g.lf[:, r, :], 0.0, ALU.mult, ALU.add)
                last.then_inc(S["scan"], 1)
                dve.wait_ge(S["scan"], m + 1)
                b4 = g.b.rearrange(flat, c=SUB)
                V.tensor_tensor(g.e2.rearrange(flat, c=SUB), b4,
                                b4[:, :, SUB - 1:SUB].broadcast_to([P, R * NSUB, SUB]), ALU.subtract).then_inc(S["scan_end"], 1)
                yield
                dve.wait_ge(S["exp_b"], m + 1)
                V.tensor_tensor(g.qe, g.q, g.eb, ALU.mult).then_inc(S["q_decayed"], 1)
                dve.wait_ge(S["kd_exp"], m + 1)
                V.tensor_tensor(g.kd, g.k, g.e2, ALU.mult).then_inc(S["kdT"], 1)
                yield
                name = g.name + "_kdt"
                dve.wait_ge(*psum.filled(name))
                V.tensor_copy(g.kdtok, shaped(psum.bank(name)[:, 0:NT * R * P], NT, R * P)).then_inc(*psum.freed(name))
                dve.drain().then_inc(S["kd_tok"], 1)
                dve.wait_ge(S["vtok"], m + 1)
                for t in range(NT):
                    last = V.tensor_tensor(g.vexp[:, t, :, :], g.vtok[:, t:t + 1, :].broadcast_to([P, SUBP, GW]),
                                           C("sub").unsqueeze(2).broadcast_to([P, SUBP, GW]), ALU.mult)
                last.then_inc(S["vexp"], 1)
                V.memset(g.S[:, :, 0, :], 0.0)
                dve.drain()
                yield
                for s in range(NSUB - 1):
                    t = s // SUBP
                    if s == SUBP:
                        yield
                    for r in range(R):
                        name = f"{g.name}_G{r}{t}"
                        if s % SUBP == 0:
                            dve.wait_ge(*psum.filled(name))
                        ins = V.scalar_tensor_tensor(g.S[:, r, s + 1, :], g.S[:, r, s, :], g.eb[:, r, SUB * s + SUB - 1:SUB * s + SUB],
                                                     shaped(psum.bank(name), SUBP, HD)[:, s % SUBP, :], ALU.mult, ALU.add)
                        if s % SUBP == SUBP - 1 or s == NSUB - 2:
                            ins.then_inc(*psum.freed(name))
                            dve.drain()
                        elif r == R - 1:
                            step(ins)
                dve.drain().then_inc(S["state"], 1)
                yield
                for p in range(2):
                    name = f"{g.name}_o{p}"
                    dve.wait_ge(*psum.filled(name))
                    V.tensor_copy(g.oT[:, p, :], psum.bank(name)[:, 0:T]).then_inc(*psum.freed(name))

                yield

                def view(kind, i, n):
                    return g.band[kind][:, i % 2, 0:n * NSUB * (SUB - i)].rearrange("p (a c) -> p a c", c=SUB - i)

                def apply(i):
                    name, n = f"{g.name}_band{i}", 2 * NSUB * (SUB - i)
                    dve.wait_ge(*psum.filled(name))
                    V.tensor_tensor(view("o", i, 2), psum.bank(name)[:, 0:n].rearrange("p (a c) -> p a c", c=SUB - i),
                                    shifted(g.vT, i), ALU.mult).then_inc(*psum.freed(name))
                    dve.drain()
                    V.tensor_tensor(bands(g.oT, i), bands(g.oT, i), view("o", i, 2), ALU.add)

                for i in range(SUB + 1):
                    n = SUB * m + i
                    if i < SUB:
                        V.tensor_tensor(view("diff", i, R), bands(g.b, i), shifted(g.b, i), ALU.subtract).then_inc(S["diff"], 1)
                    if i > 0:
                        dve.wait_ge(S["decay"], n)
                        dve.wait_ge(S["qk"], n)
                        V.tensor_tensor(view("w", i - 1, R), view("qk", i - 1, R), view("exp", i - 1, R), ALU.mult).then_inc(S["weighted"], 1)
                    if i > 1:
                        apply(i - 2)
                    yield
                apply(SUB - 1)
                dve.drain().then_inc(S["oT_ready"], 1)
                yield
                head_out(g, m, ("hgrn_norm", "gla_norm")[m], 2 * m)
                if m:
                    dve.drain().then_inc(S["gla_done"], 1)
                yield

            def project(a, bb, lower, rest, step):
                yield
                yield
                dve.wait_ge(S["aq_tanh"], 1)
                ins = V.scalar_tensor_tensor(a.q, a.q, 1.0, shaped(psum.bank("a_q"), 2, T), ALU.add, ALU.mult)
                ins.then_inc(*psum.freed("a_q"))
                dve.drain()
                V.tensor_scalar(a.q, a.q, 0.5 * HD ** -0.5, None, ALU.mult)
                yield
                yield
                dve.wait_ge(S["af_sig"], 1)
                for r in range(2):
                    V.tensor_scalar(a.k[:, r, :], a.k[:, r, :], rest[:, r:r + 1], None, ALU.mult)
                    last = V.tensor_scalar(a.lf[:, r, :], a.lf[:, r, :], rest[:, r:r + 1], lower[:, r:r + 1], ALU.mult, ALU.add)
                step(last)
                step(V.tensor_scalar(a.b, a.lf, 1e-30, 2.0 ** -40, ALU.max, ALU.min))
                V.tensor_scalar(a.lf, a.lf, 2.0 ** -40, None, ALU.max).then_inc(S["af_f"], 1)
                for _ in range(4):
                    yield
                dve.wait_ge(S["gate_th"], 1)
                V.tensor_scalar(a.gate, a.gate, 0.5, 0.5, ALU.mult, ALU.add)
                yield
                yield
                dve.wait_ge(*psum.filled("b_qk"))
                V.tensor_scalar(bb.q[:, 0, :], psum.bank("b_qk")[:, 0:T], 32 ** -0.5, None, ALU.mult)
                V.tensor_copy(bb.k[:, 0, :], psum.bank("b_qk")[:, T:2 * T]).then_inc(*psum.freed("b_qk"))
                for _ in range(5):
                    yield
                silu_gate(bb, "b_g", "bg_th", step)
                for _ in range(4):
                    yield
                V.memset(cin[:, :, 0:3], 0.0)
                for i, name in enumerate(("d_q", "d_k", "d_v")):
                    yield
                    yield
                    dve.wait_ge(*psum.filled(name))
                    V.tensor_copy(cin[:, 2 * i:2 * i + 2, 3:3 + T], shaped(psum.bank(name), 2, T)).then_inc(*psum.freed(name))
                yield
                yield
                dve.wait_ge(*psum.filled("d_ba"))
                V.tensor_copy(zb, shaped(psum.bank("d_ba")[:, 0:16], NT, 8)).then_inc(*psum.freed("d_ba"))
                silu_gate(oD, "d_z", "dz_th", step)
                yield

            def mla(step):
                yield
                yield
                dve.wait_ge(S["mla_rstd"], 1)
                for i in range(3):
                    gain = PAR("q_norm", i) if i < 2 else PAR("kv_norm")
                    last = V.scalar_tensor_tensor(cn[:, i, :], cT[:, i, :], gain, crs[:, i // 2, :], ALU.mult, ALU.mult)
                last.then_inc(S["mla_cn"], 1)
                cos, sin = C("cos96"), C("sin96")
                dve.wait_ge(*psum.filled("kr_rot"))
                V.tensor_tensor(rtmp[64:96, 1, :], psum.bank("kr_rot")[64:96, 0:T], sin[64:96, :], ALU.mult).then_inc(*psum.freed("kr_rot"))
                step(V.tensor_tensor(rtmp[64:96, 2, :], kr[64:96, :], cos[64:96, :], ALU.mult))
                V.tensor_tensor(kT[64:96, :, :], rtmp[64:96, 1:2, :].broadcast_to([32, 4, T]),
                                rtmp[64:96, 2:3, :].broadcast_to([32, 4, T]), ALU.add).then_inc(S["kr_done"], 1)
                yield
                for j in range(2):
                    name = f"kT{j}"
                    dve.wait_ge(*psum.filled(name))
                    V.tensor_copy(kT[0:64, 2 * j:2 * j + 2, :], shaped(psum.bank(name), 2, T)[0:64]).then_inc(*psum.freed(name))
                    dve.drain().then_inc(S["kT"], 1)
                yield
                for j in range(2):
                    name = f"rot{j}"
                    dve.wait_ge(*psum.filled(name))
                    V.tensor_tensor(rtmp[0:96, 2 * j:2 * j + 2, :], shaped(psum.bank(name), 2, T)[0:96],
                                    sin[0:96, :].unsqueeze(1).broadcast_to([96, 2, T]), ALU.mult).then_inc(*psum.freed(name))
                step(V.tensor_tensor(qT[0:96], qT[0:96], cos[0:96, :].unsqueeze(1).broadcast_to([96, 4, T]), ALU.mult))
                V.tensor_tensor(qT[0:96], qT[0:96], rtmp[0:96], ALU.add).then_inc(S["qT"], 1)
                mask = shaped(C("causal"), NT, T)
                for t in range(NT):
                    n = P * (t + 1)
                    yield
                    if t:
                        dve.wait_ge(*psum.filled("c_pt00"))
                        dve.wait_ge(S["exps"], t)
                    for j in range(2):
                        name = f"c_sc{t}{j}"
                        dve.wait_ge(*psum.filled(name))
                        V.scalar_tensor_tensor(L[:, 2 * j:2 * j + 2, 0:n], shaped(psum.bank(name)[:, 0:2 * n], 2, n), 96 ** -0.5,
                                               mask[:, t:t + 1, 0:n].broadcast_to([P, 2, n]), ALU.mult, ALU.add).then_inc(*psum.freed(name))
                    dve.drain()
                    step(V.tensor_reduce(stat[:, 32:36], L[:, :, 0:n], AX.X, ALU.max))
                    V.tensor_scalar(stat[:, 16 + 4 * t:20 + 4 * t], stat[:, 32:36], -1.0, None, ALU.mult).then_inc(S["scores_max"], 1)
                    yield
                    dve.wait_ge(S["exps"], t + 1)
                    step(V.reciprocal(stat[:, 36:40], stat[:, 24 + 4 * t:28 + 4 * t]))
                    V.tensor_tensor(Pr[:, :, 0:n], Pr[:, :, 0:n], stat[:, 36:40].unsqueeze(2).broadcast_to([P, 4, n]), ALU.mult)
                    dve.drain().then_inc(S["probs"], 1)
                    yield
                yield
                yield

            def gdn(step):
                w = shaped(PAR("conv"), 6, 4)
                for r in range(6):
                    V.tensor_scalar(cv[:, r, :], cin[:, r, 3:3 + T], w[:, r, 3:4], None, ALU.mult)
                for i in range(3):
                    dve.drain()
                    for r in range(6):
                        V.scalar_tensor_tensor(cv[:, r, :], cin[:, r, i:i + T], w[:, r, i:i + 1], cv[:, r, :], ALU.mult, ALU.add)
                dve.drain().then_inc(S["conv"], 1)
                V.tensor_tensor(sm["x"], zb[:, :, 4:8], PAR("dt_bias").unsqueeze(1).broadcast_to([P, NT, 4]), ALU.add)
                dve.drain()
                V.scalar_tensor_tensor(sm["e"], sm["x"], -1.0, sm["x"], ALU.mult, ALU.max)
                dve.drain().then_inc(S["ba_in"], 1)
                yield
                dve.wait_ge(S["conv_th"], 1)
                step(V.tensor_scalar(cth, cth, 0.5, 0.5, ALU.mult, ALU.add))
                V.tensor_tensor(cv, cv, cth, ALU.mult).then_inc(S["conv_silu"], 1)
                yield
                yield
                dve.wait_ge(S["ba_exp"], 1)
                V.tensor_scalar(sm["beta"], sm["beta"], 0.5, 0.5, ALU.mult, ALU.add)
                step(V.scalar_tensor_tensor(sm["g"], sm["x"], 0.0, sm["l"], ALU.max, ALU.add))
                V.scalar_tensor_tensor(sm["g"], sm["g"], -1.0, ea.unsqueeze(1).broadcast_to([P, NT, 4]), ALU.mult, ALU.mult).then_inc(S["g_ready"], 1)
                yield
                yield
                dve.wait_ge(S["l2_rstd"], 1)
                V.scalar_tensor_tensor(cv[:, 0:2, :], cv[:, 0:2, :], HD ** -0.5, lrs[:, 0:2, :], ALU.mult, ALU.mult)
                V.tensor_tensor(cv[:, 2:4, :], cv[:, 2:4, :], lrs[:, 2:4, :], ALU.mult)
                dve.drain().then_inc(S["qk_norm"], 1)
                dve.wait_ge(*psum.filled("bsum"))
                bs = psum.bank("bsum")
                V.tensor_copy(sm["b"], shaped(bs[:, 0:8], NT, 4))
                V.tensor_copy(sm["x"], shaped(bs[:, 8:16], NT, 4)).then_inc(*psum.freed("bsum"))
                dve.drain()
                V.tensor_scalar(sm["nb"], sm["b"], -1.0, None, ALU.mult)
                V.tensor_tensor(sm["bl"], sm["x"], sm["b"], ALU.subtract)
                dve.drain().then_inc(S["b_small"], 1)
                yield
                dve.wait_ge(S["b_exp"], 1)
                step(V.tensor_tensor(sm["be"], sm["beta"], sm["eb"], ALU.mult))
                dve.wait_ge(S["erow"], 1)
                for j in range(2):
                    name = f"brow{j}"
                    brow = shaped(psum.bank(name), 4, P)
                    V.tensor_tensor(lstr[:, 4 * j:4 * j + 4, :], brow, C("hide_strict").unsqueeze(1).broadcast_to([P, 4, P]), ALU.add)
                    V.tensor_tensor(lincT[:, 4 * j:4 * j + 4, :], brow, C("hide_incl").unsqueeze(1).broadcast_to([P, 4, P]), ALU.add).then_inc(*psum.freed(name))
                dve.drain().then_inc(S["hid"], 1)
                V.memset(SD[:, 0], 0.0)
                dve.drain().then_inc(S["state_D"], 1)

                def per_head(sc):
                    return sc.rearrange("p t h -> p (t h)").unsqueeze(2).broadcast_to([P, 8, HD])

                def by_head(tok):
                    return tok.rearrange("p t (h d) -> p (t h) d", d=HD)

                yield
                dve.wait_ge(*psum.filled("k_tok"))
                V.tensor_copy(ktok, shaped(psum.bank("k_tok"), NT, GW)).then_inc(*psum.freed("k_tok"))
                dve.wait_ge(*psum.filled("v_tok"))
                V.tensor_copy(vtokD, shaped(psum.bank("v_tok"), NT, GW)).then_inc(*psum.freed("v_tok"))
                dve.drain()
                V.tensor_tensor(by_head(kbe), by_head(ktok), per_head(sm["be"]), ALU.mult)
                V.tensor_tensor(by_head(vb), by_head(vtokD), per_head(sm["beta"]), ALU.mult)
                dve.drain()
                V.tensor_tensor(by_head(kdec), by_head(ktok), per_head(sm["fd"]), ALU.mult)
                dve.drain().then_inc(S["tok_D"], 1)
                for par_ in range(2):
                    rows = slice(HD * par_, HD * par_ + HD)
                    ev = erow[:, :, :].rearrange("p (q t h) c -> p q h t c", q=2, t=NT)
                    for hp in range(2):
                        V.tensor_tensor(qeD[rows, hp, :].rearrange("p (t c) -> p t c", t=NT), cv[rows, hp, :].rearrange("p (t c) -> p t c", t=NT),
                                        ev[rows, par_, hp, :, :], ALU.mult)
                dve.drain().then_inc(S["qe"], 1)
                yield
                dve.wait_ge(S["decays"], 1)
                for par_ in range(2):
                    name = f"kk{par_}"
                    dve.wait_ge(*psum.filled(name))
                    for t in range(NT):
                        for hp in range(2):
                            h, i = 2 * hp + par_, 2 * t + hp
                            e = 4 * par_ + i
                            last = V.scalar_tensor_tensor(lstr[:, e, :], psum.bank(name)[:, i * P:(i + 1) * P], sm["beta"][:, t, h:h + 1],
                                                          lstr[:, e, :], ALU.mult, ALU.mult)
                    last.then_inc(*psum.freed(name))
                dve.drain().then_inc(S["lmat"], 1)
                for par_ in range(2):
                    name = f"kq{par_}"
                    dve.wait_ge(*psum.filled(name))
                    V.tensor_tensor(lincT[:, 4 * par_:4 * par_ + 4, :], shaped(psum.bank(name), 4, P),
                                    lincT[:, 4 * par_:4 * par_ + 4, :], ALU.mult).then_inc(*psum.freed(name))

                yield
                yield

                lvl = shaped(C("level"), 7, P)

                def eight_of(m):
                    return m.unsqueeze(1).broadcast_to([P, 8, P])

                V.tensor_tensor(Tm, lstr, eight_of(lvl[:, 6, :]), ALU.mult)
                dve.wait_ge(S["nt"], 2)
                V.tensor_tensor(Um, NTm, eight_of(lvl[:, 0, :]), ALU.mult)
                dve.drain()
                V.tensor_tensor(Tm, eight_of(C("ident")), Tm, ALU.subtract)
                V.tensor_tensor(Um, eight_of(C("ident")), Um, ALU.subtract)
                V.tensor_tensor(pm, NTm, eight_of(lvl[:, 1, :]), ALU.mult)
                dve.drain().then_inc(S["level_T"], 1)
                yield
                for n in range(1, 6):
                    yield
                    if n < 5:
                        dve.wait_ge(*psum.filled(f"X{n}_1"))
                        V.tensor_tensor(pm, NTm, eight_of(lvl[:, n + 1, :]), ALU.mult)
                    yield
                    for what, m in (("TX", Tm), ("UX", Um)):
                        if what == "TX" and n == 5:
                            continue
                        for j in range(2):
                            name = f"{what}{n}_{j}"
                            dve.wait_ge(*psum.filled(name))
                            mj = m[:, 4 * j:4 * j + 4, :]
                            V.tensor_tensor(mj, mj, shaped(psum.bank(name), 4, P), ALU.subtract).then_inc(*psum.freed(name))
                    dve.drain().then_inc(S["level_T"], 1)
                    yield

                yield
                dve.wait_ge(S["uw"], 2)
                for c in range(4):
                    t, tok0 = c // 2, CHUNK * (c % 2)
                    toks = slice(tok0, tok0 + CHUNK)
                    for par_ in range(2):
                        name = f"ws{c}{par_}"
                        dve.wait_ge(*psum.filled(name))
                        hv = "p (h q d) -> p q h d"
                        un, vn = (z[toks, t, :].rearrange(hv, q=2, d=HD)[:, par_] for z in (uD, vnew))
                        V.tensor_tensor(vn, un, shaped(psum.bank(name)[:, 0:P], 2, HD)[toks], ALU.subtract).then_inc(*psum.freed(name))
                    dve.drain().then_inc(S["v_new"], 1)
                    yield
                    if c < 3:
                        name = f"su{c}"
                        dve.wait_ge(*psum.filled(name))
                        for par_ in range(2):
                            rows = slice(HD * par_, HD * par_ + HD)
                            for hp in range(2):
                                e = 4 * par_ + 2 * t + hp
                                last = V.scalar_tensor_tensor(SD[rows, c + 1, hp, :], SD[rows, c, hp, :], erow[rows, e, tok0 + CHUNK - 1:tok0 + CHUNK],
                                                              psum.bank(name)[rows, hp * HD:(hp + 1) * HD], ALU.mult, ALU.add)
                        last.then_inc(*psum.freed(name))
                        dve.drain().then_inc(S["state_D"], 1)
                        yield
                dve.wait_ge(*psum.filled("D_o"))
                V.tensor_copy(oD.oT, shaped(psum.bank("D_o"), 2, T)).then_inc(*psum.freed("D_o"))
                dve.wait_ge(*psum.filled("D_o2"))
                dve.drain()
                V.tensor_tensor(oD.oT, oD.oT, shaped(psum.bank("D_o2"), 2, T), ALU.add).then_inc(*psum.freed("D_o2"))
                dve.drain().then_inc(S["oT_ready"], 1)
                yield
                head_out(oD, 2, "gdn_norm", 6)
                yield

            def split_mix():
                dve.wait_ge(S["mixT_C"], 1)
                split(hT[:, 0:6, :], mixT[:, 0:6, :], mixT[:, 0:6, :])
                yield

            with dve.Fori(0, DEPTH) as layer:
                step = Chain(dve, S["dve"])
                dve.wait_ge(once, 16)
                dve.wait_ge(S["params"], 64)
                a, bb = G["A"], G["B"]
                lg = shaped(PAR("lb_logits"), 2, DEPTH)
                step(V.tensor_reduce(lb[:, 8:10], lg, AX.X, ALU.max))
                V.tensor_tensor(shaped(lb[:, 0:4], 2, DEPTH), lg, lb[:, 8:10].unsqueeze(2).broadcast_to([P, 2, DEPTH]),
                                ALU.subtract).then_inc(S["lb_max"], 1)
                for t in range(NT):
                    scale_rows(0, t)
                half_of_hT("hT0", "pre_mix")
                dve.wait_ge(S["lb_exp"], 1)
                step(V.tensor_reduce(lb[:, 8:10], shaped(lb[:, 0:4], 2, DEPTH), AX.X, ALU.add))
                step(V.tensor_tensor(lb[:, 0:4], lb[:, 0:4], PAR("lb_of"), ALU.mult))
                V.tensor_reduce(lb[:, 10:12], shaped(lb[:, 0:4], 2, DEPTH), AX.X, ALU.add)
                step(V.reciprocal(lb[:, 12:14], lb[:, 8:10]))
                step(V.tensor_tensor(lb[:, 14:16], lb[:, 10:12], lb[:, 12:14], ALU.mult))
                step(V.tensor_scalar(lb[:, 16:18], lb[:, 14:16], -1.0, 1.0, ALU.mult, ALU.add))
                lower, rest = lb[:, 14:16], lb[:, 16:18]

                emit(ORDER, {"in": project(a, bb, lower, rest, step), "A": gla(a, 0, step), "B": gla(bb, 1, step), "C": mla(step),
                             "D": gdn(step), "out": iter(range(4)), "mix": split_mix()})
                split(hT[:, 6:8, :], mixT[:, 6:8, :], mixT[:, 6:8, :])
                dve.drain().then_inc(S["mix_split"], 1)
                for t in range(NT):
                    residual(0, t, [f"mix{half}{t}" for half in range(2)], "post_mix")
                    scale_rows(1, t)
                half_of_hT("hT1", "pre_ffn")
                dve.wait_ge(S["hT"], 8)
                split(mixT, hT, hT)
                dve.drain().then_inc(S["h_split"], 1)
                subtract_rounded("up0")

                fw = shaped(PAR("ffn_conv"), FT, 3)

                def finish(j):
                    dve.wait_ge(S["ff_gelu"], j + 1)
                    V.tensor_tensor(gcv[:, j % 2, 0, :], gcv[:, j % 2, 2, :], psum.bank(f"ff{j}")[:, T:2 * T], ALU.mult).then_inc(*psum.freed(f"ff{j}"))
                    split(gh[:, j, :], gl[:, j, :], gcv[:, j % 2, 0, :])
                    dve.drain().then_inc(S["gT"], 1)

                V.memset(gpad[:, :, 0:2], 0.0)
                dve.drain().then_inc(S["gpad_zero"], 1)
                for j in range(FT):
                    q = j // 2 + 1
                    name = f"{('gate', 'up')[j % 2]}{q}" if q < FT // 2 else f"down{j - FT + 2}"
                    if name not in POOLED:
                        subtract_rounded(name)
                    dve.wait_ge(S["ff_gate"], j + 1)
                    step(V.tensor_scalar(gcv[:, j % 2, 0, :], gpad[:, j % 2, 2:2 + T], fw[:, j, 2:3], None, ALU.mult))
                    step(V.scalar_tensor_tensor(gcv[:, j % 2, 1, :], gpad[:, j % 2, 1:1 + T], fw[:, j, 1:2], gcv[:, j % 2, 0, :], ALU.mult, ALU.add))
                    V.scalar_tensor_tensor(gcv[:, j % 2, 1, :], gpad[:, j % 2, 0:T], fw[:, j, 0:1], gcv[:, j % 2, 1, :], ALU.mult, ALU.add).then_inc(S["ff_conv"], 1)
                    if j:
                        finish(j - 1)
                finish(FT - 1)
                subtract_rounded(*[f"down{i}" for i in range(2, FT // 2)])
                for t in range(NT):
                    residual(1, t, [f"y{2 * t + half}" for half in range(2)], "post_ffn")
                dve.drain().then_inc(layer_done, 1)
                dve.wait_ge(layer_open, layer + 1)

        @block.gpsimd
        def _(pool):
            def subtract_rounded(*names):
                for name in names:
                    pool.wait_ge(S["w_hi"], ring.split.index(name) + 1)
                    nc.gpsimd.tensor_tensor(rounded(ring.view(name)), ring.view(name), as_float32(rounded(ring.view(name + "_hi"))),
                                            ALU.subtract).then_inc(S["w_split_pool"], 1)

            with pool.Fori(0, DEPTH) as layer:
                for m, g in enumerate((G["A"], G["B"])):
                    pool.wait_ge(S["state"], m + 1)
                    for i in range(SUB):
                        n = SUB * m + i
                        if n >= 2:
                            pool.wait_ge(S["weighted"], n - 1)
                        out = g.band["qk"][:, i % 2, 0:g.R * NSUB * (SUB - i)].rearrange("p (a c) -> p a c", c=SUB - i)
                        nc.gpsimd.tensor_tensor(out, bands(g.q, i), shifted(g.k, i), ALU.mult).then_inc(S["qk"], 1)
                subtract_rounded(*POOLED)
                pool.wait_ge(layer_done, 3 * layer + 3)
                pool.sem_inc(barrier_taken, 1)
                for r in sem_ranges([s.num for s in S.values()] + [s.num for s in psum.full + psum.free]):
                    pool.sem_clear(r)
                pool.sem_inc(layer_open, 1)

        psum.check()


D_FF2 = 4096
UT = D_FF2 // P
IDX_HEADS = 8
TOPK = 64
TAKEN = -3e38
TWO_PI = (6.28125, 0.0019350051879882812, 3.0199159819e-07)
BY_PARITY = (0, 2, 1, 3)
CONST2, N_CONST2 = table([
    ("ident", P), ("cum", P), ("ones", P), ("heads64", P), ("rot64", P), ("rot32", P),
    ("causal", NT * T), ("window", NT * T), ("inv_freq", 2), ("eps", 1),
])
PAR2, N_PAR2 = table([
    ("pre_mix", KT), ("pre_mlp", KT), ("subln", 1), ("lam_q", 64), ("lam_k", 64), ("b_forget", 4),
    ("sinks", 4), ("lam_init", 1), ("lam_rest", 1), ("post_mix", DM), ("post_mlp", DM),
])
IN2 = [(0, 256), (256, 512), (512, 768), (768, 1024), (1024, 1280), (1280, 1352), (1352, 1608), (1608, 1864),
       (1864, 2124), (2124, 2380), (2380, 2636), (2636, 2892), (2892, 3148), (3148, 3404)]
IN2_ORDER = [3, 4, 5, 8, 6, 7, 9, 10, 11, 12, 13, 0, 1, 2]


def shape_constants2():
    c = np.zeros((P, N_CONST2), np.float32)

    def put(name, a):
        lo, hi = CONST2[name]
        c[:a.shape[0], lo:hi] = a.reshape(a.shape[0], -1)

    i = np.arange(P)
    put("ident", np.eye(P, dtype=np.float32))
    put("cum", (i[:, None] <= i[None, :]).astype(np.float32))
    put("ones", np.ones((P, P), np.float32))
    put("heads64", ((i[:, None] // 64) == (i[None, :] // 64)).astype(np.float32))
    inv = np.zeros((P, 2), np.float32)
    for n, (name, half) in enumerate((("rot64", 32), ("rot32", 16))):
        rot = np.zeros((P, P), np.float32)
        for m in range(P):
            if m % (2 * half) < half:
                rot[m + half, m] = -1.0
            else:
                rot[m - half, m] = 1.0
        put(name, rot)
        f = (np.float32(10000.0) ** (-np.arange(half, dtype=np.float32) / np.float32(half))).astype(np.float32)
        inv[:, n] = f[i % half]
    put("inv_freq", inv)
    key, q = np.arange(T)[None, :], i[:, None]
    put("causal", np.stack([np.where(key <= q + P * t, 0.0, NEG) for t in range(NT)], 1).astype(np.float32))
    put("window", np.stack([np.where((key <= q + P * t) & (q + P * t - key < P), 0.0, NEG) for t in range(NT)], 1).astype(np.float32))
    put("eps", np.full((P, 1), EPS, np.float32))
    return c


def params2(a):
    out = np.zeros((DEPTH, P, N_PAR2), np.float32)

    def put(name, layer, v):
        lo, hi = PAR2[name]
        out[layer, :, lo:hi] = v

    def cols(v):
        return np.asarray(v).reshape(-1, P).T

    def rows(v):
        v = np.asarray(v)
        return np.broadcast_to(v, (P,) + v.shape)

    for l in range(DEPTH):
        lam_init = 0.8 - 0.6 * float(np.exp(-0.3 * l))
        put("pre_mix", l, cols(a["norm_pre_mix_2"][l]))
        put("pre_mlp", l, cols(a["norm_pre_mlp_2"][l]))
        put("subln", l, np.concatenate([a["diff_subln_2"][l]] * 2)[:, None])
        put("lam_q", l, rows(np.concatenate([a["lambda_q1_2"][l], a["lambda_q2_2"][l]])))
        put("lam_k", l, rows(np.concatenate([a["lambda_k1_2"][l], a["lambda_k2_2"][l]])))
        put("b_forget", l, rows(a["b_forget_2"][l]))
        put("sinks", l, rows(np.asarray(a["sinks_2"][l])[list(BY_PARITY)]))
        put("lam_init", l, np.float32(lam_init))
        put("lam_rest", l, np.float32(1.0 - lam_init))
        put("post_mix", l, rows(a["norm_post_mix_2"][l]))
        put("post_mlp", l, rows(a["norm_post_mlp_2"][l]))
    return out

SIGNALS2 = """params w_split x_new diagonal raw hT copied roped probs PT o_sq nlf mix_split h_split gT p_split
w_hi rstd y_ss y_sum y_rstd score_max exps gate_abs gate_ln relu_used relu c_oT o_rstd mixT lam_sum
lam_exp pT_in ff_relu ff_squared g_hi proj gates cosined""".split()


def block2(nc, kept, banks, x, A):
    with ExitStack() as ctx:
        QKV, WORK = 28 * T, 16128
        memory = Memory(nc, ctx, "b2", {"ring": SLOTS * KT * PANEL, "zone": QKV + WORK,
                                        "small": N_CONST2 + N_PAR2 + 2 * KT * T + 128 + 4 * T + 4 * T + NT * (8 + 4 * 4) + 80})
        rounded, buf = memory.rounded, memory.area("small")

        S = {n: ctx.enter_context(nc.semaphore("b2_" + n)) for n in SIGNALS2}
        psum = Psum(nc, ctx, "b2", banks)
        layer_done = kept.enter_context(nc.semaphore("b2_layer_done"))
        layer_open = kept.enter_context(nc.semaphore("b2_layer_open"))
        barrier_taken = kept.enter_context(nc.semaphore("b2_barrier_taken"))
        once = kept.enter_context(nc.semaphore("b2_constants_in"))
        tables_made = kept.enter_context(nc.semaphore("b2_tables_made"))
        angles = kept.enter_context(nc.semaphore("b2_angles"))

        def cols(src):
            return src.rearrange("l (k p) n -> l p k n", p=P)

        win, wout, wup, wgate = cols(A["w_in_2"]), cols(A["w_out_2"]), cols(A["w_mlp_up_2"]), cols(A["w_ple_gate_2"])
        wdown, wproj = cols(A["w_mlp_down_2"]), cols(A["w_ple_proj_2"])
        panels = [(f"in{i}", lambda l, c0=c0, c1=c1: win[l, :, :, c0:c1], KT, c0, c1) for i, (c0, c1) in ((i, IN2[i]) for i in IN2_ORDER)]
        late = [(f"out{i}", lambda l, i=i: wout[l, :, :, 256 * i:256 * i + 256], KT, 0, 256) for i in range(4)]
        late += [(f"up{i}", lambda l, i=i: wup[l, :, :, 256 * i:256 * i + 256], KT, 0, 256) for i in range(UT // 2)]
        late += [(f"down{i}", lambda l, i=i: wdown[l, :, 2 * i:2 * i + 2, :], 2, 0, DM) for i in range(UT // 2)]
        late += [("proj", lambda l: wproj[l, :, :, :], 2, 0, DM)]
        late += [(f"ple{i}", lambda l, i=i: wgate[l, :, :, 256 * i:256 * i + 256], KT, 0, 256) for i in range(4)]
        panels += with_parts(late)
        ring = Ring(nc, kept, "b2", panels, memory.area("ring")(SLOTS, KT * PANEL))

        const = buf(N_CONST2)
        par = buf(N_PAR2)

        def C(name, rows=P):
            lo, hi = CONST2[name]
            return const[0:rows, lo:hi]

        def PAR(name, i=None, n=1):
            lo, hi = PAR2[name]
            return par[:, lo:hi] if i is None else par[:, lo + i:lo + i + n]

        hT = buf(KT, T)
        mixT = buf(KT, T)
        stat = buf(128)
        ptok = buf(NT, T)
        pT = buf(2, T)
        pT_lo = ptok.rearrange("p a b -> p (a b)").rearrange("p (a b) -> p a b", a=2)
        rope = buf(2, 2, T)
        iw = buf(NT, IDX_HEADS)
        fl = {n: buf(NT, 4) for n in ("x", "e", "n", "cum")}
        lam = buf(80)

        zone = memory.plain["zone"][:, :]
        positions = zone[:, 0:T].bitcast(mybir.dt.int32)
        area = Area(zone, QKV)
        qk = {n: area(w, T) for n, w in (("a_q", 2), ("a_k", 2), ("a_iq", 4), ("a_ik", 1), ("b_q", 2), ("b_k", 2),
                                           ("c_q", 2), ("c_k", 2), ("d_q", 2), ("d_k", 2))}
        vtok = {n: area(NT, w) for n, w in (("a_v", GW), ("b_v", GW), ("c_v", GW), ("d_v", P))}
        work = zone[:, QKV:QKV + WORK]
        area = Area(work, WORK)
        raw, turned = area(2, 2, T), area(2, 2, T)
        LN = 8 * P * 3
        Ls = [area(LN), area(LN)]
        PTs = [area(NT, 4, T), area(NT, 4, T)]
        Dm = area(4 * P * 3)
        sel, acc = [area(P), area(T)], [area(P), area(T)]
        dots = area(2, 512)
        area.at -= 1024 + 2 * 3 * P + 4 * P * 3
        oT, osq, ors = area(2, T), area(2, T), area(2, T)
        area.at = 0
        xn, diagonal = area(NT, DM), area(NT, P)
        area = Area(zone, QKV + WORK)
        gh, gl = area(UT, T), area(UT, T)
        gates, proj, yn = area(4, 512), area(4, 512), area(4, 512)
        ysq = area(512)

        def scores_of(buffer, t, maps):
            n = P * (t + 1)
            lo = maps * P * t
            return buffer[:, lo:lo + maps * n].rearrange("p (e n) -> p e n", n=n)

        IN_USES = [
            ("a_iq0", "in3", "T", [(0, P, 0, 768), (0, P, 1, 896)]), ("a_iq1", "in4", "T", [(0, P, 0, 1024), (0, P, 1, 1152)]),
            ("a_ik", "in5", "T", [(0, 64, 0, 1280), (64, 64, 0, 1280)]), ("a_iw", "in5", "tok", (1344, 8)),
            ("b_v", "in8", "tok", (1864, GW)), ("b_f", "in8", "tok", (2120, 4)),
            ("b_q", "in6", "T", [(0, P, 0, 1352), (0, P, 1, 1480)]), ("b_k", "in7", "T", [(0, P, 0, 1608), (0, P, 1, 1736)]),
            ("c_q", "in9", "T", [(0, P, 0, 2124), (0, P, 1, 2252)]), ("c_k", "in10", "T", [(0, P, 0, 2380), (0, P, 1, 2508)]),
            ("c_v", "in11", "tok", (2636, GW)),
            ("d_q", "in12", "T", [(0, P, 0, 2892), (0, P, 1, 3020)]),
            ("d_k", "in13", "T", [(0, 64, 0, 3148), (64, 64, 0, 3148), (0, 64, 1, 3212), (64, 64, 1, 3212)]),
            ("d_v", "in13", "tok", (3276, P)),
            ("a_q", "in0", "T", [(0, P, 0, 0), (0, P, 1, 128)]), ("a_k", "in1", "T", [(0, P, 0, 256), (0, P, 1, 384)]),
            ("a_v", "in2", "tok", (512, GW)),
        ]
        ROPED = [("a_iq0", qk["a_iq"][:, 0:2, :], 0, 2), ("a_iq1", qk["a_iq"][:, 2:4, :], 0, 2), ("a_ik", qk["a_ik"], 0, 1),
                 ("c_q", qk["c_q"], 1, 2), ("c_k", qk["c_k"], 1, 2), ("d_q", qk["d_q"], 0, 2), ("d_k", qk["d_k"], 0, 2),
                 ("a_q", qk["a_q"], 0, 2), ("a_k", qk["a_k"], 0, 2)]
        ROPED_AT = {r[0]: i for i, r in enumerate(ROPED)}
        ATTENDED = [("b", 4, HD ** -0.5, 2), ("c", 8, 32 ** -0.5, 4), ("d", 4, HD ** -0.5, 6), ("a", 4, HD ** -0.5, 0)]
        COPIED = [name for name, *_ in IN_USES if name in ("b_q", "b_k") or name in vtok]
        ORDER = ["in"] * 6 + """index in index in select forget in select forget in forget b in b in b in b c in b c in
            b c in c c in d c in d c in d c d a d a out a d out a out a out a""".split()
        block = ctx.enter_context(nc.Block())

        @block.sync
        def _(sp):
            sp.dma_start(const[:, :], A["const2"]).then_inc(once, 16)
            sp.dma_start(positions[:, :], A["positions_2"][0, :].partition_broadcast(P)).then_inc(once, 16)
            sp.wait_ge(once, 32)
            sp.wait_ge(S["params"], 32)
            for s in range(SLOTS):
                sp.sem_inc(ring.free[s], 1)
            with sp.Fori(0, DEPTH) as layer:
                ring.load_all(sp, layer)

        @block.tensor
        def _(pe):
            used = []

            def mm(out, lhsT, rhs, start=True, stop=True):
                ins = nc.tensor.matmul(out, lhsT, rhs, start=start, stop=stop)
                if used:
                    ins.then_inc(*ring.freed(used.pop(0)))
                return ins

            def mm3(out, a, b, start, stop):
                mm(out, a[0], b[0], start, False)
                mm(out, a[0], b[1], False, False)
                return mm(out, a[1], b[0], False, stop)

            def split_panel(name):
                pe.wait_ge(S["w_split"], ring.split.index(name) + 1)
                return rounded(ring.view(name + "_hi")), rounded(ring.view(name))

            def give_back():
                for name in used:
                    pe.drain().then_inc(*ring.freed(name))
                used.clear()

            def transpose(out, a):
                return nc.tensor.transpose(out, a, C("ident"))

            def transposes(name):
                for t in range(NT):
                    pe.wait_ge(S["x_new"], NT + t + 1)
                    for j in range(2):
                        b = psum.claim(pe, f"{name}_{t}{j}")
                        for i in range(4):
                            last = transpose(b[:, i * P:(i + 1) * P], x[:, t, (4 * j + i) * P:(4 * j + i + 1) * P])
                        last.then_inc(psum.full_of(f"{name}_{t}{j}"), 1)

            def normed_transposes(name, k):
                for t in range(NT):
                    pe.wait_ge(S["diagonal"], NT * k + t + 1)
                    for j in range(2):
                        b = psum.claim(pe, f"{name}_{t}{j}")
                        for i in range(4):
                            c = (4 * j + i) * P
                            last = mm(b[:, i * P:(i + 1) * P], x[:, t, c:c + P], diagonal[:, t, :])
                        last.then_inc(psum.full_of(f"{name}_{t}{j}"), 1)

            def turn(i):
                name, _, width, tiles = ROPED[i]
                pe.wait_ge(S["raw"], i + 1)
                b = psum.claim(pe, name + "_rot")
                mm(b[:, 0:tiles * T], C(("rot64", "rot32")[width]), raw[:, i % 2, 0:tiles, :]).then_inc(psum.full_of(name + "_rot"), 1)

            def project(layer):
                pe.wait_ge(S["hT"], 4)
                held, waiting = None, []
                for name, panel, kind, parts in IN_USES:
                    if panel != held:
                        if held:
                            used.append(held)
                        held = panel
                        w = ring.wait(pe, layer, panel)
                        base = IN2[int(panel[2:])][0]
                    b = psum.claim(pe, name)
                    if kind == "T":
                        for row0, m, half, c0 in parts:
                            for k in range(KT):
                                last = mm(b[row0:row0 + m, half * T:(half + 1) * T], w[:, k, c0 - base:c0 - base + m],
                                          hT[:, k, :], k == 0, k == KT - 1)
                    else:
                        c0, n = parts
                        for t in range(NT):
                            for k in range(KT):
                                last = mm(b[:, t * n:(t + 1) * n], hT[:, k, t * P:(t + 1) * P], w[:, k, c0 - base:c0 - base + n],
                                          k == 0, k == KT - 1)
                    last.then_inc(psum.full_of(name), 1)
                    for i in waiting:
                        turn(i)
                    waiting = [ROPED_AT[name]] if name in ROPED_AT else []
                    yield
                used.append(held)
                give_back()
                for i in waiting:
                    turn(i)
                yield
                yield

            def scores(name):
                size = 32 if name == "c" else HD
                if name == "b":
                    pe.wait_ge(S["copied"], COPIED.index("b_k") + 1)
                else:
                    pe.wait_ge(S["roped"], ROPED_AT[name + "_k"] + 1)
                q, k = qk[name + "_q"], qk[name + "_k"]
                for t in range(NT):
                    n = P * (t + 1)
                    for g in range(P // size):
                        b = psum.claim(pe, f"{name}_sc{t}{g}")
                        rows = slice(size * g, size * (g + 1))
                        for hp in range(2):
                            last = mm(b[:, hp * n:(hp + 1) * n], q[rows, hp, t * P:(t + 1) * P], k[rows, hp, 0:n])
                        last.then_inc(psum.full_of(f"{name}_sc{t}{g}"), 1)
                    yield

            def values(i):
                name, maps, _, _ = ATTENDED[i]
                L, PT = Ls[i % 2], PTs[i % 2]
                for t in range(NT):
                    pe.wait_ge(S["probs"], 2 * i + t + 1)
                    for kt in range(t + 1):
                        b = psum.claim(pe, f"{name}_pt{t}{kt}")
                        for e in range(4):
                            m = e if maps == 4 else 4 * (e // 2) + e % 2
                            last = transpose(b[:, e * P:(e + 1) * P], scores_of(L, t, maps)[:, m, kt * P:(kt + 1) * P])
                        last.then_inc(psum.full_of(f"{name}_pt{t}{kt}"), 1)
                yield
                pe.wait_ge(S["PT"], 3 * i + 3)
                pe.wait_ge(S["copied"], COPIED.index(name + "_v") + 1)
                b = psum.claim(pe, name + "_o")
                v = vtok[name + "_v"]
                for e, h in enumerate(BY_PARITY):
                    c = HD * (h // 2) if name == "d" else HD * h
                    o = b[HD * (h % 2):HD * (h % 2) + HD, T * (h // 2):T * (h // 2) + T]
                    mm(o, v[:, 0, c:c + HD], PT[:, 0, e, :], True, False)
                    last = mm(o[:, P:T], v[:, 1, c:c + HD], PT[:, 1, e, P:T], False, True)
                last.then_inc(psum.full_of(name + "_o"), 1)
                yield

            def attend(i):
                yield from scores(ATTENDED[i][0])
                yield
                yield
                yield from values(i)
                if ATTENDED[i][0] == "c":
                    pe.wait_ge(S["o_sq"], 1)
                    b = psum.claim(pe, "c_ss")
                    mm(b[:, :], C("heads64"), osq).then_inc(psum.full_of("c_ss"), 1)
                    yield
                    yield

            def forget_sums():
                yield
                yield
                pe.wait_ge(S["nlf"], 1)
                b = psum.claim(pe, "f_col")
                mm(b[:, 0:4], C("cum"), fl["n"][:, 0, :])
                mm(b[:, 4:8], C("ones"), fl["n"][:, 0, :], True, False)
                mm(b[:, 4:8], C("cum"), fl["n"][:, 1, :], False, True).then_inc(psum.full_of("f_col"), 1)
                for g in range(2):
                    b = psum.claim(pe, f"f_row{g}")
                    for hp in range(2):
                        h = BY_PARITY[2 * g + hp]
                        first, second = (fl["n"][:, t, h:h + 1].broadcast_to([P, P]) for t in range(NT))
                        mm(b[:, hp * T:hp * T + P], first, C("cum"))
                        mm(b[:, hp * T + P:(hp + 1) * T], first, C("ones"), True, False)
                        last = mm(b[:, hp * T + P:(hp + 1) * T], second, C("cum"), False, True)
                    last.then_inc(psum.full_of(f"f_row{g}"), 1)
                yield

            def index_dots():
                pe.wait_ge(S["roped"], ROPED_AT["a_ik"] + 1)
                for t in range(NT):
                    n = P * (t + 1)
                    each = 512 // n
                    for g in range(2):
                        rows = slice(HD * g, HD * (g + 1))
                        for j in range(4 // each):
                            name = f"dots{t}{g}{j}"
                            b = psum.claim(pe, name)
                            for i in range(each):
                                last = mm(b[:, i * n:(i + 1) * n], qk["a_iq"][rows, each * j + i, t * P:(t + 1) * P],
                                          qk["a_ik"][rows, 0, 0:n])
                            last.then_inc(psum.full_of(name), 1)
                    yield

            def wide(what, lhs, panels):
                banks = [psum.claim(pe, f"{what}{i}") for i in range(4)]
                for n, name in enumerate(panels):
                    w = split_panel(name)
                    end = n == len(panels) - 1
                    for t in range(NT):
                        for cut in range(2):
                            for half in range(2):
                                last = mm3(banks[2 * t + half], [a[:, 2 * n + cut, t * P:(t + 1) * P] for a in lhs],
                                           [a[:, cut, half * 512:half * 512 + 512] for a in w], n == cut == 0, end and cut == 1)
                                if end and cut:
                                    last.then_inc(psum.full_of(f"{what}{2 * t + half}"), 1)
                    used.extend((name, name + "_hi"))
                give_back()

            def rows_by(what, lhs, panel):
                for t in range(NT):
                    banks = [psum.claim(pe, f"{what}{half}{t}") for half in range(2)]
                    for q in range(4):
                        name = f"{panel}{q}"
                        w = split_panel(name)
                        for k in range(KT):
                            last = mm3(banks[q // 2][:, (q % 2) * 256:(q % 2) * 256 + 256], [a[:, k, t * P:(t + 1) * P] for a in lhs],
                                       [a[:, k, :] for a in w], k == 0, k == KT - 1)
                        if q % 2:
                            last.then_inc(psum.full_of(f"{what}{q // 2}{t}"), 1)
                        if t == NT - 1:
                            used.extend((name, name + "_hi"))
                give_back()

            with pe.Fori(0, DEPTH) as layer:
                pe.wait_ge(once, 32)
                normed_transposes("hT0", 0)
                emit(ORDER, {"in": project(layer), "index": index_dots(), "select": iter(range(2)), "forget": forget_sums(),
                             "b": attend(0), "c": attend(1), "d": attend(2), "a": attend(3), "out": iter(range(4))})
                pe.wait_ge(S["mix_split"], 1)
                rows_by("mix", (rounded(hT), rounded(mixT)), "out")
                pe.wait_ge(S["params"], 32)
                b = psum.claim(pe, "pT")
                for i in range(4):
                    last = transpose(b[:, i * P:(i + 1) * P], ptok[:, i % 2, (i // 2) * P:(i // 2 + 1) * P])
                last.then_inc(psum.full_of("pT"), 1)
                normed_transposes("hT1", 1)
                pe.wait_ge(S["h_split"], 1)
                h = (rounded(mixT), rounded(hT))
                for c in range(UT // 2):
                    w = split_panel(f"up{c}")
                    b = psum.claim(pe, f"ff{c}")
                    for half in range(2):
                        for k in range(KT):
                            last = mm3(b[:, half * T:(half + 1) * T], [a[:, k, half * P:(half + 1) * P] for a in w],
                                       [a[:, k, :] for a in h], k == 0, k == KT - 1)
                    last.then_inc(psum.full_of(f"ff{c}"), 1)
                    used.extend((f"up{c}", f"up{c}_hi"))
                pe.wait_ge(S["gT"], UT // 2)
                wide("y", (rounded(gh), rounded(gl)), [f"down{i}" for i in range(UT // 2)])
                pe.wait_ge(S["p_split"], 1)
                wide("proj", (rounded(pT), rounded(pT_lo)), ["proj"])
                transposes("xT")
                pe.wait_ge(S["h_split"], 2)
                rows_by("ple", h, "ple")
                pe.drain().then_inc(layer_done, 1)
                pe.wait_ge(layer_open, layer + 1)

        def stat_of(i, t, what, n):
            lo = 16 + 48 * (i % 2) + 8 * t + {"neg": 0, "den": 16, "rec": 32, "sink": 36}[what]
            return stat[:, lo:lo + n]

        @block.scalar
        def _(act):
            A_ = nc.scalar.activation

            def round_weights(layer, *names):
                for name in names:
                    raw = ring.wait(act, layer, name)
                    ring.wait_free(act, layer, name + "_hi")
                    A_(rounded(ring.view(name + "_hi")), raw, ACT.Copy).then_inc(S["w_hi"], 1)

            def norm_stats(k, t):
                A_(xn[:, t, :], x[:, t, :], ACT.Square, accum_out=stat[:, t:t + 1])
                act.drain()
                A_(stat[:, 2 + t:3 + t], stat[:, t:t + 1], ACT.Ln, bias=C("eps"), scale=1.0 / DM)
                act.drain()
                A_(stat[:, 4 + t:5 + t], stat[:, 2 + t:3 + t], ACT.Exp, scale=-0.5).then_inc(S["rstd"], 1)

            def half_of_hT(name, gain):
                for t in range(NT):
                    act.wait_ge(*psum.filled(f"{name}_{t}1"))
                    for i in range(4):
                        last = A_(hT[:, 4 + i, t * P:(t + 1) * P], psum.bank(f"{name}_{t}1")[:, i * P:(i + 1) * P], ACT.Copy,
                                  scale=PAR(gain, 4 + i) if gain else 1.0)
                    last.then_inc(*psum.freed(f"{name}_{t}1"))
                    act.drain().then_inc(S["hT"], 1)

            def y_stats(k, t, names):
                for half, name in enumerate(names):
                    act.wait_ge(*psum.filled(name))
                    A_(ysq[:, 0:512], psum.bank(name), ACT.Square, accum_out=stat[:, 112 + 2 * half + t:113 + 2 * half + t])
                    act.drain()
                act.drain().then_inc(S["y_ss"], 1)
                act.wait_ge(S["y_sum"], NT * k + t + 1)
                A_(stat[:, 118 + t:119 + t], stat[:, 116 + t:117 + t], ACT.Ln, bias=C("eps"), scale=1.0 / DM)
                act.drain()
                A_(stat[:, 120 + t:121 + t], stat[:, 118 + t:119 + t], ACT.Exp, scale=-0.5).then_inc(S["y_rstd"], 1)

            def drain_bank(name, out, signal, rows=slice(0, P), part=slice(0, 512)):
                act.wait_ge(*psum.filled(name))
                A_(out, psum.bank(name)[rows, part], ACT.Copy).then_inc(*psum.freed(name))
                act.drain().then_inc(S[signal], 1)

            def exps(i):
                name, maps, _, _ = ATTENDED[i]
                for t in range(NT):
                    act.wait_ge(S["score_max"], 2 * i + t + 1)
                    L = scores_of(Ls[i % 2], t, maps)
                    for e in range(maps):
                        A_(L[:, e, :], L[:, e, :], ACT.Exp, bias=stat_of(i, t, "neg", maps)[:, e:e + 1],
                           accum_out=stat_of(i, t, "den", maps)[:, e:e + 1])
                    if name == "d":
                        A_(stat_of(i, t, "sink", 4), stat_of(i, t, "sink", 4), ACT.Exp)
                    act.drain().then_inc(S["exps"], 1)
                    yield

            def project():
                yield
                for name, panel, kind, parts in IN_USES:
                    if name in ROPED_AT:
                        i = ROPED_AT[name]
                        tiles = ROPED[i][3]
                        if i >= 2:
                            act.wait_ge(S["roped"], i - 1)
                        drain_bank(name, raw[:, i % 2, 0:tiles, :], "raw", part=slice(0, tiles * T))
                    elif name in ("b_q", "b_k"):
                        drain_bank(name, qk[name], "copied")
                    elif name in vtok:
                        drain_bank(name, vtok[name], "copied", part=slice(0, NT * parts[1]))
                    yield
                yield

            def forget():
                act.wait_ge(S["gate_abs"], 1)
                A_(fl["e"], fl["e"], ACT.Exp, scale=-1.0)
                act.drain()
                A_(fl["e"], fl["e"], ACT.Ln, bias=C("ones")[:, 0:1]).then_inc(S["gate_ln"], 1)
                yield
                yield
                yield

            def index():
                at = 0
                for t in range(NT):
                    for g in range(2):
                        for j in range(t + 1):
                            if at >= 2:
                                act.wait_ge(S["relu_used"], at - 1)
                            act.wait_ge(*psum.filled(f"dots{t}{g}{j}"))
                            A_(dots[:, at % 2, :], psum.bank(f"dots{t}{g}{j}"), ACT.Relu).then_inc(*psum.freed(f"dots{t}{g}{j}"))
                            act.drain().then_inc(S["relu"], 1)
                            at += 1
                    yield

            def attend(i):
                yield
                yield from exps(i)
                yield
                yield from turned_probs(i)

            def split_out(layer):
                for i in range(4):
                    round_weights(layer, f"out{i}")
                    yield

            def turned_probs(i):
                name, _, _, tile = ATTENDED[i]
                for t, kt in ((0, 0), (1, 0), (1, 1)):
                    drain_bank(f"{name}_pt{t}{kt}", PTs[i % 2][:, kt, :, t * P:(t + 1) * P], "PT")
                yield
                if name == "c":
                    drain_bank("c_o", oT, "c_oT")
                    A_(osq, oT, ACT.Square).then_inc(S["o_sq"], 1)
                    yield
                    act.wait_ge(*psum.filled("c_ss"))
                    A_(ors, shaped(psum.bank("c_ss"), 2, T), ACT.Ln, bias=C("eps"), scale=1.0 / HD).then_inc(*psum.freed("c_ss"))
                    act.drain()
                    A_(ors, ors, ACT.Exp, scale=-0.5).then_inc(S["o_rstd"], 1)
                    yield
                    yield
                else:
                    drain_bank(name + "_o", mixT[:, tile:tile + 2, :], "mixT")
                    yield

            act.wait_ge(angles, 1)
            A_(rope, rope, ACT.Sin).then_inc(tables_made, 1)
            with act.Fori(0, DEPTH) as layer:
                act.dma_start(par[:, :], A["par2"][layer, :, :]).then_inc(S["params"], 16)
                act.dma_start(ptok, A["p_2"][layer, 0, :, :].rearrange("(t q) n -> q t n", q=P)).then_inc(S["params"], 16)
                act.wait_ge(once, 32)
                for t in range(NT):
                    norm_stats(0, t)
                act.wait_ge(S["params"], 32)
                act.wait_ge(S["lam_sum"], 1)
                A_(lam[:, 66:68], lam[:, 64:66], ACT.Exp).then_inc(S["lam_exp"], 1)
                half_of_hT("hT0", "pre_mix")
                emit(ORDER, {"in": project(), "index": index(), "select": iter(range(2)), "forget": forget(),
                             "b": attend(0), "c": attend(1), "d": attend(2), "a": attend(3), "out": split_out(layer)})
                for t in range(NT):
                    y_stats(0, t, [f"mix{half}{t}" for half in range(2)])
                    act.wait_ge(S["x_new"], t + 1)
                    norm_stats(1, t)
                drain_bank("pT", pT_lo, "pT_in")
                half_of_hT("hT1", "pre_mlp")
                round_weights(layer, "up0", "up1")
                for c in range(UT // 2 + 1):
                    if c < UT // 2:
                        round_weights(layer, f"up{c + 2}" if c + 2 < UT // 2 else f"down{c + 2 - UT // 2}")
                        act.wait_ge(*psum.filled(f"ff{c}"))
                        A_(gh[:, 2 * c:2 * c + 2, :], shaped(psum.bank(f"ff{c}"), 2, T), ACT.Relu).then_inc(*psum.freed(f"ff{c}"))
                        act.drain().then_inc(S["ff_relu"], 1)
                    if c:
                        act.wait_ge(S["ff_squared"], c)
                        A_(rounded(gh[:, 2 * c - 2:2 * c, :]), gl[:, 2 * c - 2:2 * c, :], ACT.Copy).then_inc(S["g_hi"], 1)
                round_weights(layer, *[f"down{i}" for i in range(2, UT // 2)])
                round_weights(layer, "proj", "ple0", "ple1")
                for t in range(NT):
                    y_stats(1, t, [f"y{2 * t + half}" for half in range(2)])
                for i in range(4):
                    drain_bank(f"proj{i}", proj[:, i, :], "proj")
                half_of_hT("xT", None)
                round_weights(layer, "ple2", "ple3")
                for t in range(NT):
                    for half in range(2):
                        name = f"ple{half}{t}"
                        act.wait_ge(*psum.filled(name))
                        A_(gates[:, 2 * t + half, :], psum.bank(name), ACT.Sigmoid).then_inc(*psum.freed(name))
                        act.drain().then_inc(S["gates"], 1)
                act.drain().then_inc(layer_done, 1)
                act.wait_ge(layer_open, layer + 1)

        @block.vector
        def _(dve):
            V = nc.vector

            def subtract_rounded(*names):
                for name in names:
                    dve.wait_ge(S["w_hi"], ring.split.index(name) + 1)
                    V.tensor_tensor(rounded(ring.view(name)), ring.view(name), as_float32(rounded(ring.view(name + "_hi"))), ALU.subtract).then_inc(S["w_split"], 1)

            def split(hi, lo, a):
                dve.drain()
                V.tensor_copy(rounded(hi), a)
                dve.drain()
                V.tensor_tensor(rounded(lo), a, as_float32(rounded(hi)), ALU.subtract)

            def scale_rows(k, t):
                dve.wait_ge(S["rstd"], NT * k + t + 1)
                V.tensor_scalar(diagonal[:, t, :], C("ident"), stat[:, 4 + t:5 + t], None, ALU.mult).then_inc(S["diagonal"], 1)

            def half_of_hT(name, gain):
                for t in range(NT):
                    dve.wait_ge(*psum.filled(f"{name}_{t}0"))
                    out, bank = hT[:, 0:4, t * P:(t + 1) * P], shaped(psum.bank(f"{name}_{t}0"), 4, P)
                    if gain:
                        last = V.tensor_tensor(out, bank, PAR(gain)[:, 0:4].unsqueeze(2).broadcast_to([P, 4, P]), ALU.mult)
                    else:
                        last = V.tensor_copy(out, bank)
                    last.then_inc(*psum.freed(f"{name}_{t}0"))
                    dve.drain().then_inc(S["hT"], 1)

            def residual(k, t, names, gain):
                dve.wait_ge(S["y_ss"], NT * k + t + 1)
                V.tensor_tensor(stat[:, 116 + t:117 + t], stat[:, 112 + t:113 + t], stat[:, 114 + t:115 + t],
                                ALU.add).then_inc(S["y_sum"], 1)
                dve.wait_ge(S["y_rstd"], NT * k + t + 1)
                lo = PAR2[gain][0]
                for half, name in enumerate(names):
                    V.scalar_tensor_tensor(yn[:, 2 * t + half, :], psum.bank(name), stat[:, 120 + t:121 + t],
                                           par[:, lo + 512 * half:lo + 512 * half + 512], ALU.mult, ALU.mult).then_inc(*psum.freed(name))
                add_to_x(t)

            def add_to_x(t):
                dve.drain()
                for half in range(2):
                    xs = x[:, t, 512 * half:512 * half + 512]
                    V.tensor_tensor(xs, xs, yn[:, 2 * t + half, :], ALU.add)
                dve.drain().then_inc(S["x_new"], 1)

            def turn(i):
                name, out, width, tiles = ROPED[i]
                dve.wait_ge(*psum.filled(name + "_rot"))
                if i >= 2:
                    dve.drain()
                sin = rope[:, width, 1:2, :].broadcast_to([P, tiles, T])
                V.tensor_tensor(turned[:, i % 2, 0:tiles, :], shaped(psum.bank(name + "_rot")[:, 0:tiles * T], tiles, T), sin,
                                ALU.mult).then_inc(*psum.freed(name + "_rot"))
                dve.wait_ge(S["cosined"], i + 1)
                dve.drain()
                V.tensor_tensor(out, out, turned[:, i % 2, 0:tiles, :], ALU.add).then_inc(S["roped"], 1)

            def masked_scores(i):
                name, maps, scale, _ = ATTENDED[i]
                if i >= 2:
                    dve.wait_ge(*psum.filled(ATTENDED[i - 2][0] + "_pt11"))
                for t in range(NT):
                    n = P * (t + 1)
                    L = scores_of(Ls[i % 2], t, maps)
                    for g in range(maps // 2):
                        bank = f"{name}_sc{t}{g}"
                        dve.wait_ge(*psum.filled(bank))
                        if name == "a":
                            mask = sel[t].unsqueeze(1).broadcast_to([P, 2, n])
                        elif name == "b":
                            mask = scores_of(Dm, t, 4)[:, 2 * g:2 * g + 2, :]
                        else:
                            all_ = shaped(C("window" if name == "d" else "causal"), NT, T)
                            mask = all_[:, t:t + 1, 0:n].broadcast_to([P, 2, n])
                        V.scalar_tensor_tensor(L[:, 2 * g:2 * g + 2, :], shaped(psum.bank(bank)[:, 0:2 * n], 2, n), scale, mask,
                                               ALU.mult, ALU.add).then_inc(*psum.freed(bank))
                    dve.drain()
                    neg, rec = stat_of(i, t, "neg", maps), stat_of(i, t, "rec", maps)
                    V.tensor_reduce(rec, L, AX.X, ALU.max)
                    dve.drain()
                    if name == "d":
                        V.tensor_tensor(rec, rec, PAR("sinks"), ALU.max)
                        dve.drain()
                    V.tensor_scalar(neg, rec, -1.0, None, ALU.mult)
                    if name == "d":
                        dve.drain()
                        V.tensor_tensor(stat_of(i, t, "sink", 4), PAR("sinks"), neg, ALU.add)
                    dve.drain().then_inc(S["score_max"], 1)
                    yield

            def probs(i):
                name, maps, _, _ = ATTENDED[i]
                for t in range(NT):
                    n = P * (t + 1)
                    L = scores_of(Ls[i % 2], t, maps)
                    den, rec = stat_of(i, t, "den", maps), stat_of(i, t, "rec", maps)
                    dve.wait_ge(S["exps"], 2 * i + t + 1)
                    if name == "d":
                        V.tensor_tensor(den, den, stat_of(i, t, "sink", 4), ALU.add)
                        dve.drain()
                    V.reciprocal(rec, den)
                    dve.drain()
                    V.tensor_tensor(L, L, rec.unsqueeze(2).broadcast_to([P, maps, n]), ALU.mult)
                    if name == "c":
                        dve.drain()
                        for g in range(2):
                            V.scalar_tensor_tensor(L[:, 4 * g:4 * g + 2, :], L[:, 4 * g + 2:4 * g + 4, :], lam[:, 68:69],
                                                   L[:, 4 * g:4 * g + 2, :], ALU.mult, ALU.add)
                    dve.drain().then_inc(S["probs"], 1)
                    yield

            def select(t):
                n = P * (t + 1)
                best = stat[:, 8:16]
                V.tensor_tensor(acc[t], acc[t], shaped(C("causal"), NT, T)[:, t, 0:n], ALU.add)
                for _ in range(TOPK // 8):
                    dve.drain()
                    V.max(best, acc[t])
                    dve.drain()
                    V.match_replace(acc[t], best, acc[t], TAKEN)
                dve.drain()
                V.tensor_scalar(sel[t], acc[t], -1e35, NEG, ALU.is_gt, ALU.mult)
                dve.drain()
                V.tensor_tensor(sel[t], sel[t], shaped(C("causal"), NT, T)[:, t, 0:n], ALU.add)
                dve.drain()

            def project():
                yield
                yield
                for name, *_ in IN_USES:
                    if name in ROPED_AT:
                        turn(ROPED_AT[name])
                    elif name == "a_iw":
                        dve.wait_ge(*psum.filled("a_iw"))
                        V.tensor_scalar(iw, shaped(psum.bank("a_iw")[:, 0:16], NT, 8), IDX_HEADS ** -0.5 * 64 ** -0.5, None,
                                        ALU.mult).then_inc(*psum.freed("a_iw"))
                    elif name == "b_f":
                        dve.wait_ge(*psum.filled("b_f"))
                        V.tensor_tensor(fl["x"], shaped(psum.bank("b_f")[:, 0:8], NT, 4),
                                        PAR("b_forget").unsqueeze(1).broadcast_to([P, NT, 4]), ALU.add).then_inc(*psum.freed("b_f"))
                        dve.drain()
                        V.scalar_tensor_tensor(fl["e"], fl["x"], -1.0, fl["x"], ALU.mult, ALU.max)
                        dve.drain().then_inc(S["gate_abs"], 1)
                    yield

            def forget():
                yield
                dve.wait_ge(S["gate_ln"], 1)
                V.tensor_scalar(fl["x"], fl["x"], 0.0, None, ALU.min)
                dve.drain()
                V.tensor_tensor(fl["n"], fl["e"], fl["x"], ALU.subtract).then_inc(S["nlf"], 1)
                yield
                dve.wait_ge(*psum.filled("f_col"))
                V.tensor_scalar(fl["cum"], shaped(psum.bank("f_col")[:, 0:8], NT, 4), -1.0, None, ALU.mult).then_inc(*psum.freed("f_col"))
                dve.drain()
                for g in range(2):
                    name = f"f_row{g}"
                    dve.wait_ge(*psum.filled(name))
                    for t in range(NT):
                        n = P * (t + 1)
                        for hp in range(2):
                            h = BY_PARITY[2 * g + hp]
                            last = V.scalar_tensor_tensor(scores_of(Dm, t, 4)[:, 2 * g + hp, :], psum.bank(name)[:, hp * T:hp * T + n],
                                                          fl["cum"][:, t, h:h + 1], shaped(C("causal"), NT, T)[:, t, 0:n], ALU.add, ALU.add)
                    last.then_inc(*psum.freed(name))
                dve.drain()
                yield

            def index():
                at = 0
                for t in range(NT):
                    n = P * (t + 1)
                    each = 512 // n
                    for g in range(2):
                        for j in range(4 // each):
                            dve.wait_ge(S["relu"], at + 1)
                            for i in range(each):
                                head = 2 * (each * j + i) + g
                                r, weight = dots[:, at % 2, i * n:(i + 1) * n], iw[:, t, head:head + 1]
                                dve.drain()
                                if g == j == i == 0:
                                    last = V.tensor_scalar(acc[t], r, weight, None, ALU.mult)
                                else:
                                    last = V.scalar_tensor_tensor(acc[t], r, weight, acc[t], ALU.mult, ALU.add)
                            last.then_inc(S["relu_used"], 1)
                            at += 1
                    yield

            def choose():
                for t in range(NT):
                    select(t)
                    yield

            def attend(i):
                yield from masked_scores(i)
                yield from probs(i)
                yield
                yield
                if ATTENDED[i][0] == "c":
                    yield
                    dve.wait_ge(S["o_rstd"], 1)
                    V.scalar_tensor_tensor(oT, oT, PAR("subln"), ors, ALU.mult, ALU.mult)
                    dve.drain()
                    V.tensor_scalar(mixT[:, 4:6, :], oT, PAR("lam_rest"), None, ALU.mult)
                    yield

            dve.wait_ge(once, 32)
            pos, turns = acc[1], sel[1]
            V.tensor_copy(pos, positions[:, :])
            for w in range(2):
                ang = rope[:, w, 1, :]
                dve.drain()
                V.tensor_scalar(ang, pos, C("inv_freq")[:, w:w + 1], None, ALU.mult)
                dve.drain()
                V.tensor_scalar(turns, ang, float(1 / (2 * np.pi)), 1.5 * 2.0 ** 23, ALU.mult, ALU.add)
                dve.drain()
                V.tensor_scalar(turns, turns, -1.5 * 2.0 ** 23, None, ALU.add)
                for part in TWO_PI:
                    dve.drain()
                    V.scalar_tensor_tensor(ang, turns, -part, ang, ALU.mult, ALU.add)
                dve.drain()
                V.tensor_scalar(ang, ang, -3.1415925, 3.1415925, ALU.max, ALU.min)
                dve.drain()
                V.scalar_tensor_tensor(rope[:, w, 0, :], ang, -1.0, ang, ALU.mult, ALU.max)
                dve.drain()
                V.tensor_scalar(rope[:, w, 0, :], rope[:, w, 0, :], -1.0, float(np.pi / 2), ALU.mult, ALU.add)
            dve.drain().then_inc(angles, 1)
            with dve.Fori(0, DEPTH) as layer:
                dve.wait_ge(tables_made, 1)
                dve.wait_ge(S["params"], 32)
                V.tensor_tensor(lam[:, 0:64], PAR("lam_q"), PAR("lam_k"), ALU.mult)
                dve.drain()
                V.tensor_reduce(lam[:, 64:66], shaped(lam[:, 0:64], 2, 32), AX.X, ALU.add).then_inc(S["lam_sum"], 1)
                for t in range(NT):
                    scale_rows(0, t)
                half_of_hT("hT0", "pre_mix")
                dve.wait_ge(S["lam_exp"], 1)
                V.tensor_tensor(lam[:, 68:69], lam[:, 67:68], lam[:, 66:67], ALU.subtract)
                dve.drain()
                V.tensor_tensor(lam[:, 68:69], lam[:, 68:69], PAR("lam_init"), ALU.subtract)
                emit(ORDER, {"in": project(), "index": index(), "select": choose(), "forget": forget(),
                             "b": attend(0), "c": attend(1), "d": attend(2), "a": attend(3), "out": iter(range(4))})
                dve.wait_ge(S["mixT"], 3)
                split(hT, mixT, mixT)
                dve.drain().then_inc(S["mix_split"], 1)
                for t in range(NT):
                    residual(0, t, [f"mix{half}{t}" for half in range(2)], "post_mix")
                    scale_rows(1, t)
                half_of_hT("hT1", "pre_mlp")
                dve.wait_ge(S["hT"], 8)
                split(mixT, hT, hT)
                dve.drain().then_inc(S["h_split"], 1)
                subtract_rounded("up0", "up1")
                dve.wait_ge(S["pT_in"], 1)
                split(pT, pT_lo, pT_lo)
                dve.drain().then_inc(S["p_split"], 1)
                for c in range(UT // 2 + 1):
                    if c < UT // 2:
                        subtract_rounded(f"up{c + 2}" if c + 2 < UT // 2 else f"down{c + 2 - UT // 2}")
                        dve.wait_ge(S["ff_relu"], c + 1)
                        V.tensor_tensor(gl[:, 2 * c:2 * c + 2, :], gh[:, 2 * c:2 * c + 2, :], gh[:, 2 * c:2 * c + 2, :],
                                        ALU.mult).then_inc(S["ff_squared"], 1)
                    if c:
                        dve.wait_ge(S["g_hi"], c)
                        V.tensor_tensor(rounded(gl[:, 2 * c - 2:2 * c, :]), gl[:, 2 * c - 2:2 * c, :],
                                        as_float32(rounded(gh[:, 2 * c - 2:2 * c, :])), ALU.subtract).then_inc(S["gT"], 1)
                subtract_rounded(*[f"down{i}" for i in range(2, UT // 2)])
                subtract_rounded("proj", "ple0", "ple1")
                for t in range(NT):
                    residual(1, t, [f"y{2 * t + half}" for half in range(2)], "post_mlp")
                half_of_hT("xT", None)
                dve.wait_ge(S["hT"], 12)
                split(mixT, hT, hT)
                dve.drain().then_inc(S["h_split"], 1)
                subtract_rounded("ple2", "ple3")
                for t in range(NT):
                    for i in (2 * t, 2 * t + 1):
                        dve.wait_ge(S["gates"], i + 1)
                        V.tensor_tensor(yn[:, i, :], gates[:, i, :], proj[:, i, :], ALU.mult)
                    add_to_x(t)
                dve.drain().then_inc(layer_done, 1)
                dve.wait_ge(layer_open, layer + 1)

        @block.gpsimd
        def _(pool):
            def subtract_rounded(*names):
                for name in names:
                    pool.wait_ge(S["w_hi"], ring.split.index(name) + 1)
                    nc.gpsimd.tensor_tensor(rounded(ring.view(name)), ring.view(name), as_float32(rounded(ring.view(name + "_hi"))),
                                            ALU.subtract).then_inc(S["w_split"], 1)

            pool.wait_ge(tables_made, 1)
            with pool.Fori(0, DEPTH) as layer:
                for i, (name, out, width, tiles) in enumerate(ROPED):
                    pool.wait_ge(S["raw"], i + 1)
                    cos = rope[:, width, 0:1, :].broadcast_to([P, tiles, T])
                    nc.gpsimd.tensor_tensor(out, raw[:, i % 2, 0:tiles, :], cos, ALU.mult).then_inc(S["cosined"], 1)
                subtract_rounded(*[f"out{i}" for i in range(4)])
                pool.wait_ge(layer_done, 3 * layer + 3)
                pool.sem_inc(barrier_taken, 1)
                for r in sem_ranges([s.num for s in S.values()] + [s.num for s in psum.full + psum.free]):
                    pool.sem_clear(r)
                pool.sem_inc(layer_open, 1)

        psum.check()


def two_blocks(nc, A, out):
    with ExitStack() as ctx:
        x = shaped(ctx.enter_context(nc.sbuf_tensor("x_state", [P, NT * DM], F32))[:, :], NT, DM)
        banks = ctx.enter_context(nc.psum_tensor("banks", [P, 8, 512], F32))
        x_in = ctx.enter_context(nc.semaphore("x_in"))
        x_out = ctx.enter_context(nc.semaphore("x_out"))
        with nc.Block() as block:
            @block.sync
            def _(sp):
                for t in range(NT):
                    sp.dma_start(x[:, t, :], A["x"][0, t * P:(t + 1) * P, :]).then_inc(x_in, 16)
                sp.wait_ge(x_in, 16 * NT)
        block1(nc, ctx, banks, x, x_in, A)
        block2(nc, ctx, banks, x, A)
        with nc.Block() as block:
            @block.sync
            def _(sp):
                for t in range(NT):
                    sp.dma_start(out[0, t * P:(t + 1) * P, :], x[:, t, :]).then_inc(x_out, 16)
                sp.wait_ge(x_out, 16 * NT)


_LARGE = ["x", "w_in", "w_out", "mla_w_uq", "mla_w_ukv", "gla_w_gk2", "ffn_w_gate", "ffn_w_up", "ffn_w_down",
          "p_2", "positions_2", "w_in_2", "w_out_2", "w_mlp_up_2", "w_mlp_down_2", "w_ple_proj_2", "w_ple_gate_2"]


def kernel(**inputs):
    import concourse.bacc as bacc
    from concourse.bass_utils import run_bass_kernel_spmd

    nc = bacc.Bacc("TRN2", target_bir_lowering=False, num_devices=1)
    host = {name: np.ascontiguousarray(inputs[name]) for name in _LARGE}
    host["const1"], host["const2"] = shape_constants1(), shape_constants2()
    host["par1"], host["par2"] = params1(inputs), params2(inputs)
    arrays, A = {}, {}
    for name, a in host.items():
        arrays[f"in_{name}"] = a
        A[name] = nc.dram_tensor(f"in_{name}", a.shape, mybir.dt.from_np(a.dtype), kind="ExternalInput").ap()
    out = nc.dram_tensor("out_x", (1, T, DM), F32, kind="ExternalOutput").ap()
    two_blocks(nc, A, out)
    result = run_bass_kernel_spmd(nc, [arrays], core_ids=[0])
    return result.results[0]["out_x"]
```
